# Optimizing a Trainium2 kernel written in Bass

```python
import math
import jax, jax.numpy as jnp
from jax import lax
import numpy as np

D_MODEL = 1024
BATCH = 1
SEQ = 512
DEPTH = 2

HEAD_DIM = 64
ROPE_DIM = HEAD_DIM // 4
ROPE_THETA = 500000.0
Q_BLOCK = 128
LN_EPS = 1e-5
DIFF_HEADS = 4
NSA_HEADS = 8
NSA_KV_HEADS = 2
NSA_CMP_LEN = 32
NSA_CMP_STRIDE = 16
NSA_CMP_HIDDEN = 256
NSA_SEL_LEN = 64
NSA_TOPK = 8
NSA_WINDOW = 512
NSA_Q_BLOCK = 64
NSA_N_BRANCH = 3
NSA_BIG = 1e4
NEG = -1e30
FOX_HEADS = D_MODEL // HEAD_DIM
FOX_WIDTH = FOX_HEADS * HEAD_DIM
D_FF = 4 * D_MODEL
ALPHA = (2 * DEPTH) ** 0.25
BETA = (8 * DEPTH) ** -0.25
N_EVEN = (DEPTH + 1) // 2
N_ODD = DEPTH // 2

DIFF_QK = DIFF_HEADS * 2 * HEAD_DIM
DIFF_V = DIFF_HEADS * 2 * HEAD_DIM
NSA_Q = NSA_HEADS * HEAD_DIM
NSA_KV = NSA_KV_HEADS * HEAD_DIM
EVEN_SPLITS = (DIFF_QK, DIFF_QK, DIFF_V, NSA_Q, NSA_KV, NSA_KV, NSA_KV, NSA_KV, NSA_KV, NSA_KV, NSA_HEADS * NSA_N_BRANCH)
EVEN_COLS = sum(EVEN_SPLITS)
EVEN_MIX = DIFF_V + NSA_Q
ODD_SPLITS = (FOX_WIDTH, FOX_WIDTH, FOX_WIDTH, FOX_HEADS)
ODD_COLS = sum(ODD_SPLITS)


def _split(h, sizes):
    offsets = [int(o) for o in np.cumsum(sizes)[:-1]]
    return jnp.split(h, offsets, axis=-1)

def layer_norm(x, g, b):
    xf = x.astype(jnp.float32)
    mu = jnp.mean(xf, axis=-1, keepdims=True)
    var = jnp.mean(jnp.square(xf - mu), axis=-1, keepdims=True)
    return ((xf - mu) * lax.rsqrt(var + LN_EPS) * g.astype(jnp.float32) + b.astype(jnp.float32)).astype(x.dtype)

def rms_norm(x, g):
    xf = x.astype(jnp.float32)
    return xf * lax.rsqrt(jnp.mean(jnp.square(xf), axis=-1, keepdims=True) + LN_EPS) * g.astype(jnp.float32)

def partial_rope(x, pos):
    half = ROPE_DIM // 2
    inv = ROPE_THETA ** (-jnp.arange(half, dtype=jnp.float32) / half)
    ang = pos.astype(jnp.float32)[:, None] * inv[None, :]
    shape = (pos.shape[0],) + (1,) * (x.ndim - 3) + (half,)
    cos = jnp.cos(ang).reshape(shape)
    sin = jnp.sin(ang).reshape(shape)
    xf = x.astype(jnp.float32)
    x1 = xf[..., :half]
    x2 = xf[..., half:ROPE_DIM]
    return jnp.concatenate([x1 * cos - x2 * sin, x2 * cos + x1 * sin, xf[..., ROPE_DIM:]], axis=-1)

def _sweep(fn, seq_len, block):
    out = lax.map(fn, jnp.arange(seq_len // block))
    out = jnp.moveaxis(out, 0, 1)
    return out.reshape((out.shape[0], seq_len) + out.shape[3:])

def diff_attention(q, k, v, lam_params, subln_g, layer_idx):
    B, S = q.shape[:2]
    pos = jnp.arange(S)
    scale = HEAD_DIM ** -0.5
    qr = partial_rope(q, pos) * scale
    kr = partial_rope(k, pos)
    vf = v.astype(jnp.float32)
    lam_init = 0.8 - 0.6 * math.exp(-0.3 * layer_idx)
    lp = lam_params.astype(jnp.float32)
    lam = jnp.exp(jnp.sum(lp[0] * lp[1])) - jnp.exp(jnp.sum(lp[2] * lp[3])) + lam_init

    def blk(i):
        q0 = i * Q_BLOCK
        qb = lax.dynamic_slice_in_dim(qr, q0, Q_BLOCK, axis=1)
        tq = q0 + jnp.arange(Q_BLOCK)
        mask = pos[None, :] <= tq[:, None]
        s = jnp.einsum('bqhcd,bshcd->bhcqs', qb, kr)
        p = jax.nn.softmax(jnp.where(mask, s, -jnp.inf), axis=-1)
        pd = p[:, :, 0] - lam * p[:, :, 1]
        return jnp.einsum('bhqs,bshe->bqhe', pd, vf)

    o = _sweep(blk, S, Q_BLOCK)
    o = rms_norm(o, subln_g) * (1.0 - lam_init)
    return o.reshape(B, S, -1).astype(v.dtype)

def nsa_attention(q, k_cmp, v_cmp, k_slc, v_slc, k_win, v_win, gate_logits, pe, w1, b1, w2):
    B, S, H, d = q.shape
    G = NSA_KV_HEADS
    HPG = H // G
    W = NSA_WINDOW
    pos = jnp.arange(S)
    scale = HEAD_DIM ** -0.5
    qr = (partial_rope(q, pos) * scale).reshape(B, S, G, HPG, d)

    n_cmp = (S - NSA_CMP_LEN) // NSA_CMP_STRIDE + 1
    cmp_start = jnp.arange(n_cmp) * NSA_CMP_STRIDE
    cmp_end = cmp_start + NSA_CMP_LEN - 1
    cmp_idx = cmp_start[:, None] + jnp.arange(NSA_CMP_LEN)[None, :]

    def compress(t, j):
        blocks = t[:, cmp_idx] + pe[j][None, None, :, None, :]
        blocks = jnp.moveaxis(blocks, 3, 2).reshape(B, n_cmp, G, NSA_CMP_LEN * d)
        h = jax.nn.gelu(blocks @ w1[j] + b1[j])
        return h @ w2[j]

    kc = partial_rope(compress(k_cmp, 0), cmp_end)
    vc = compress(v_cmp, 1).astype(jnp.float32)

    n_sel = S // NSA_SEL_LEN
    topk = min(NSA_TOPK, n_sel)
    ks = partial_rope(k_slc, pos)
    ks_blk = ks.reshape(B, n_sel, NSA_SEL_LEN, G, d).transpose(0, 3, 1, 2, 4)
    vs_blk = v_slc.astype(jnp.float32).reshape(B, n_sel, NSA_SEL_LEN, G, d).transpose(0, 3, 1, 2, 4)
    sel_start = jnp.arange(n_sel) * NSA_SEL_LEN
    overlap = ((cmp_start[:, None] <= sel_start[None, :] + NSA_SEL_LEN - 1)
               & (cmp_end[:, None] >= sel_start[None, :])).astype(jnp.float32)
    bi = jnp.arange(B)[:, None, None, None]
    gi = jnp.arange(G)[None, :, None, None]
    jb = jnp.arange(n_sel)

    kw_pad = jnp.pad(partial_rope(k_win, pos), ((0, 0), (W, 0), (0, 0), (0, 0)))
    vw_pad = jnp.pad(v_win.astype(jnp.float32), ((0, 0), (W, 0), (0, 0), (0, 0)))

    gate = jax.nn.sigmoid(gate_logits.astype(jnp.float32)).reshape(B, S, G, HPG, NSA_N_BRANCH)

    def blk(i):
        q0 = i * NSA_Q_BLOCK
        qb = lax.dynamic_slice_in_dim(qr, q0, NSA_Q_BLOCK, axis=1)
        tq = q0 + jnp.arange(NSA_Q_BLOCK)
        valid_c = cmp_end[None, :] <= tq[:, None]
        sc = jnp.einsum('bqghd,bngd->bghqn', qb, kc)
        pc = jax.nn.softmax(jnp.where(valid_c, sc, NEG), axis=-1) * valid_c
        o_c = jnp.einsum('bghqn,bngd->bqghd', pc, vc)
        imp = jnp.einsum('bghqn,nj->bgqj', pc, overlap)
        cur = tq // NSA_SEL_LEN
        forced = (jb[None, :] == 0) | (jb[None, :] == cur[:, None]) | (jb[None, :] == cur[:, None] - 1)
        future = jb[None, :] > cur[:, None]
        imp = jnp.where(forced, NSA_BIG, jnp.where(future, -NSA_BIG, imp))
        _, idx = lax.top_k(imp, topk)
        kg = ks_blk[bi, gi, idx]
        vg = vs_blk[bi, gi, idx]
        tok = idx[..., None] * NSA_SEL_LEN + jnp.arange(NSA_SEL_LEN)
        valid_s = (tok <= tq[None, None, :, None, None])[:, :, None]
        ss = jnp.where(valid_s, jnp.einsum('bqghd,bgqkld->bghqkl', qb, kg), -jnp.inf)
        ps = jax.nn.softmax(ss.reshape(ss.shape[:4] + (-1,)), axis=-1).reshape(ss.shape)
        o_s = jnp.einsum('bghqkl,bgqkld->bqghd', ps, vg)
        kwb = lax.dynamic_slice_in_dim(kw_pad, q0, W + NSA_Q_BLOCK, axis=1)
        vwb = lax.dynamic_slice_in_dim(vw_pad, q0, W + NSA_Q_BLOCK, axis=1)
        sk = q0 - W + jnp.arange(W + NSA_Q_BLOCK)
        valid_w = (sk[None, :] <= tq[:, None]) & (sk[None, :] > tq[:, None] - W) & (sk[None, :] >= 0)
        sw = jnp.einsum('bqghd,bsgd->bghqs', qb, kwb)
        pw = jax.nn.softmax(jnp.where(valid_w, sw, -jnp.inf), axis=-1)
        o_w = jnp.einsum('bghqs,bsgd->bqghd', pw, vwb)
        gb = lax.dynamic_slice_in_dim(gate, q0, NSA_Q_BLOCK, axis=1)
        return gb[..., 0:1] * o_c + gb[..., 1:2] * o_s + gb[..., 2:3] * o_w

    o = _sweep(blk, S, NSA_Q_BLOCK)
    return o.reshape(B, S, H * d).astype(q.dtype)

def forgetting_attention(q, k, v, f_logit, f_bias):
    B, S, H, d = q.shape
    pos = jnp.arange(S)
    qf = q.astype(jnp.float32) * (HEAD_DIM ** -0.5)
    kf = k.astype(jnp.float32)
    vf = v.astype(jnp.float32)
    log_f = jax.nn.log_sigmoid(f_logit.astype(jnp.float32) + f_bias.astype(jnp.float32))
    c = jnp.cumsum(log_f, axis=1).transpose(0, 2, 1)

    def blk(i):
        q0 = i * Q_BLOCK
        qb = lax.dynamic_slice_in_dim(qf, q0, Q_BLOCK, axis=1)
        cq = lax.dynamic_slice_in_dim(c, q0, Q_BLOCK, axis=2)
        tq = q0 + jnp.arange(Q_BLOCK)
        mask = pos[None, :] <= tq[:, None]
        s = jnp.einsum('bqhd,bshd->bhqs', qb, kf) + cq[..., None] - c[:, :, None, :]
        p = jax.nn.softmax(jnp.where(mask, s, -jnp.inf), axis=-1)
        return jnp.einsum('bhqs,bshd->bqhd', p, vf)

    o = _sweep(blk, S, Q_BLOCK)
    return o.reshape(B, S, H * d).astype(q.dtype)

def sqrelu_mlp(x, w_up, w_down):
    return jnp.square(jax.nn.relu(x @ w_up)) @ w_down

def first_inputs(seed: int = 0) -> dict:
    key = jax.random.key(seed)
    ks = jax.random.split(key, 16)

    def nrm(k, shape, scale):
        return jax.random.normal(k, shape, jnp.float32) * scale

    return {
        'x': nrm(ks[0], (BATCH, SEQ, D_MODEL), 1.0),
        'ln_gain': 1.0 + nrm(ks[1], (DEPTH, 2, D_MODEL), 0.02),
        'ln_bias': nrm(ks[2], (DEPTH, 2, D_MODEL), 0.02),
        'mlp_w_up': nrm(ks[3], (DEPTH, D_MODEL, D_FF), D_MODEL ** -0.5),
        'mlp_w_down': nrm(ks[4], (DEPTH, D_FF, D_MODEL), BETA * D_FF ** -0.5),
        'w_in_even': nrm(ks[5], (N_EVEN, D_MODEL, EVEN_COLS), D_MODEL ** -0.5),
        'w_out_even': nrm(ks[6], (N_EVEN, EVEN_MIX, D_MODEL), BETA * EVEN_MIX ** -0.5),
        'diff_lambda': nrm(ks[7], (N_EVEN, 4, HEAD_DIM), 0.1),
        'diff_subln': 1.0 + nrm(ks[8], (N_EVEN, 2 * HEAD_DIM), 0.02),
        'nsa_pe': nrm(ks[9], (N_EVEN, 2, NSA_CMP_LEN, HEAD_DIM), 0.1),
        'nsa_cmp_w1': nrm(ks[10], (N_EVEN, 2, NSA_CMP_LEN * HEAD_DIM, NSA_CMP_HIDDEN), (NSA_CMP_LEN * HEAD_DIM) ** -0.5),
        'nsa_cmp_b1': nrm(ks[11], (N_EVEN, 2, NSA_CMP_HIDDEN), 0.02),
        'nsa_cmp_w2': nrm(ks[12], (N_EVEN, 2, NSA_CMP_HIDDEN, HEAD_DIM), NSA_CMP_HIDDEN ** -0.5),
        'w_in_odd': nrm(ks[13], (N_ODD, D_MODEL, ODD_COLS), D_MODEL ** -0.5),
        'fox_f_bias': jnp.linspace(1.0, 6.0, FOX_HEADS, dtype=jnp.float32)[None, :] + nrm(ks[14], (N_ODD, FOX_HEADS), 0.1),
        'w_out_odd': nrm(ks[15], (N_ODD, FOX_WIDTH, D_MODEL), BETA * FOX_WIDTH ** -0.5),
    }

def first_block(x, ln_gain, ln_bias, mlp_w_up, mlp_w_down, w_in_even, w_out_even, diff_lambda, diff_subln,
              nsa_pe, nsa_cmp_w1, nsa_cmp_b1, nsa_cmp_w2, w_in_odd, fox_f_bias, w_out_odd):
    B, S, _ = x.shape
    for layer in range(DEPTH):
        li = layer // 2
        if layer % 2 == 0:
            h = x @ w_in_even[li]
            qa, ka, va, qn, kc, vc, ksl, vsl, kw, vw, g = _split(h, EVEN_SPLITS)
            o_a = diff_attention(qa.reshape(B, S, DIFF_HEADS, 2, HEAD_DIM),
                                 ka.reshape(B, S, DIFF_HEADS, 2, HEAD_DIM),
                                 va.reshape(B, S, DIFF_HEADS, 2 * HEAD_DIM),
                                 diff_lambda[li], diff_subln[li], layer)
            kv = lambda t: t.reshape(B, S, NSA_KV_HEADS, HEAD_DIM)
            o_b = nsa_attention(qn.reshape(B, S, NSA_HEADS, HEAD_DIM), kv(kc), kv(vc), kv(ksl), kv(vsl),
                                kv(kw), kv(vw), g, nsa_pe[li], nsa_cmp_w1[li], nsa_cmp_b1[li], nsa_cmp_w2[li])
            mix = jnp.concatenate([o_a, o_b], axis=-1) @ w_out_even[li]
        else:
            h = x @ w_in_odd[li]
            qf, kf, vf, fl = _split(h, ODD_SPLITS)
            hd = lambda t: t.reshape(B, S, FOX_HEADS, HEAD_DIM)
            mix = forgetting_attention(hd(qf), hd(kf), hd(vf), fl, fox_f_bias[li]) @ w_out_odd[li]
        x = layer_norm(ALPHA * x + mix, ln_gain[layer, 0], ln_bias[layer, 0])
        x = layer_norm(ALPHA * x + sqrelu_mlp(x, mlp_w_up[layer], mlp_w_down[layer]), ln_gain[layer, 1], ln_bias[layer, 1])
    return x


DEPTH_2 = 1

GRID_W = 64
CTX_LEN = 256
D_MIX = D_MODEL
SSD_WIDTH = D_MIX // 2
SSD_HEADDIM = 64
SSD_HEADS = SSD_WIDTH // SSD_HEADDIM
SSD_GROUPS = 2
HEADS_PER_GROUP = SSD_HEADS // SSD_GROUPS
SSD_STATE = 128
SSD_CONV = 3
SSD_CHUNK = 128
XBC_WIDTH = SSD_WIDTH + 2 * SSD_GROUPS * SSD_STATE
FNET_WIDTH = D_MIX // 4
FNET_GROUPS = 4
FNET_GDIM = FNET_WIDTH // FNET_GROUPS
POOL_WINDOWS = (2, 4, 8, 16)
POOL_WIDTH = D_MIX // 4
POOL_GDIM = POOL_WIDTH // len(POOL_WINDOWS)
D_FF_2 = 256 * ((8 * D_MODEL // 3 + 255) // 256)
FFN_CONV = 3
OFF_Z = 0
OFF_XBC = OFF_Z + SSD_WIDTH
OFF_DT = OFF_XBC + XBC_WIDTH
OFF_FNET = OFF_DT + 2 * SSD_HEADS
OFF_POOL = OFF_FNET + FNET_WIDTH
N_IN = OFF_POOL + POOL_WIDTH
ALPHA_2 = (2.0 * DEPTH_2) ** 0.25
BETA_2 = (8.0 * DEPTH_2) ** -0.25
EPS = 1e-6


def layer_norm_2(x):
    xf = x.astype(jnp.float32)
    mu = jnp.mean(xf, -1, keepdims=True)
    var = jnp.mean(jnp.square(xf - mu), -1, keepdims=True)
    return ((xf - mu) * lax.rsqrt(var + EPS)).astype(x.dtype)

def ada(cvec, w, b):
    m = jax.nn.silu(cvec) @ w + b
    return [mi[:, None, :] for mi in jnp.split(m, 6, axis=-1)]

def modulate(x, shift, scale):
    return layer_norm_2(x) * (1 + scale) + shift

def post_norm(x, y, gate, g, b):
    return layer_norm_2(ALPHA_2 * x + gate * y) * g + b

def dwconv1d(x, w, b):
    k = w.shape[0]
    left = (k - 1) // 2
    y = lax.conv_general_dilated(x, w[:, None, :], window_strides=(1,), padding=[(left, k - 1 - left)],
                                 dimension_numbers=("NWC", "WIO", "NWC"), feature_group_count=x.shape[-1])
    return y + b

def dwconv2d_grid(x, w, b):
    bsz, L, C = x.shape
    rows = L // GRID_W
    xg = x.reshape(bsz, rows, GRID_W, C)
    y = lax.conv_general_dilated(xg, w[:, :, None, :], window_strides=(1, 1), padding=[(1, 1), (1, 1)],
                                 dimension_numbers=("NHWC", "HWIO", "NHWC"), feature_group_count=C)
    return y.reshape(bsz, L, C) + b

def segsum(a):
    T = a.shape[-1]
    cs = jnp.cumsum(a, axis=-1)
    seg = cs[..., :, None] - cs[..., None, :]
    mask = jnp.tril(jnp.ones((T, T), dtype=bool))
    return jnp.where(mask, seg, -jnp.inf)

def ssd_chunked(X, dA, B, C, init_state):
    b, L, h, p = X.shape
    n = B.shape[-1]
    nc = L // SSD_CHUNK
    X = X.astype(jnp.float32).reshape(b, nc, SSD_CHUNK, h, p)
    B = B.astype(jnp.float32).reshape(b, nc, SSD_CHUNK, h, n)
    C = C.astype(jnp.float32).reshape(b, nc, SSD_CHUNK, h, n)
    A = dA.astype(jnp.float32).reshape(b, nc, SSD_CHUNK, h).transpose(0, 3, 1, 2)
    A_cs = jnp.cumsum(A, axis=-1)
    Lmat = jnp.exp(segsum(A))
    y_diag = jnp.einsum("bclhn,bcshn,bhcls,bcshp->bclhp", C, B, Lmat, X)
    decay_states = jnp.exp(A_cs[..., -1:] - A_cs)
    states = jnp.einsum("bclhn,bhcl,bclhp->bchpn", B, decay_states, X)
    states = jnp.concatenate([init_state[:, None].astype(jnp.float32), states], axis=1)
    chunk_decay = jnp.exp(segsum(jnp.pad(A_cs[..., -1], ((0, 0), (0, 0), (1, 0)))))
    new_states = jnp.einsum("bhzc,bchpn->bzhpn", chunk_decay, states)
    states, final_state = new_states[:, :-1], new_states[:, -1]
    y_off = jnp.einsum("bclhn,bchpn,bhcl->bclhp", C, states, jnp.exp(A_cs))
    return (y_diag + y_off).reshape(b, L, h, p), final_state

def ssd_final_state(X, dA, B):
    cs = jnp.cumsum(dA, axis=1)
    return jnp.einsum("blh,blhn,blhp->bhpn", jnp.exp(cs[:, -1:] - cs), B.astype(jnp.float32), X)

def rev(a):
    return jnp.flip(a, axis=1)

def ssd_prep(u, conv_w, conv_b, dt_bias, a_log):
    bsz, L, _ = u.shape
    xbc = jax.nn.silu(dwconv1d(u[..., OFF_XBC:OFF_DT], conv_w, conv_b))
    xs = xbc[..., :SSD_WIDTH].reshape(bsz, L, SSD_HEADS, SSD_HEADDIM)
    gn = SSD_GROUPS * SSD_STATE
    bm = xbc[..., SSD_WIDTH:SSD_WIDTH + gn].reshape(bsz, L, SSD_GROUPS, SSD_STATE)
    cm = xbc[..., SSD_WIDTH + gn:].reshape(bsz, L, SSD_GROUPS, SSD_STATE)
    bm = jnp.repeat(bm, HEADS_PER_GROUP, axis=2)
    cm = jnp.repeat(cm, HEADS_PER_GROUP, axis=2)
    dt_raw = u[..., OFF_DT:OFF_FNET].reshape(bsz, L, 2, SSD_HEADS)
    dt = jax.nn.softplus((dt_raw + dt_bias).astype(jnp.float32))
    dA = dt * (-jnp.exp(a_log.astype(jnp.float32)))
    return xs, bm, cm, dt, dA

def ssd_bidir(xs, bm, cm, dt, dA, init_f, init_b):
    x32 = xs.astype(jnp.float32)
    y_f, s_f = ssd_chunked(x32 * dt[:, :, 0, :, None], dA[:, :, 0], bm, cm, init_f)
    y_b, s_b = ssd_chunked(rev(x32 * dt[:, :, 1, :, None]), rev(dA[:, :, 1]), rev(bm), rev(cm), init_b)
    return y_f + rev(y_b), s_f, s_b

def ssd_gate_norm(y, xs, z, d_skip, norm_w):
    bsz, L = z.shape[:2]
    y = (y + xs.astype(jnp.float32) * d_skip.astype(jnp.float32)[:, None]).reshape(bsz, L, SSD_WIDTH)
    y = (y * jax.nn.silu(z.astype(jnp.float32))).reshape(bsz, L, SSD_GROUPS, SSD_WIDTH // SSD_GROUPS)
    y = (y * lax.rsqrt(jnp.mean(y * y, -1, keepdims=True) + EPS)).reshape(bsz, L, SSD_WIDTH)
    return (y * norm_w).astype(z.dtype)

def fourier_mix(f, w):
    bsz, L, _ = f.shape
    fg = f.astype(jnp.float32).reshape(bsz, L, FNET_GROUPS, FNET_GDIM)
    spec = jnp.fft.fft2(fg, axes=(1, 3), norm="ortho").real
    y = jnp.einsum("blgc,gcd->blgd", spec.astype(f.dtype), w)
    return y.reshape(bsz, L, FNET_WIDTH)

def pool_mix(p, w, scale):
    bsz, L, _ = p.shape
    pf = p.astype(jnp.float32)
    cs = jnp.pad(jnp.cumsum(pf, axis=1), ((0, 0), (1, 0), (0, 0)))
    pos = jnp.arange(L)
    outs = []
    for gi, win in enumerate(POOL_WINDOWS):
        left = win // 2
        right = win - 1 - left
        hi = jnp.minimum(pos + right + 1, L)
        lo = jnp.maximum(pos - left, 0)
        sl = slice(gi * POOL_GDIM, (gi + 1) * POOL_GDIM)
        csg = cs[..., sl]
        mean = (csg[:, hi] - csg[:, lo]) / (hi - lo).astype(jnp.float32)[None, :, None]
        outs.append(mean - pf[..., sl])
    pooled = jnp.stack(outs, axis=2).astype(p.dtype)
    y = jnp.einsum("blgc,gcd->blgd", pooled, w).reshape(bsz, L, POOL_WIDTH)
    return y * scale

def token_mixer(u, init_f, init_b, conv_w, conv_b, dt_bias, a_log, d_skip, norm_w, fnet_w, pool_w, pool_scale, w_out):
    xs, bm, cm, dt, dA = ssd_prep(u, conv_w, conv_b, dt_bias, a_log)
    y, s_f, s_b = ssd_bidir(xs, bm, cm, dt, dA, init_f, init_b)
    y_ssd = ssd_gate_norm(y, xs, u[..., OFF_Z:OFF_XBC], d_skip, norm_w)
    y_fnet = fourier_mix(u[..., OFF_FNET:OFF_POOL], fnet_w)
    y_pool = pool_mix(u[..., OFF_POOL:N_IN], pool_w, pool_scale)
    return jnp.concatenate([y_ssd, y_fnet, y_pool], axis=-1) @ w_out, s_f, s_b

def ctx_scan_states(u, conv_w, conv_b, dt_bias, a_log):
    xs, bm, _, dt, dA = ssd_prep(u, conv_w, conv_b, dt_bias, a_log)
    x32 = xs.astype(jnp.float32)
    s_f = ssd_final_state(x32 * dt[:, :, 0, :, None], dA[:, :, 0], bm)
    s_b = ssd_final_state(rev(x32 * dt[:, :, 1, :, None]), rev(dA[:, :, 1]), rev(bm))
    return s_f, s_b

def conv_ffn(h, w_up, conv_w, conv_b, w_down, grid):
    a = h @ w_up
    a = dwconv2d_grid(a, conv_w, conv_b) if grid else dwconv1d(a, conv_w[1], conv_b)
    val, gate = jnp.split(a, 2, axis=-1)
    return (jax.nn.gelu(gate) * val) @ w_down

def second_inputs(seed: int = 0) -> dict:
    key = jax.random.key(seed)
    ks = jax.random.split(key, 25)
    f32 = jnp.float32

    def nrm(k, shape, s):
        return s * jax.random.normal(k, shape, f32)

    dt0 = jnp.exp(jax.random.uniform(ks[9], (DEPTH_2, 2, SSD_HEADS), f32, np.log(1e-3), np.log(1e-1)))
    return {
        "x": nrm(ks[0], (BATCH, SEQ, D_MODEL), 1.0),
        "c": nrm(ks[1], (BATCH, D_MODEL), 1.0),
        "ctx": nrm(ks[2], (BATCH, CTX_LEN, D_MODEL), 1.0),
        "c_ctx": nrm(ks[3], (D_MODEL,), 1.0),
        "w_ada": nrm(ks[4], (DEPTH_2, D_MODEL, 6 * D_MODEL), 0.5 * D_MODEL ** -0.5),
        "b_ada": nrm(ks[5], (DEPTH_2, 6 * D_MODEL), 0.02),
        "w_in": nrm(ks[6], (DEPTH_2, D_MODEL, N_IN), D_MODEL ** -0.5),
        "ssd_conv_w": nrm(ks[7], (DEPTH_2, SSD_CONV, XBC_WIDTH), SSD_CONV ** -0.5),
        "ssd_conv_b": nrm(ks[8], (DEPTH_2, XBC_WIDTH), 0.02),
        "ssd_dt_bias": dt0 + jnp.log(-jnp.expm1(-dt0)),
        "ssd_a_log": jnp.log(jax.random.uniform(ks[10], (DEPTH_2, 2, SSD_HEADS), f32, 1.0, 16.0)),
        "ssd_d": 1.0 + nrm(ks[11], (DEPTH_2, SSD_HEADS), 0.1),
        "ssd_norm_w": 1.0 + nrm(ks[12], (DEPTH_2, SSD_WIDTH), 0.1),
        "fnet_w": nrm(ks[13], (DEPTH_2, FNET_GROUPS, FNET_GDIM, FNET_GDIM), FNET_GDIM ** -0.5),
        "pool_w": nrm(ks[14], (DEPTH_2, len(POOL_WINDOWS), POOL_GDIM, POOL_GDIM), POOL_GDIM ** -0.5),
        "pool_scale": 1.0 + nrm(ks[15], (DEPTH_2, POOL_WIDTH), 0.1),
        "w_out": nrm(ks[16], (DEPTH_2, D_MIX, D_MODEL), BETA_2 * D_MIX ** -0.5),
        "ln1_g": 1.0 + nrm(ks[17], (DEPTH_2, D_MODEL), 0.1),
        "ln1_b": nrm(ks[18], (DEPTH_2, D_MODEL), 0.02),
        "ffn_w_up": nrm(ks[19], (DEPTH_2, D_MODEL, 2 * D_FF_2), D_MODEL ** -0.5),
        "ffn_conv_w": nrm(ks[20], (DEPTH_2, FFN_CONV, FFN_CONV, 2 * D_FF_2), 1.0 / FFN_CONV),
        "ffn_conv_b": nrm(ks[21], (DEPTH_2, 2 * D_FF_2), 0.02),
        "ffn_w_down": nrm(ks[22], (DEPTH_2, D_FF_2, D_MODEL), BETA_2 * D_FF_2 ** -0.5),
        "ln2_g": 1.0 + nrm(ks[23], (DEPTH_2, D_MODEL), 0.1),
        "ln2_b": nrm(ks[24], (DEPTH_2, D_MODEL), 0.02),
    }

def second_block(x, c, ctx, c_ctx, w_ada, b_ada, w_in, ssd_conv_w, ssd_conv_b, ssd_dt_bias, ssd_a_log, ssd_d,
              ssd_norm_w, fnet_w, pool_w, pool_scale, w_out, ln1_g, ln1_b, ffn_w_up, ffn_conv_w, ffn_conv_b,
              ffn_w_down, ln2_g, ln2_b):
    bsz = x.shape[0]
    zero_state = jnp.zeros((bsz, SSD_HEADS, SSD_HEADDIM, SSD_STATE), jnp.float32)
    for l in range(DEPTH_2):
        last = l == DEPTH_2 - 1
        sh1, sc1, g1, sh2, sc2, g2 = ada(c, w_ada[l], b_ada[l])
        csh1, csc1, cg1, csh2, csc2, cg2 = ada(c_ctx[None, :], w_ada[l], b_ada[l])
        mixer_p = (ssd_conv_w[l], ssd_conv_b[l], ssd_dt_bias[l], ssd_a_log[l], ssd_d[l], ssd_norm_w[l],
                   fnet_w[l], pool_w[l], pool_scale[l], w_out[l])
        u_ctx = modulate(ctx, csh1, csc1) @ w_in[l]
        u_lat = modulate(x, sh1, sc1) @ w_in[l]
        if last:
            s_f, s_b = ctx_scan_states(u_ctx, ssd_conv_w[l], ssd_conv_b[l], ssd_dt_bias[l], ssd_a_log[l])
        else:
            mix_ctx, s_f, s_b = token_mixer(u_ctx, zero_state, zero_state, *mixer_p)
        mix_lat, _, _ = token_mixer(u_lat, s_f, s_b, *mixer_p)
        x = post_norm(x, mix_lat, g1, ln1_g[l], ln1_b[l])
        ffn_lat = conv_ffn(modulate(x, sh2, sc2), ffn_w_up[l], ffn_conv_w[l], ffn_conv_b[l], ffn_w_down[l], True)
        x = post_norm(x, ffn_lat, g2, ln2_g[l], ln2_b[l])
        if not last:
            ctx = post_norm(ctx, mix_ctx, cg1, ln1_g[l], ln1_b[l])
            ffn_ctx = conv_ffn(modulate(ctx, csh2, csc2), ffn_w_up[l], ffn_conv_w[l], ffn_conv_b[l], ffn_w_down[l], False)
            ctx = post_norm(ctx, ffn_ctx, cg2, ln2_g[l], ln2_b[l])
    return x


def setup_inputs(seed=0):
    out = dict(first_inputs(seed))
    for name, value in second_inputs(seed + 1).items():
        if name != "x":
            out[name + "_2"] = value
    return out


def reference(
    x, ln_gain, ln_bias, mlp_w_up, mlp_w_down, w_in_even, w_out_even, diff_lambda, diff_subln,
    nsa_pe, nsa_cmp_w1, nsa_cmp_b1, nsa_cmp_w2, w_in_odd, fox_f_bias, w_out_odd, c_2, ctx_2,
    c_ctx_2, w_ada_2, b_ada_2, w_in_2, ssd_conv_w_2, ssd_conv_b_2, ssd_dt_bias_2, ssd_a_log_2,
    ssd_d_2, ssd_norm_w_2, fnet_w_2, pool_w_2, pool_scale_2, w_out_2, ln1_g_2, ln1_b_2,
    ffn_w_up_2, ffn_conv_w_2, ffn_conv_b_2, ffn_w_down_2, ln2_g_2, ln2_b_2,
):
    x = first_block(
        x, ln_gain, ln_bias, mlp_w_up, mlp_w_down, w_in_even, w_out_even, diff_lambda,
        diff_subln, nsa_pe, nsa_cmp_w1, nsa_cmp_b1, nsa_cmp_w2, w_in_odd, fox_f_bias, w_out_odd,
    )
    return second_block(
        x, c_2, ctx_2, c_ctx_2, w_ada_2, b_ada_2, w_in_2, ssd_conv_w_2, ssd_conv_b_2,
        ssd_dt_bias_2, ssd_a_log_2, ssd_d_2, ssd_norm_w_2, fnet_w_2, pool_w_2, pool_scale_2,
        w_out_2, ln1_g_2, ln1_b_2, ffn_w_up_2, ffn_conv_w_2, ffn_conv_b_2, ffn_w_down_2,
        ln2_g_2, ln2_b_2,
    )


_drawn_inputs = setup_inputs


def setup_inputs(seed=0):
    import zlib

    import numpy as np

    out = dict(_drawn_inputs(seed))
    spreads = {}
    factors = {'diff_subln': 23.651,
     'nsa_pe': 30.325,
     'nsa_cmp_b1': 56.516,
     'ctx_2': 8.0,
     'c_ctx_2': 8.0,
     'b_ada_2': 4.245,
     'ssd_conv_b_2': 8.0,
     'ssd_dt_bias_2': 3.251,
     'ssd_d_2': 35.161,
     'ssd_norm_w_2': 4.602,
     'pool_scale_2': 8.0,
     'ln1_b_2': 2.776,
     'ffn_conv_b_2': 8.0,
     'ln2_b_2': 2.852,
     'nsa_cmp_w1': 2.95}
    for name, (base, spread) in spreads.items():
        noise = np.random.default_rng([zlib.crc32(name.encode()), seed]).standard_normal(out[name].shape)
        drawn = base * np.exp(spread * noise) if base else spread * noise
        out[name] = __import__('jax').numpy.asarray(drawn.astype(out[name].dtype))
    for name, factor in factors.items():
        out[name] = (out[name] * factor).astype(out[name].dtype)
    return out
```

```python
import math
from contextlib import ExitStack

import numpy as np
import concourse.bass as bass
from concourse import mybir

F32 = mybir.dt.float32
ALU = mybir.AluOpType
ACT = mybir.ActivationFunctionType
AX = mybir.AxisListType

P = 128
D = 1024
S = 512
TT = S // P
KT = D // P
HD = 64
D_FF = 4 * D
N_EVEN_COLS = 2840
ALPHA = 4.0 ** 0.25
LN_EPS = 1e-5
BIG = 2.0 ** 100
N_CMP = 31
LAM_INIT = 0.8 - 0.6 * math.exp(0.0)

D_FF_2 = 2816
CTX = 256
ALPHA_2 = 2.0 ** 0.25
EPS_2 = 1e-6
N_IN = 2064
OFF_XS, OFF_BC, OFF_DT, OFF_FP = 512, 1024, 1536, 1552
GRID_W = 64


def shape_constants():
    half = 8
    inv = (np.float32(500000.0) ** (-np.arange(half, dtype=np.float32) / np.float32(half))).astype(np.float32)

    def rope(pos):
        ang = pos.astype(np.float32)[:, None] * inv[None, :]
        c, s = np.cos(ang), np.sin(ang)
        cos, sin = np.ones((P, len(pos)), np.float32), np.zeros((P, len(pos)), np.float32)
        for p in range(P):
            d = p % HD
            if d < 2 * half:
                cos[p] = c[:, d % half]
                sin[p] = s[:, d % half] * (-1 if d < half else 1)
        return cos, sin

    cos, sin = rope(np.arange(S))
    cmp_end = np.arange(N_CMP) * 16 + 31
    cc, cs = rope(np.concatenate([cmp_end, cmp_end]))
    swap = np.zeros((P, P), np.float32)
    for m in range(P):
        d = m % HD
        if d < 16:
            swap[(m - 8 if d >= 8 else m + 8), m] = 1
    q, k = np.arange(P)[:, None], np.arange(P)[None, :]
    causal = np.zeros((P, S), np.float32)
    causal[:, S - P:] = np.where(k > q, BIG, 0)
    tok = np.arange(TT)[None, :, None] * P + np.arange(P)[:, None, None]
    ok = cmp_end[None, None, :] <= tok
    inv_count = np.zeros((P, 2, S), np.float32)
    t = np.arange(S)
    for g, w in enumerate((2, 4, 8, 16)):
        n = np.minimum(t + (w - 1 - w // 2) + 1, S) - np.maximum(t - w // 2, 0)
        inv_count[(g % 2) * HD:(g % 2) * HD + HD, g // 2] = 1.0 / n.astype(np.float32)
    parts = [("cos", cos), ("sin", sin), ("ident", np.eye(P)), ("swap", swap), ("causal", causal),
             ("cmp_cos", cc), ("cmp_sin", cs),
             ("cmp_mask", np.where(ok, 0, BIG).reshape(P, -1)), ("cmp_ok", ok.reshape(P, -1)),
             ("lower", (q >= k)), ("upper", (q <= k)), ("inv_count", inv_count.reshape(P, -1))]
    at, where = 0, {}
    for name, a in parts:
        where[name] = (at, at + a.shape[1])
        at += a.shape[1]
    table = np.concatenate([np.asarray(a, np.float32) for _, a in parts], axis=1)
    n = np.arange(S)
    ang = 2 * np.pi * ((n[:, None] * n[None, :]) % S) / S
    scale = 1.0 / math.sqrt(S * HD)
    dft_len = np.stack([np.cos(ang) * scale, -np.sin(ang) * scale]).astype(np.float32)
    c = np.arange(HD)
    angc = 2 * np.pi * ((c[:, None] * c[None, :]) % HD) / HD
    dft_ch = np.stack([np.cos(angc), np.sin(angc)]).astype(np.float32)
    heads = np.zeros((16, 16 * P), np.float32)
    for h in range(16):
        heads[h, h * P:(h + 1) * P] = 1
    return table, where, dft_len, dft_ch, heads


class Stages:

    def __init__(self):
        self.total, self.base, self.before = {}, {}, {}

    def add(self, stage, **counts):
        self.before[stage] = dict(self.total)
        for what, n in counts.items():
            self.base[stage, what] = self.total.get(what, 0)
            self.total[what] = self.total.get(what, 0) + n

    def __call__(self, stage, what):
        return self.base[stage, what]


def build(nc, A, out, debug=None):
    where = A["where"]
    st = Stages()
    st.add("x0", tr=8)
    st.add("proj0", quarters=24, act=24)
    st.add("cmp", quarters=8, act=4)
    st.add("diff", units=8, loads=2)
    st.add("nsa", units=16, loads=1)
    st.add("mixed0", tr=8)
    st.add("out0", quarters=8, dve=8, ln=26, std=1)
    st.add("x1", tr=8)
    st.add("up0", quarters=32, act=32, squares=32)
    st.add("down0", quarters=32, dve=8, ln=26, std=1)
    st.add("x2", tr=8)
    st.add("proj1", quarters=28, act=25)
    st.add("fox", units=16)
    st.add("mixed1", tr=8)
    st.add("out1", quarters=8, dve=8, ln=26, std=1)
    st.add("x3", tr=8)
    st.add("up1", quarters=32, act=32, squares=32)
    st.add("down1", quarters=32, dve=8, ln=26, std=1)
    st.add("ln_ctx", ln=10, std=1)
    st.add("x_ctx", tr=8)
    st.add("ln_x", ln=18, std=1)
    st.add("x4", tr=8)
    st.add("w_in", quarters=20)
    st.add("dft", quarters=4)
    st.add("out2", quarters=8, dve=8, ln=26, std=1)
    st.add("ln_ffn", ln=18, std=1)
    st.add("x5", tr=8)
    st.add("up2", quarters=44, act=44)
    st.add("down2", quarters=32, dve=8, ln=26, std=1)
    DOWN2_K = (6, 6, 5, 5)
    N_SLABS = st.total["quarters"] // 4

    CONSTS = 2 * 16
    SMALL_INPUTS = 5 * 16
    GROUPS0 = ([("F", (m * P, m * P + P), (None, 1.0)) for m in range(4)]
               + [("F", (m * P, m * P + P), (None, -0.125)) for m in range(4)] * 2
               + [("T", (0, 512), (("V", t, 0, 512), 1.0)) for t in range(TT)]
               + [("F", (m * P, m * P + P), (("K", 4 + m) if m < 2 else None, 1.0)) for m in range(4)]
               + [("T", (0, 280), (("V", t, 512, 792), 1.0)) for t in range(TT)])
    ROPED0 = ([(g, "k", g) for g in range(4)] + [(4 + g, "q", g) for g in range(8)]
              + [(18, "k", 6), (19, "k", 7)])
    SMALL = dict(lam=2, windows=7, gelu_in=12, gelu=14, kraw=16, krope=19, scmp=29, pcmp=41, rms=53,
                 mixed0=61, fabs=63, fox=67)
    SMALLA = dict(ptc=4, fexp=14)
    LOADS = {"diff": 0, "nsa": 128, "fox": 256}
    STEP0 = {"diff": 0, "nsa": 16, "fox": 64}

    ctx = ExitStack()
    with ctx:
        def sb(name, shape):
            return ctx.enter_context(nc.sbuf_tensor(name + "_sb", shape, F32))

        def pb(name):
            return ctx.enter_context(nc.psum_tensor(name, [P, 512], F32))

        def sem(name):
            return ctx.enter_context(nc.semaphore(name))

        X = sb("X", [P, TT, D])
        XT = sb("XT", [P, KT, S])
        ring = sb("ring", [P, 2, 4096])
        wide = sb("wide", [P, 32, S])
        QT, KTT = wide[:, 0:8, :], wide[:, 8:16, :]
        V = wide[:, 16:24, :].rearrange("p (t h) n -> p t (h n)", t=TT)
        O = wide[:, 24:32, :].rearrange("p (t h) n -> p t (h n)", t=TT)
        SC = sb("SC", [P, 2, TT, S])
        PT = sb("PT", [P, TT, S])
        qb = sb("qb", [P, 2, S])
        kb = sb("kb", [P, 2, S])
        table = sb("table", [P, A["table"].shape[1]])
        cols = sb("cols", [P, A["cols"].shape[1]])
        rows = sb("rows", [P, 2, D])
        stat = sb("stat", [P, TT, 2, 6])
        agg = sb("agg", [P, TT, 2])
        rstd = sb("rstd", [P, 3, TT])
        mn = sb("mn", [P, 2, TT])
        sm = sb("sm", [P, 2, TT])
        rs = sb("rs", [P, 2, TT])
        og = sb("og", [P, TT, P])
        lamrow = og[:, 0:2, :].rearrange("p a (b n) -> p a b n", b=2)
        KS4 = sb("KS4", [P, 4, S])
        KSW = KS4[0:HD, :, :].rearrange("p (a b) n -> p a b n", a=2)
        lam = sb("lam", [P, 8])
        subln = sb("subln", [P, P])
        gate = sb("gate", [P, TT, 24])
        w2 = sb("w2", [P, 2, 2, P])
        hc = SC[:, 1, 3, 0:248].rearrange("p (a b) -> p a b", a=4)
        hc2 = SC[:, 1, 3, 248:496].rearrange("p (a b) -> p a b", a=4)
        kcc = sb("kcc", [P, 2, 62])
        vcc = sb("vcc", [N_CMP, 2, HD])
        crow = rows[0:16, :, :].rearrange("p a (b n) -> p (a b) n", n=S)
        ones = sb("ones", [P, P])
        cols2 = sb("cols2", [P, A["cols2"].shape[1]])
        modc = sb("modc", [P, 64])
        csil = sb("csil", [P, 2, 2, KT])
        bd = sb("bd", [P, 2, 256])
        poolw = sb("poolw", [P, 2, P])
        tks = sb("tks", [P, 160])
        ncs = sb("ncs", [P, TT, 16])
        ecs = sb("ecs", [P, TT, 16])
        nega = sb("nega", [16, 4])
        drow = sb("drow", [P, 8])
        ys = sb("ys", [P, 3, TT, 2])
        pcm = sb("pcm", [P, 2, 32])
        rmsq = sb("rmsq", [P, 2, 16])
        PC = SC[:, 0, 0:2, :].rearrange("p a b -> p (a b)")[:, 0:8 * TT * N_CMP].rearrange("p (h t n) -> p h t n", h=8, t=TT)

        def WIN(j):
            w = PT[:, 2 * j:2 * j + 2, :].rearrange("p a b -> p (a b)")
            return w[:, 0:16 * 62].rearrange("p (m n) -> p m n", m=16)

        G = [pb(f"G{i}") for i in range(4)]
        TR = [pb(f"TR{i}") for i in range(2)]
        OB = [pb(f"OB{i}") for i in range(2)]

        def tab(name, n=P):
            a, b = where[name]
            return table[0:n, a:b]

        ident = tab("ident")

        s_const = sem("constants_in")
        s_small_in = sem("small_inputs_in")
        s_x = sem("x_in")
        slab_in = [sem("slab_in_even"), sem("slab_in_odd")]
        quarters = sem("slab_quarters_used")
        act_out = sem("psum_emptied_by_scalar")
        dve_out = sem("psum_emptied_by_vector")
        tr_ready = sem("transposed_in_psum")
        tr_out = sem("transposed_copied")
        rope_swapped = sem("rope_partners_in_psum")
        rope_cos = sem("rope_cos_products")
        rope_dve = sem("rope_vector_steps")
        gb_in = sem("gain_bias_in")
        ln_dve = sem("layer_norm_vector_steps")
        ln_std = sem("layer_norm_deviations")
        squared = sem("hidden_squared")
        qk_in = [sem("qk_in_even"), sem("qk_in_odd")]
        sc_seen = sem("scores_seen_by_vector")
        sc_ready = sem("scores_in_psum")
        sc_used = sem("scores_copied_with_min")
        pr_ready = sem("probabilities_ready")
        pt_ready = sem("probabilities_transposed")
        pt_dve = sem("transposed_probabilities_by_vector")
        pt_act = sem("transposed_probabilities_by_scalar")
        pv_ready = sem("attended_in_psum")
        o_steps = sem("attended_vector_steps")
        o_used = sem("attended_copied")
        s_small = sem("vector_small_steps")
        s_smalla = sem("scalar_small_steps")
        s_smallp = sem("tensor_small_steps")
        ksw_in = sem("shared_keys_moved")
        cmp_in = sem("compression_windows_in")
        crow_in = sem("forget_rows_stored")
        s_out = sem("stored")
        ada_in = [sem("ada_half_0_in"), sem("ada_half_1_in")]
        ada_steps = sem("ada_accumulated")
        ada_cols = sem("ada_columns_summed")
        s_two = sem("vector_steps_second")
        s_twoa = sem("scalar_steps_second")
        s_twop = sem("tensor_steps_second")
        s_twog = sem("gpsimd_steps_second")
        s_twod = sem("second_inputs_in")
        conv_first = sem("ffn_conv_padded")
        conv_steps = sem("ffn_conv_taps")
        gelu_done = sem("ffn_gelu")
        gated = sem("ffn_gated")
        res_steps = sem("residual_gated")
        s_ctx = sem("context_in")

        def ADW(h):
            return SC[:, h, :, :].rearrange("p k c -> p (k c)")

        STEPS = {"diff": (0, 1, 4), "nsa": tuple(range(0, 25, 3)), "fox": (0, 1, 2)}

        block = ctx.enter_context(nc.Block())

        def slab(s):
            return ring[:, s % 2, :].rearrange("p (k c) -> p k c", k=KT)

        C2 = dict(bada=16, dt_bias=80, a_log=81, fwd=82, bwd=83, conv=84, conv_b=108, norm=116, pool=120, ffn=122)

        def col(name, n=0, rows_=P):
            return cols2[0:rows_, C2[name] + n:C2[name] + n + 1]

        def tiles(a, b):
            return wide[:, a:b, :].rearrange("p a b -> p (a b)")

        xbcT, Z, Btok = wide[:, 0:8, :], wide[:, 11:15, :], wide[:, 15, :]
        CX = tiles(8, 11).rearrange("p (a b) -> p a b", b=CTX)
        STATE = wide[:, 8:10, :]
        CT = tiles(16, 20).rearrange("p (a b) -> p a b", b=CTX)
        fnetT, CXT = wide[:, 16:18, :], wide[:, 18:20, :]
        ctok = tiles(20, 24).rearrange("p (t n) -> p t n", t=2)
        XW = wide[:, 20:24, :]
        Hn = O
        XS, Y, FAB = wide[:, 24:28, :], wide[:, 28:32, :], wide[:, 28:32, :]
        XF, XB = wide[:, 0:4, :], wide[:, 16:20, :]
        MB = [PT, wide[:, 20:24, :]]
        gbc = KS4[:, :, :].rearrange("p a b -> p (a b)")
        SCF = SC[:, :, :, :].rearrange("p a b c -> p (a b c)")
        PAD_L = 528
        PB, D1, D2 = (SCF[:, n * 2 * PAD_L:(n + 1) * 2 * PAD_L].rearrange("p (a b) -> p a b", a=2) for n in range(3))
        D8 = SCF[:, 6 * PAD_L:7 * PAD_L]
        R = kb
        CR = rows[0:16, :, :].rearrange("p a b -> p (a b)")
        DT, DA = CR[:, 0:768], CR[:, 768:1536]
        PTF = PT[0:16, :, :].rearrange("p a b -> p (a b)")
        CF, RV = PTF[:, 0:768], PTF[:, 768:1536]
        PADS = SCF[:, 0:4 * 660].rearrange("p (m r c) -> p m r c", m=4, r=10)
        dch = w2[0:HD, 0, :, :]
        fw = w2[0:HD, 1, :, :].rearrange("p a b -> p (a b)")

        class Steps:

            def __init__(self, sem_, names):
                self.sem, self.names, self.next = sem_, names, 0
                self.place = {n: i + 1 for i, n in enumerate(names)}
                assert len(self.place) == len(names)

            def do(self, name, ins):
                assert self.names[self.next] == name, (name, self.names[self.next])
                self.next += 1
                ins.then_inc(self.sem, 1)

            def of(self, name):
                return self.place[name]

        def names(*parts):
            out_ = []
            for x in parts:
                out_ += [x] if isinstance(x, str) else list(x)
            return out_

        CONV = [(m, who) for m in range(8) for who in ("c", "l") if who == "l" or m < 6]

        def conv_order(first, second):
            out_ = []
            for m in range(9):
                for k, w in CONV:
                    if k == m:
                        out_ += [x.format(w=w, m=m) for x in first]
                for k, w in CONV:
                    if k == m - 1:
                        out_ += [x.format(w=w, m=m - 1) for x in second]
            return out_

        V2 = Steps(s_two, names(
            "modc", "mod1", "mod2", "mod3", [f"dgb{b}" for b in range(16)], "halfw", "bdz", "pwz",
            conv_order(["{w}{m}a", "{w}{m}b"], ["{w}{m}s"]),
            "dneg", "dabs", "dmax", "dt", "nega", "dA", "cf", "cfc", "rv", "rvc", "c0", "cs", "tt0", "tt1", "wc",
            [f"bd{n}" for n in range(8)], [f"z{t}" for t in range(4)], "tks", "ncs", [f"xw{n}" for n in range(8)],
            [f"xf{t}" for t in range(4)], [f"xb{t}" for t in range(4)],
            [f"yo{g}{t}{x}" for g in range(2) for t in range(4) for x in "abc"],
            [x for h in range(9) for x in ([f"da{h}", f"db{h}", f"dm{h}"] if h < 8 else []) + ([f"mm{h-1}", f"df{h-1}", f"dr{h-1}"] if h else [])
             + ([f"ya{h-2}"] if h >= 2 else [])], "ya7",
            [f"{x}{t}" for t in range(4) for x in ("sk", "sa", "sz", "sq", "sr")], "sv", "si", [f"sn{t}" for t in range(4)]))
        A2 = Steps(s_twoa, names(
            [f"gb{q}" for q in range(4)], "dtc", "dtl", conv_order(["{w}{m}f"], ["{w}{m}t"]),
            "alog", "dexp", "dln", "fn0", "fn1", "po0", "po1", "wexp",
            [f"z{t}{x}" for t in range(4) for x in "ht"], [f"fab{t}" for t in range(4)], "yf0", "yf1", "ecs",
            [f"xt{t}" for t in range(4)], "ct0", "ct1", "bt", "yp0", "yp1", "st0", "st1", [f"g{g}{j}" for g in range(2) for j in range(4)],
            [f"{x}{h}" for h in range(8) for x in ("of", "ed")], "ss", [f"ym{b}" for b in range(4)]))
        P2 = Steps(s_twop, names(
            [f"gb{q}" for q in range(4)], "dtc", "bdp", "tks", [f"fab{t}" for t in range(4)],
            [f"xt{t}" for t in range(4)], "ct0", "ct1", "bt", "yp0", "yp1", "st0", "st1",
            [f"g{g}{j}" for g in range(2) for j in range(4)], [f"yo{g}{t}" for g in range(2) for t in range(4)],
            "rw0", [x for h in range(8) for x in ([f"rw{h+1}"] if h < 7 else []) + [f"y{h}"]], [f"ym{b}" for b in range(4)]))
        G2 = Steps(s_twog, names("pz", "d2", "d4", "d8", "d16", "m0", "m1", "m2", "m3", "sub", "padz"))

        def XBC(w, m):
            return xbcT[:, m, :] if w == "l" else CX[:, m, :]

        def TH(w, m):
            return qb[:, m % 2, :] if w == "l" else PT[:, 3, (m % 2) * CTX:(m % 2 + 1) * CTX]

        def DGB(b):
            return qb[:, (b % 8) // 4, (b % 4) * P:(b % 4 + 1) * P]

        def DFB(h):
            return kb[:, 0, :], kb[:, 1, :]

        def diagonal(m):
            a = m[:, 0, 0:P]
            return bass.AP(tensor=a.tensor, offset=a.offset, ap=[list(a.ap[0]), [S + P, TT], [1, P]])

        def gpsimd_second(gp, gain_bias):
            gp.wait_ge(quarters, st("down1", "quarters") + 32)
            gp.dma_start(ctok, A["ctx_2"].rearrange("o (t p) d -> p (o t) d", p=P)).then_inc(s_ctx, 16)
            gp.dma_start(dch, A["dft_ch"]).then_inc(s_twod, 16)
            gp.dma_start(fw.rearrange("p (g d) -> p g d", g=4), A["fnet_w_2"].rearrange("o g c d -> c (o g) d")).then_inc(s_twod, 16)
            gp.dma_start(drow[:, :], A["ssd_d_2"].partition_broadcast(P).rearrange("p o h -> p (o h)")).then_inc(s_twod, 16)
            gp.wait_ge(s_two, V2.of("pwz"))
            for g in range(4):
                r = (g % 2) * HD
                gp.dma_start(poolw[r:r + HD, g // 2, r:r + HD], A["pool_w_2"][0, g, :, :]).then_inc(s_twod, 16)
            gp.wait_ge(ada_steps, 128)
            G2.do("pz", nc.gpsimd.memset(SCF[:, 0:2 * PAD_L], 0.0))
            gp.wait_ge(s_twoa, A2.of("po1"))
            tt = nc.gpsimd.tensor_tensor
            G2.do("d2", tt(out=D1[:, :, 0:526], in0=PB[:, :, 0:526], in1=PB[:, :, 1:527], op=ALU.add))
            gp.wait_ge(s_twog, G2.of("d2"))
            G2.do("d4", tt(out=D2[:, :, 0:524], in0=D1[:, :, 0:524], in1=D1[:, :, 2:526], op=ALU.add))
            gp.wait_ge(s_twog, G2.of("d4"))
            G2.do("d8", tt(out=D8[:, 0:520], in0=D2[:, 1, 0:520], in1=D2[:, 1, 4:524], op=ALU.add))
            gp.wait_ge(s_twog, G2.of("d8"))
            G2.do("d16", tt(out=D1[:, 1, 0:S], in0=D8[:, 0:S], in1=D8[:, 8:S + 8], op=ALU.add))
            gp.wait_ge(s_twog, G2.of("d16"))
            inv = tab("inv_count").rearrange("p (a n) -> p a n", a=2)
            for n, (p0, i, src) in enumerate([(0, 0, D1[0:HD, 0, 7:7 + S]), (HD, 0, D2[HD:P, 0, 6:6 + S]),
                                              (0, 1, D8[0:HD, 4:4 + S]), (HD, 1, D1[HD:P, 1, 0:S])]):
                G2.do(f"m{n}", tt(out=R[p0:p0 + HD, i, :], in0=src, in1=inv[p0:p0 + HD, i, :], op=ALU.mult))
            gp.wait_ge(s_twog, G2.of("m3"))
            G2.do("sub", tt(out=R[:, :, :], in0=R[:, :, :], in1=PB[:, :, 8:8 + S], op=ALU.subtract))
            gp.wait_ge(s_twop, P2.of("y7"))
            gp.wait_ge(s_two, V2.of("mm7"))
            gain_bias(4, A["ln1_g_2"][0, :], A["ln1_b_2"][0, :])
            G2.do("padz", nc.gpsimd.memset(SCF[:, 0:4 * 660], 0.0))
            gain_bias(5, A["ln2_g_2"][0, :], A["ln2_b_2"][0, :])

        def tensor_second(pe, stage_start, slab_wait, transposes, out_products):
            mm_, tr_ = nc.tensor.matmul, nc.tensor.transpose

            def by_feature(stage, src, n_tiles, ready):
                base = st(stage, "tr")
                ready()
                for b in range(KT):
                    if base + b >= 2:
                        pe.wait_ge(tr_out, base + b - 1)
                    for t in range(n_tiles):
                        m = tr_(TR[b % 2][:, t * P:(t + 1) * P], src[:, t, b * P:(b + 1) * P], ident)
                    m.then_inc(tr_ready, 1)

            for q in range(4):
                pe.wait_ge(s_two, V2.of(f"dgb{4 * q + 3}"))
                pe.wait_ge(ln_dve, st("ln_ctx", "ln"))
                for n in range(4):
                    m = mm_(G[q][:, n * P:(n + 1) * P], lhsT=ones[:, :], rhs=DGB(4 * q + n), start=True, stop=True)
                P2.do(f"gb{q}", m)
            by_feature("x_ctx", ctok, 2, lambda: pe.wait_ge(ln_dve, st("ln_ctx", "ln") + 10))
            by_feature("x4", Hn, TT, lambda: pe.wait_ge(ln_dve, st("ln_x", "ln") + 18))

            s0 = st("w_in", "quarters") // 4
            pe.wait_ge(tr_out, st("x4", "tr") + 8)
            pe.wait_ge(s_twoa, A2.of("gb3"))
            slab_wait(s0)
            for k in range(KT):
                m = mm_(G[2][0:16, 0:CTX], lhsT=slab(s0)[:, k, 0:16], rhs=CT[:, k, :], start=(k == 0), stop=(k == KT - 1))
            P2.do("dtc", m)
            for k in range(KT):
                m = mm_(G[0][0:16, :], lhsT=slab(s0)[:, k, 0:16], rhs=XT[:, k, :], start=(k == 0), stop=(k == KT - 1))
            m.then_inc(quarters, 4)
            for n in range(16):
                if n % 4 == 0:
                    slab_wait(s0 + 1 + n // 4)
                sl = slab(s0 + 1 + n // 4)
                c = slice((n % 4) * P, (n % 4 + 1) * P)
                if n < 2:
                    pe.wait_ge(s_twoa, A2.of("dtl"))
                elif n < 10:
                    pe.wait_ge(s_two, V2.of(f"l{n - 2}b"))
                elif n < 14:
                    pe.wait_ge(s_twoa, A2.of(("fn0", "fn1", "po0", "po1")[n - 10]))
                else:
                    pe.wait_ge(s_twoa, A2.of(f"z{n - 14}h"))
                if n < 6:
                    for k in range(KT):
                        mm_(G[2 + n % 2][:, 0:CTX], lhsT=sl[:, k, c], rhs=CT[:, k, :], start=(k == 0), stop=(k == KT - 1))
                for k in range(KT):
                    if n < 12:
                        m = mm_(G[n % 2][:, :], lhsT=sl[:, k, c], rhs=XT[:, k, :], start=(k == 0), stop=(k == KT - 1))
                    else:
                        m = mm_(G[n % 2][:, :], lhsT=XT[:, k, c], rhs=sl[:, k, :], start=(k == 0), stop=(k == KT - 1))
                m.then_inc(quarters, 1)

            pe.wait_ge(s_twod, 112)
            for cs in range(2):
                m = mm_(TR[0][:, cs * 256:(cs + 1) * 256], lhsT=dch[:, cs, :], rhs=fw, start=True, stop=True)
            P2.do("bdp", m)
            pe.wait_ge(s_two, V2.of("wc"))
            for n in range(10):
                src = DA[:, n * P:(n + 1) * P] if n < 4 else DT[:, (n - 4) * P:(n - 3) * P] if n < 8 else CF[:, S + (n - 8) * P:S + (n - 7) * P]
                m = tr_(OB[1][:, n * 16:(n + 1) * 16], src, ident[0:16, 0:16])
            P2.do("tks", m)
            pe.wait_ge(s_two, V2.of("bd7"))
            for t in range(TT):
                pe.wait_ge(s_twoa, A2.of("z3h"))
                for ft in range(2):
                    m = mm_(G[t][:, ft * 256:(ft + 1) * 256], lhsT=fnetT[:, ft, t * P:(t + 1) * P], rhs=bd[:, ft, :], start=True, stop=True)
                P2.do(f"fab{t}", m)
            sd = st("dft", "quarters") // 4
            slab_wait(sd)
            for ft in range(2):
                for n in range(8):
                    cs, t = n // 4, n % 4
                    pe.wait_ge(s_twoa, A2.of("fab3"))
                    m = mm_(TR[ft][:, :], lhsT=FAB[:, t, ft * 256 + cs * P:ft * 256 + (cs + 1) * P], rhs=slab(sd)[:, n, :],
                            start=(n == 0), stop=(n == 7))
                m.then_inc(quarters, 2)
            pe.wait_ge(s_two, V2.of("l7s"))
            for t in range(TT):
                for b in range(4):
                    m = tr_(G[t][:, b * P:(b + 1) * P], xbcT[:, b, t * P:(t + 1) * P], ident)
                P2.do(f"xt{t}", m)
            for t in range(2):
                pe.wait_ge(s_twoa, A2.of(f"yf{t}"))
                for b in range(4):
                    m = tr_(TR[t][:, b * P:(b + 1) * P], CX[:, b, t * P:(t + 1) * P], ident)
                P2.do(f"ct{t}", m)
            for n in range(4):
                m = tr_(OB[0][:, n * P:(n + 1) * P], CX[:, 4 + n % 2, (n // 2) * P:(n // 2 + 1) * P], ident)
            P2.do("bt", m)
            pe.wait_ge(s_twog, G2.of("sub"))
            pe.wait_ge(s_twod, 112)
            for i in range(2):
                pe.wait_ge(s_twoa, A2.of(f"xt{i}"))
                P2.do(f"yp{i}", mm_(G[i][:, :], lhsT=poolw[:, i, :], rhs=R[:, i, :], start=True, stop=True))
            pe.wait_ge(s_two, V2.of("xw7"))
            pe.wait_ge(s_twoa, A2.of("bt"))
            for g in range(2):
                for t in range(2):
                    m = mm_(OB[g][:, :], lhsT=Btok[:, (2 * t + g) * P:(2 * t + g + 1) * P], rhs=XW[:, 2 * t + g, :], start=(t == 0), stop=(t == 1))
                P2.do(f"st{g}", m)
            for g in range(2):
                for j in range(TT):
                    if g == 0:
                        pe.wait_ge(s_twoa, A2.of(f"yp{j}" if j < 2 else f"xt{j}"))
                    else:
                        pe.wait_ge(s_twoa, A2.of(f"g0{j}"))
                    P2.do(f"g{g}{j}", mm_(G[j][:, :], lhsT=xbcT[:, 4 + g, j * P:(j + 1) * P], rhs=xbcT[:, 6 + g, :], start=True, stop=True))
            pe.wait_ge(s_twoa, A2.of("st1"))
            for g in range(2):
                for t in range(TT):
                    if g or t >= 2:
                        pe.wait_ge(s_two, V2.of(f"yo{g if t >= 2 else 0}{(t - 2) % 4}b"))
                    P2.do(f"yo{g}{t}", mm_(TR[t % 2][:, :], lhsT=xbcT[:, 6 + g, t * P:(t + 1) * P], rhs=STATE[:, g, :], start=True, stop=True))

            def decay_rows(h):
                if h >= 2:
                    pe.wait_ge(s_two, V2.of(f"db{h - 2}"))
                    pe.wait_ge(s_twoa, A2.of(f"of{h - 2}"))
                else:
                    pe.wait_ge(s_twoa, A2.of("g13"))
                for x in range(2):
                    m = mm_(G[2 * (h % 2) + x][:, :], lhsT=ident[0:16, 8 * x + h:8 * x + h + 1].to_broadcast([16, P]), rhs=DA[:, 0:S],
                            start=True, stop=True)
                P2.do(f"rw{h}", m)

            decay_rows(0)
            for h in range(8):
                if h < 7:
                    decay_rows(h + 1)
                pe.wait_ge(s_two, V2.of(f"dr{h}"))
                if h >= 2:
                    pe.wait_ge(s_two, V2.of(f"ya{h - 2}"))
                M = MB[h % 2]
                c = slice(h * HD, (h + 1) * HD)
                for t in range(TT):
                    T_ = slice(t * P, (t + 1) * P)
                    terms = [(M[:, j, T_], (XF if j < t else XB)[:, j, c]) for j in range(TT) if j != t]
                    terms += [(DFB(h)[0][:, T_], XF[:, t, c]), (DFB(h)[1][:, T_], XB[:, t, c])]
                    for n, (a, b) in enumerate(terms):
                        m = mm_(OB[h % 2][:, t * HD:(t + 1) * HD], lhsT=a, rhs=b, start=(n == 0), stop=(n == len(terms) - 1))
                P2.do(f"y{h}", m)
            pe.wait_ge(s_two, V2.of("sn3"))
            for b in range(4):
                if b >= 2:
                    pe.wait_ge(s_twoa, A2.of(f"ym{b - 2}"))
                for t in range(TT):
                    m = tr_(TR[b % 2][:, t * P:(t + 1) * P], Y[:, t, b * P:(b + 1) * P], ident)
                P2.do(f"ym{b}", m)

            pe.wait_ge(s_twoa, A2.of("ym3"))
            out_products("out2", "x4")
            by_feature("x5", Hn, TT, lambda: pe.wait_ge(ln_dve, st("ln_ffn", "ln") + 18))

            pe.wait_ge(tr_out, st("x5", "tr") + 8)
            stage_start("up2")
            s0, a0 = st("up2", "quarters") // 4, st("up2", "act")

            def up_slab(s, i):
                slab_wait(s0 + s, i)
                for m in range(4):
                    pe.wait_ge(act_out, i * 8 + (a0 + 4 * s + m - 3))
                    for k in range(KT):
                        x = mm_(G[m][:, :], lhsT=slab(s0 + s)[:, k, m * P:(m + 1) * P], rhs=XT[:, k, :], start=(k == 0), stop=(k == KT - 1))
                    x.then_inc(quarters, 1)

            with pe.Fori(0, 5) as i:
                up_slab(0, i)
                up_slab(1, i)
            up_slab(0, 5)
            stage_start("down2")
            s0, v0 = st("down2", "quarters") // 4, st("down2", "dve")
            with pe.Fori(0, 2) as n:
                k0 = 0
                for kb_, nk in enumerate(DOWN2_K):
                    slab_wait(s0 + kb_, n * 2)
                    for t in range(TT):
                        if kb_ == 0:
                            pe.wait_ge(dve_out, n * 4 + (v0 + t - 3))
                        for k in range(nk):
                            if t == 0:
                                pe.wait_ge(gated, k0 + k + 1)
                            x = mm_(G[t][:, :], lhsT=wide[:, k0 + k, t * P:(t + 1) * P], rhs=slab(s0 + kb_)[:, k, :],
                                    start=(k0 + k == 0), stop=(k0 + k == 21))
                        x.then_inc(quarters, 1)
                    k0 += nk

        def scalar_second(act, copies, deviation):
            ac = nc.scalar.activation

            def modulated(stage, dst, n_tiles, scale0, shift0):
                base = st(stage, "tr")
                for b in range(KT):
                    act.wait_ge(tr_ready, base + b + 1)
                    ac(dst[:, b, :], TR[b % 2][:, 0:n_tiles * P], ACT.Identity, scale=modc[:, scale0 + b:scale0 + b + 1],
                       bias=modc[:, shift0 + b:shift0 + b + 1]).then_inc(tr_out, 1)

            for q in range(4):
                act.wait_ge(s_twop, P2.of(f"gb{q}"))
                A2.do(f"gb{q}", ac(gbc[:, q * 512:(q + 1) * 512], G[q][:, :], ACT.Copy))
            deviation("ln_ctx", 8)
            modulated("x_ctx", CT, 2, 56, 48)
            deviation("ln_x")
            modulated("x4", XT, TT, 8, 0)
            q0 = st("w_in", "quarters")
            act.wait_ge(s_twop, P2.of("dtc"))
            A2.do("dtc", ac(DT[:, S:S + CTX], G[2][0:16, 0:CTX], ACT.Identity, bias=col("dt_bias", 0, 16)))
            act.wait_ge(quarters, q0 + 4)
            A2.do("dtl", ac(DT[:, 0:S], G[0][0:16, :], ACT.Identity, bias=col("dt_bias", 0, 16)))

            def conv_tanh(m, w):
                act.wait_ge(s_two, V2.of(f"{w}{m}b"))
                if m >= 2:
                    act.wait_ge(s_two, V2.of(f"{w}{m - 2}s"))
                A2.do(f"{w}{m}t", ac(TH(w, m), XBC(w, m), ACT.Tanh))

            act.wait_ge(s_two, V2.of("halfw"))
            for m in range(9):
                if m < 8:
                    act.wait_ge(quarters, q0 + 4 + m + 1)
                for k, w in CONV:
                    if k == m:
                        ps = G[m % 2][:, :] if w == "l" else G[2 + m % 2][:, 0:CTX]
                        A2.do(f"{w}{m}f", ac(XBC(w, m), ps, ACT.Identity, scale=col("conv", 3 * m + 1), bias=col("conv_b", m)))
                for k, w in CONV:
                    if k == m - 1:
                        conv_tanh(k, w)
            A2.do("alog", ac(nega[:, 0:1], col("a_log", 0, 16), ACT.Exp))
            act.wait_ge(s_two, V2.of("dabs"))
            A2.do("dexp", ac(DA, DA, ACT.Exp, scale=-1.0))
            act.wait_ge(s_twoa, A2.of("dexp"))
            A2.do("dln", ac(DA, DA, ACT.Ln, bias=1.0))
            for n in range(4):
                act.wait_ge(quarters, q0 + 12 + n + 1)
                if n < 2:
                    A2.do(f"fn{n}", ac(fnetT[:, n, :], G[n % 2][:, :], ACT.Copy))
                else:
                    act.wait_ge(s_twog, G2.of("pz"))
                    A2.do(f"po{n - 2}", ac(PB[:, n - 2, 8:8 + S], G[n % 2][:, :], ACT.Copy))
            act.wait_ge(s_two, V2.of("tt1"))
            A2.do("wexp", ac(CF[:, S:S + CTX], DA[:, S:S + CTX], ACT.Exp, scale=-1.0, bias=nega[:, 3:4]))
            for t in range(TT):
                act.wait_ge(quarters, q0 + 16 + t + 1)
                A2.do(f"z{t}h", ac(Z[:, t, :], G[t % 2][:, :], ACT.Copy, scale=0.5))
                act.wait_ge(s_twoa, A2.of(f"z{t}h"))
                act.wait_ge(s_two, V2.of("l7s") if t < 2 else V2.of(f"z{t - 2}"))
                A2.do(f"z{t}t", ac(qb[:, t % 2, :], Z[:, t, :], ACT.Tanh))
            for t in range(TT):
                act.wait_ge(s_twop, P2.of(f"fab{t}"))
                A2.do(f"fab{t}", ac(FAB[:, t, :], G[t][:, :], ACT.Copy))
            for ft in range(2):
                act.wait_ge(quarters, st("dft", "quarters") + 2 * ft + 2)
                A2.do(f"yf{ft}", ac(XT[:, 4 + ft, :], TR[ft][:, :], ACT.Copy))
            act.wait_ge(s_two, V2.of("tks"))
            A2.do("ecs", ac(ecs[:, :, :].rearrange("p a b -> p (a b)"), tks[:, 0:64], ACT.Exp))
            for t in range(TT):
                act.wait_ge(s_twop, P2.of(f"xt{t}"))
                A2.do(f"xt{t}", ac(XS[:, t, :], G[t][:, :], ACT.Copy))
            for t in range(2):
                act.wait_ge(s_twop, P2.of(f"ct{t}"))
                A2.do(f"ct{t}", ac(CXT[:, t, :], TR[t][:, :], ACT.Copy))
            act.wait_ge(s_twop, P2.of("bt"))
            A2.do("bt", ac(Btok, OB[0][:, :], ACT.Copy))
            for i in range(2):
                act.wait_ge(s_twop, P2.of(f"yp{i}"))
                A2.do(f"yp{i}", ac(XT[:, 6 + i, :], G[i][:, :], ACT.Copy, scale=col("pool", i)))
            for g in range(2):
                act.wait_ge(s_twop, P2.of(f"st{g}"))
                A2.do(f"st{g}", ac(STATE[:, g, :], OB[g][:, :], ACT.Copy))
            act.wait_ge(s_twog, G2.of("sub"))
            for g in range(2):
                for j in range(TT):
                    act.wait_ge(s_twop, P2.of(f"g{g}{j}"))
                    A2.do(f"g{g}{j}", ac(SC[:, g, j, :], G[j][:, :], ACT.Copy))
            for h in range(8):
                act.wait_ge(s_twop, P2.of(f"rw{h}"))
                act.wait_ge(s_two, V2.of("ncs"))
                if h >= 2:
                    act.wait_ge(s_twop, P2.of(f"y{h - 2}"))
                elif h == 1:
                    act.wait_ge(s_twop, P2.of("st1"))
                M = MB[h % 2]
                for j in range(TT):
                    if j:
                        m = ac(M[:, j, 0:j * P], G[2 * (h % 2) + 1][:, 0:j * P], ACT.Exp, bias=ncs[:, j, 8 + h:9 + h])
                    if j < 3:
                        m = ac(M[:, j, (j + 1) * P:S], G[2 * (h % 2)][:, (j + 1) * P:S], ACT.Exp, bias=ncs[:, j, h:h + 1])
                A2.do(f"of{h}", m)
                act.wait_ge(s_two, V2.of(f"dm{h}"))
                A2.do(f"ed{h}", ac(diagonal(M), qb[:, h % 2, :].rearrange("p (a b) -> p a b", a=TT), ACT.Exp))
            act.wait_ge(s_two, V2.of("si"))
            A2.do("ss", ac(ys[:, 2, :, :], ys[:, 0, :, :], ACT.Sqrt))
            for b in range(4):
                act.wait_ge(s_twop, P2.of(f"ym{b}"))
                A2.do(f"ym{b}", ac(XT[:, b, :], TR[b % 2][:, :], ACT.Copy, scale=col("norm", b)))
            deviation("out2")
            deviation("ln_ffn")
            modulated("x5", XT, TT, 32, 24)

            q0 = st("up2", "quarters")

            def grids(i, s):
                for m in range(4):
                    n = 4 * s + m
                    act.wait_ge(quarters, i * 8 + (q0 + n + 1))
                    if not (isinstance(i, int) and i == 0 and n < 4):
                        act.wait_ge(gated, i * 4 + (2 * s - 2 + m // 2 + 1))
                    else:
                        act.wait_ge(s_twog, G2.of("padz"))
                    ps = G[m][:, :].rearrange("p (r c) -> p r c", c=GRID_W)
                    ac(PADS[:, m, 1:9, 1:65], ps, ACT.Copy).then_inc(conv_first, 1)
                    f = C2["ffn"] + 40 * s + 10 * m
                    w, b = (cols2[:, bass.ds(i * 80 + (f + x), 1)] for x in (4, 9))
                    ac(PT[:, m, :], G[m][:, :], ACT.Identity, scale=w, bias=b).then_inc(act_out, 1)
                    if m % 2:
                        act.wait_ge(conv_steps, i * 64 + 8 * (n + 1))
                        ac(PT[:, m, :], PT[:, m, :], ACT.Gelu_apprx_tanh).then_inc(gelu_done, 1)

            for s in range(2):
                grids(0, s)
            with act.Fori(1, 5) as i:
                for s in range(2):
                    grids(i, s)
            grids(5, 0)
            deviation("down2")

        def vector_second(dve, residual, layer_norm):
            tt, ts, stt = nc.vector.tensor_tensor, nc.vector.tensor_scalar, nc.vector.scalar_tensor_tensor

            def own(name):
                dve.wait_ge(s_two, V2.of(name))

            dve.wait_ge(ada_cols, 16)
            V2.do("modc", tt(out=modc[:, :], in0=OB[0][:, 0:64], in1=cols2[:, 16:80], op=ALU.add))
            own("modc")
            for n, c in enumerate((8, 32, 56)):
                V2.do(f"mod{n + 1}", ts(modc[:, c:c + 8], modc[:, c:c + 8], 1.0, None, ALU.add))
            for b in range(16):
                c = 16 + b if b < 8 else 32 + b
                if b >= 8:
                    dve.wait_ge(s_twop, P2.of(f"gb{(b - 8) // 4}"))
                V2.do(f"dgb{b}", ts(DGB(b), ident, modc[:, c:c + 1], None, ALU.mult))
            V2.do("halfw", ts(cols2[:, 84:116], cols2[:, 84:116], 0.5, None, ALU.mult))
            V2.do("bdz", nc.vector.memset(bd[:, :, :], 0.0))
            V2.do("pwz", nc.vector.memset(poolw[:, :, :], 0.0))
            dve.wait_ge(s_ctx, 16)
            own("mod3")
            layer_norm("ln_ctx", EPS_2, n_tiles=2, src=ctok, dst=ctok)
            layer_norm("ln_x", EPS_2, src=X, dst=Hn)

            own("halfw")
            for m in range(9):
                for k, w in CONV:
                    if k == m:
                        n = S if w == "l" else CTX
                        ps = G[m % 2] if w == "l" else G[2 + m % 2]
                        y = XBC(w, m)
                        dve.wait_ge(s_twoa, A2.of(f"{w}{m}f"))
                        V2.do(f"{w}{m}a", stt(out=y[:, 1:n], in0=ps[:, 0:n - 1], scalar=col("conv", 3 * m), in1=y[:, 1:n], op0=ALU.mult, op1=ALU.add))
                        own(f"{w}{m}a")
                        V2.do(f"{w}{m}b", stt(out=y[:, 0:n - 1], in0=ps[:, 1:n], scalar=col("conv", 3 * m + 2), in1=y[:, 0:n - 1], op0=ALU.mult, op1=ALU.add))
                for k, w in CONV:
                    if k == m - 1:
                        y = XBC(w, k)
                        dve.wait_ge(s_twoa, A2.of(f"{w}{k}t"))
                        V2.do(f"{w}{k}s", stt(out=y, in0=TH(w, k), scalar=1.0, in1=y, op0=ALU.add, op1=ALU.mult))
            dve.wait_ge(s_twoa, A2.of("dtl"))
            V2.do("dneg", ts(DA, DT, -1.0, None, ALU.mult))
            own("dneg")
            V2.do("dabs", tt(out=DA, in0=DA, in1=DT, op=ALU.max))
            own("dabs")
            V2.do("dmax", ts(DT, DT, 0.0, None, ALU.max))
            dve.wait_ge(s_twoa, A2.of("dln"))
            own("dmax")
            V2.do("dt", tt(out=DT, in0=DT, in1=DA, op=ALU.add))
            V2.do("nega", ts(nega[:, 1:2], nega[:, 0:1], -1.0, None, ALU.mult))
            own("nega")
            V2.do("dA", ts(DA, DT, nega[:, 1:2], None, ALU.mult))
            own("dA")
            scan = nc.vector.tensor_tensor_scan
            for name, o, a, b, flip in (("cf", CF, 0, S, 0), ("cfc", CF, S, S + CTX, 0), ("rv", RV, 0, S, 1), ("rvc", RV, S, S + CTX, 1)):
                src, dst = DA[:, a:b], o[:, a:b]
                if flip:
                    src, dst = src[:, ::-1], dst[:, ::-1]
                V2.do(name, scan(out=dst, data0=src, data1=src, initial=0.0, op0=ALU.add, op1=ALU.bypass))
            own("rvc")
            V2.do("c0", ts(CF, CF, col("fwd", 0, 16), None, ALU.mult))
            own("c0")
            V2.do("cs", stt(out=DA, in0=RV, scalar=col("bwd", 0, 16), in1=CF, op0=ALU.mult, op1=ALU.add))
            own("cs")
            V2.do("tt0", ts(nega[:, 2:3], DA[:, S + CTX - 1:S + CTX], col("fwd", 0, 16), None, ALU.mult))
            own("tt0")
            V2.do("tt1", stt(out=nega[:, 3:4], in0=DA[:, S:S + 1], scalar=col("bwd", 0, 16), in1=nega[:, 2:3], op0=ALU.mult, op1=ALU.add))
            dve.wait_ge(s_twoa, A2.of("wexp"))
            V2.do("wc", tt(out=CF[:, S:S + CTX], in0=CF[:, S:S + CTX], in1=DT[:, S:S + CTX], op=ALU.mult))
            dve.wait_ge(s_twop, P2.of("bdp"))
            own("bdz")
            for n in range(8):
                cs, g = n // 4, n % 4
                r = (g % 2) * HD
                V2.do(f"bd{n}", nc.vector.tensor_copy(bd[r:r + HD, g // 2, cs * P + r:cs * P + r + HD],
                                                      TR[0][r:r + HD, cs * 256 + g * HD:cs * 256 + (g + 1) * HD]))
            for t in range(TT):
                dve.wait_ge(s_twoa, A2.of(f"z{t}t"))
                V2.do(f"z{t}", stt(out=Z[:, t, :], in0=qb[:, t % 2, :], scalar=1.0, in1=Z[:, t, :], op0=ALU.add, op1=ALU.mult))
            dve.wait_ge(s_twop, P2.of("tks"))
            V2.do("tks", nc.vector.tensor_copy(tks[:, :], OB[1][:, 0:160]))
            own("tks")
            V2.do("ncs", ts(ncs[:, :, :].rearrange("p a b -> p (a b)"), tks[:, 0:64], -1.0, None, ALU.mult))
            dtt = tks[:, 64:128].rearrange("p (t n) -> p t n", t=TT)
            wct = tks[:, 128:160].rearrange("p (t n) -> p t n", t=2)

            def heads_(ap, n=4):
                return ap.rearrange("p (h d) -> p h d", h=n)

            def over(ap, n, d):
                return ap.unsqueeze(2).to_broadcast([P, n, d])

            for n in range(8):
                t, g, x = n // 4, (n // 2) % 2, n % 2
                dve.wait_ge(s_twoa, A2.of(f"ct{t}"))
                V2.do(f"xw{n}", tt(out=heads_(XW[:, 2 * t + g, x * 256:(x + 1) * 256]), in0=heads_(CXT[:, t, g * 256:(g + 1) * 256]),
                                   in1=over(wct[:, t, 8 * x + 4 * g:8 * x + 4 * g + 4], 4, HD), op=ALU.mult))
            own("xw7")
            dve.wait_ge(s_twoa, A2.of("fab3"))
            for x, dst in ((0, XF), (1, XB)):
                for t in range(TT):
                    dve.wait_ge(s_twoa, A2.of(f"xt{t}"))
                    V2.do(f"x{'fb'[x]}{t}", tt(out=heads_(dst[:, t, :], 8), in0=heads_(XS[:, t, :], 8),
                                              in1=over(dtt[:, t, 8 * x:8 * x + 8], 8, HD), op=ALU.mult))
            dve.wait_ge(s_twoa, A2.of("ecs"))
            ogf = og[:, :, :].rearrange("p a b -> p (a b)")
            for g in range(2):
                for t in range(TT):
                    dve.wait_ge(s_twop, P2.of(f"yo{g}{t}"))
                    y = heads_(Y[:, t, g * 256:(g + 1) * 256])
                    if g or t:
                        own(f"yo{g if t else g - 1}{(t - 1) % 4}c")
                    V2.do(f"yo{g}{t}a", tt(out=y, in0=heads_(TR[t % 2][:, 0:256]), in1=over(ecs[:, t, 4 * g:4 * g + 4], 4, HD), op=ALU.mult))
                    V2.do(f"yo{g}{t}b", tt(out=heads_(ogf[:, 0:256]), in0=heads_(TR[t % 2][:, 256:512]), in1=over(ecs[:, t, 8 + 4 * g:12 + 4 * g], 4, HD), op=ALU.mult))
                    own(f"yo{g}{t}b")
                    V2.do(f"yo{g}{t}c", tt(out=y, in0=y, in1=heads_(ogf[:, 0:256]), op=ALU.add))

            def head_out(h):
                y = Y[:, :, h * HD:(h + 1) * HD]
                dve.wait_ge(s_twop, P2.of(f"y{h}"))
                V2.do(f"ya{h}", tt(out=y, in0=y, in1=OB[h % 2][:, 0:256].rearrange("p (t d) -> p t d", t=TT), op=ALU.add))

            for h in range(9):
                if h < 8:
                    q = [qb[:, h % 2, :].rearrange("p (a b) -> p a b", a=TT), ogf.rearrange("p (a b) -> p a b", a=TT)]
                    dve.wait_ge(s_twoa, A2.of(f"of{h}"))
                    own(f"dm{h - 1}" if h else "yo13c")
                    if h >= 2:
                        dve.wait_ge(s_twoa, A2.of(f"ed{h - 2}"))
                    for x, name in enumerate(("da", "db")):
                        V2.do(f"{name}{h}", tt(out=q[x], in0=G[2 * (h % 2) + x][:, :].rearrange("p (a b) -> p a b", a=TT),
                                               in1=over(ncs[:, :, 8 * x + h], TT, P), op=ALU.add))
                    own(f"db{h}")
                    V2.do(f"dm{h}", tt(out=q[0], in0=q[0], in1=q[1], op=ALU.min))
                if h:
                    e = h - 1
                    M = MB[e % 2]
                    dve.wait_ge(s_twoa, A2.of(f"ed{e}"))
                    V2.do(f"mm{e}", tt(out=M[:, :, :], in0=M[:, :, :], in1=SC[:, e // 4, :, :], op=ALU.mult))
                    own(f"mm{e}")
                    if e:
                        dve.wait_ge(s_twop, P2.of(f"y{e - 1}"))
                    for x, (name, mask) in enumerate((("df", "upper"), ("dr", "lower"))):
                        V2.do(f"{name}{e}", tt(out=DFB(e)[x].rearrange("p (a b) -> p a b", a=TT), in0=diagonal(M),
                                               in1=tab(mask).unsqueeze(1).to_broadcast([P, TT, P]), op=ALU.mult))
                if h >= 2:
                    head_out(h - 2)
            head_out(7)
            for t in range(TT):
                y = Y[:, t, :]
                own(f"sr{t - 1}" if t else "ya7")
                V2.do(f"sk{t}", tt(out=heads_(ogf, 8), in0=heads_(XS[:, t, :], 8), in1=over(drow[:, :], 8, HD), op=ALU.mult))
                own(f"sk{t}")
                V2.do(f"sa{t}", tt(out=y, in0=y, in1=ogf, op=ALU.add))
                own(f"sa{t}")
                V2.do(f"sz{t}", tt(out=y, in0=y, in1=Z[:, t, :], op=ALU.mult))
                own(f"sz{t}")
                V2.do(f"sq{t}", tt(out=ogf, in0=y, in1=y, op=ALU.mult))
                own(f"sq{t}")
                V2.do(f"sr{t}", nc.vector.tensor_reduce(ys[:, 0, t, :], heads_(ogf, 2), AX.X, ALU.add))
            own("sr3")
            V2.do("sv", ts(ys[:, 1, :, :], ys[:, 0, :, :], 1.0 / 256, EPS_2, ALU.mult, ALU.add))
            own("sv")
            V2.do("si", nc.vector.reciprocal(ys[:, 0, :, :], ys[:, 1, :, :]))
            dve.wait_ge(s_twoa, A2.of("ss"))
            for t in range(TT):
                V2.do(f"sn{t}", tt(out=heads_(Y[:, t, :], 2), in0=heads_(Y[:, t, :], 2), in1=over(ys[:, 2, t, :], 2, 256), op=ALU.mult))

            def gated_residual(x, ps, g, at):
                dve.wait_ge(dve_out, at + (st("out2", "dve") - 1))
                tt(out=ogf, in0=ps, in1=g, op=ALU.mult).then_inc(res_steps, 1)
                dve.wait_ge(res_steps, at)
                stt(out=x, in0=x, scalar=ALPHA_2, in1=ogf, op0=ALU.mult, op1=ALU.add).then_inc(dve_out, 1)

            q0 = st("out2", "quarters")
            for n in range(8):
                h, t = n // 4, n % 4
                dve.wait_ge(quarters, q0 + n + 1)
                gated_residual(X[:, t, h * 512:(h + 1) * 512], G[t][:, :], gbc[:, h * 512:(h + 1) * 512], n + 1)
            layer_norm("out2", EPS_2)
            layer_norm("ln_ffn", EPS_2, src=X, dst=Hn, again=True)

            a0 = st("up2", "act")

            def taps(i, s):
                for m in range(4):
                    n = 4 * s + m
                    y = PT[:, m, :].rearrange("p (r c) -> p r c", c=GRID_W)
                    dve.wait_ge(act_out, i * 8 + (a0 + n + 1))
                    for x, tap in enumerate((0, 1, 2, 3, 5, 6, 7, 8)):
                        if x:
                            dve.wait_ge(conv_steps, i * 64 + 8 * n + x)
                        w = cols2[:, bass.ds(i * 80 + (C2["ffn"] + 40 * s + 10 * m + tap), 1)]
                        r, c = tap // 3, tap % 3
                        stt(out=y, in0=PADS[:, m, r:r + 8, c:c + GRID_W], scalar=w, in1=y, op0=ALU.mult, op1=ALU.add).then_inc(conv_steps, 1)
                    if m % 2:
                        dve.wait_ge(gelu_done, i * 4 + (2 * s + m // 2 + 1))
                        tt(out=wide[:, bass.ds(i * 4 + (2 * s + m // 2), 1), :].rearrange("p o n -> p (o n)"), in0=PT[:, m - 1, :], in1=PT[:, m, :], op=ALU.mult).then_inc(gated, 1)

            with dve.Fori(0, 5) as i:
                for s in range(2):
                    taps(i, s)
            taps(5, 0)
            q0 = st("down2", "quarters")
            with dve.Fori(0, 2) as n:
                for t in range(TT):
                    dve.wait_ge(quarters, n * 16 + (q0 + 12 + t + 1))
                    gated_residual(X[:, t, bass.ds(n * 512, 512)], G[t][:, :], gbc[:, bass.ds(n * 512 + 1024, 512)], n * 4 + (8 + t + 1))
            layer_norm("down2", EPS_2)

        @block.sync
        def _(sp):
            sp.dma_start(X[:, :, :], A["x"].rearrange("o (t p) d -> p (o t) d", p=P)).then_inc(s_x, 16)
            sp.dma_start(table[:, :], A["table"]).then_inc(s_const, 16)
            sp.dma_start(cols[:, :], A["cols"]).then_inc(s_const, 16)
            for s in range(2):
                sp.dma_start(ring[:, s, :], A["slabs"][s]).then_inc(slab_in[s], 16)
            with sp.Fori(1, N_SLABS // 2) as i:
                for s in range(2):
                    sp.wait_ge(quarters, i * 8 + (4 * s - 4))
                    sp.wait_ge(s_x, 16)
                    sp.dma_start(ring[:, s, :], A["slabs"][bass.ds(i * 2 + s, 1), :, :].rearrange("o p c -> p (o c)")).then_inc(slab_in[s], 16)
            if N_SLABS % 2:
                sp.wait_ge(quarters, 4 * (N_SLABS - 2))
                sp.dma_start(ring[:, 0, :], A["slabs"][N_SLABS - 1]).then_inc(slab_in[0], 16)
            sp.wait_ge(ln_dve, st.total["ln"])
            sp.dma_start(out.rearrange("o (t p) d -> p (o t) d", p=P), X[:, :, :]).then_inc(s_out, 16)
            sp.wait_ge(s_out, 16)

        @block.gpsimd
        def _(gp):
            gp.dma_start(w2[:, :, :, 0:HD], A["nsa_cmp_w2"].rearrange("o j (h p) d -> p (o j) h d", p=P)).then_inc(s_small_in, 16)
            gp.dma_start(w2[:, :, :, HD:P], A["nsa_cmp_w2"].rearrange("o j (h p) d -> p (o j) h d", p=P)).then_inc(s_small_in, 16)
            gp.dma_start(lamrow[:, :, :, :], A["diff_lambda"].rearrange("o (a b) d -> o (a b d)", a=2).partition_broadcast(P)
                         .rearrange("p o (a b d) -> p (o a) b d", a=2, b=2)).then_inc(s_small_in, 16)
            gp.dma_start(subln[:, :], A["diff_subln"].partition_broadcast(P).rearrange("p o d -> p (o d)")).then_inc(s_small_in, 16)
            gp.dma_start(cols2[:, :], A["cols2"]).then_inc(s_small_in, 16)

            def gain_bias(n, gain, bias):
                if n:
                    gp.wait_ge(ln_dve, 26 * n if n < 5 else st("ln_ffn", "ln"))
                gp.dma_start(rows[:, 0, :], gain.partition_broadcast(P)).then_inc(gb_in, 16)
                gp.dma_start(rows[:, 1, :], bias.partition_broadcast(P)).then_inc(gb_in, 16)

            gain_bias(0, A["ln_gain"][0, 0, :], A["ln_bias"][0, 0, :])

            gp.wait_ge(s_const, CONSTS)
            for r, (g, *_) in enumerate(ROPED0):
                gp.wait_ge(act_out, st("proj0", "act") + g + 1)
                if r >= 2:
                    gp.wait_ge(rope_dve, 2 * (r - 2) + 2)
                nc.gpsimd.tensor_tensor(out=SC[:, 0, 2 + r % 2, :], in0=SC[:, 0, r % 2, :], in1=tab("cos"),
                                        op=ALU.mult).then_inc(rope_cos, 1)

            gp.wait_ge(act_out, st("proj0", "act") + 24)
            gp.wait_ge(quarters, 24)
            for j in range(2):
                for g in range(2):
                    src = KTT[g * HD:(g + 1) * HD, 4 + j, :]
                    gp.dma_start(XT[0:HD, 2 * j + g, :], src).then_inc(cmp_in, 16)
                    gp.dma_start(XT[HD:P, 2 * j + g, 0:S - 1], src[:, 1:S]).then_inc(cmp_in, 16)
            gp.wait_ge(rope_dve, 2 * len(ROPED0))
            for kind in range(2):
                for g in range(2):
                    gp.dma_start(KSW[:, kind, g, :], KTT[g * HD:(g + 1) * HD, 6 + kind, :]).then_inc(ksw_in, 16)

            def tile(ap):
                return ap.rearrange("p o n -> p (o n)")

            def feed(name, n_iter, n, loads, lead=None):
                def unit(i, j):
                    u0 = st(name, "units")
                    aps = [(d, s) for d, s in loads(i, j)]
                    for d, s in aps:
                        gp.dma_start(d, s).then_inc(qk_in[j % 2], 16)
                for j in range(2):
                    if st(name, "units"):
                        gp.wait_ge(sc_ready, 4 * (st(name, "units") + j - 1))
                    unit(0, j)
                for j in range(2, n):
                    gp.wait_ge(sc_ready, 4 * (st(name, "units") + j - 1))
                    unit(0, j)
                with gp.Fori(1, n_iter) as i:
                    for j in range(n):
                        gp.wait_ge(sc_ready, i * (4 * n) + 4 * (st(name, "units") + j - 1))
                        unit(i, j)

            feed("diff", 4, 2, lambda i, c: [
                (qb[0:HD, c, :], tile(QT[c * HD:(c + 1) * HD, bass.ds(i, 1), :])),
                (kb[0:HD, c, :], tile(KTT[c * HD:(c + 1) * HD, bass.ds(i, 1), :]))])
            feed("nsa", 2, 8, lambda r, j: [
                (qb[0:HD, j % 2, :], tile(QT[((j // 2) % 2) * HD:((j // 2) % 2) * HD + HD, bass.ds(r + (4 + 2 * (j // 4)), 1), :]))])

            gp.wait_ge(gb_in, 32)
            gain_bias(1, A["ln_gain"][0, 1, :], A["ln_bias"][0, 1, :])

            gp.wait_ge(s_small, SMALL["fox"])
            gp.wait_ge(s_small_in, SMALL_INPUTS)
            gp.dma_start(A["crow"], crow[:, 1:3, :]).then_inc(crow_in, 16)
            gp.wait_ge(crow_in, 16)
            for e in range(2):
                gp.dma_start(qb[HD:HD + 1, e, :], A["ones"][0:1, :]).then_inc(crow_in, 16)
                gp.dma_start(kb[HD + 1:HD + 2, e, :], A["ones"][1:2, :]).then_inc(crow_in, 16)
            gp.wait_ge(act_out, st("proj1", "act") + 16)
            feed("fox", 8, 2, lambda i, e: [
                (qb[0:HD, e, :], tile(QT[e * HD:(e + 1) * HD, bass.ds(i, 1), :])),
                (kb[0:HD, e, :], tile(KTT[e * HD:(e + 1) * HD, bass.ds(i, 1), :])),
                (qb[HD + 1:HD + 2, e, :], A["crow"][bass.ds(i * 2 + e, 1), 1, :]),
                (kb[HD:HD + 1, e, :], A["crow"][bass.ds(i * 2 + e, 1), 0, :])])
            gain_bias(2, A["ln_gain"][1, 0, :], A["ln_bias"][1, 0, :])
            gp.wait_ge(o_used, 40)
            gp.wait_ge(pt_ready, 160)

            def ada_load(i, j, h, first=False):
                if not first:
                    gp.wait_ge(ada_steps, i * 32 + 8 * j - (4 if h == 0 else 0))
                src = A["ada"][bass.ds(i * 3 + j, 1) if j < 3 else bass.ds(i, 1), :, h * 2048:(h + 1) * 2048]
                gp.dma_start(ADW(h), src.rearrange("o p c -> p (o c)")).then_inc(ada_in[h], 16)

            for j in range(4):
                for h in range(2):
                    ada_load(0, j, h, j == 0)
            with gp.Fori(1, 4) as i:
                for j in range(4):
                    for h in range(2):
                        ada_load(i, j, h)
            gain_bias(3, A["ln_gain"][1, 1, :], A["ln_bias"][1, 1, :])
            gpsimd_second(gp, gain_bias)

        def pe_attend(pe, name, n_iter, n, depth, q_of, k_of, v_of, hd, per_slot):
            u0 = st(name, "units")
            in0 = LOADS[name]

            def scores(i, j):
                e = j % 2
                pe.wait_ge(qk_in[e], in0 + i * (per_slot * 16 * (n // 2)) + per_slot * 16 * (j // 2 + 1))
                for t in range(TT):
                    if name != "diff" or not isinstance(i, int) or i or 4 * j + t >= 2:
                        pe.wait_ge(sc_used, i * (4 * n) + 4 * (u0 + j) + t - 1)
                    nc.tensor.matmul(G[t % 2][:, 0:(t + 1) * P], lhsT=q_of(i, j)[0:depth, t * P:(t + 1) * P],
                                     rhs=k_of(i, j)[0:depth, 0:(t + 1) * P], start=True, stop=True).then_inc(sc_ready, 1)

            def values(i, j):
                e = j % 2
                u = 4 * (u0 + j)

                def transposes(t):
                    pe.wait_ge(pr_ready, i * (4 * n) + u + t + 1)
                    if t >= 2:
                        pe.wait_ge(pt_dve, i * (3 * n) + 3 * (u0 + j) + t - 1)
                    elif not (name == "diff" and isinstance(i, int) and i == 0 and j == 0):
                        if t == 0:
                            pe.wait_ge(pt_dve, i * (3 * n) + 3 * (u0 + j))
                        else:
                            pe.wait_ge(pt_act, i * n + u0 + j)
                    for b in range(t + 1):
                        mm = nc.tensor.transpose(TR[t % 2][:, b * P:(b + 1) * P], SC[:, e, t, b * P:(b + 1) * P], ident)
                    mm.then_inc(pt_ready, 1)

                def products(t):
                    if t < 3:
                        pe.wait_ge(pt_dve, i * (3 * n) + 3 * (u0 + j) + t + 1)
                    else:
                        pe.wait_ge(pt_act, i * n + u0 + j + 1)
                    if t == 0 and not (name == "diff" and isinstance(i, int) and i == 0 and j < 2):
                        pe.wait_ge(o_used, i * n + u0 + j - 1)
                    for b in range(t + 1):
                        mm = nc.tensor.matmul(OB[e][:, t * hd:(t + 1) * hd], lhsT=PT[:, t, b * P:(b + 1) * P],
                                              rhs=v_of(i, j, b), start=(b == 0), stop=(b == t))
                    mm.then_inc(pv_ready, 1)

                transposes(0)
                for t in range(1, TT):
                    transposes(t)
                    products(t - 1)
                products(TT - 1)

            scores(0, 0)
            start = 0 if u0 else 1
            for j in range(n * start):
                scores(*((0, j + 1) if j + 1 < n else (1, 0)))
                values(0, j)
            with pe.Fori(start, n_iter - 1) as i:
                for j in range(n):
                    scores(*((i, j + 1) if j + 1 < n else (i + 1, 0)))
                    values(i, j)
            for j in range(n):
                if j + 1 < n:
                    scores(n_iter - 1, j + 1)
                values(n_iter - 1, j)

        def act_attend(act, name, n_iter, n):
            u0 = st(name, "units")

            def exps(i, j):
                e = j % 2
                for t in range(TT):
                    act.wait_ge(sc_used, i * (4 * n) + 4 * (u0 + j) + t + 1)
                    if t == 0 and not (name == "diff" and isinstance(i, int) and i == 0 and j < 2):
                        act.wait_ge(o_used, i * n + u0 + j - 1)
                    nc.scalar.activation(SC[:, e, t, 0:(t + 1) * P], SC[:, e, t, 0:(t + 1) * P], ACT.Exp,
                                         scale=-1.0, bias=mn[:, e, t:t + 1], accum_out=sm[:, e, t:t + 1]).then_inc(pr_ready, 1)

            def copy(i, j):
                act.wait_ge(pt_ready, i * (4 * n) + 4 * (u0 + j) + 4)
                nc.scalar.activation(PT[:, 3, :], TR[1][:, :], ACT.Copy).then_inc(pt_act, 1)

            exps(0, 0)
            start = 0 if u0 else 1
            for j in range(n * start):
                exps(*((0, j + 1) if j + 1 < n else (1, 0)))
                copy(0, j)
            with act.Fori(start, n_iter - 1) as i:
                for j in range(n):
                    exps(*((i, j + 1) if j + 1 < n else (i + 1, 0)))
                    copy(i, j)
            for j in range(n):
                if j + 1 < n:
                    exps(n_iter - 1, j + 1)
                copy(n_iter - 1, j)

        def dve_attend(dve, name, n_iter, n, hd, finish):
            u0 = st(name, "units")
            step0, per = STEP0[name], STEPS[name]

            def mins(i, j):
                e = j % 2
                for t in range(TT):
                    if t == 0 and not (name == "diff" and isinstance(i, int) and i == 0 and j < 2):
                        dve.wait_ge(pt_ready, i * (4 * n) + 4 * (u0 + j - 1))
                    dve.wait_ge(sc_ready, i * (4 * n) + 4 * (u0 + j) + t + 1)
                    dve.sem_inc(sc_seen, 1)
                    a, b = where["causal"]
                    nc.vector.tensor_tensor_reduce(
                        out=SC[:, e, t, 0:(t + 1) * P], in0=G[t % 2][:, 0:(t + 1) * P], in1=table[:, b - (t + 1) * P:b],
                        scale=1.0, scalar=3.0e38, op0=ALU.add, op1=ALU.min, accum_out=mn[:, e, t:t + 1]).then_inc(sc_used, 1)

            def rest(i, j):
                e = j % 2
                for t in range(3):
                    if t == 0 and not (name == "diff" and isinstance(i, int) and i == 0 and j == 0):
                        dve.wait_ge(pv_ready, i * (4 * n) + 4 * (u0 + j))
                    dve.wait_ge(pt_ready, i * (4 * n) + 4 * (u0 + j) + t + 1)
                    nc.vector.tensor_copy(PT[:, t, 0:(t + 1) * P], TR[t % 2][:, 0:(t + 1) * P]).then_inc(pt_dve, 1)
                at = i * per[n] + (step0 + per[j])
                dve.wait_ge(pr_ready, i * (4 * n) + 4 * (u0 + j) + 4)
                nc.vector.reciprocal(rs[:, e, :], sm[:, e, :]).then_inc(o_steps, 1)
                dve.wait_ge(pv_ready, i * (4 * n) + 4 * (u0 + j) + 4)
                dve.wait_ge(o_steps, at + 1)
                finish(i, j, at + 1)

            mins(0, 0)
            start = 0 if u0 else 1
            for j in range(n * start):
                mins(*((0, j + 1) if j + 1 < n else (1, 0)))
                rest(0, j)
            with dve.Fori(start, n_iter - 1) as i:
                for j in range(n):
                    mins(*((i, j + 1) if j + 1 < n else (i + 1, 0)))
                    rest(i, j)
            for j in range(n):
                if j + 1 < n:
                    mins(n_iter - 1, j + 1)
                rest(n_iter - 1, j)

        @block.tensor
        def _(pe):
            def slab_wait(s, pairs=0):
                pe.wait_ge(slab_in[s % 2], pairs * 16 + 16 * (s // 2 + 1))

            def stage_start(stage):
                a = st.before[stage].get("act", 0)
                v = st.before[stage].get("dve", 0)
                if a:
                    pe.wait_ge(act_out, a)
                if v:
                    pe.wait_ge(dve_out, v)

            def transposes(stage, src, ready):
                base = st(stage, "tr")
                for t in range(TT):
                    ready(t)
                    for h in range(2):
                        n = base + 2 * t + h
                        if n >= 2:
                            pe.wait_ge(tr_out, n - 1)
                        for b in range(4):
                            c = (4 * h + b) * P
                            mm = nc.tensor.transpose(TR[h][:, b * P:(b + 1) * P], src[:, t, c:c + P], ident)
                        mm.then_inc(tr_ready, 1)

            def token_groups(stage, s, bank0, half, pos):
                for t in range(TT):
                    if bank0 + t >= 4:
                        pe.wait_ge(dve_out, st(stage, "dve") + bank0 + t - 3)
                    for k in range(KT):
                        mm = nc.tensor.matmul(G[t][:, :], lhsT=XT[:, k, t * P:(t + 1) * P], rhs=slab(s)[:, k, :],
                                              start=(k == 0), stop=(k == KT - 1))
                    mm.then_inc(quarters, 1)

            def out_products(stage, tr_stage):
                stage_start(stage)
                pe.wait_ge(tr_out, st(tr_stage, "tr") + 8)
                s = st(stage, "quarters") // 4
                for h in range(2):
                    slab_wait(s + h)
                    token_groups(stage, s + h, 4 * h, h, 0)

            def ada_sums(i, j):
                pe.wait_ge(ada_steps, i * 32 + 8 * (j + 1))
                at = 12 * i + 4 * j if j < 3 else 48 + 4 * i
                for q in range(4):
                    col = (i * 12 + (4 * j + q)) if j < 3 else (i * 4 + (48 + q))
                    mm = nc.tensor.matmul(OB[0][:, bass.ds(col, 1)], lhsT=qb[:, j % 2, q * P:(q + 1) * P], rhs=ones[:, 0:1],
                                          start=True, stop=True)
                mm.then_inc(ada_cols, 1)

            def mlp_products(up, down, tr_stage, ada=False):
                stage_start(up)
                pe.wait_ge(tr_out, st(tr_stage, "tr") + 8)
                s0 = st(up, "quarters") // 4
                a0 = st(up, "act")
                with pe.Fori(0, 4) as i:
                    for s in range(2):
                        slab_wait(s0 + s, i)
                        for m in range(4):
                            pe.wait_ge(act_out, i * 8 + (a0 + 4 * s + m - 3))
                            for k in range(KT):
                                mm = nc.tensor.matmul(G[m][:, :], lhsT=slab(s0 + s)[:, k, m * P:(m + 1) * P], rhs=XT[:, k, :],
                                                      start=(k == 0), stop=(k == KT - 1))
                            mm.then_inc(quarters, 1)
                            if ada and m % 2:
                                ada_sums(i, (4 * s + m) // 2)
                stage_start(down)
                s0 = st(down, "quarters") // 4
                v0 = st(down, "dve")
                q0 = st(up, "squares")
                with pe.Fori(0, 2) as n:
                    for kb_ in range(4):
                        slab_wait(s0 + kb_, n * 2)
                        for t in range(TT):
                            if kb_ == 0:
                                pe.wait_ge(dve_out, n * 4 + (v0 + t - 3))
                            for k in range(KT):
                                if t == 0:
                                    pe.wait_ge(squared, q0 + 8 * kb_ + k + 1)
                                mm = nc.tensor.matmul(G[t][:, :], lhsT=wide[:, 8 * kb_ + k, t * P:(t + 1) * P], rhs=slab(s0 + kb_)[:, k, :],
                                                      start=(kb_ == 0 and k == 0), stop=(kb_ == 3 and k == KT - 1))
                            mm.then_inc(quarters, 1)

            pe.wait_ge(s_const, CONSTS)
            transposes("x0", X, lambda t: pe.wait_ge(s_x, 16))

            pe.wait_ge(tr_out, 8)
            roped = {g: r for r, (g, *_) in enumerate(ROPED0)}

            def rope_swap(g):
                r = roped[g]
                pe.wait_ge(act_out, g + 1)
                if r >= 2:
                    pe.wait_ge(rope_dve, 2 * (r - 2) + 1)
                else:
                    pe.wait_ge(tr_out, 8)
                nc.tensor.matmul(TR[r % 2][:, :], lhsT=tab("swap"), rhs=SC[:, 0, r % 2, :], start=True, stop=True).then_inc(rope_swapped, 1)

            for g in range(24):
                if g % 4 == 0:
                    slab_wait(g // 4)
                if g >= 4:
                    pe.wait_ge(act_out, g - 3)
                kind, cols_, _ = GROUPS0[g]
                for k in range(KT):
                    w = slab(g // 4)[:, k, cols_[0]:cols_[1]]
                    if kind == "F":
                        mm = nc.tensor.matmul(G[g % 4][:, :], lhsT=w, rhs=XT[:, k, :], start=(k == 0), stop=(k == KT - 1))
                    else:
                        t = g % 4
                        mm = nc.tensor.matmul(G[g % 4][:, 0:cols_[1] - cols_[0]], lhsT=XT[:, k, t * P:(t + 1) * P], rhs=w,
                                              start=(k == 0), stop=(k == KT - 1))
                mm.then_inc(quarters, 1)
                if g - 1 in roped:
                    rope_swap(g - 1)
            if 23 in roped:
                rope_swap(23)

            a0 = st("cmp", "act")
            pe.wait_ge(act_out, 24)
            for j in range(2):
                pe.wait_ge(s_small, SMALL["windows"] + j + 1)
                slab_wait(6 + j)
                for h in range(2):
                    for m in range(16):
                        mm = nc.tensor.matmul(G[2 * j + h][:, 0:62], lhsT=ring[:, j, m * 256 + h * P:m * 256 + (h + 1) * P],
                                              rhs=WIN(j)[:, m, :], start=(m == 0), stop=(m == 15))
                    mm.then_inc(quarters, 2)
            pe.wait_ge(s_small, SMALL["gelu"])
            pe.wait_ge(s_small_in, SMALL_INPUTS)
            pe.wait_ge(rope_dve, 2 * len(ROPED0))
            for h in range(2):
                mm = nc.tensor.matmul(TR[0][:, 0:62], lhsT=w2[:, 0, h, :], rhs=hc2[:, h, :], start=(h == 0), stop=(h == 1))
            mm.then_inc(s_smallp, 1)
            for g in range(2):
                for h in range(2):
                    mm = nc.tensor.matmul(TR[1][0:N_CMP, g * HD:(g + 1) * HD], lhsT=hc2[:, 2 + h, g * N_CMP:(g + 1) * N_CMP],
                                          rhs=w2[:, 1, h, 0:HD], start=(h == 0), stop=(h == 1))
            mm.then_inc(s_smallp, 1)
            pe.wait_ge(s_small, SMALL["kraw"])
            nc.tensor.matmul(TR[0][:, 0:62], lhsT=tab("swap"), rhs=kcc[:, 0, :], start=True, stop=True).then_inc(s_smallp, 1)
            pe.wait_ge(s_small, SMALL["krope"])
            for h in range(8):
                r = (h % 2) * HD
                for t in range(TT):
                    c = (h // 2) * P + t * 32
                    mm = nc.tensor.matmul(G[h % 2][:, c:c + N_CMP], lhsT=QT[r:r + HD, 4 + h // 2, t * P:(t + 1) * P],
                                          rhs=kcc[r:r + HD, 1, (h // 4) * N_CMP:(h // 4 + 1) * N_CMP], start=True, stop=True)
                if h >= 6:
                    mm.then_inc(s_smallp, 1)
            for h in range(8):
                pe.wait_ge(s_small, SMALL["pcmp"])
                if h >= 2:
                    pe.wait_ge(s_smalla, SMALLA["ptc"] + h - 1)
                for t in range(TT):
                    mm = nc.tensor.transpose(TR[h % 2][0:N_CMP, t * P:(t + 1) * P], PC[:, h, t, 0:N_CMP], ident)
                mm.then_inc(s_smallp, 1)
                pe.wait_ge(s_smalla, SMALLA["ptc"] + h + 1)
                if h >= 2:
                    pe.wait_ge(s_small, SMALL["pcmp"] + h - 1)
                for t in range(TT):
                    mm = nc.tensor.matmul(OB[h % 2][:, t * HD:(t + 1) * HD], lhsT=PT[0:N_CMP, h % 2, t * P:(t + 1) * P],
                                          rhs=vcc[:, h // 4, :], start=True, stop=True)
                mm.then_inc(s_smallp, 1)

            pe.wait_ge(s_small, SMALL["pcmp"] + 8)
            pe_attend(pe, "diff", 4, 2, HD, lambda i, j: qb[:, j % 2, :], lambda i, j: kb[:, j % 2, :],
                      lambda i, j, b: V[:, b, bass.ds(i * P, P)] if not isinstance(i, int) else V[:, b, i * P:(i + 1) * P], P, 2)
            pe.wait_ge(ksw_in, 64)
            pe_attend(pe, "nsa", 2, 8, HD, lambda i, j: qb[:, j % 2, :], lambda i, j: KSW[:, j % 2, j // 4, :],
                      lambda i, j, b: V[:, b, 512 + (j % 2) * P + (j // 4) * HD:512 + (j % 2) * P + (j // 4) * HD + HD], HD, 1)

            transposes("mixed0", O, lambda t: pe.wait_ge(s_small, SMALL["rms"] + 2 * (t + 1)))
            out_products("out0", "mixed0")
            transposes("x1", X, lambda t: pe.wait_ge(ln_dve, 14 + 3 * (t + 1)))
            mlp_products("up0", "down0", "x1")
            transposes("x2", X, lambda t: pe.wait_ge(ln_dve, 26 + 14 + 3 * (t + 1)))

            stage_start("proj1")
            pe.wait_ge(tr_out, st("x2", "tr") + 8)
            s0, a0 = st("proj1", "quarters") // 4, st("proj1", "act")
            for g in range(25):
                if g % 4 == 0:
                    slab_wait(s0 + g // 4)
                if g >= 4:
                    pe.wait_ge(act_out, a0 + g - 3)
                sl = slab(s0 + g // 4)
                for k in range(KT):
                    if g < 16:
                        mm = nc.tensor.matmul(G[g % 4][:, :], lhsT=sl[:, k, (g % 4) * P:(g % 4 + 1) * P], rhs=XT[:, k, :],
                                              start=(k == 0), stop=(k == KT - 1))
                    elif g < 24:
                        t = g % 4
                        mm = nc.tensor.matmul(G[t][:, :], lhsT=XT[:, k, t * P:(t + 1) * P], rhs=sl[:, k, :],
                                              start=(k == 0), stop=(k == KT - 1))
                    else:
                        mm = nc.tensor.matmul(G[0][0:16, :], lhsT=sl[:, k, 0:16], rhs=XT[:, k, :],
                                              start=(k == 0), stop=(k == KT - 1))
                mm.then_inc(quarters, 4 if g == 24 else 1)
            pe.wait_ge(act_out, a0 + 25)
            pe.wait_ge(tr_out, st("x2", "tr") + 8)
            pe.wait_ge(crow_in, 80)
            pe_attend(pe, "fox", 8, 2, HD + 2, lambda i, j: qb[:, j % 2, :], lambda i, j: kb[:, j % 2, :],
                      lambda i, j, b: V[:, b, bass.ds(i * P + j * HD, HD)] if not isinstance(i, int) else V[:, b, i * P + j * HD:i * P + (j + 1) * HD], HD, 4)
            transposes("mixed1", O, lambda t: pe.wait_ge(o_used, st("fox", "units") + 16))
            out_products("out1", "mixed1")
            transposes("x3", X, lambda t: pe.wait_ge(ln_dve, 52 + 14 + 3 * (t + 1)))
            mlp_products("up1", "down1", "x3", ada=True)
            tensor_second(pe, stage_start, slab_wait, transposes, out_products)

        @block.scalar
        def _(act):
            def copies(stage):
                base = st(stage, "tr")
                for n in range(8):
                    act.wait_ge(tr_ready, base + n + 1)
                    t, h = n // 2, n % 2
                    nc.scalar.activation(XT[:, 4 * h:4 * h + 4, t * P:(t + 1) * P], TR[h][:, :].rearrange("p (b c) -> p b c", b=4),
                                         ACT.Copy).then_inc(tr_out, 1)

            def deviation(stage, steps=14):
                act.wait_ge(ln_dve, st(stage, "ln") + steps)
                nc.scalar.activation(rstd[:, 2, :], rstd[:, 1, :], ACT.Sqrt).then_inc(ln_std, 1)

            def relu(up):
                a0, q0 = st(up, "act"), st(up, "quarters")
                with act.Fori(0, 4) as i:
                    for g in range(8):
                        act.wait_ge(quarters, i * 8 + (q0 + g + 1))
                        nc.scalar.activation(wide[:, bass.ds(i * 8 + g, 1), :], G[g % 4][:, :].unsqueeze(1), ACT.Relu).then_inc(act_out, 1)

            act.wait_ge(s_const, CONSTS)
            copies("x0")
            r = 0
            for g in range(24):
                kind, c, (dst, scale) = GROUPS0[g]
                act.wait_ge(quarters, g + 1)
                if dst is None:
                    if r >= 2:
                        act.wait_ge(rope_swapped, r - 1)
                        act.wait_ge(rope_cos, r - 1)
                    dst_ap, r = SC[:, 0, r % 2, :], r + 1
                else:
                    dst_ap = KTT[:, dst[1], :] if dst[0] == "K" else V[:, dst[1], dst[2]:dst[3]]
                nc.scalar.activation(dst_ap, G[g % 4][:, 0:dst_ap.free_size()], ACT.Copy, scale=scale).then_inc(act_out, 1)
            act.wait_ge(s_small, SMALL["lam"])
            nc.scalar.activation(lam[:, 2:4], lam[:, 0:2], ACT.Exp).then_inc(s_smalla, 1)
            act.wait_ge(act_out, 24)
            nc.scalar.activation(gate[:, :, :], V[:, :, 768:792], ACT.Exp, scale=-1.0).then_inc(s_smalla, 1)
            for n in range(4):
                act.wait_ge(quarters, 24 + 2 * (n + 1))
                nc.scalar.activation(hc[:, n, :], G[n][:, 0:62], ACT.Identity, bias=cols[:, n:n + 1]).then_inc(act_out, 1)
            act.wait_ge(s_small, SMALL["gelu_in"])
            nc.scalar.activation(SC[:, 1, 2, 0:248], SC[:, 1, 1, 0:248], ACT.Tanh, scale=math.sqrt(2 / math.pi)).then_inc(s_smalla, 1)
            act.wait_ge(s_small, SMALL["scmp"])
            nc.scalar.activation(PC[:, :, :, :], PC[:, :, :, :], ACT.Exp, scale=-1.0).then_inc(s_smalla, 1)
            for h in range(8):
                act.wait_ge(s_smallp, 6 + 2 * h)
                if h >= 2:
                    act.wait_ge(s_smallp, 7 + 2 * (h - 2))
                nc.scalar.activation(PT[0:N_CMP, h % 2, :], TR[h % 2][0:N_CMP, :], ACT.Copy).then_inc(s_smalla, 1)
            act.wait_ge(s_smallp, 21)
            act_attend(act, "diff", 4, 2)
            act_attend(act, "nsa", 2, 8)
            act.wait_ge(s_small, SMALL["rms"])
            nc.scalar.activation(rmsq[:, 1, :], rmsq[:, 0, :], ACT.Sqrt).then_inc(s_smalla, 1)
            copies("mixed0")
            deviation("out0")
            copies("x1")
            relu("up0")
            deviation("down0")
            copies("x2")
            a0, q0 = st("proj1", "act"), st("proj1", "quarters")
            for g in range(25):
                act.wait_ge(quarters, q0 + (g + 1 if g < 24 else 28))
                if g < 8:
                    o, i_, sc_ = KTT[:, g, :], G[g % 4][:, :], 1.0
                elif g < 16:
                    o, i_, sc_ = QT[:, g - 8, :], G[g % 4][:, :], -0.125
                elif g < 24:
                    o, i_, sc_ = V[:, g % 4, ((g - 16) // 4) * 512:((g - 16) // 4 + 1) * 512], G[g % 4][:, :], 1.0
                else:
                    o, i_ = crow[:, 0, :], G[0][0:16, :]
                    nc.scalar.activation(o, i_, ACT.Identity, bias=cols[0:16, 4:5]).then_inc(act_out, 1)
                    continue
                nc.scalar.activation(o, i_, ACT.Copy, scale=sc_).then_inc(act_out, 1)
            act.wait_ge(s_small, SMALL["fabs"])
            nc.scalar.activation(crow[:, 2, :], crow[:, 1, :], ACT.Exp, scale=-1.0).then_inc(s_smalla, 1)
            act.wait_ge(s_smalla, SMALLA["fexp"])
            nc.scalar.activation(crow[:, 1, :], crow[:, 2, :], ACT.Ln, bias=1.0).then_inc(s_smalla, 1)
            act_attend(act, "fox", 8, 2)
            act.wait_ge(s_small_in, SMALL_INPUTS)
            nc.scalar.activation(csil[:, 0, :, :].rearrange("p a k -> p (a k)"), cols2[:, 0:16], ACT.Exp, scale=-1.0).then_inc(s_smalla, 1)
            copies("mixed1")
            deviation("out1")
            copies("x3")
            relu("up1")
            deviation("down1")
            scalar_second(act, copies, deviation)

        @block.vector
        def _(dve):
            small = [0]

            def step(ins, wait=True):
                small[0] += 1
                ins.then_inc(s_small, 1)
                if wait:
                    dve.wait_ge(s_small, small[0])

            def mark(name, add=0):
                assert SMALL[name] == small[0] + add, (name, SMALL[name], small[0] + add)

            def residual(stage, alpha):
                q0 = st(stage, "quarters")
                for h in range(2):
                    for t in range(TT):
                        dve.wait_ge(quarters, q0 + 4 * h + t + 1)
                        nc.vector.scalar_tensor_tensor(out=X[:, t, h * 512:(h + 1) * 512], in0=X[:, t, h * 512:(h + 1) * 512], scalar=alpha,
                                                       in1=G[t][:, :], op0=ALU.mult, op1=ALU.add).then_inc(dve_out, 1)

            def ada_job(i, j):
                a = qb[:, j % 2, :]
                if not (isinstance(i, int) and 4 * i + j < 2):
                    dve.wait_ge(ada_cols, i * 4 + (j - 1))
                for k in range(KT):
                    if k % 4 == 0:
                        dve.wait_ge(ada_in[k // 4], i * 64 + 16 * (j + 1))
                    w = SC[:, k // 4, k % 4, :]
                    c = csil[:, 1, 0 if j < 3 else 1, k:k + 1]
                    if k == 0:
                        nc.vector.tensor_scalar(a, w, c, None, ALU.mult).then_inc(ada_steps, 1)
                    else:
                        dve.wait_ge(ada_steps, i * 32 + 8 * j + k)
                        nc.vector.scalar_tensor_tensor(out=a, in0=w, scalar=c, in1=a, op0=ALU.mult, op1=ALU.add).then_inc(ada_steps, 1)

            def mlp(up, down, alpha, ada=False):
                a0, q0 = st(up, "act"), st(down, "quarters")

                def squares(i):
                    for g in range(8):
                        dve.wait_ge(act_out, i * 8 + (a0 + g + 1))
                        h = wide[:, bass.ds(i * 8 + g, 1), :]
                        nc.vector.tensor_tensor(out=h, in0=h, in1=h, op=ALU.mult).then_inc(squared, 1)
                        if ada and g % 2 == 0:
                            ada_job(i, g // 2)

                if ada:
                    squares(0)
                with dve.Fori(1 if ada else 0, 4) as i:
                    squares(i)
                with dve.Fori(0, 2) as n:
                    for t in range(TT):
                        dve.wait_ge(quarters, n * 16 + (q0 + 12 + t + 1))
                        x = X[:, t, bass.ds(n * 512, 512)]
                        nc.vector.scalar_tensor_tensor(out=x, in0=x, scalar=alpha, in1=G[t][:, :],
                                                       op0=ALU.mult, op1=ALU.add).then_inc(dve_out, 1)

            norms = [0]

            def layer_norm(stage, eps, n_tiles=TT, src=X, dst=None, again=False):
                b = st(stage, "ln")
                for t in range(n_tiles):
                    if (stage, "dve") in st.base:
                        dve.wait_ge(dve_out, st(stage, "dve") + 4 + t + 1)
                    elif again and t == 0:
                        dve.wait_ge(ln_dve, b)
                    for h in range(2):
                        nc.vector.bn_stats(stat[:, t, h, :], src[:, t, h * 512:(h + 1) * 512]).then_inc(ln_dve, 1)
                for t in range(n_tiles):
                    dve.wait_ge(ln_dve, b + 2 * t + 2)
                    nc.vector.bn_aggr(agg[:, t, :], stat[:, t, :, :]).then_inc(ln_dve, 1)
                b += 3 * n_tiles
                dve.wait_ge(ln_dve, b)
                nc.vector.tensor_scalar(rstd[:, 0, :], agg[:, :, 1], eps, None, ALU.add).then_inc(ln_dve, 1)
                dve.wait_ge(ln_dve, b + 1)
                nc.vector.reciprocal(rstd[:, 1, :], rstd[:, 0, :]).then_inc(ln_dve, 1)
                b += 2
                dve.wait_ge(ln_std, st(stage, "std") + 1)
                if dst is None:
                    norms[0] += 1
                    dve.wait_ge(gb_in, 32 * norms[0])
                for t in range(n_tiles):
                    nc.vector.tensor_scalar((src if dst is None else dst)[:, t, :], src[:, t, :], agg[:, t, 0:1], rstd[:, 2, t:t + 1],
                                            ALU.subtract, ALU.mult).then_inc(ln_dve, 1)
                    if dst is None:
                        dve.wait_ge(ln_dve, b + 3 * t + 1)
                        nc.vector.tensor_tensor(out=X[:, t, :], in0=X[:, t, :], in1=rows[:, 0, :], op=ALU.mult).then_inc(ln_dve, 1)
                        dve.wait_ge(ln_dve, b + 3 * t + 2)
                        nc.vector.tensor_tensor(out=X[:, t, :], in0=X[:, t, :], in1=rows[:, 1, :], op=ALU.add).then_inc(ln_dve, 1)

            dve.wait_ge(s_const, CONSTS)
            dve.wait_ge(s_small_in, SMALL_INPUTS)
            step(nc.vector.tensor_tensor(out=lamrow[:, :, 0, :], in0=lamrow[:, :, 0, :], in1=lamrow[:, :, 1, :], op=ALU.mult))
            step(nc.vector.tensor_reduce(lam[:, 0:2], lamrow[:, :, 0, :], AX.X, ALU.add))
            mark("lam")
            step(nc.vector.tensor_scalar(subln[:, :], subln[:, :], 1.0 - LAM_INIT, None, ALU.mult))

            for r, (g, *dst) in enumerate(ROPED0):
                which, idx = dst
                o = (QT if which == "q" else KTT)[:, idx, :]
                dve.wait_ge(rope_swapped, r + 1)
                if r >= 2:
                    dve.wait_ge(rope_dve, 2 * (r - 2) + 2)
                nc.vector.tensor_tensor(out=SC[:, 1, r % 2, :], in0=TR[r % 2][:, :], in1=tab("sin"), op=ALU.mult).then_inc(rope_dve, 1)
                dve.wait_ge(rope_cos, r + 1)
                dve.wait_ge(rope_dve, 2 * r + 1)
                nc.vector.tensor_tensor(out=o, in0=SC[:, 0, 2 + r % 2, :], in1=SC[:, 1, r % 2, :], op=ALU.add).then_inc(rope_dve, 1)
            dve.wait_ge(rope_dve, 2 * len(ROPED0))
            dve.wait_ge(s_smalla, 2)
            step(nc.vector.tensor_tensor(out=lam[:, 4:5], in0=lam[:, 3:4], in1=lam[:, 2:3], op=ALU.subtract))
            step(nc.vector.tensor_scalar(lam[:, 5:6], lam[:, 4:5], -LAM_INIT, None, ALU.add))
            step(nc.vector.tensor_scalar(gate[:, :, :], gate[:, :, :], 1.0, None, ALU.add))
            step(nc.vector.reciprocal(gate[:, :, :], gate[:, :, :]))
            mark("windows")
            dve.wait_ge(cmp_in, 128)
            for j in range(2):
                for g in range(2):
                    src = XT[:, 2 * j + g, :]
                    for m in range(16):
                        ins = nc.vector.tensor_scalar(WIN(j)[:, m, g * N_CMP:(g + 1) * N_CMP], src[:, 2 * m:2 * m + 16 * 30 + 1:16],
                                                      cols[:, 5 + 16 * j + m:6 + 16 * j + m], None, ALU.add)
                step(ins, wait=False)
            dve.wait_ge(act_out, 28)
            x_ = hc[:, :, :].rearrange("p a b -> p (a b)")
            a_, b_ = SC[:, 1, 0, 0:248], SC[:, 1, 1, 0:248]
            step(nc.vector.tensor_tensor(out=a_, in0=x_, in1=x_, op=ALU.mult))
            step(nc.vector.tensor_scalar(a_, a_, 0.044715, 1.0, ALU.mult, ALU.add))
            step(nc.vector.tensor_tensor(out=b_, in0=a_, in1=x_, op=ALU.mult))
            mark("gelu_in")
            dve.wait_ge(s_smalla, 3)
            step(nc.vector.tensor_scalar(a_, SC[:, 1, 2, 0:248], 1.0, 0.5, ALU.add, ALU.mult))
            step(nc.vector.tensor_tensor(out=hc2[:, :, :].rearrange("p a b -> p (a b)"), in0=a_, in1=x_, op=ALU.mult))
            mark("gelu")
            dve.wait_ge(s_smallp, 2)
            step(nc.vector.tensor_copy(vcc[:, :, :], TR[1][0:N_CMP, 0:P].rearrange("p (g d) -> p g d", g=2)))
            step(nc.vector.tensor_copy(kcc[:, 0, :], TR[0][:, 0:62]))
            mark("kraw")
            step(nc.vector.tensor_tensor(out=SC[:, 1, 0, 0:62], in0=kcc[:, 0, :], in1=tab("cmp_cos"), op=ALU.mult))
            dve.wait_ge(s_smallp, 3)
            step(nc.vector.tensor_tensor(out=SC[:, 1, 1, 0:62], in0=TR[0][:, 0:62], in1=tab("cmp_sin"), op=ALU.mult))
            step(nc.vector.tensor_tensor(out=kcc[:, 1, :], in0=SC[:, 1, 0, 0:62], in1=SC[:, 1, 1, 0:62], op=ALU.add))
            mark("krope")
            okt = tab("cmp_ok").rearrange("p (t n) -> p t n", t=TT)
            mkt = tab("cmp_mask").rearrange("p (t n) -> p t n", t=TT)
            for b in range(2):
                dve.wait_ge(s_smallp, 4 + b)
                for h in range(4):
                    ins = nc.vector.tensor_tensor(out=PC[:, 2 * h + b, :, :], in0=G[b][:, h * P:(h + 1) * P].rearrange("p (t n) -> p t n", t=TT)[:, :, 0:N_CMP],
                                                  in1=mkt, op=ALU.add)
                    step(ins, wait=False)
            dve.wait_ge(s_small, small[0])
            step(nc.vector.tensor_reduce(pcm[:, 0, :], PC[:, :, :, :].rearrange("p h t n -> p (h t) n"), AX.X, ALU.min))
            pcv = PC[:, :, :, :].rearrange("p h t n -> p (h t) n")
            step(nc.vector.tensor_tensor(out=pcv, in0=pcv, in1=pcm[:, 0, :].unsqueeze(2).to_broadcast([P, 32, N_CMP]), op=ALU.subtract))
            mark("scmp")
            dve.wait_ge(s_smalla, 4)
            step(nc.vector.tensor_reduce(pcm[:, 1, :], pcv, AX.X, ALU.add))
            step(nc.vector.reciprocal(pcm[:, 0, :], pcm[:, 1, :]))
            step(nc.vector.tensor_tensor(out=pcm[:, 1, :].rearrange("p (h t) -> p h t", h=8), in0=pcm[:, 0, :].rearrange("p (h t) -> p h t", h=8),
                                         in1=gate[:, :, 0:24:3].rearrange("p t h -> p h t"), op=ALU.mult))
            step(nc.vector.tensor_tensor(out=pcv, in0=pcv, in1=pcm[:, 1, :].unsqueeze(2).to_broadcast([P, 32, N_CMP]), op=ALU.mult))
            for h in range(8):
                step(nc.vector.tensor_tensor(out=PC[:, h, :, :], in0=PC[:, h, :, :], in1=okt, op=ALU.mult), wait=False)
            mark("pcmp")
            for h in range(8):
                dve.wait_ge(s_smallp, 7 + 2 * h)
                step(nc.vector.tensor_copy(O[:, :, 512 + h * HD:512 + (h + 1) * HD], OB[h % 2][:, 0:256].rearrange("p (t d) -> p t d", t=TT)), wait=False)
            dve.wait_ge(s_small, small[0])

            def fin_diff(i, j, at):
                o = O[:, :, bass.ds(i * P, P)] if not isinstance(i, int) else O[:, :, i * P:(i + 1) * P]
                ps = OB[j][:, :].rearrange("p (t d) -> p t d", t=TT)
                if j == 0:
                    nc.vector.tensor_tensor(out=o, in0=ps, in1=rs[:, 0, :].unsqueeze(2).to_broadcast([P, TT, P]), op=ALU.mult).then_inc(o_used, 1)
                else:
                    nc.vector.tensor_scalar(rs[:, 1, :], rs[:, 1, :], lam[:, 5:6], None, ALU.mult).then_inc(o_steps, 1)
                    dve.wait_ge(o_steps, at + 1)
                    nc.vector.tensor_tensor(out=og[:, :, :], in0=ps, in1=rs[:, 1, :].unsqueeze(2).to_broadcast([P, TT, P]), op=ALU.mult).then_inc(o_steps, 1)
                    dve.wait_ge(o_steps, at + 2)
                    nc.vector.tensor_tensor(out=o, in0=o, in1=og[:, :, :], op=ALU.add).then_inc(o_used, 1)

            def fin_nsa(r, j, at):
                g, par, kind = j // 4, (j // 2) % 2, j % 2
                if isinstance(r, int):
                    c = 512 + (4 * g + 2 * r + par) * HD
                    o = O[:, :, c:c + HD]
                    c = 3 * (4 * g + 2 * r + par) + 1 + kind
                    gt = gate[:, :, c:c + 1]
                else:
                    o = O[:, :, bass.ds(r * (2 * HD) + (512 + (4 * g + par) * HD), HD)]
                    gt = gate[:, :, bass.ds(r * 6 + (3 * (4 * g + par) + 1 + kind), 1)]
                ps = OB[kind][:, 0:256].rearrange("p (t d) -> p t d", t=TT)
                nc.vector.tensor_tensor(out=rs[:, kind, :].unsqueeze(2), in0=rs[:, kind, :].unsqueeze(2), in1=gt, op=ALU.mult).then_inc(o_steps, 1)
                dve.wait_ge(o_steps, at + 1)
                nc.vector.tensor_tensor(out=og[:, :, 0:HD], in0=ps, in1=rs[:, kind, :].unsqueeze(2).to_broadcast([P, TT, HD]), op=ALU.mult).then_inc(o_steps, 1)
                dve.wait_ge(o_steps, at + 2)
                nc.vector.tensor_tensor(out=o, in0=o, in1=og[:, :, 0:HD], op=ALU.add).then_inc(o_used, 1)

            def fin_fox(i, j, at):
                o = O[:, :, bass.ds(i * P + j * HD, HD)] if not isinstance(i, int) else O[:, :, i * P + j * HD:i * P + (j + 1) * HD]
                ps = OB[j][:, 0:256].rearrange("p (t d) -> p t d", t=TT)
                nc.vector.tensor_tensor(out=o, in0=ps, in1=rs[:, j, :].unsqueeze(2).to_broadcast([P, TT, HD]), op=ALU.mult).then_inc(o_used, 1)

            dve_attend(dve, "diff", 4, 2, P, fin_diff)
            dve_attend(dve, "nsa", 2, 8, HD, fin_nsa)
            dve.wait_ge(o_used, 24)
            sq = SC[:, 0, :, :]
            step(nc.vector.tensor_tensor(out=sq, in0=O[:, :, 0:512], in1=O[:, :, 0:512], op=ALU.mult))
            step(nc.vector.tensor_reduce(rmsq[:, 0, :], sq.rearrange("p t (h d) -> p (t h) d", h=4), AX.X, ALU.add))
            step(nc.vector.tensor_scalar(rmsq[:, 1, :], rmsq[:, 0, :], 1.0 / P, LN_EPS, ALU.mult, ALU.add))
            step(nc.vector.reciprocal(rmsq[:, 0, :], rmsq[:, 1, :]))
            mark("rms")
            dve.wait_ge(s_smalla, 13)
            for t in range(TT):
                o = O[:, t, 0:512].rearrange("p (h d) -> p h d", h=4)
                step(nc.vector.tensor_tensor(out=o, in0=o, in1=rmsq[:, 1, 4 * t:4 * t + 4].unsqueeze(2).to_broadcast([P, 4, P]), op=ALU.mult))
                step(nc.vector.tensor_tensor(out=o, in0=o, in1=subln[:, :].unsqueeze(1).to_broadcast([P, 4, P]), op=ALU.mult), wait=False)
            mark("mixed0")
            residual("out0", ALPHA)
            layer_norm("out0", LN_EPS)
            mlp("up0", "down0", ALPHA)
            layer_norm("down0", LN_EPS)
            dve.wait_ge(act_out, st("proj1", "act") + 25)
            step(nc.vector.tensor_scalar(crow[:, 2, :], crow[:, 0, :], -1.0, None, ALU.mult))
            step(nc.vector.tensor_tensor(out=crow[:, 1, :], in0=crow[:, 0, :], in1=crow[:, 2, :], op=ALU.max))
            mark("fabs")
            dve.wait_ge(s_smalla, SMALLA["fexp"])
            step(nc.vector.tensor_scalar(crow[:, 0, :], crow[:, 0, :], 0.0, None, ALU.min))
            dve.wait_ge(s_smalla, SMALLA["fexp"] + 1)
            step(nc.vector.tensor_tensor(out=crow[:, 0, :], in0=crow[:, 0, :], in1=crow[:, 1, :], op=ALU.subtract))
            step(nc.vector.tensor_tensor_scan(out=crow[:, 1, :], data0=crow[:, 0, :], data1=crow[:, 0, :], initial=0.0,
                                              op0=ALU.add, op1=ALU.bypass))
            step(nc.vector.tensor_scalar(crow[:, 2, :], crow[:, 1, :], -1.0, None, ALU.mult))
            mark("fox")
            dve_attend(dve, "fox", 8, 2, HD, fin_fox)
            cc = csil[:, 0, :, :].rearrange("p a k -> p (a k)")
            cs_ = csil[:, 1, :, :].rearrange("p a k -> p (a k)")
            dve.wait_ge(s_smalla, 16)
            step(nc.vector.tensor_scalar(cc, cc, 1.0, None, ALU.add))
            step(nc.vector.reciprocal(cc, cc))
            step(nc.vector.tensor_tensor(out=cs_, in0=cc, in1=cols2[:, 0:16], op=ALU.mult))
            step(nc.vector.memset(ones[:, :], 1.0))
            residual("out1", ALPHA)
            layer_norm("out1", LN_EPS)
            mlp("up1", "down1", ALPHA, ada=True)
            layer_norm("down1", LN_EPS)
            vector_second(dve, residual, layer_norm)


def slab_layout(w, width=512):
    K, n = w.shape
    w = np.pad(w, ((0, 0), (0, -n % width)))
    out = []
    for c in range(0, w.shape[1], width):
        for r in range(0, K, 1024):
            out.append(w[r:r + 1024, c:c + width].reshape(8, P, width).transpose(1, 0, 2).reshape(P, 4096))
    return out


def kernel(**inputs):
    import concourse.bacc as bacc
    from concourse.bass_utils import run_bass_kernel_spmd

    a = {k: np.asarray(v) for k, v in inputs.items()}
    table, where, dft_len, dft_ch, heads = shape_constants()
    we, wo = a["w_in_even"][0], a["w_in_odd"][0]
    up = [slab_layout(a["mlp_w_up"][i]) for i in range(2)]
    down = [slab_layout(a["mlp_w_down"][i]) for i in range(2)]
    kv = np.concatenate([we[:, 2048:2176], we[:, 2176:2304], we[:, 2304:2432], we[:, 2560:2688]], axis=1)
    vg = np.concatenate([we[:, 2432:2560], we[:, 2688:2816], we[:, 2816:2840]], axis=1)
    w1 = a["nsa_cmp_w1"][0]
    slabs = (slab_layout(we[:, 512:1024]) + slab_layout(we[:, 0:512]) + slab_layout(we[:, 1536:2048])
             + slab_layout(we[:, 1024:1536]) + slab_layout(kv) + slab_layout(vg)
             + [w1[j].reshape(16, P, 256).transpose(1, 0, 2).reshape(P, 4096) for j in range(2)]
             + slab_layout(a["w_out_even"][0]) + up[0] + down[0]
             + slab_layout(wo[:, 1024:2048]) + slab_layout(wo[:, 0:1024]) + slab_layout(wo[:, 2048:3072]) + slab_layout(wo[:, 3072:])
             + slab_layout(a["w_out_odd"][0]) + up[1] + down[1])
    cols = np.zeros((P, 37), np.float32)
    cols[:, 0:4] = a["nsa_cmp_b1"][0].reshape(4, P).T
    cols[0:16, 4] = a["fox_f_bias"][0]
    cols[:, 5:37] = a["nsa_pe"][0].reshape(2 * 16, P).T

    wi = a["w_in_2"][0]
    fu = a["ffn_w_up_2"][0].reshape(D, 2, 11, 256).transpose(0, 2, 1, 3)
    fu = fu.reshape(D, 11, 2, 2, P).transpose(0, 1, 3, 2, 4).reshape(D, 2 * D_FF_2)
    fd = a["ffn_w_down_2"][0]
    slabs += (slab_layout(wi[:, OFF_DT:OFF_DT + 16]) + slab_layout(wi[:, OFF_XS:OFF_BC]) + slab_layout(wi[:, OFF_BC:OFF_DT])
              + slab_layout(wi[:, OFF_FP:]) + slab_layout(wi[:, 0:512])
              + [dft_len.reshape(8, P, S).transpose(1, 0, 2).reshape(P, 4096)]
              + slab_layout(a["w_out_2"][0]) + slab_layout(fu))
    for c in range(0, D, 512):
        r = 0
        for nk in (6, 6, 5, 5):
            slabs += slab_layout(np.pad(fd[r * P:(r + nk) * P, c:c + 512], ((0, (8 - nk) * P), (0, 0))))
            r += nk
    bada = a["b_ada_2"][0].reshape(48, P).T
    cols2 = np.zeros((P, 122 + 480), np.float32)
    cols2[:, 0:8] = a["c_2"].reshape(KT, P).T
    cols2[:, 8:16] = a["c_ctx_2"].reshape(KT, P).T
    cols2[:, 16:64] = bada
    cols2[:, 64:80] = bada[:, 0:16]
    cols2[0:16, 80] = a["ssd_dt_bias_2"].reshape(16)
    cols2[0:16, 81] = a["ssd_a_log_2"].reshape(16)
    cols2[0:8, 82] = 1
    cols2[8:16, 83] = 1
    cols2[:, 84:108] = a["ssd_conv_w_2"][0].reshape(3, 8, P).transpose(2, 1, 0).reshape(P, 24)
    cols2[:, 108:116] = a["ssd_conv_b_2"].reshape(8, P).T
    cols2[:, 116:120] = a["ssd_norm_w_2"].reshape(4, P).T
    cols2[:, 120:122] = a["pool_scale_2"].reshape(2, P).T
    ffn = np.concatenate([a["ffn_conv_w_2"][0].reshape(9, 2 * D_FF_2), a["ffn_conv_b_2"]])
    ffn = ffn.reshape(10, 2, 11, 2, P).transpose(4, 2, 3, 1, 0)
    cols2[:, 122:562] = ffn.reshape(P, 440)
    ada = np.stack(slab_layout(a["w_ada_2"][0]))

    nc = bacc.Bacc("TRN2", target_bir_lowering=False, num_devices=1)
    arrays = {"slabs": np.stack(slabs), "cols": cols, "table": table, "ones": np.ones((2, S), np.float32),
              "cols2": cols2, "ada": ada, "dft_ch": np.concatenate([dft_ch, dft_ch], axis=2).transpose(1, 0, 2).copy()}
    for n in ("x", "ln_gain", "ln_bias", "diff_lambda", "diff_subln", "nsa_cmp_w2", "ctx_2", "fnet_w_2", "pool_w_2",
              "ssd_d_2", "ln1_g_2", "ln1_b_2", "ln2_g_2", "ln2_b_2"):
        arrays[n] = a[n]
    A = {n: nc.dram_tensor(n, v.shape, F32, kind="ExternalInput").ap() for n, v in arrays.items()}
    A["where"] = where
    A["crow"] = nc.dram_tensor("forget_rows", (16, 2, S), F32, kind="Internal").ap()
    out = nc.dram_tensor("out", (1, S, D), F32, kind="ExternalOutput").ap()
    build(nc, A, out)
    r = run_bass_kernel_spmd(nc, [arrays], core_ids=[0])
    return r.results[0]["out"]
```

```python
import math
from contextlib import ExitStack

import numpy as np
import concourse.bass as bass
from concourse import mybir

F32 = mybir.dt.float32
F32R = mybir.dt.float32r
ALU = mybir.AluOpType
ACT = mybir.ActivationFunctionType
AX = mybir.AxisListType

P = 128
D = 1024
S = 512
TT = S // P
KT = D // P
HD = 64
D_FF = 4 * D
N_EVEN_COLS = 2840
ALPHA = 4.0 ** 0.25
LN_EPS = 1e-5
BIG = 2.0 ** 100
N_CMP = 31
LAM_INIT = 0.8 - 0.6 * math.exp(0.0)

D_FF_2 = 2816
CTX = 256
ALPHA_2 = 2.0 ** 0.25
EPS_2 = 1e-6
N_IN = 2064
OFF_XS, OFF_BC, OFF_DT, OFF_FP = 512, 1024, 1536, 1552
GRID_W = 64


def shape_constants():
    half = 8
    inv = (np.float32(500000.0) ** (-np.arange(half, dtype=np.float32) / np.float32(half))).astype(np.float32)

    def rope(pos):
        ang = pos.astype(np.float32)[:, None] * inv[None, :]
        c, s = np.cos(ang), np.sin(ang)
        cos, sin = np.ones((P, len(pos)), np.float32), np.zeros((P, len(pos)), np.float32)
        for p in range(P):
            d = p % HD
            if d < 2 * half:
                cos[p] = c[:, d % half]
                sin[p] = s[:, d % half] * (-1 if d < half else 1)
        return cos, sin

    cos, sin = rope(np.arange(S))
    cmp_end = np.arange(N_CMP) * 16 + 31
    cc, cs = rope(np.concatenate([cmp_end, cmp_end]))
    swap = np.zeros((P, P), np.float32)
    for m in range(P):
        d = m % HD
        if d < 16:
            swap[(m - 8 if d >= 8 else m + 8), m] = 1
    q, k = np.arange(P)[:, None], np.arange(P)[None, :]
    causal = np.zeros((P, S), np.float32)
    causal[:, S - P:] = np.where(k > q, BIG, 0)
    tok = np.arange(TT)[None, :, None] * P + np.arange(P)[:, None, None]
    ok = cmp_end[None, None, :] <= tok
    inv_count = np.zeros((P, 2, S), np.float32)
    t = np.arange(S)
    for g, w in enumerate((2, 4, 8, 16)):
        n = np.minimum(t + (w - 1 - w // 2) + 1, S) - np.maximum(t - w // 2, 0)
        inv_count[(g % 2) * HD:(g % 2) * HD + HD, g // 2] = 1.0 / n.astype(np.float32)
    parts = [("cos", cos), ("sin", sin), ("ident", np.eye(P)), ("swap", swap), ("causal", causal),
             ("cmp_cos", cc), ("cmp_sin", cs),
             ("cmp_mask", np.where(ok, 0, BIG).reshape(P, -1)), ("cmp_ok", ok.reshape(P, -1)),
             ("lower", (q >= k)), ("upper", (q <= k)), ("inv_count", inv_count.reshape(P, -1))]
    at, where = 0, {}
    for name, a in parts:
        where[name] = (at, at + a.shape[1])
        at += a.shape[1]
    table = np.concatenate([np.asarray(a, np.float32) for _, a in parts], axis=1)
    n = np.arange(S)
    ang = 2 * np.pi * ((n[:, None] * n[None, :]) % S) / S
    scale = 1.0 / math.sqrt(S * HD)
    dft_len = np.stack([np.cos(ang) * scale, -np.sin(ang) * scale]).astype(np.float32)
    c = np.arange(HD)
    angc = 2 * np.pi * ((c[:, None] * c[None, :]) % HD) / HD
    dft_ch = np.stack([np.cos(angc), np.sin(angc)]).astype(np.float32)
    heads = np.zeros((16, 16 * P), np.float32)
    for h in range(16):
        heads[h, h * P:(h + 1) * P] = 1
    return table, where, dft_len, dft_ch, heads


class Stages:

    def __init__(self):
        self.total, self.base, self.before = {}, {}, {}

    def add(self, stage, **counts):
        self.before[stage] = dict(self.total)
        for what, n in counts.items():
            self.base[stage, what] = self.total.get(what, 0)
            self.total[what] = self.total.get(what, 0) + n

    def __call__(self, stage, what):
        return self.base[stage, what]


def build(nc, A, out, debug=None):
    where = A["where"]
    st = Stages()
    st.add("x0", tr=8)
    st.add("proj0", quarters=24, act=24)
    st.add("cmp", quarters=8, act=4)
    st.add("diff", units=8, loads=2)
    st.add("nsa", units=16, loads=1)
    st.add("mixed0", tr=8)
    st.add("out0", quarters=8, dve=8, ln=26, std=1)
    st.add("x1", tr=8)
    st.add("mlp0", quarters=64, act=32, hidden=32, dve=16, ln=26, std=1)
    st.add("x2", tr=8)
    st.add("proj1", quarters=28, act=25)
    st.add("fox", units=16)
    st.add("mixed1", tr=8)
    st.add("out1", quarters=8, dve=8, ln=26, std=1)
    st.add("x3", tr=8)
    st.add("mlp1", quarters=64, act=32, hidden=32, dve=16, ln=26, std=1)
    st.add("ln_ctx", ln=10, std=1)
    st.add("x_ctx", tr=8)
    st.add("ln_x", ln=18, std=1)
    st.add("x4", tr=8)
    st.add("w_in", quarters=20)
    st.add("dft", quarters=4)
    st.add("out2", quarters=8, dve=8, ln=26, std=1)
    st.add("ln_ffn", ln=18, std=1)
    st.add("x5", tr=8)
    st.add("ffn2", quarters=66, act=44, hidden=22, dve=16, ln=26, std=1)
    SLAB = {}
    for stage, n in (("proj0", 6), ("cmp", 2), ("out0", 2), ("proj1", 7), ("out1", 2), ("w_in", 5), ("dft", 1), ("out2", 2)):
        SLAB[stage] = sum(n_ for _, n_ in SLAB.values()), n
    PARTS = {"mlp0": ((16, 16), (16, 16)), "mlp1": ((16, 16), (16, 16)), "ffn2": ((24, 12), (20, 10))}
    SPLIT0 = {"mlp0": 0, "mlp1": 64, "ffn2": 128}

    CONSTS = 2 * 16
    SMALL_INPUTS = 5 * 16
    GROUPS0 = ([("F", (m * P, m * P + P), (None, 1.0)) for m in range(4)]
               + [("F", (m * P, m * P + P), (None, -0.125)) for m in range(4)] * 2
               + [("T", (0, 512), (("V", t, 0, 512), 1.0)) for t in range(TT)]
               + [("F", (m * P, m * P + P), (("K", 4 + m) if m < 2 else None, 1.0)) for m in range(4)]
               + [("T", (0, 280), (("V", t, 512, 792), 1.0)) for t in range(TT)])
    ROPED0 = ([(g, "k", g) for g in range(4)] + [(4 + g, "q", g) for g in range(8)]
              + [(18, "k", 6), (19, "k", 7)])
    SMALL = dict(lam=2, windows=7, gelu_in=12, gelu=14, kraw=16, krope=19, scmp=29, pcmp=41, rms=53,
                 mixed0=61, fabs=67, fox=71)
    SMALLA = dict(ptc=4, silu=14, fexp=15)
    LOADS = {"diff": 0, "nsa": 128, "fox": 256}
    STEP0 = {"diff": 0, "nsa": 8, "fox": 40}

    ctx = ExitStack()
    with ctx:
        def sb(name, shape):
            return ctx.enter_context(nc.sbuf_tensor(name + "_sb", shape, F32))

        def pb(name):
            return ctx.enter_context(nc.psum_tensor(name, [P, 512], F32))

        def sem(name):
            return ctx.enter_context(nc.semaphore(name))

        X = sb("X", [P, TT, D])
        with ExitStack() as overlay:
            Hh, Hl, Wh, Wl, XTh, XTl = (overlay.enter_context(nc.sbuf_tensor(name, shape, F32R)) for name, shape in (
                ("hidden_high", [P, 16, S]), ("hidden_low", [P, 16, S]), ("weights_high", [P, 4, 1024]),
                ("weights_low", [P, 4, 1024]), ("xt_high", [P, KT, S]), ("xt_low", [P, KT, S])))
        wide = sb("wide", [P, 32, S])
        SC = sb("SC", [P, 2, TT, S])
        PT = sb("PT", [P, TT, S])
        qb = sb("qb", [P, 2, S])
        kb = sb("kb", [P, 2, S])
        XT = sb("XT", [P, KT, S])
        ring = sb("ring", [P, 2, 4096])
        raw = ring[:, 1, :].rearrange("p (s q n) -> p s q n", s=2, q=2)
        QT, KTT = wide[:, 0:8, :], wide[:, 8:16, :]
        V = wide[:, 16:24, :].rearrange("p (t h) n -> p t (h n)", t=TT)
        O = wide[:, 24:32, :].rearrange("p (t h) n -> p t (h n)", t=TT)
        table = sb("table", [P, A["table"].shape[1]])
        cols = sb("cols", [P, A["cols"].shape[1]])
        rows = sb("rows", [P, 2, D])
        stat = sb("stat", [P, TT, 2, 6])
        agg = sb("agg", [P, TT, 2])
        rstd = sb("rstd", [P, 3, TT])
        mn = sb("mn", [P, 2, TT])
        sm = sb("sm", [P, 2, TT])
        rs = sb("rs", [P, 2, TT])
        og = sb("og", [P, TT, P])
        lamrow = og[:, 0:2, :].rearrange("p a (b n) -> p a b n", b=2)
        KS4 = sb("KS4", [P, 4, S])
        KSW = KS4[0:HD, :, :].rearrange("p (a b) n -> p a b n", a=2)
        lam = sb("lam", [P, 8])
        subln = sb("subln", [P, P])
        gate = sb("gate", [P, TT, 24])
        w2 = sb("w2", [P, 2, 2, P])
        hc = SC[:, 1, 3, 0:248].rearrange("p (a b) -> p a b", a=4)
        hc2 = SC[:, 1, 3, 248:496].rearrange("p (a b) -> p a b", a=4)
        kcc = sb("kcc", [P, 2, 62])
        vcc = sb("vcc", [N_CMP, 2, HD])
        crow = rows[0:16, :, :].rearrange("p a (b n) -> p (a b) n", n=S)
        ones = sb("ones", [P, P])
        cols2 = sb("cols2", [P, A["cols2"].shape[1]])
        modc = sb("modc", [P, 64])
        csil = sb("csil", [P, 2, 2, KT])
        bd = sb("bd", [P, 2, 256])
        poolw = sb("poolw", [P, 2, P])
        tks = sb("tks", [P, 160])
        ncs = sb("ncs", [P, TT, 16])
        ecs = sb("ecs", [P, TT, 16])
        nega = sb("nega", [16, 4])
        drow = sb("drow", [P, 8])
        ys = sb("ys", [P, 3, TT, 2])
        pcm = sb("pcm", [P, 2, 32])
        rmsq = sb("rmsq", [P, 2, 16])
        PC = SC[:, 0, 0:2, :].rearrange("p a b -> p (a b)")[:, 0:8 * TT * N_CMP].rearrange("p (h t n) -> p h t n", h=8, t=TT)

        def WIN(j):
            w = PT[:, 2 * j:2 * j + 2, :].rearrange("p a b -> p (a b)")
            return w[:, 0:16 * 62].rearrange("p (m n) -> p m n", m=16)

        G = [pb(f"G{i}") for i in range(4)]
        TR = [pb(f"TR{i}") for i in range(2)]
        OB = [pb(f"OB{i}") for i in range(2)]

        def tab(name, n=P):
            a, b = where[name]
            return table[0:n, a:b]

        act_buf = [tab("cos"), tab("sin")]
        ogf = og[:, :, :].rearrange("p a b -> p (a b)")

        ident = tab("ident")
        BANKS = [G, [TR[0], TR[1], OB[1], OB[0]]]

        s_const = sem("constants_in")
        s_small_in = sem("small_inputs_in")
        s_x = sem("x_in")
        slab_in = [sem("slab_in_even"), sem("slab_in_odd")]
        quarters = sem("slab_quarters_used")
        act_out = sem("psum_emptied_by_scalar")
        dve_out = sem("psum_emptied_by_vector")
        tr_ready = sem("transposed_in_psum")
        tr_out = sem("transposed_copied")
        rope_swapped = sem("rope_partners_in_psum")
        rope_cos = sem("rope_cos_products")
        rope_dve = sem("rope_vector_steps")
        gb_in = sem("gain_bias_in")
        ln_dve = sem("layer_norm_vector_steps")
        ln_std = sem("layer_norm_deviations")
        raw_in = [sem("raw_even_in"), sem("raw_odd_in")]
        w_hi = sem("weight_high_parts")
        w_lo = sem("weight_low_parts")
        xt_hi = sem("xt_high_parts")
        hid_hi = sem("hidden_high_parts")
        hid_steps = sem("hidden_float32")
        hidden = sem("hidden_low_parts")
        ada_moved = sem("ada_columns_moved")
        qk_in = [sem("qk_in_even"), sem("qk_in_odd")]
        sc_seen = sem("scores_seen_by_vector")
        sc_ready = sem("scores_in_psum")
        sc_used = sem("scores_copied_with_min")
        pr_ready = sem("probabilities_ready")
        pt_ready = sem("probabilities_transposed")
        pt_dve = sem("transposed_probabilities_by_vector")
        pt_act = sem("transposed_probabilities_by_scalar")
        pv_ready = sem("attended_in_psum")
        o_steps = sem("attended_vector_steps")
        rec_done = sem("sums_inverted")
        o_used = sem("attended_copied")
        s_small = sem("vector_small_steps")
        s_smalla = sem("scalar_small_steps")
        s_smallp = sem("tensor_small_steps")
        ksw_in = sem("shared_keys_moved")
        cmp_in = sem("compression_windows_in")
        crow_in = sem("forget_rows_stored")
        s_out = sem("stored")
        ada_in = [sem("ada_half_0_in"), sem("ada_half_1_in")]
        ada_steps = sem("ada_accumulated")
        ada_cols = sem("ada_columns_summed")
        s_two = sem("vector_steps_second")
        s_twoa = sem("scalar_steps_second")
        s_twop = sem("tensor_steps_second")
        s_twog = sem("gpsimd_steps_second")
        s_twod = sem("second_inputs_in")
        conv_first = sem("ffn_conv_padded")
        conv_steps = sem("ffn_conv_taps")
        gelu_done = sem("ffn_gelu")
        x_val = sem("modulated_float32")
        res_steps = sem("residual_gated")
        s_ctx = sem("context_in")

        def ADW(h):
            return KS4[:, 2 * h:2 * h + 2, :].rearrange("p k c -> p (k c)")

        STEPS = {"diff": (0, 0, 2), "nsa": tuple(range(0, 17, 2)), "fox": (0, 0, 0)}

        block = ctx.enter_context(nc.Block())

        def slab(s):
            return ring[:, s % 2, :].rearrange("p (k c) -> p k c", k=KT)

        def split_products(out, terms):
            n = 3 * len(terms)
            for i, (ah, al, bh, bl) in enumerate(terms):
                for j, (a, b) in enumerate(((ah, bh), (ah, bl), (al, bh))):
                    mm = nc.tensor.matmul(out, lhsT=a, rhs=b, start=(3 * i + j == 0), stop=(3 * i + j == n - 1))
            return mm

        def raw_quarter(Q):
            return raw[:, (Q // 2) % 2, Q % 2, :]

        def high_split(act, stage, n, i=0, first=False):
            Q = SPLIT0[stage] + n
            act.wait_ge(raw_in[(Q // 2) % 2], i * 16 + 16 * (Q // 4 + 1))
            if not first:
                act.wait_ge(quarters, i * 4 + (st(stage, "quarters") + n - 3))
            nc.scalar.activation(Wh[:, n % 4, :], raw_quarter(Q), ACT.Copy).then_inc(w_hi, 1)

        def low_split(eng, tt_, stage, n, i=0):
            Q = SPLIT0[stage] + n
            eng.wait_ge(w_hi, i * 4 + (Q + 1))
            tt_(out=Wl[:, n % 4, :], in0=raw_quarter(Q), in1=Wh[:, n % 4, :], op=ALU.subtract).then_inc(w_lo, 1)

        def n_quarters(stage):
            return sum(a + b for a, b in PARTS[stage])

        C2 = dict(bada=16, dt_bias=80, a_log=81, fwd=82, bwd=83, conv=84, conv_b=108, norm=116, pool=120, ffn=122)

        def col(name, n=0, rows_=P):
            return cols2[0:rows_, C2[name] + n:C2[name] + n + 1]

        def tiles(a, b):
            return wide[:, a:b, :].rearrange("p a b -> p (a b)")

        xbcT, Z, Btok = wide[:, 0:8, :], wide[:, 11:15, :], wide[:, 15, :]
        CX = tiles(8, 11).rearrange("p (a b) -> p a b", b=CTX)
        STATE = wide[:, 8:10, :]
        CT = tiles(16, 20).rearrange("p (a b) -> p a b", b=CTX)
        fnetT, CXT = wide[:, 16:18, :], wide[:, 18:20, :]
        ctok = tiles(20, 24).rearrange("p (t n) -> p t n", t=2)
        XW = wide[:, 20:24, :]
        Hn = O
        XS, Y, FAB = wide[:, 24:28, :], wide[:, 28:32, :], wide[:, 28:32, :]
        XF, XB = wide[:, 0:4, :], wide[:, 16:20, :]
        MB = [PT, wide[:, 20:24, :]]
        gbc = KS4[:, :, :].rearrange("p a b -> p (a b)")
        SCF = SC[:, :, :, :].rearrange("p a b c -> p (a b c)")
        PAD_L = 528
        PB, D1, D2 = (SCF[:, n * 2 * PAD_L:(n + 1) * 2 * PAD_L].rearrange("p (a b) -> p a b", a=2) for n in range(3))
        D8 = SCF[:, 6 * PAD_L:7 * PAD_L]
        R = kb
        CR = rows[0:16, :, :].rearrange("p a b -> p (a b)")
        DT, DA = CR[:, 0:768], CR[:, 768:1536]
        PTF = PT[0:16, :, :].rearrange("p a b -> p (a b)")
        CF, RV = PTF[:, 0:768], PTF[:, 768:1536]
        PAIR = [wide[:, a:a + 4, :].rearrange("p a b -> p (a b)") for a in (12, 28)]
        PADS = [PAIR[m // 2][:, (m % 2) * 660:(m % 2 + 1) * 660].rearrange("p (r c) -> p r c", r=10) for m in range(4)]
        SUMS = [PAIR[m // 2][:, 1320:1832] if m % 2 == 0 else KS4[:, m // 2, :] for m in range(4)]
        dch = w2[0:HD, 0, :, :]
        fw = w2[0:HD, 1, :, :].rearrange("p a b -> p (a b)")

        class Steps:

            def __init__(self, sem_, names):
                self.sem, self.names, self.next = sem_, names, 0
                self.place = {n: i + 1 for i, n in enumerate(names)}
                assert len(self.place) == len(names)

            def do(self, name, ins):
                assert self.names[self.next] == name, (name, self.names[self.next])
                self.next += 1
                ins.then_inc(self.sem, 1)

            def of(self, name):
                return self.place[name]

        def names(*parts):
            out_ = []
            for x in parts:
                out_ += [x] if isinstance(x, str) else list(x)
            return out_

        CONV = [(m, who) for m in range(8) for who in ("c", "l") if who == "l" or m < 6]

        def conv_order(first, second):
            out_ = []
            for m in range(9):
                for k, w in CONV:
                    if k == m:
                        out_ += [x.format(w=w, m=m) for x in first]
                for k, w in CONV:
                    if k == m - 1:
                        out_ += [x.format(w=w, m=m - 1) for x in second]
            return out_

        V2 = Steps(s_two, names(
            "mod1", "mod2", "mod3", [f"dgb{b}" for b in range(16)], "halfw", "bdz", "pwz",
            conv_order(["{w}{m}a", "{w}{m}b"], ["{w}{m}s"]),
            "dneg", "dabs", "dmax", "dt", "nega", "dA", "cf", "cfc", "rv", "rvc", "c0", "cs", "tt0", "tt1", "wc",
            [f"bd{n}" for n in range(8)], [f"z{t}" for t in range(4)], "tks", "ncs", [f"xw{n}" for n in range(8)],
            [f"xf{t}" for t in range(4)], [f"xb{t}" for t in range(4)],
            [f"yo{g}{t}{x}" for g in range(2) for t in range(4) for x in "abc"],
            "da0", "db0", "dm0", [x for h in range(8) for x in ([f"da{h+1}", f"db{h+1}", f"dm{h+1}"] if h < 7 else [])
                                  + [f"mm{h}", f"df{h}", f"dr{h}"] + ([f"ya{h-1}"] if h else [])], "ya7",
            [f"{x}{t}" for t in range(4) for x in ("sk", "sa", "sz", "sq", "sr")], "sv", "si", [f"sn{t}" for t in range(4)]))
        A2 = Steps(s_twoa, names(
            [f"gb{q}" for q in range(4)], "dtc", "dtl", conv_order(["{w}{m}f"], ["{w}{m}t"]),
            "alog", "dexp", "dln", "fn0", "fn1", "po0", "po1", "wexp",
            [f"z{t}{x}" for t in range(4) for x in "ht"], [f"fab{t}" for t in range(4)], "yf0", "yf1", "ecs",
            [f"xt{t}" for t in range(4)], "ct0", "ct1", "bt", "yp0", "yp1", "st0", "st1", [f"g{g}{j}" for g in range(2) for j in range(4)],
            [f"{x}{h}" for h in range(8) for x in ("of", "ed")], "ss", [f"ym{b}" for b in range(4)]))
        P2 = Steps(s_twop, names(
            [f"gb{q}" for q in range(4)], "dtc", "bdp", "tks", [f"fab{t}" for t in range(4)],
            [f"xt{t}" for t in range(4)], "ct0", "ct1", "bt", "yp0", "yp1", "st0", "st1",
            [f"g{g}{j}" for g in range(2) for j in range(4)], [f"yo{g}{t}" for g in range(2) for t in range(4)],
            "rw0", "rw1", [x for h in range(8) for x in ([f"rw{h+2}"] if h < 6 else []) + [f"y{h}"]], [f"ym{b}" for b in range(4)]))
        G2 = Steps(s_twog, names("pz", "d2", "d4", "d8", "d16", "m0", "m1", "m2", "m3", "sub", "padz"))

        def XBC(w, m):
            return xbcT[:, m, :] if w == "l" else CX[:, m, :]

        def TH(w, m):
            return qb[:, m % 2, :] if w == "l" else PT[:, 3, (m % 2) * CTX:(m % 2 + 1) * CTX]

        def DGB(b):
            return qb[:, (b % 8) // 4, (b % 4) * P:(b % 4 + 1) * P]

        def DFB(h):
            return (kb[:, 0, :], kb[:, 1, :]) if h % 2 == 0 else (XT[:, 0, :], XT[:, 1, :])

        def diagonal(m):
            a = m[:, 0, 0:P]
            return bass.AP(tensor=a.tensor, offset=a.offset, ap=[list(a.ap[0]), [S + P, TT], [1, P]])

        def gpsimd_second(gp, gain_bias):
            gp.wait_ge(quarters, st("mlp1", "quarters") + 64)
            gp.dma_start(ctok, A["ctx_2"].rearrange("o (t p) d -> p (o t) d", p=P)).then_inc(s_ctx, 16)
            gp.dma_start(dch, A["dft_ch"]).then_inc(s_twod, 16)
            gp.dma_start(fw.rearrange("p (g d) -> p g d", g=4), A["fnet_w_2"].rearrange("o g c d -> c (o g) d")).then_inc(s_twod, 16)
            gp.dma_start(drow[:, :], A["ssd_d_2"].partition_broadcast(P).rearrange("p o h -> p (o h)")).then_inc(s_twod, 16)
            gp.wait_ge(s_two, V2.of("pwz"))
            for g in range(4):
                r = (g % 2) * HD
                gp.dma_start(poolw[r:r + HD, g // 2, r:r + HD], A["pool_w_2"][0, g, :, :]).then_inc(s_twod, 16)
            gp.wait_ge(quarters, st("mlp1", "quarters") + 64)
            G2.do("pz", nc.gpsimd.memset(SCF[:, 0:2 * PAD_L], 0.0))
            gp.wait_ge(s_twoa, A2.of("po1"))
            tt = nc.gpsimd.tensor_tensor
            G2.do("d2", tt(out=D1[:, :, 0:526], in0=PB[:, :, 0:526], in1=PB[:, :, 1:527], op=ALU.add))
            gp.wait_ge(s_twog, G2.of("d2"))
            G2.do("d4", tt(out=D2[:, :, 0:524], in0=D1[:, :, 0:524], in1=D1[:, :, 2:526], op=ALU.add))
            gp.wait_ge(s_twog, G2.of("d4"))
            G2.do("d8", tt(out=D8[:, 0:520], in0=D2[:, 1, 0:520], in1=D2[:, 1, 4:524], op=ALU.add))
            gp.wait_ge(s_twog, G2.of("d8"))
            G2.do("d16", tt(out=D1[:, 1, 0:S], in0=D8[:, 0:S], in1=D8[:, 8:S + 8], op=ALU.add))
            gp.wait_ge(s_twog, G2.of("d16"))
            inv = tab("inv_count").rearrange("p (a n) -> p a n", a=2)
            for n, (p0, i, src) in enumerate([(0, 0, D1[0:HD, 0, 7:7 + S]), (HD, 0, D2[HD:P, 0, 6:6 + S]),
                                              (0, 1, D8[0:HD, 4:4 + S]), (HD, 1, D1[HD:P, 1, 0:S])]):
                G2.do(f"m{n}", tt(out=R[p0:p0 + HD, i, :], in0=src, in1=inv[p0:p0 + HD, i, :], op=ALU.mult))
            gp.wait_ge(s_twog, G2.of("m3"))
            G2.do("sub", tt(out=R[:, :, :], in0=R[:, :, :], in1=PB[:, :, 8:8 + S], op=ALU.subtract))
            gp.wait_ge(s_twop, P2.of("y7"))
            gp.wait_ge(s_two, V2.of("mm7"))
            gain_bias(4, A["ln1_g_2"][0, :], A["ln1_b_2"][0, :])
            gain_bias(5, A["ln2_g_2"][0, :], A["ln2_b_2"][0, :])
            gp.wait_ge(tr_ready, st("x5", "tr") + 8)
            nc.gpsimd.memset(PAIR[0][:, 0:1320], 0.0)
            G2.do("padz", nc.gpsimd.memset(PAIR[1][:, 0:1320], 0.0))
            for n in range(3):
                low_split(gp, tt, "ffn2", n)
            n0 = 0
            for up, down in PARTS["ffn2"]:
                with gp.Fori(0, up // 4) as i:
                    for m in range(4):
                        low_split(gp, tt, "ffn2", n0 + m + 3, i)
                n0 += up
                for n in range(n0, n0 + down):
                    if n + 3 < n_quarters("ffn2"):
                        low_split(gp, tt, "ffn2", n + 3)
                n0 += down

        def tensor_second(pe, stage_start, slab_wait, mlp_products, out_products):
            mm_, tr_ = nc.tensor.matmul, nc.tensor.transpose

            def by_feature(stage, src, n_tiles, ready):
                base = st(stage, "tr")
                ready()
                for b in range(KT):
                    if base + b >= 2:
                        pe.wait_ge(tr_out, base + b - 1)
                    for t in range(n_tiles):
                        m = tr_(TR[b % 2][:, t * P:(t + 1) * P], src[:, t, b * P:(b + 1) * P], ident)
                    m.then_inc(tr_ready, 1)

            for q in range(4):
                pe.wait_ge(s_two, V2.of(f"dgb{4 * q + 3}"))
                pe.wait_ge(ln_dve, st("ln_ctx", "ln"))
                for n in range(4):
                    m = mm_(G[q][:, n * P:(n + 1) * P], lhsT=ones[:, :], rhs=DGB(4 * q + n), start=True, stop=True)
                P2.do(f"gb{q}", m)
            by_feature("x_ctx", ctok, 2, lambda: pe.wait_ge(ln_dve, st("ln_ctx", "ln") + 10))
            by_feature("x4", Hn, TT, lambda: pe.wait_ge(ln_dve, st("ln_x", "ln") + 18))

            s0 = SLAB["w_in"][0]
            pe.wait_ge(tr_out, st("x4", "tr") + 8)
            pe.wait_ge(s_twoa, A2.of("gb3"))
            slab_wait(s0)
            for k in range(KT):
                m = mm_(G[2][0:16, 0:CTX], lhsT=slab(s0)[:, k, 0:16], rhs=CT[:, k, :], start=(k == 0), stop=(k == KT - 1))
            P2.do("dtc", m)
            for k in range(KT):
                m = mm_(G[0][0:16, :], lhsT=slab(s0)[:, k, 0:16], rhs=XT[:, k, :], start=(k == 0), stop=(k == KT - 1))
            m.then_inc(quarters, 4)
            for n in range(16):
                if n % 4 == 0:
                    slab_wait(s0 + 1 + n // 4)
                sl = slab(s0 + 1 + n // 4)
                c = slice((n % 4) * P, (n % 4 + 1) * P)
                if n < 2:
                    pe.wait_ge(s_twoa, A2.of("dtl"))
                elif n < 10:
                    pe.wait_ge(s_two, V2.of(f"l{n - 2}b"))
                elif n < 14:
                    pe.wait_ge(s_twoa, A2.of(("fn0", "fn1", "po0", "po1")[n - 10]))
                else:
                    pe.wait_ge(s_twoa, A2.of(f"z{n - 14}h"))
                if n < 6:
                    for k in range(KT):
                        mm_(G[2 + n % 2][:, 0:CTX], lhsT=sl[:, k, c], rhs=CT[:, k, :], start=(k == 0), stop=(k == KT - 1))
                for k in range(KT):
                    if n < 12:
                        m = mm_(G[n % 2][:, :], lhsT=sl[:, k, c], rhs=XT[:, k, :], start=(k == 0), stop=(k == KT - 1))
                    else:
                        m = mm_(G[n % 2][:, :], lhsT=XT[:, k, c], rhs=sl[:, k, :], start=(k == 0), stop=(k == KT - 1))
                m.then_inc(quarters, 1)

            pe.wait_ge(s_twod, 112)
            for cs in range(2):
                m = mm_(TR[0][:, cs * 256:(cs + 1) * 256], lhsT=dch[:, cs, :], rhs=fw, start=True, stop=True)
            P2.do("bdp", m)
            pe.wait_ge(s_two, V2.of("wc"))
            for n in range(10):
                src = DA[:, n * P:(n + 1) * P] if n < 4 else DT[:, (n - 4) * P:(n - 3) * P] if n < 8 else CF[:, S + (n - 8) * P:S + (n - 7) * P]
                m = tr_(OB[1][:, n * 16:(n + 1) * 16], src, ident[0:16, 0:16])
            P2.do("tks", m)
            pe.wait_ge(s_two, V2.of("bd7"))
            for t in range(TT):
                pe.wait_ge(s_twoa, A2.of("z3h"))
                for ft in range(2):
                    m = mm_(G[t][:, ft * 256:(ft + 1) * 256], lhsT=fnetT[:, ft, t * P:(t + 1) * P], rhs=bd[:, ft, :], start=True, stop=True)
                P2.do(f"fab{t}", m)
            sd = SLAB["dft"][0]
            slab_wait(sd)
            for ft in range(2):
                for n in range(8):
                    cs, t = n // 4, n % 4
                    pe.wait_ge(s_twoa, A2.of("fab3"))
                    m = mm_(TR[ft][:, :], lhsT=FAB[:, t, ft * 256 + cs * P:ft * 256 + (cs + 1) * P], rhs=slab(sd)[:, n, :],
                            start=(n == 0), stop=(n == 7))
                m.then_inc(quarters, 2)
            pe.wait_ge(s_two, V2.of("l7s"))
            for t in range(TT):
                for b in range(4):
                    m = tr_(G[t][:, b * P:(b + 1) * P], xbcT[:, b, t * P:(t + 1) * P], ident)
                P2.do(f"xt{t}", m)
            for t in range(2):
                pe.wait_ge(s_twoa, A2.of(f"yf{t}"))
                for b in range(4):
                    m = tr_(TR[t][:, b * P:(b + 1) * P], CX[:, b, t * P:(t + 1) * P], ident)
                P2.do(f"ct{t}", m)
            for n in range(4):
                m = tr_(OB[0][:, n * P:(n + 1) * P], CX[:, 4 + n % 2, (n // 2) * P:(n // 2 + 1) * P], ident)
            P2.do("bt", m)
            pe.wait_ge(s_twog, G2.of("sub"))
            pe.wait_ge(s_twod, 112)
            for i in range(2):
                pe.wait_ge(s_twoa, A2.of(f"xt{i}"))
                P2.do(f"yp{i}", mm_(G[i][:, :], lhsT=poolw[:, i, :], rhs=R[:, i, :], start=True, stop=True))
            pe.wait_ge(s_two, V2.of("xw7"))
            pe.wait_ge(s_twoa, A2.of("bt"))
            for g in range(2):
                for t in range(2):
                    m = mm_(OB[g][:, :], lhsT=Btok[:, (2 * t + g) * P:(2 * t + g + 1) * P], rhs=XW[:, 2 * t + g, :], start=(t == 0), stop=(t == 1))
                P2.do(f"st{g}", m)
            for g in range(2):
                for j in range(TT):
                    if g == 0:
                        pe.wait_ge(s_twoa, A2.of(f"yp{j}" if j < 2 else f"xt{j}"))
                    else:
                        pe.wait_ge(s_twoa, A2.of(f"g0{j}"))
                    P2.do(f"g{g}{j}", mm_(G[j][:, :], lhsT=xbcT[:, 4 + g, j * P:(j + 1) * P], rhs=xbcT[:, 6 + g, :], start=True, stop=True))
            pe.wait_ge(s_twoa, A2.of("st1"))
            for g in range(2):
                for t in range(TT):
                    if g or t >= 2:
                        pe.wait_ge(s_two, V2.of(f"yo{g if t >= 2 else 0}{(t - 2) % 4}b"))
                    P2.do(f"yo{g}{t}", mm_(TR[t % 2][:, :], lhsT=xbcT[:, 6 + g, t * P:(t + 1) * P], rhs=STATE[:, g, :], start=True, stop=True))

            def decay_rows(h):
                if h >= 2:
                    pe.wait_ge(s_two, V2.of(f"db{h - 2}"))
                    pe.wait_ge(s_twoa, A2.of(f"of{h - 2}"))
                else:
                    pe.wait_ge(s_twoa, A2.of("g13"))
                for x in range(2):
                    m = mm_(G[2 * (h % 2) + x][:, :], lhsT=ident[0:16, 8 * x + h:8 * x + h + 1].to_broadcast([16, P]), rhs=DA[:, 0:S],
                            start=True, stop=True)
                P2.do(f"rw{h}", m)

            decay_rows(0)
            decay_rows(1)
            for h in range(8):
                if h < 6:
                    decay_rows(h + 2)
                pe.wait_ge(s_two, V2.of(f"dr{h}"))
                if h >= 2:
                    pe.wait_ge(s_two, V2.of(f"ya{h - 2}"))
                M = MB[h % 2]
                c = slice(h * HD, (h + 1) * HD)
                for t in range(TT):
                    T_ = slice(t * P, (t + 1) * P)
                    terms = [(M[:, j, T_], (XF if j < t else XB)[:, j, c]) for j in range(TT) if j != t]
                    terms += [(DFB(h)[0][:, T_], XF[:, t, c]), (DFB(h)[1][:, T_], XB[:, t, c])]
                    for n, (a, b) in enumerate(terms):
                        m = mm_(OB[h % 2][:, t * HD:(t + 1) * HD], lhsT=a, rhs=b, start=(n == 0), stop=(n == len(terms) - 1))
                P2.do(f"y{h}", m)
            pe.wait_ge(s_two, V2.of("sn3"))
            for b in range(4):
                if b >= 2:
                    pe.wait_ge(s_twoa, A2.of(f"ym{b - 2}"))
                for t in range(TT):
                    m = tr_(TR[b % 2][:, t * P:(t + 1) * P], Y[:, t, b * P:(b + 1) * P], ident)
                P2.do(f"ym{b}", m)

            pe.wait_ge(s_twoa, A2.of("ym3"))
            out_products("out2", "x4")
            by_feature("x5", Hn, TT, lambda: pe.wait_ge(ln_dve, st("ln_ffn", "ln") + 18))

            mlp_products("ffn2", "x5")

        def hidden_tile(x, i, e):
            at = 2 * i + e if isinstance(i, int) else i * 2 + e if e >= 0 else (i - 1) * 2 + (e + 2)
            return x[:, at:at + 1, :] if isinstance(at, int) else x[:, bass.ds(at, 1), :]

        def scalar_second(act, first_splits, deviation):
            ac = nc.scalar.activation

            def modulated(stage, dst, n_tiles, scale0, shift0):
                base = st(stage, "tr")
                for b in range(KT):
                    act.wait_ge(tr_ready, base + b + 1)
                    ac(dst[:, b, :], TR[b % 2][:, 0:n_tiles * P], ACT.Identity, scale=modc[:, scale0 + b:scale0 + b + 1],
                       bias=modc[:, shift0 + b:shift0 + b + 1]).then_inc(tr_out, 1)

            for q in range(4):
                act.wait_ge(s_twop, P2.of(f"gb{q}"))
                A2.do(f"gb{q}", ac(gbc[:, q * 512:(q + 1) * 512], G[q][:, :], ACT.Copy))
            deviation("ln_ctx", 8)
            modulated("x_ctx", CT, 2, 56, 48)
            deviation("ln_x")
            modulated("x4", XT, TT, 8, 0)
            q0 = st("w_in", "quarters")
            act.wait_ge(s_twop, P2.of("dtc"))
            A2.do("dtc", ac(DT[:, S:S + CTX], G[2][0:16, 0:CTX], ACT.Identity, bias=col("dt_bias", 0, 16)))
            act.wait_ge(quarters, q0 + 4)
            A2.do("dtl", ac(DT[:, 0:S], G[0][0:16, :], ACT.Identity, bias=col("dt_bias", 0, 16)))

            def conv_tanh(m, w):
                act.wait_ge(s_two, V2.of(f"{w}{m}b"))
                if m >= 2:
                    act.wait_ge(s_two, V2.of(f"{w}{m - 2}s"))
                A2.do(f"{w}{m}t", ac(TH(w, m), XBC(w, m), ACT.Tanh))

            act.wait_ge(s_two, V2.of("halfw"))
            for m in range(9):
                if m < 8:
                    act.wait_ge(quarters, q0 + 4 + m + 1)
                for k, w in CONV:
                    if k == m:
                        ps = G[m % 2][:, :] if w == "l" else G[2 + m % 2][:, 0:CTX]
                        A2.do(f"{w}{m}f", ac(XBC(w, m), ps, ACT.Identity, scale=col("conv", 3 * m + 1), bias=col("conv_b", m)))
                for k, w in CONV:
                    if k == m - 1:
                        conv_tanh(k, w)
            A2.do("alog", ac(nega[:, 0:1], col("a_log", 0, 16), ACT.Exp))
            act.wait_ge(s_two, V2.of("dabs"))
            A2.do("dexp", ac(DA, DA, ACT.Exp, scale=-1.0))
            act.wait_ge(s_twoa, A2.of("dexp"))
            A2.do("dln", ac(DA, DA, ACT.Ln, bias=1.0))
            for n in range(4):
                act.wait_ge(quarters, q0 + 12 + n + 1)
                if n < 2:
                    A2.do(f"fn{n}", ac(fnetT[:, n, :], G[n % 2][:, :], ACT.Copy))
                else:
                    act.wait_ge(s_twog, G2.of("pz"))
                    A2.do(f"po{n - 2}", ac(PB[:, n - 2, 8:8 + S], G[n % 2][:, :], ACT.Copy))
            act.wait_ge(s_two, V2.of("tt1"))
            A2.do("wexp", ac(CF[:, S:S + CTX], DA[:, S:S + CTX], ACT.Exp, scale=-1.0, bias=nega[:, 3:4]))
            for t in range(TT):
                act.wait_ge(quarters, q0 + 16 + t + 1)
                A2.do(f"z{t}h", ac(Z[:, t, :], G[t % 2][:, :], ACT.Copy, scale=0.5))
                act.wait_ge(s_twoa, A2.of(f"z{t}h"))
                act.wait_ge(s_two, V2.of("l7s") if t < 2 else V2.of(f"z{t - 2}"))
                A2.do(f"z{t}t", ac(qb[:, t % 2, :], Z[:, t, :], ACT.Tanh))
            for t in range(TT):
                act.wait_ge(s_twop, P2.of(f"fab{t}"))
                A2.do(f"fab{t}", ac(FAB[:, t, :], G[t][:, :], ACT.Copy))
            for ft in range(2):
                act.wait_ge(quarters, st("dft", "quarters") + 2 * ft + 2)
                A2.do(f"yf{ft}", ac(XT[:, 4 + ft, :], TR[ft][:, :], ACT.Copy))
            act.wait_ge(s_two, V2.of("tks"))
            A2.do("ecs", ac(ecs[:, :, :].rearrange("p a b -> p (a b)"), tks[:, 0:64], ACT.Exp))
            for t in range(TT):
                act.wait_ge(s_twop, P2.of(f"xt{t}"))
                A2.do(f"xt{t}", ac(XS[:, t, :], G[t][:, :], ACT.Copy))
            for t in range(2):
                act.wait_ge(s_twop, P2.of(f"ct{t}"))
                A2.do(f"ct{t}", ac(CXT[:, t, :], TR[t][:, :], ACT.Copy))
            act.wait_ge(s_twop, P2.of("bt"))
            A2.do("bt", ac(Btok, OB[0][:, :], ACT.Copy))
            for i in range(2):
                act.wait_ge(s_twop, P2.of(f"yp{i}"))
                A2.do(f"yp{i}", ac(XT[:, 6 + i, :], G[i][:, :], ACT.Copy, scale=col("pool", i)))
            for g in range(2):
                act.wait_ge(s_twop, P2.of(f"st{g}"))
                A2.do(f"st{g}", ac(STATE[:, g, :], OB[g][:, :], ACT.Copy))
            act.wait_ge(s_twog, G2.of("sub"))
            for g in range(2):
                for j in range(TT):
                    act.wait_ge(s_twop, P2.of(f"g{g}{j}"))
                    A2.do(f"g{g}{j}", ac(SC[:, g, j, :], G[j][:, :], ACT.Copy))
            for h in range(8):
                act.wait_ge(s_two, V2.of(f"db{h}"))
                if h >= 2:
                    act.wait_ge(s_twop, P2.of(f"y{h - 2}"))
                elif h == 1:
                    act.wait_ge(s_twop, P2.of("st1"))
                M = MB[h % 2]
                for j in range(TT):
                    if j:
                        m = ac(M[:, j, 0:j * P], G[2 * (h % 2) + 1][:, 0:j * P], ACT.Exp, bias=ncs[:, j, 8 + h:9 + h])
                    if j < 3:
                        m = ac(M[:, j, (j + 1) * P:S], G[2 * (h % 2)][:, (j + 1) * P:S], ACT.Exp, bias=ncs[:, j, h:h + 1])
                A2.do(f"of{h}", m)
                act.wait_ge(s_two, V2.of(f"dm{h}"))
                A2.do(f"ed{h}", ac(diagonal(M), qb[:, h % 2, :].rearrange("p (a b) -> p a b", a=TT), ACT.Exp))
            act.wait_ge(s_two, V2.of("si"))
            A2.do("ss", ac(ys[:, 2, :, :], ys[:, 0, :, :], ACT.Sqrt))
            for b in range(4):
                act.wait_ge(s_twop, P2.of(f"ym{b}"))
                A2.do(f"ym{b}", ac(XT[:, b, :], TR[b % 2][:, :], ACT.Copy, scale=col("norm", b)))
            deviation("out2")
            deviation("ln_ffn")
            base, v = st("x5", "tr"), 0
            for b in range(KT):
                act.wait_ge(tr_ready, base + b + 1)
                if b >= 2:
                    act.wait_ge(tr_out, base + b - 1)
                for dst, sem_ in ((act_buf[b % 2], x_val), (XTh[:, b, :], xt_hi)):
                    ac(dst, TR[b % 2][:, :], ACT.Identity, scale=modc[:, 32 + b:33 + b], bias=modc[:, 24 + b:25 + b]).then_inc(sem_, 1)
            first_splits("ffn2")

            n, u, q, a0, h = 0, 0, st("ffn2", "quarters"), st("ffn2", "act"), st("ffn2", "hidden")
            Q = SPLIT0["ffn2"]

            def grids(i, first=False):
                pads(i, 0)
                pads(i, 1)
                if not first:
                    gelu(i, -1)
                    high_hidden(i, -1)
                pads(i, 2)
                pads(i, 3)
                gelu(i, 1)
                high_hidden(i, 0)

            def pads(i, m):
                high_split(act, "ffn2", n + m + 3, i)
                act.wait_ge(quarters, i * 4 + (q + n + m + 1))
                if m % 2 == 0:
                    act.wait_ge(hidden, i * 2 + (h + (u + m) // 2 - 1))
                ps = G[m][:, :].rearrange("p (r c) -> p r c", c=GRID_W)
                ac(PADS[m][:, 1:9, 1:65], ps, ACT.Copy).then_inc(conv_first, 1)
                f = C2["ffn"] + 10 * (u + m)
                w, b = (cols2[:, bass.ds(i * 40 + (f + x), 1)] for x in (4, 9))
                ac(SUMS[m], G[m][:, :], ACT.Identity, scale=w, bias=b).then_inc(act_out, 1)

            def gelu(i, m):
                act.wait_ge(conv_steps, i * 32 + 8 * (u + m + 1))
                ac(SUMS[m % 4], SUMS[m % 4], ACT.Gelu_apprx_tanh).then_inc(gelu_done, 1)

            def high_hidden(i, e):
                act.wait_ge(hid_steps, i * 2 + (h + u // 2 + e + 1))
                ac(hidden_tile(Hh, i, e), SUMS[2 * (e % 2)].unsqueeze(1), ACT.Copy).then_inc(hid_hi, 1)

            act.wait_ge(s_twog, G2.of("padz"))
            for up, down in PARTS["ffn2"]:
                grids(0, True)
                with act.Fori(1, up // 4) as i:
                    grids(i)
                gelu(up // 4, -1)
                high_hidden(up // 4, -1)
                n, u = n + up, u + up
                for j in range(down):
                    if n + j + 3 < n_quarters("ffn2"):
                        high_split(act, "ffn2", n + j + 3)
                n += down
            deviation("ffn2")

        def vector_second(dve, residual, layer_norm):
            tt, ts, stt = nc.vector.tensor_tensor, nc.vector.tensor_scalar, nc.vector.scalar_tensor_tensor

            def own(name):
                dve.wait_ge(s_two, V2.of(name))

            dve.wait_ge(ada_moved, 16)
            for n, c in enumerate((8, 32, 56)):
                V2.do(f"mod{n + 1}", ts(modc[:, c:c + 8], modc[:, c:c + 8], 1.0, None, ALU.add))
            for b in range(16):
                c = 16 + b if b < 8 else 32 + b
                if b >= 8:
                    dve.wait_ge(s_twop, P2.of(f"gb{(b - 8) // 4}"))
                V2.do(f"dgb{b}", ts(DGB(b), ident, modc[:, c:c + 1], None, ALU.mult))
            V2.do("halfw", ts(cols2[:, 84:116], cols2[:, 84:116], 0.5, None, ALU.mult))
            V2.do("bdz", nc.vector.memset(bd[:, :, :], 0.0))
            V2.do("pwz", nc.vector.memset(poolw[:, :, :], 0.0))
            dve.wait_ge(s_ctx, 16)
            own("mod3")
            layer_norm("ln_ctx", EPS_2, n_tiles=2, src=ctok, dst=ctok)
            layer_norm("ln_x", EPS_2, src=X, dst=Hn)

            own("halfw")
            for m in range(9):
                for k, w in CONV:
                    if k == m:
                        n = S if w == "l" else CTX
                        ps = G[m % 2] if w == "l" else G[2 + m % 2]
                        y = XBC(w, m)
                        dve.wait_ge(s_twoa, A2.of(f"{w}{m}f"))
                        V2.do(f"{w}{m}a", stt(out=y[:, 1:n], in0=ps[:, 0:n - 1], scalar=col("conv", 3 * m), in1=y[:, 1:n], op0=ALU.mult, op1=ALU.add))
                        own(f"{w}{m}a")
                        V2.do(f"{w}{m}b", stt(out=y[:, 0:n - 1], in0=ps[:, 1:n], scalar=col("conv", 3 * m + 2), in1=y[:, 0:n - 1], op0=ALU.mult, op1=ALU.add))
                for k, w in CONV:
                    if k == m - 1:
                        y = XBC(w, k)
                        dve.wait_ge(s_twoa, A2.of(f"{w}{k}t"))
                        V2.do(f"{w}{k}s", stt(out=y, in0=TH(w, k), scalar=1.0, in1=y, op0=ALU.add, op1=ALU.mult))
            dve.wait_ge(s_twoa, A2.of("dtl"))
            V2.do("dneg", ts(DA, DT, -1.0, None, ALU.mult))
            own("dneg")
            V2.do("dabs", tt(out=DA, in0=DA, in1=DT, op=ALU.max))
            own("dabs")
            V2.do("dmax", ts(DT, DT, 0.0, None, ALU.max))
            dve.wait_ge(s_twoa, A2.of("dln"))
            own("dmax")
            V2.do("dt", tt(out=DT, in0=DT, in1=DA, op=ALU.add))
            V2.do("nega", ts(nega[:, 1:2], nega[:, 0:1], -1.0, None, ALU.mult))
            own("nega")
            V2.do("dA", ts(DA, DT, nega[:, 1:2], None, ALU.mult))
            own("dA")
            scan = nc.vector.tensor_tensor_scan
            for name, o, a, b, flip in (("cf", CF, 0, S, 0), ("cfc", CF, S, S + CTX, 0), ("rv", RV, 0, S, 1), ("rvc", RV, S, S + CTX, 1)):
                src, dst = DA[:, a:b], o[:, a:b]
                if flip:
                    src, dst = src[:, ::-1], dst[:, ::-1]
                V2.do(name, scan(out=dst, data0=src, data1=src, initial=0.0, op0=ALU.add, op1=ALU.bypass))
            own("rvc")
            V2.do("c0", ts(CF, CF, col("fwd", 0, 16), None, ALU.mult))
            own("c0")
            V2.do("cs", stt(out=DA, in0=RV, scalar=col("bwd", 0, 16), in1=CF, op0=ALU.mult, op1=ALU.add))
            own("cs")
            V2.do("tt0", ts(nega[:, 2:3], DA[:, S + CTX - 1:S + CTX], col("fwd", 0, 16), None, ALU.mult))
            own("tt0")
            V2.do("tt1", stt(out=nega[:, 3:4], in0=DA[:, S:S + 1], scalar=col("bwd", 0, 16), in1=nega[:, 2:3], op0=ALU.mult, op1=ALU.add))
            dve.wait_ge(s_twoa, A2.of("wexp"))
            V2.do("wc", tt(out=CF[:, S:S + CTX], in0=CF[:, S:S + CTX], in1=DT[:, S:S + CTX], op=ALU.mult))
            dve.wait_ge(s_twop, P2.of("bdp"))
            own("bdz")
            for n in range(8):
                cs, g = n // 4, n % 4
                r = (g % 2) * HD
                V2.do(f"bd{n}", nc.vector.tensor_copy(bd[r:r + HD, g // 2, cs * P + r:cs * P + r + HD],
                                                      TR[0][r:r + HD, cs * 256 + g * HD:cs * 256 + (g + 1) * HD]))
            for t in range(TT):
                dve.wait_ge(s_twoa, A2.of(f"z{t}t"))
                V2.do(f"z{t}", stt(out=Z[:, t, :], in0=qb[:, t % 2, :], scalar=1.0, in1=Z[:, t, :], op0=ALU.add, op1=ALU.mult))
            dve.wait_ge(s_twop, P2.of("tks"))
            V2.do("tks", nc.vector.tensor_copy(tks[:, :], OB[1][:, 0:160]))
            own("tks")
            V2.do("ncs", ts(ncs[:, :, :].rearrange("p a b -> p (a b)"), tks[:, 0:64], -1.0, None, ALU.mult))
            dtt = tks[:, 64:128].rearrange("p (t n) -> p t n", t=TT)
            wct = tks[:, 128:160].rearrange("p (t n) -> p t n", t=2)

            def heads_(ap, n=4):
                return ap.rearrange("p (h d) -> p h d", h=n)

            def over(ap, n, d):
                return ap.unsqueeze(2).to_broadcast([P, n, d])

            for n in range(8):
                t, g, x = n // 4, (n // 2) % 2, n % 2
                dve.wait_ge(s_twoa, A2.of(f"ct{t}"))
                V2.do(f"xw{n}", tt(out=heads_(XW[:, 2 * t + g, x * 256:(x + 1) * 256]), in0=heads_(CXT[:, t, g * 256:(g + 1) * 256]),
                                   in1=over(wct[:, t, 8 * x + 4 * g:8 * x + 4 * g + 4], 4, HD), op=ALU.mult))
            own("xw7")
            dve.wait_ge(s_twoa, A2.of("fab3"))
            for x, dst in ((0, XF), (1, XB)):
                for t in range(TT):
                    dve.wait_ge(s_twoa, A2.of(f"xt{t}"))
                    V2.do(f"x{'fb'[x]}{t}", tt(out=heads_(dst[:, t, :], 8), in0=heads_(XS[:, t, :], 8),
                                              in1=over(dtt[:, t, 8 * x:8 * x + 8], 8, HD), op=ALU.mult))
            dve.wait_ge(s_twoa, A2.of("ecs"))
            for g in range(2):
                for t in range(TT):
                    dve.wait_ge(s_twop, P2.of(f"yo{g}{t}"))
                    y = heads_(Y[:, t, g * 256:(g + 1) * 256])
                    if g or t:
                        own(f"yo{g if t else g - 1}{(t - 1) % 4}c")
                    V2.do(f"yo{g}{t}a", tt(out=y, in0=heads_(TR[t % 2][:, 0:256]), in1=over(ecs[:, t, 4 * g:4 * g + 4], 4, HD), op=ALU.mult))
                    V2.do(f"yo{g}{t}b", tt(out=heads_(ogf[:, 0:256]), in0=heads_(TR[t % 2][:, 256:512]), in1=over(ecs[:, t, 8 + 4 * g:12 + 4 * g], 4, HD), op=ALU.mult))
                    own(f"yo{g}{t}b")
                    V2.do(f"yo{g}{t}c", tt(out=y, in0=y, in1=heads_(ogf[:, 0:256]), op=ALU.add))

            def head_out(h):
                y = Y[:, :, h * HD:(h + 1) * HD]
                dve.wait_ge(s_twop, P2.of(f"y{h}"))
                V2.do(f"ya{h}", tt(out=y, in0=y, in1=OB[h % 2][:, 0:256].rearrange("p (t d) -> p t d", t=TT), op=ALU.add))

            def diagonal_exponents(h):
                q = [qb[:, h % 2, :].rearrange("p (a b) -> p a b", a=TT), ogf.rearrange("p (a b) -> p a b", a=TT)]
                dve.wait_ge(s_twop, P2.of(f"rw{h}"))
                own(f"dm{h - 1}" if h else "yo13c")
                if h >= 2:
                    dve.wait_ge(s_twoa, A2.of(f"ed{h - 2}"))
                for x, name in enumerate(("da", "db")):
                    V2.do(f"{name}{h}", tt(out=q[x], in0=G[2 * (h % 2) + x][:, :].rearrange("p (a b) -> p a b", a=TT),
                                           in1=over(ncs[:, :, 8 * x + h], TT, P), op=ALU.add))
                own(f"db{h}")
                V2.do(f"dm{h}", tt(out=q[0], in0=q[0], in1=q[1], op=ALU.min))

            diagonal_exponents(0)
            for h in range(8):
                if h < 7:
                    diagonal_exponents(h + 1)
                M = MB[h % 2]
                dve.wait_ge(s_twoa, A2.of(f"ed{h}"))
                V2.do(f"mm{h}", tt(out=M[:, :, :], in0=M[:, :, :], in1=SC[:, h // 4, :, :], op=ALU.mult))
                own(f"mm{h}")
                if h >= 2:
                    dve.wait_ge(s_twop, P2.of(f"y{h - 2}"))
                for x, (name, mask) in enumerate((("df", "upper"), ("dr", "lower"))):
                    V2.do(f"{name}{h}", tt(out=DFB(h)[x].rearrange("p (a b) -> p a b", a=TT), in0=diagonal(M),
                                           in1=tab(mask).unsqueeze(1).to_broadcast([P, TT, P]), op=ALU.mult))
                if h:
                    head_out(h - 1)
            head_out(7)
            for t in range(TT):
                y = Y[:, t, :]
                own(f"sr{t - 1}" if t else "ya7")
                V2.do(f"sk{t}", tt(out=heads_(ogf, 8), in0=heads_(XS[:, t, :], 8), in1=over(drow[:, :], 8, HD), op=ALU.mult))
                own(f"sk{t}")
                V2.do(f"sa{t}", tt(out=y, in0=y, in1=ogf, op=ALU.add))
                own(f"sa{t}")
                V2.do(f"sz{t}", tt(out=y, in0=y, in1=Z[:, t, :], op=ALU.mult))
                own(f"sz{t}")
                V2.do(f"sq{t}", tt(out=ogf, in0=y, in1=y, op=ALU.mult))
                own(f"sq{t}")
                V2.do(f"sr{t}", nc.vector.tensor_reduce(ys[:, 0, t, :], heads_(ogf, 2), AX.X, ALU.add))
            own("sr3")
            V2.do("sv", ts(ys[:, 1, :, :], ys[:, 0, :, :], 1.0 / 256, EPS_2, ALU.mult, ALU.add))
            own("sv")
            V2.do("si", nc.vector.reciprocal(ys[:, 0, :, :], ys[:, 1, :, :]))
            dve.wait_ge(s_twoa, A2.of("ss"))
            for t in range(TT):
                V2.do(f"sn{t}", tt(out=heads_(Y[:, t, :], 2), in0=heads_(Y[:, t, :], 2), in1=over(ys[:, 2, t, :], 2, 256), op=ALU.mult))

            def gated_residual(x, ps, g, at, alpha=ALPHA_2):
                dve.wait_ge(dve_out, at + (st("out2", "dve") - 1))
                tt(out=ogf, in0=ps, in1=g, op=ALU.mult).then_inc(res_steps, 1)
                dve.wait_ge(res_steps, at)
                stt(out=x, in0=x, scalar=alpha, in1=ogf, op0=ALU.mult, op1=ALU.add).then_inc(dve_out, 1)

            q0 = st("out2", "quarters")
            for n in range(8):
                h, t = n // 4, n % 4
                dve.wait_ge(quarters, q0 + n + 1)
                gated_residual(X[:, t, h * 512:(h + 1) * 512], G[t][:, :], gbc[:, h * 512:(h + 1) * 512], n + 1)
            layer_norm("out2", EPS_2)
            layer_norm("ln_ffn", EPS_2, src=X, dst=Hn, again=True)

            base = st("x5", "tr")
            for b in range(KT):
                dve.wait_ge(x_val, b + 1)
                dve.wait_ge(xt_hi, 16 + b + 1)
                tt(out=XTl[:, b, :], in0=act_buf[b % 2], in1=XTh[:, b, :], op=ALU.subtract).then_inc(tr_out, 1)

            a0, q0, h0, u = st("ffn2", "act"), st("ffn2", "quarters"), st("ffn2", "hidden"), 0

            def taps(i, pair, xs):
                for x in xs:
                    for e in range(2):
                        m = 2 * pair + e
                        if x == 0:
                            dve.wait_ge(act_out, i * 4 + (a0 + u + m + 1))
                        else:
                            dve.wait_ge(conv_steps, i * 32 + (8 * u + 16 * pair + 2 * x + e - 1))
                        tap = (0, 1, 2, 3, 5, 6, 7, 8)[x]
                        r, c = tap // 3, tap % 3
                        w = cols2[:, bass.ds(i * 40 + (C2["ffn"] + 10 * (u + m) + tap), 1)] if not isinstance(i, int) else \
                            cols2[:, C2["ffn"] + 10 * (u + m) + tap:C2["ffn"] + 10 * (u + m) + tap + 1]
                        y = SUMS[m].rearrange("p (r c) -> p r c", c=GRID_W)
                        stt(out=y, in0=PADS[m][:, r:r + 8, c:c + GRID_W], scalar=w, in1=y, op0=ALU.mult, op1=ALU.add).then_inc(conv_steps, 1)

            def product(i, e):
                dve.wait_ge(gelu_done, i * 2 + (u // 2 + e + 1))
                m = 2 * (e % 2)
                tt(out=SUMS[m], in0=SUMS[m], in1=SUMS[m + 1], op=ALU.mult).then_inc(hid_steps, 1)

            def low_hidden(i, e):
                dve.wait_ge(hid_hi, i * 2 + (h0 + u // 2 + e + 1))
                tt(out=hidden_tile(Hl, i, e), in0=SUMS[2 * (e % 2)].unsqueeze(1), in1=hidden_tile(Hh, i, e), op=ALU.subtract).then_inc(hidden, 1)

            def four_tiles(i, first=False):
                for pair in range(2):
                    taps(i, pair, range(0, 2))
                    if not (first and pair == 0):
                        product(i, pair - 1)
                    taps(i, pair, range(2, 5))
                    if not (first and pair == 0):
                        low_hidden(i, pair - 1)
                    taps(i, pair, range(5, 8))

            q = q0
            for part, (up, down) in enumerate(PARTS["ffn2"]):
                four_tiles(0, True)
                with dve.Fori(1, up // 4) as i:
                    four_tiles(i)
                product(up // 4, -1)
                low_hidden(up // 4, -1)
                q, u = q + up + down, u + up
                for half in range(2):
                    dve.wait_ge(quarters, q - 1 + half)
                    for t in range(TT):
                        gated_residual(X[:, t, half * 512:(half + 1) * 512], BANKS[half][t][:, :], gbc[:, 1024 + half * 512:1536 + half * 512],
                                       8 + 8 * part + 4 * half + t + 1, 1.0 if part else ALPHA_2)
            layer_norm("ffn2", EPS_2)

        @block.sync
        def _(sp):
            sp.dma_start(X[:, :, :], A["x"].rearrange("o (t p) d -> p (o t) d", p=P)).then_inc(s_x, 16)
            sp.dma_start(table[:, :], A["table"]).then_inc(s_const, 16)
            sp.dma_start(cols[:, :], A["cols"]).then_inc(s_const, 16)
            def load(s):
                sp.dma_start(ring[:, s % 2, :], A["slabs"][s]).then_inc(slab_in[s % 2], 16)

            def slabs(first, last, q0):
                with sp.Fori(0, (last - first) // 2) as i:
                    for e in range(2):
                        s = first + e
                        sp.wait_ge(quarters, i * 8 + (q0 + 4 * e - 4))
                        sp.wait_ge(s_x, 16)
                        sp.dma_start(ring[:, s % 2, :], A["slabs"][bass.ds(i * 2 + s, 1), :, :].rearrange("o p c -> p (o c)")).then_inc(slab_in[s % 2], 16)
                if (last - first) % 2:
                    sp.wait_ge(quarters, q0 + 4 * (last - first) - 8)
                    load(last - 1)

            def raw_chunks(stage):
                c0, n = SPLIT0[stage] // 2, n_quarters(stage) // 2
                sp.wait_ge(quarters, st(stage, "quarters"))
                for s in range(2):
                    sp.dma_start(ring[:, 1, s * 2048:(s + 1) * 2048], A["chunks"][c0 + s]).then_inc(raw_in[s], 16)
                with sp.Fori(1, n // 2) as i:
                    for s in range(2):
                        sp.wait_ge(w_lo, i * 4 + (2 * c0 + 2 * s - 2))
                        sp.wait_ge(s_x, 16)
                        sp.dma_start(ring[:, 1, s * 2048:(s + 1) * 2048], A["chunks"][bass.ds(i * 2 + (c0 + s), 1), :, :].rearrange("o p c -> p (o c)")).then_inc(raw_in[s], 16)
                if n % 2:
                    sp.wait_ge(w_lo, 2 * (c0 + n - 1) - 2)
                    sp.dma_start(ring[:, 1, 0:2048], A["chunks"][c0 + n - 1]).then_inc(raw_in[0], 16)

            def after_mlp(stage, s):
                for e in range(2):
                    if (s + e) % 2:
                        sp.wait_ge(w_lo, SPLIT0[stage] + 64)
                    else:
                        sp.wait_ge(quarters, st(stage, "quarters") + 48)
                    load(s + e)

            def tile(ap):
                return ap.rearrange("p o n -> p (o n)")

            def feed(name, n_iter, n, loads, lead=None):
                def unit(i, j):
                    u0 = st(name, "units")
                    aps = [(d, s) for d, s in loads(i, j)]
                    for d, s in aps:
                        sp.dma_start(d, s).then_inc(qk_in[j % 2], 16)
                for j in range(2):
                    if st(name, "units"):
                        sp.wait_ge(sc_ready, 4 * (st(name, "units") + j - 1))
                    unit(0, j)
                for j in range(2, n):
                    sp.wait_ge(sc_ready, 4 * (st(name, "units") + j - 1))
                    unit(0, j)
                with sp.Fori(1, n_iter) as i:
                    for j in range(n):
                        sp.wait_ge(sc_ready, i * (4 * n) + 4 * (st(name, "units") + j - 1))
                        unit(i, j)

            load(0)
            load(1)
            slabs(2, SLAB["proj1"][0], 8)
            sp.wait_ge(act_out, st("proj0", "act") + 24)
            sp.wait_ge(rope_dve, 2 * len(ROPED0))
            feed("diff", 4, 2, lambda i, c: [
                (qb[0:HD, c, :], tile(QT[c * HD:(c + 1) * HD, bass.ds(i, 1), :])),
                (kb[0:HD, c, :], tile(KTT[c * HD:(c + 1) * HD, bass.ds(i, 1), :]))])
            feed("nsa", 2, 8, lambda r, j: [
                (qb[0:HD, j % 2, :], tile(QT[((j // 2) % 2) * HD:((j // 2) % 2) * HD + HD, bass.ds(r + (4 + 2 * (j // 4)), 1), :]))])
            raw_chunks("mlp0")
            after_mlp("mlp0", SLAB["proj1"][0])
            slabs(SLAB["proj1"][0] + 2, SLAB["w_in"][0], st("proj1", "quarters") + 8)
            sp.wait_ge(act_out, st("proj1", "act") + 16)
            sp.wait_ge(crow_in, 80)
            feed("fox", 8, 2, lambda i, e: [
                (qb[0:HD, e, :], tile(QT[e * HD:(e + 1) * HD, bass.ds(i, 1), :])),
                (kb[0:HD, e, :], tile(KTT[e * HD:(e + 1) * HD, bass.ds(i, 1), :])),
                (qb[HD + 1:HD + 2, e, :], A["crow"][bass.ds(i * 2 + e, 1), 1, :]),
                (kb[HD:HD + 1, e, :], A["crow"][bass.ds(i * 2 + e, 1), 0, :])])
            raw_chunks("mlp1")
            after_mlp("mlp1", SLAB["w_in"][0])
            slabs(SLAB["w_in"][0] + 2, SLAB["out2"][0] + 2, st("w_in", "quarters") + 8)
            raw_chunks("ffn2")
            sp.wait_ge(ln_dve, st.total["ln"])
            sp.dma_start(out.rearrange("o (t p) d -> p (o t) d", p=P), X[:, :, :]).then_inc(s_out, 16)
            sp.wait_ge(s_out, 16)

        @block.gpsimd
        def _(gp):
            gp.dma_start(w2[:, :, :, 0:HD], A["nsa_cmp_w2"].rearrange("o j (h p) d -> p (o j) h d", p=P)).then_inc(s_small_in, 16)
            gp.dma_start(w2[:, :, :, HD:P], A["nsa_cmp_w2"].rearrange("o j (h p) d -> p (o j) h d", p=P)).then_inc(s_small_in, 16)
            gp.dma_start(lamrow[:, :, :, :], A["diff_lambda"].rearrange("o (a b) d -> o (a b d)", a=2).partition_broadcast(P)
                         .rearrange("p o (a b d) -> p (o a) b d", a=2, b=2)).then_inc(s_small_in, 16)
            gp.dma_start(subln[:, :], A["diff_subln"].partition_broadcast(P).rearrange("p o d -> p (o d)")).then_inc(s_small_in, 16)
            gp.dma_start(cols2[:, :], A["cols2"]).then_inc(s_small_in, 16)

            def gain_bias(n, gain, bias):
                if n:
                    gp.wait_ge(ln_dve, 26 * n if n < 5 else st("ln_ffn", "ln"))
                gp.dma_start(rows[:, 0, :], gain.partition_broadcast(P)).then_inc(gb_in, 16)
                gp.dma_start(rows[:, 1, :], bias.partition_broadcast(P)).then_inc(gb_in, 16)

            gain_bias(0, A["ln_gain"][0, 0, :], A["ln_bias"][0, 0, :])

            gp.wait_ge(s_const, CONSTS)
            for r, (g, *_) in enumerate(ROPED0):
                gp.wait_ge(act_out, st("proj0", "act") + g + 1)
                if r >= 2:
                    gp.wait_ge(rope_dve, 2 * (r - 2) + 2)
                nc.gpsimd.tensor_tensor(out=SC[:, 0, 2 + r % 2, :], in0=SC[:, 0, r % 2, :], in1=tab("cos"),
                                        op=ALU.mult).then_inc(rope_cos, 1)

            gp.wait_ge(act_out, st("proj0", "act") + 24)
            gp.wait_ge(quarters, 24)
            for j in range(2):
                for g in range(2):
                    src = KTT[g * HD:(g + 1) * HD, 4 + j, :]
                    gp.dma_start(XT[0:HD, 2 * j + g, :], src).then_inc(cmp_in, 16)
                    gp.dma_start(XT[HD:P, 2 * j + g, 0:S - 1], src[:, 1:S]).then_inc(cmp_in, 16)
            gp.wait_ge(rope_dve, 2 * len(ROPED0))
            for kind in range(2):
                for g in range(2):
                    gp.dma_start(KSW[:, kind, g, :], KTT[g * HD:(g + 1) * HD, 6 + kind, :]).then_inc(ksw_in, 16)

            gp.wait_ge(gb_in, 32)
            gain_bias(1, A["ln_gain"][0, 1, :], A["ln_bias"][0, 1, :])

            def ada_loads(parts):
                def job(part, j):
                    for q in range(4):
                        if part or q > 1 or not isinstance(j, int) or j:
                            gp.wait_ge(ada_steps, j * 8 + (32 * part + 2 * q - 2))
                        src = A["ada"][part if isinstance(j, int) and j == 3 else j + 3 * part if isinstance(j, int) else bass.ds(j + 3 * part, 1), :, q * 1024:(q + 1) * 1024]
                        if len(src.shape) == 3:
                            src = src.rearrange("o p c -> p (o c)")
                        gp.dma_start(ADW(q % 2), src).then_inc(ada_in[q % 2], 16)

                for part in parts:
                    job(part, 0)
                    with gp.Fori(1, 3) as j:
                        job(part, j)
                    job(part, 3)

            gp.wait_ge(o_used, 24)
            ada_loads((0, 1))
            gp.wait_ge(s_small, SMALL["fox"])
            gp.wait_ge(s_small_in, SMALL_INPUTS)
            gp.dma_start(A["crow"], crow[:, 1:3, :]).then_inc(crow_in, 16)
            gp.wait_ge(crow_in, 16)
            for e in range(2):
                gp.dma_start(qb[HD:HD + 1, e, :], A["ones"][0:1, :]).then_inc(crow_in, 16)
                gp.dma_start(kb[HD + 1:HD + 2, e, :], A["ones"][1:2, :]).then_inc(crow_in, 16)
            gain_bias(2, A["ln_gain"][1, 0, :], A["ln_bias"][1, 0, :])
            ada_loads((2, 3))
            gain_bias(3, A["ln_gain"][1, 1, :], A["ln_bias"][1, 1, :])
            gpsimd_second(gp, gain_bias)

        PTS = [XT[:, 0:4, :], XT[:, 4:8, :]]
        TRS = [TR[0], TR[1], G[2], G[3]]

        def units(engine, n_iter, n, slot):
            for j in range(n):
                slot(0, j, (0, j + 1) if j + 1 < n else (1, 0), (0, j - 1) if j else None)
            if n_iter > 2:
                with engine.Fori(1, n_iter - 1) as i:
                    for j in range(n):
                        slot(i, j, (i, j + 1) if j + 1 < n else (i + 1, 0), (i, j - 1))
            i = n_iter - 1
            for j in range(n):
                slot(i, j, (i, j + 1) if j + 1 < n else None, (i, j - 1) if j else (i - 1, n - 1))

        def pe_attend(pe, name, n_iter, n, depth, q_of, k_of, v_of, hd, per_slot):
            u0 = st(name, "units")
            in0 = LOADS[name]

            def number(i, j, times):
                return i * (times * n) + times * (u0 + j)

            def first(i, j, before):
                return isinstance(i, int) and i * n + u0 + j < before

            def score(unit, t):
                if unit is None:
                    return
                i, j = unit
                if t == 0:
                    pe.wait_ge(qk_in[j % 2], in0 + i * (per_slot * 16 * (n // 2)) + per_slot * 16 * (j // 2 + 1))
                if not first(i, j, 1) or t >= 2:
                    pe.wait_ge(sc_used, number(i, j, 4) + t - 1)
                nc.tensor.matmul(G[t % 2][:, 0:(t + 1) * P], lhsT=q_of(i, j)[0:depth, t * P:(t + 1) * P],
                                 rhs=k_of(i, j)[0:depth, 0:(t + 1) * P], start=True, stop=True).then_inc(sc_ready, 1)

            def transposed(i, j, t):
                pe.wait_ge(pr_ready, number(i, j, 4) + t + 1)
                if not first(i, j, 1):
                    pe.wait_ge(pt_dve if t < 2 else pt_act, number(i, j, 2) + t % 2 - 1)
                for b in range(t + 1):
                    mm = nc.tensor.transpose(TRS[t][:, b * P:(b + 1) * P], SC[:, j % 2, t, b * P:(b + 1) * P], ident)
                mm.then_inc(pt_ready, 1)

            def attended(unit):
                if unit is None:
                    return
                i, j = unit
                if not first(i, j, 2):
                    pe.wait_ge(o_used, number(i, j, 1) - 1)
                for t in range(TT):
                    pe.wait_ge(pt_dve if t < 2 else pt_act, number(i, j, 2) + t % 2 + 1)
                    for b in range(t + 1):
                        mm = nc.tensor.matmul(OB[j % 2][:, t * hd:(t + 1) * hd], lhsT=PTS[j % 2][:, t, b * P:(b + 1) * P],
                                              rhs=v_of(i, j, b), start=(b == 0), stop=(b == t))
                mm.then_inc(pv_ready, 1)

            def slot(i, j, after, before):
                score(after, 0)
                score(after, 1)
                transposed(i, j, 0)
                transposed(i, j, 1)
                score(after, 2)
                score(after, 3)
                transposed(i, j, 2)
                transposed(i, j, 3)
                attended(before)

            for t in range(TT):
                score((0, 0), t)
            units(pe, n_iter, n, slot)
            attended((n_iter - 1, n - 1))

        def act_attend(act, name, n_iter, n):
            u0 = st(name, "units")

            def number(i, j, times):
                return i * (times * n) + times * (u0 + j)

            def exp(unit, t):
                if unit is None:
                    return
                i, j = unit
                e = j % 2
                act.wait_ge(sc_used, number(i, j, 4) + t + 1)
                if t == 0 and not (isinstance(i, int) and i * n + u0 + j < 2):
                    act.wait_ge(rec_done, number(i, j, 1) - 1)
                nc.scalar.activation(SC[:, e, t, 0:(t + 1) * P], SC[:, e, t, 0:(t + 1) * P], ACT.Exp,
                                     scale=-1.0, bias=mn[:, e, t:t + 1], accum_out=sm[:, e, t:t + 1]).then_inc(pr_ready, 1)

            def copy(i, j, t):
                act.wait_ge(pt_ready, number(i, j, 4) + t + 1)
                if t == 2 and not (isinstance(i, int) and i * n + u0 + j < 2):
                    act.wait_ge(pv_ready, number(i, j, 1) - 1)
                nc.scalar.activation(PTS[j % 2][:, t, 0:(t + 1) * P], TRS[t][:, 0:(t + 1) * P], ACT.Copy).then_inc(pt_act, 1)

            def slot(i, j, after, before):
                exp(after, 0)
                exp(after, 1)
                exp(after, 2)
                copy(i, j, 2)
                exp(after, 3)
                copy(i, j, 3)

            for t in range(TT):
                exp((0, 0), t)
            units(act, n_iter, n, slot)

        def dve_attend(dve, name, n_iter, n, hd, finish):
            u0 = st(name, "units")
            step0, per = STEP0[name], STEPS[name]

            def number(i, j, times):
                return i * (times * n) + times * (u0 + j)

            def first(i, j):
                return isinstance(i, int) and i * n + u0 + j < 2

            def least(unit, t):
                if unit is None:
                    return
                i, j = unit
                e = j % 2
                if t == 0 and not first(i, j):
                    dve.wait_ge(pt_ready, number(i, j, 4) - 4)
                dve.wait_ge(sc_ready, number(i, j, 4) + t + 1)
                dve.sem_inc(sc_seen, 1)
                a, b = where["causal"]
                nc.vector.tensor_tensor_reduce(
                    out=SC[:, e, t, 0:(t + 1) * P], in0=G[t % 2][:, 0:(t + 1) * P], in1=table[:, b - (t + 1) * P:b],
                    scale=1.0, scalar=3.0e38, op0=ALU.add, op1=ALU.min, accum_out=mn[:, e, t:t + 1]).then_inc(sc_used, 1)

            def copy(i, j, t):
                if t == 0 and not first(i, j):
                    dve.wait_ge(pv_ready, number(i, j, 1) - 1)
                dve.wait_ge(pt_ready, number(i, j, 4) + t + 1)
                nc.vector.tensor_copy(PTS[j % 2][:, t, 0:(t + 1) * P], TRS[t][:, 0:(t + 1) * P]).then_inc(pt_dve, 1)

            def invert(i, j):
                dve.wait_ge(pr_ready, number(i, j, 4) + 4)
                if not first(i, j):
                    dve.wait_ge(o_used, number(i, j, 1) - 1)
                nc.vector.reciprocal(rs[:, j % 2, :], sm[:, j % 2, :]).then_inc(rec_done, 1)

            def output(unit):
                if unit is None:
                    return
                i, j = unit
                dve.wait_ge(pv_ready, number(i, j, 1) + 1)
                dve.wait_ge(rec_done, number(i, j, 1) + 1)
                finish(i, j, i * per[n] + (step0 + (per[j] if j >= 0 else per[n - 1] - per[n])))

            def slot(i, j, after, before):
                least(after, 0)
                least(after, 1)
                copy(i, j, 0)
                copy(i, j, 1)
                least(after, 2)
                least(after, 3)
                invert(i, j)
                output(before)

            for t in range(TT):
                least((0, 0), t)
            units(dve, n_iter, n, slot)
            output((n_iter - 1, n - 1))

        @block.tensor
        def _(pe):
            def slab_wait(s, pairs=0):
                pe.wait_ge(slab_in[s % 2], pairs * 16 + 16 * (s // 2 + 1))

            def stage_start(stage):
                a = st.before[stage].get("act", 0)
                v = st.before[stage].get("dve", 0)
                if a:
                    pe.wait_ge(act_out, a)
                if v:
                    pe.wait_ge(dve_out, v)

            def transposes(stage, src, ready):
                base = st(stage, "tr")
                for t in range(TT):
                    ready(t)
                    for h in range(2):
                        n = base + 2 * t + h
                        if n >= 2:
                            pe.wait_ge(tr_out, n - 1)
                        for b in range(4):
                            c = (4 * h + b) * P
                            mm = nc.tensor.transpose(TR[h][:, b * P:(b + 1) * P], src[:, t, c:c + P], ident)
                        mm.then_inc(tr_ready, 1)

            def token_groups(stage, s, bank0, half, pos):
                for t in range(TT):
                    if bank0 + t >= 4:
                        pe.wait_ge(dve_out, st(stage, "dve") + bank0 + t - 3)
                    for k in range(KT):
                        mm = nc.tensor.matmul(G[t][:, :], lhsT=XT[:, k, t * P:(t + 1) * P], rhs=slab(s)[:, k, :],
                                              start=(k == 0), stop=(k == KT - 1))
                    mm.then_inc(quarters, 1)

            def out_products(stage, tr_stage):
                stage_start(stage)
                pe.wait_ge(tr_out, st(tr_stage, "tr") + 8)
                s = SLAB[stage][0]
                for h in range(2):
                    slab_wait(s + h)
                    token_groups(stage, s + h, 4 * h, h, 0)

            def ada_sums(part, j):
                pe.wait_ge(ada_steps, j * 8 + (32 * part + 8))
                for q in range(4):
                    mm = nc.tensor.matmul(OB[0][:, q:q + 1], lhsT=ogf[:, q * P:(q + 1) * P], rhs=ones[:, 0:1], start=True, stop=True)
                mm.then_inc(ada_cols, 1)

            def mlp_products(stage, tr_stage, ada=None):
                stage_start(stage)
                pe.wait_ge(tr_out, st(tr_stage, "tr") + 8)
                Q, a, v, h = SPLIT0[stage], st(stage, "act"), st(stage, "dve"), st(stage, "hidden")
                per = 2 if stage == "ffn2" else 1
                for part, (up, down) in enumerate(PARTS[stage]):
                    if part:
                        pe.wait_ge(dve_out, v + 4)
                    with pe.Fori(0, up // 4) as i:
                        for m in range(4):
                            pe.wait_ge(w_lo, i * 4 + (Q + m + 1))
                            pe.wait_ge(act_out, i * 4 + (a + m - 3))
                            w = [x[:, m, :].rearrange("p (k c) -> p k c", k=KT) for x in (Wh, Wl)]
                            split_products(G[m][:, :], [(w[0][:, k, :], w[1][:, k, :], XTh[:, k, :], XTl[:, k, :])
                                                        for k in range(KT)]).then_inc(quarters, 1)
                        if ada is not None:
                            ada_sums(ada + part, i)
                    Q, a = Q + up, a + up
                    if ada is not None:
                        pe.wait_ge(ada_moved, 4 * (ada + part) + 4)
                    if part:
                        pe.wait_ge(dve_out, v + 8)
                    for j in range(down):
                        half = 1 - j % 2 if j < down - 2 else j % 2
                        pe.wait_ge(w_lo, Q + j + 1)
                        if j == 1:
                            pe.wait_ge(act_out, a)
                        w = [x[:, (Q + j) % 4, :].rearrange("p (k c) -> p k c", k=2) for x in (Wh, Wl)]
                        for k in range(2):
                            n = 2 * (j // 2) + k
                            pe.wait_ge(hidden, h + n + 1)
                            for t in range(TT):
                                T_ = slice(t * P, (t + 1) * P)
                                for x, (lh, wx) in enumerate(((Hh, w[0]), (Hh, w[1]), (Hl, w[0]))):
                                    mm = nc.tensor.matmul(BANKS[half][t][:, :], lhsT=lh[:, n, T_], rhs=wx[:, k, :],
                                                          start=(n == 0 and x == 0), stop=(n == down - 1 and x == 2))
                        mm.then_inc(quarters, 1)
                    Q, h = Q + down, h + up // per

            pe.wait_ge(s_const, CONSTS)
            transposes("x0", X, lambda t: pe.wait_ge(s_x, 16))

            pe.wait_ge(tr_out, 8)
            roped = {g: r for r, (g, *_) in enumerate(ROPED0)}

            def rope_swap(g):
                r = roped[g]
                pe.wait_ge(act_out, g + 1)
                if r >= 2:
                    pe.wait_ge(rope_dve, 2 * (r - 2) + 1)
                else:
                    pe.wait_ge(tr_out, 8)
                nc.tensor.matmul(TR[r % 2][:, :], lhsT=tab("swap"), rhs=SC[:, 0, r % 2, :], start=True, stop=True).then_inc(rope_swapped, 1)

            for g in range(24):
                if g % 4 == 0:
                    slab_wait(g // 4)
                if g >= 4:
                    pe.wait_ge(act_out, g - 3)
                kind, cols_, _ = GROUPS0[g]
                for k in range(KT):
                    w = slab(g // 4)[:, k, cols_[0]:cols_[1]]
                    if kind == "F":
                        mm = nc.tensor.matmul(G[g % 4][:, :], lhsT=w, rhs=XT[:, k, :], start=(k == 0), stop=(k == KT - 1))
                    else:
                        t = g % 4
                        mm = nc.tensor.matmul(G[g % 4][:, 0:cols_[1] - cols_[0]], lhsT=XT[:, k, t * P:(t + 1) * P], rhs=w,
                                              start=(k == 0), stop=(k == KT - 1))
                mm.then_inc(quarters, 1)
                if g - 1 in roped:
                    rope_swap(g - 1)
            if 23 in roped:
                rope_swap(23)

            a0 = st("cmp", "act")
            pe.wait_ge(act_out, 24)
            for j in range(2):
                pe.wait_ge(s_small, SMALL["windows"] + j + 1)
                slab_wait(6 + j)
                for h in range(2):
                    for m in range(16):
                        mm = nc.tensor.matmul(G[2 * j + h][:, 0:62], lhsT=ring[:, j, m * 256 + h * P:m * 256 + (h + 1) * P],
                                              rhs=WIN(j)[:, m, :], start=(m == 0), stop=(m == 15))
                    mm.then_inc(quarters, 2)
            pe.wait_ge(s_small, SMALL["gelu"])
            pe.wait_ge(s_small_in, SMALL_INPUTS)
            pe.wait_ge(rope_dve, 2 * len(ROPED0))
            for h in range(2):
                mm = nc.tensor.matmul(TR[0][:, 0:62], lhsT=w2[:, 0, h, :], rhs=hc2[:, h, :], start=(h == 0), stop=(h == 1))
            mm.then_inc(s_smallp, 1)
            for g in range(2):
                for h in range(2):
                    mm = nc.tensor.matmul(TR[1][0:N_CMP, g * HD:(g + 1) * HD], lhsT=hc2[:, 2 + h, g * N_CMP:(g + 1) * N_CMP],
                                          rhs=w2[:, 1, h, 0:HD], start=(h == 0), stop=(h == 1))
            mm.then_inc(s_smallp, 1)
            pe.wait_ge(s_small, SMALL["kraw"])
            nc.tensor.matmul(TR[0][:, 0:62], lhsT=tab("swap"), rhs=kcc[:, 0, :], start=True, stop=True).then_inc(s_smallp, 1)
            pe.wait_ge(s_small, SMALL["krope"])
            for h in range(8):
                r = (h % 2) * HD
                for t in range(TT):
                    c = (h // 2) * P + t * 32
                    mm = nc.tensor.matmul(G[h % 2][:, c:c + N_CMP], lhsT=QT[r:r + HD, 4 + h // 2, t * P:(t + 1) * P],
                                          rhs=kcc[r:r + HD, 1, (h // 4) * N_CMP:(h // 4 + 1) * N_CMP], start=True, stop=True)
                if h >= 6:
                    mm.then_inc(s_smallp, 1)
            for h in range(8):
                pe.wait_ge(s_small, SMALL["pcmp"])
                if h >= 2:
                    pe.wait_ge(s_smalla, SMALLA["ptc"] + h - 1)
                for t in range(TT):
                    mm = nc.tensor.transpose(TR[h % 2][0:N_CMP, t * P:(t + 1) * P], PC[:, h, t, 0:N_CMP], ident)
                mm.then_inc(s_smallp, 1)
                pe.wait_ge(s_smalla, SMALLA["ptc"] + h + 1)
                if h >= 2:
                    pe.wait_ge(s_small, SMALL["pcmp"] + h - 1)
                for t in range(TT):
                    mm = nc.tensor.matmul(OB[h % 2][:, t * HD:(t + 1) * HD], lhsT=PT[0:N_CMP, h % 2, t * P:(t + 1) * P],
                                          rhs=vcc[:, h // 4, :], start=True, stop=True)
                mm.then_inc(s_smallp, 1)

            pe.wait_ge(s_small, SMALL["pcmp"] + 8)
            pe_attend(pe, "diff", 4, 2, HD, lambda i, j: qb[:, j % 2, :], lambda i, j: kb[:, j % 2, :],
                      lambda i, j, b: V[:, b, bass.ds(i * P + (j // 2) * P, P)] if not isinstance(i, int) else V[:, b, i * P:(i + 1) * P], P, 2)
            pe.wait_ge(ksw_in, 64)
            pe_attend(pe, "nsa", 2, 8, HD, lambda i, j: qb[:, j % 2, :], lambda i, j: KSW[:, j % 2, j // 4, :],
                      lambda i, j, b: V[:, b, 512 + (j % 2) * P + (j // 4) * HD:512 + (j % 2) * P + (j // 4) * HD + HD], HD, 1)

            transposes("mixed0", O, lambda t: pe.wait_ge(s_small, SMALL["rms"] + 2 * (t + 1)))
            out_products("out0", "mixed0")
            transposes("x1", X, lambda t: pe.wait_ge(ln_dve, 14 + 3 * (t + 1)))
            mlp_products("mlp0", "x1", ada=0)
            transposes("x2", X, lambda t: pe.wait_ge(ln_dve, 26 + 14 + 3 * (t + 1)))

            stage_start("proj1")
            pe.wait_ge(tr_out, st("x2", "tr") + 8)
            s0, a0 = SLAB["proj1"][0], st("proj1", "act")
            for g in range(25):
                if g % 4 == 0:
                    slab_wait(s0 + g // 4)
                if g >= 4:
                    pe.wait_ge(act_out, a0 + g - 3)
                sl = slab(s0 + g // 4)
                for k in range(KT):
                    if g < 16:
                        mm = nc.tensor.matmul(G[g % 4][:, :], lhsT=sl[:, k, (g % 4) * P:(g % 4 + 1) * P], rhs=XT[:, k, :],
                                              start=(k == 0), stop=(k == KT - 1))
                    elif g < 24:
                        t = g % 4
                        mm = nc.tensor.matmul(G[t][:, :], lhsT=XT[:, k, t * P:(t + 1) * P], rhs=sl[:, k, :],
                                              start=(k == 0), stop=(k == KT - 1))
                    else:
                        mm = nc.tensor.matmul(G[0][0:16, :], lhsT=sl[:, k, 0:16], rhs=XT[:, k, :],
                                              start=(k == 0), stop=(k == KT - 1))
                mm.then_inc(quarters, 4 if g == 24 else 1)
            pe.wait_ge(act_out, a0 + 25)
            pe.wait_ge(tr_out, st("x2", "tr") + 8)
            pe.wait_ge(crow_in, 80)
            pe_attend(pe, "fox", 8, 2, HD + 2, lambda i, j: qb[:, j % 2, :], lambda i, j: kb[:, j % 2, :],
                      lambda i, j, b: V[:, b, bass.ds(i * P + j * HD, HD)] if not isinstance(i, int) else V[:, b, i * P + j * HD:i * P + (j + 1) * HD], HD, 4)
            transposes("mixed1", O, lambda t: pe.wait_ge(o_used, st("fox", "units") + 16))
            out_products("out1", "mixed1")
            transposes("x3", X, lambda t: pe.wait_ge(ln_dve, 52 + 14 + 3 * (t + 1)))
            mlp_products("mlp1", "x3", ada=2)
            tensor_second(pe, stage_start, slab_wait, mlp_products, out_products)

        @block.scalar
        def _(act):
            def copies(stage):
                base = st(stage, "tr")
                for n in range(8):
                    act.wait_ge(tr_ready, base + n + 1)
                    t, h = n // 2, n % 2
                    nc.scalar.activation(XT[:, 4 * h:4 * h + 4, t * P:(t + 1) * P], TR[h][:, :].rearrange("p (b c) -> p b c", b=4),
                                         ACT.Copy).then_inc(tr_out, 1)

            def deviation(stage, steps=14):
                act.wait_ge(ln_dve, st(stage, "ln") + steps)
                nc.scalar.activation(rstd[:, 2, :], rstd[:, 1, :], ACT.Sqrt).then_inc(ln_std, 1)

            def first_splits(stage):
                for n in range(3):
                    high_split(act, stage, n, first=True)

            def split_copies(stage):
                base = st(stage, "tr")
                for n in range(8):
                    act.wait_ge(tr_ready, base + n + 1)
                    t, h = n // 2, n % 2
                    nc.scalar.activation(XTh[:, 4 * h:4 * h + 4, t * P:(t + 1) * P], TR[h][:, :].rearrange("p (b c) -> p b c", b=4),
                                         ACT.Copy).then_inc(xt_hi, 1)

            def relu(stage):
                n, u = 0, 0
                q, a, h = st(stage, "quarters"), st(stage, "act"), st(stage, "hidden")

                def four(i):
                    for m in range(4):
                        high_split(act, stage, n + m + 3, i)
                        act.wait_ge(quarters, i * 4 + (q + n + m + 1))
                        if h + u + m >= 2 or not (isinstance(i, int) and i == 0):
                            act.wait_ge(hidden, i * 4 + (h + u + m - 1))
                        nc.scalar.activation(act_buf[m % 2], G[m][:, :], ACT.Relu).then_inc(act_out, 1)
                        act.wait_ge(act_out, i * 4 + (a + u + m + 1))
                        nc.scalar.activation(Hh[:, bass.ds(i * 4 + m, 1), :] if not isinstance(i, int) else Hh[:, m:m + 1, :],
                                             act_buf[m % 2].unsqueeze(1), ACT.Square).then_inc(hid_hi, 1)

                for up, down in PARTS[stage]:
                    first = h + u < 2
                    if first:
                        four(0)
                    with act.Fori(1 if first else 0, up // 4) as i:
                        four(i)
                    n, u = n + up, u + up
                    for j in range(down):
                        if n + j + 3 < n_quarters(stage):
                            high_split(act, stage, n + j + 3)
                    n += down

            act.wait_ge(s_const, CONSTS)
            copies("x0")
            r = 0
            for g in range(24):
                kind, c, (dst, scale) = GROUPS0[g]
                act.wait_ge(quarters, g + 1)
                if dst is None:
                    if r >= 2:
                        act.wait_ge(rope_swapped, r - 1)
                        act.wait_ge(rope_cos, r - 1)
                    dst_ap, r = SC[:, 0, r % 2, :], r + 1
                else:
                    dst_ap = KTT[:, dst[1], :] if dst[0] == "K" else V[:, dst[1], dst[2]:dst[3]]
                nc.scalar.activation(dst_ap, G[g % 4][:, 0:dst_ap.free_size()], ACT.Copy, scale=scale).then_inc(act_out, 1)
            act.wait_ge(s_small, SMALL["lam"])
            nc.scalar.activation(lam[:, 2:4], lam[:, 0:2], ACT.Exp).then_inc(s_smalla, 1)
            act.wait_ge(act_out, 24)
            nc.scalar.activation(gate[:, :, :], V[:, :, 768:792], ACT.Exp, scale=-1.0).then_inc(s_smalla, 1)
            for n in range(4):
                act.wait_ge(quarters, 24 + 2 * (n + 1))
                nc.scalar.activation(hc[:, n, :], G[n][:, 0:62], ACT.Identity, bias=cols[:, n:n + 1]).then_inc(act_out, 1)
            act.wait_ge(s_small, SMALL["gelu_in"])
            nc.scalar.activation(SC[:, 1, 2, 0:248], SC[:, 1, 1, 0:248], ACT.Tanh, scale=math.sqrt(2 / math.pi)).then_inc(s_smalla, 1)
            act.wait_ge(s_small, SMALL["scmp"])
            nc.scalar.activation(PC[:, :, :, :], PC[:, :, :, :], ACT.Exp, scale=-1.0).then_inc(s_smalla, 1)
            for h in range(8):
                act.wait_ge(s_smallp, 6 + 2 * h)
                if h >= 2:
                    act.wait_ge(s_smallp, 7 + 2 * (h - 2))
                nc.scalar.activation(PT[0:N_CMP, h % 2, :], TR[h % 2][0:N_CMP, :], ACT.Copy).then_inc(s_smalla, 1)
            act.wait_ge(s_smallp, 21)
            act_attend(act, "diff", 4, 2)
            act_attend(act, "nsa", 2, 8)
            act.wait_ge(s_small, SMALL["rms"])
            nc.scalar.activation(rmsq[:, 1, :], rmsq[:, 0, :], ACT.Sqrt).then_inc(s_smalla, 1)
            nc.scalar.activation(csil[:, 0, :, :].rearrange("p a k -> p (a k)"), cols2[:, 0:16], ACT.Exp, scale=-1.0).then_inc(s_smalla, 1)
            copies("mixed0")
            deviation("out0")
            split_copies("x1")
            first_splits("mlp0")
            relu("mlp0")
            deviation("mlp0")
            copies("x2")
            a0, q0 = st("proj1", "act"), st("proj1", "quarters")
            for g in range(25):
                act.wait_ge(quarters, q0 + (g + 1 if g < 24 else 28))
                if g < 8:
                    o, i_, sc_ = KTT[:, g, :], G[g % 4][:, :], 1.0
                elif g < 16:
                    o, i_, sc_ = QT[:, g - 8, :], G[g % 4][:, :], -0.125
                elif g < 24:
                    o, i_, sc_ = V[:, g % 4, ((g - 16) // 4) * 512:((g - 16) // 4 + 1) * 512], G[g % 4][:, :], 1.0
                else:
                    o, i_ = crow[:, 0, :], G[0][0:16, :]
                    nc.scalar.activation(o, i_, ACT.Identity, bias=cols[0:16, 4:5]).then_inc(act_out, 1)
                    continue
                nc.scalar.activation(o, i_, ACT.Copy, scale=sc_).then_inc(act_out, 1)
            act.wait_ge(s_small, SMALL["fabs"])
            nc.scalar.activation(crow[:, 2, :], crow[:, 1, :], ACT.Exp, scale=-1.0).then_inc(s_smalla, 1)
            act.wait_ge(s_smalla, SMALLA["fexp"])
            nc.scalar.activation(crow[:, 1, :], crow[:, 2, :], ACT.Ln, bias=1.0).then_inc(s_smalla, 1)
            act_attend(act, "fox", 8, 2)
            copies("mixed1")
            deviation("out1")
            split_copies("x3")
            first_splits("mlp1")
            relu("mlp1")
            deviation("mlp1")
            scalar_second(act, first_splits, deviation)

        @block.vector
        def _(dve):
            small = [0]

            def step(ins, wait=True):
                small[0] += 1
                ins.then_inc(s_small, 1)
                if wait:
                    dve.wait_ge(s_small, small[0])

            def mark(name, add=0):
                assert SMALL[name] == small[0] + add, (name, SMALL[name], small[0] + add)

            def residual(stage, alpha):
                q0 = st(stage, "quarters")
                for h in range(2):
                    for t in range(TT):
                        dve.wait_ge(quarters, q0 + 4 * h + t + 1)
                        nc.vector.scalar_tensor_tensor(out=X[:, t, h * 512:(h + 1) * 512], in0=X[:, t, h * 512:(h + 1) * 512], scalar=alpha,
                                                       in1=G[t][:, :], op0=ALU.mult, op1=ALU.add).then_inc(dve_out, 1)

            def ada_steps_of(part, j, ks):
                for k in ks:
                    if k % 2 == 0:
                        dve.wait_ge(ada_in[(k // 2) % 2], j * 32 + 16 * (8 * part + k // 4 + 1))
                    w = ADW((k // 2) % 2)[:, (k % 2) * 512:(k % 2 + 1) * 512]
                    ctx_part = isinstance(j, int) and j == 3
                    c = csil[:, 1, 1 if ctx_part else 0, k:k + 1]
                    if k == 0:
                        nc.vector.tensor_scalar(ogf, w, c, None, ALU.mult).then_inc(ada_steps, 1)
                    else:
                        dve.wait_ge(ada_steps, j * 8 + (32 * part + k))
                        nc.vector.scalar_tensor_tensor(out=ogf, in0=w, scalar=c, in1=ogf, op0=ALU.mult, op1=ALU.add).then_inc(ada_steps, 1)

            def ada_move(part, j, less=0):
                dve.wait_ge(ada_cols, j + (4 * part + 1 - less))
                at = 48 + 4 * part if isinstance(j, int) and j - less == 3 else j * 4 + (12 * part - 4 * less)
                dst, bias = ((x[:, bass.ds(at + o, 4)] if not isinstance(at, int) else x[:, at + o:at + o + 4]) for x, o in ((modc, 0), (cols2, 16)))
                nc.vector.tensor_tensor(out=dst, in0=OB[0][:, 0:4], in1=bias, op=ALU.add).then_inc(ada_moved, 1)

            def xt_low(stage, done):
                for n in range(8):
                    dve.wait_ge(xt_hi, done + n + 1)
                    t, h = n // 2, n % 2
                    x = [y[:, 4 * h:4 * h + 4, t * P:(t + 1) * P] for y in (XTl, XTh)]
                    nc.vector.tensor_tensor(out=x[0], in0=TR[h][:, :].rearrange("p (b c) -> p b c", b=4), in1=x[1],
                                            op=ALU.subtract).then_inc(tr_out, 1)

            def mlp(stage, alpha, ada):
                n, u = 0, 0
                q, h = st(stage, "quarters"), st(stage, "hidden")

                def four(part, i):
                    if not (isinstance(i, int) and i == 0):
                        ada_move(part, i, 1)
                    for m in range(4):
                        low_split(dve, nc.vector.tensor_tensor, stage, n + m + 3, i)
                        r = act_buf[m % 2]
                        dve.wait_ge(hid_hi, i * 4 + (h + u + m + 1))
                        nc.vector.tensor_tensor(out=r, in0=r, in1=r, op=ALU.mult).then_inc(hid_steps, 1)
                        dve.wait_ge(hid_steps, i * 4 + (h + u + m + 1))
                        at = bass.ds(i * 4 + m, 1) if not isinstance(i, int) else slice(4 * i + m, 4 * i + m + 1)
                        nc.vector.tensor_tensor(out=Hl[:, at, :], in0=r.unsqueeze(1), in1=Hh[:, at, :],
                                                op=ALU.subtract).then_inc(hidden, 1)
                        ada_steps_of(part, i, ((0, 1, 2), (3, 4, 5), (6, 7), ())[m])

                for n_ in range(3):
                    low_split(dve, nc.vector.tensor_tensor, stage, n_)
                for part, (up, down) in enumerate(PARTS[stage]):
                    four(ada + part, 0)
                    with dve.Fori(1, 3) as i:
                        four(ada + part, i)
                    four(ada + part, 3)
                    n, u = n + up, u + up
                    ada_move(ada + part, 3)
                    for j in range(down):
                        if n + j + 3 < n_quarters(stage):
                            low_split(dve, nc.vector.tensor_tensor, stage, n + j + 3)
                    n += down
                    for half in range(2):
                        dve.wait_ge(quarters, q + n - 1 + half)
                        for t in range(TT):
                            if part:
                                dve.wait_ge(dve_out, st(stage, "dve") + 4 * half + t + 1)
                            nc.vector.scalar_tensor_tensor(out=X[:, t, half * 512:(half + 1) * 512], in0=X[:, t, half * 512:(half + 1) * 512],
                                                           scalar=1.0 if part else alpha, in1=BANKS[half][t][:, :],
                                                           op0=ALU.mult, op1=ALU.add).then_inc(dve_out, 1)

            norms = [0]

            def layer_norm(stage, eps, n_tiles=TT, src=X, dst=None, again=False):
                b = st(stage, "ln")
                for t in range(n_tiles):
                    if (stage, "dve") in st.base:
                        dve.wait_ge(dve_out, st(stage, "dve") + (4 if stage[:3] == "out" else 12) + t + 1)
                    elif again and t == 0:
                        dve.wait_ge(ln_dve, b)
                    for h in range(2):
                        nc.vector.bn_stats(stat[:, t, h, :], src[:, t, h * 512:(h + 1) * 512]).then_inc(ln_dve, 1)
                for t in range(n_tiles):
                    dve.wait_ge(ln_dve, b + 2 * t + 2)
                    nc.vector.bn_aggr(agg[:, t, :], stat[:, t, :, :]).then_inc(ln_dve, 1)
                b += 3 * n_tiles
                dve.wait_ge(ln_dve, b)
                nc.vector.tensor_scalar(rstd[:, 0, :], agg[:, :, 1], eps, None, ALU.add).then_inc(ln_dve, 1)
                dve.wait_ge(ln_dve, b + 1)
                nc.vector.reciprocal(rstd[:, 1, :], rstd[:, 0, :]).then_inc(ln_dve, 1)
                b += 2
                dve.wait_ge(ln_std, st(stage, "std") + 1)
                if dst is None:
                    norms[0] += 1
                    dve.wait_ge(gb_in, 32 * norms[0])
                for t in range(n_tiles):
                    nc.vector.tensor_scalar((src if dst is None else dst)[:, t, :], src[:, t, :], agg[:, t, 0:1], rstd[:, 2, t:t + 1],
                                            ALU.subtract, ALU.mult).then_inc(ln_dve, 1)
                    if dst is None:
                        dve.wait_ge(ln_dve, b + 3 * t + 1)
                        nc.vector.tensor_tensor(out=X[:, t, :], in0=X[:, t, :], in1=rows[:, 0, :], op=ALU.mult).then_inc(ln_dve, 1)
                        dve.wait_ge(ln_dve, b + 3 * t + 2)
                        nc.vector.tensor_tensor(out=X[:, t, :], in0=X[:, t, :], in1=rows[:, 1, :], op=ALU.add).then_inc(ln_dve, 1)

            dve.wait_ge(s_const, CONSTS)
            dve.wait_ge(s_small_in, SMALL_INPUTS)
            step(nc.vector.tensor_tensor(out=lamrow[:, :, 0, :], in0=lamrow[:, :, 0, :], in1=lamrow[:, :, 1, :], op=ALU.mult))
            step(nc.vector.tensor_reduce(lam[:, 0:2], lamrow[:, :, 0, :], AX.X, ALU.add))
            mark("lam")
            step(nc.vector.tensor_scalar(subln[:, :], subln[:, :], 1.0 - LAM_INIT, None, ALU.mult))

            for r, (g, *dst) in enumerate(ROPED0):
                which, idx = dst
                o = (QT if which == "q" else KTT)[:, idx, :]
                dve.wait_ge(rope_swapped, r + 1)
                if r >= 2:
                    dve.wait_ge(rope_dve, 2 * (r - 2) + 2)
                nc.vector.tensor_tensor(out=SC[:, 1, r % 2, :], in0=TR[r % 2][:, :], in1=tab("sin"), op=ALU.mult).then_inc(rope_dve, 1)
                dve.wait_ge(rope_cos, r + 1)
                dve.wait_ge(rope_dve, 2 * r + 1)
                nc.vector.tensor_tensor(out=o, in0=SC[:, 0, 2 + r % 2, :], in1=SC[:, 1, r % 2, :], op=ALU.add).then_inc(rope_dve, 1)
            dve.wait_ge(rope_dve, 2 * len(ROPED0))
            dve.wait_ge(s_smalla, 2)
            step(nc.vector.tensor_tensor(out=lam[:, 4:5], in0=lam[:, 3:4], in1=lam[:, 2:3], op=ALU.subtract))
            step(nc.vector.tensor_scalar(lam[:, 5:6], lam[:, 4:5], -LAM_INIT, None, ALU.add))
            step(nc.vector.tensor_scalar(gate[:, :, :], gate[:, :, :], 1.0, None, ALU.add))
            step(nc.vector.reciprocal(gate[:, :, :], gate[:, :, :]))
            mark("windows")
            dve.wait_ge(cmp_in, 128)
            for j in range(2):
                for g in range(2):
                    src = XT[:, 2 * j + g, :]
                    for m in range(16):
                        ins = nc.vector.tensor_scalar(WIN(j)[:, m, g * N_CMP:(g + 1) * N_CMP], src[:, 2 * m:2 * m + 16 * 30 + 1:16],
                                                      cols[:, 5 + 16 * j + m:6 + 16 * j + m], None, ALU.add)
                step(ins, wait=False)
            dve.wait_ge(act_out, 28)
            x_ = hc[:, :, :].rearrange("p a b -> p (a b)")
            a_, b_ = SC[:, 1, 0, 0:248], SC[:, 1, 1, 0:248]
            step(nc.vector.tensor_tensor(out=a_, in0=x_, in1=x_, op=ALU.mult))
            step(nc.vector.tensor_scalar(a_, a_, 0.044715, 1.0, ALU.mult, ALU.add))
            step(nc.vector.tensor_tensor(out=b_, in0=a_, in1=x_, op=ALU.mult))
            mark("gelu_in")
            dve.wait_ge(s_smalla, 3)
            step(nc.vector.tensor_scalar(a_, SC[:, 1, 2, 0:248], 1.0, 0.5, ALU.add, ALU.mult))
            step(nc.vector.tensor_tensor(out=hc2[:, :, :].rearrange("p a b -> p (a b)"), in0=a_, in1=x_, op=ALU.mult))
            mark("gelu")
            dve.wait_ge(s_smallp, 2)
            step(nc.vector.tensor_copy(vcc[:, :, :], TR[1][0:N_CMP, 0:P].rearrange("p (g d) -> p g d", g=2)))
            step(nc.vector.tensor_copy(kcc[:, 0, :], TR[0][:, 0:62]))
            mark("kraw")
            step(nc.vector.tensor_tensor(out=SC[:, 1, 0, 0:62], in0=kcc[:, 0, :], in1=tab("cmp_cos"), op=ALU.mult))
            dve.wait_ge(s_smallp, 3)
            step(nc.vector.tensor_tensor(out=SC[:, 1, 1, 0:62], in0=TR[0][:, 0:62], in1=tab("cmp_sin"), op=ALU.mult))
            step(nc.vector.tensor_tensor(out=kcc[:, 1, :], in0=SC[:, 1, 0, 0:62], in1=SC[:, 1, 1, 0:62], op=ALU.add))
            mark("krope")
            okt = tab("cmp_ok").rearrange("p (t n) -> p t n", t=TT)
            mkt = tab("cmp_mask").rearrange("p (t n) -> p t n", t=TT)
            for b in range(2):
                dve.wait_ge(s_smallp, 4 + b)
                for h in range(4):
                    ins = nc.vector.tensor_tensor(out=PC[:, 2 * h + b, :, :], in0=G[b][:, h * P:(h + 1) * P].rearrange("p (t n) -> p t n", t=TT)[:, :, 0:N_CMP],
                                                  in1=mkt, op=ALU.add)
                    step(ins, wait=False)
            dve.wait_ge(s_small, small[0])
            step(nc.vector.tensor_reduce(pcm[:, 0, :], PC[:, :, :, :].rearrange("p h t n -> p (h t) n"), AX.X, ALU.min))
            pcv = PC[:, :, :, :].rearrange("p h t n -> p (h t) n")
            step(nc.vector.tensor_tensor(out=pcv, in0=pcv, in1=pcm[:, 0, :].unsqueeze(2).to_broadcast([P, 32, N_CMP]), op=ALU.subtract))
            mark("scmp")
            dve.wait_ge(s_smalla, 4)
            step(nc.vector.tensor_reduce(pcm[:, 1, :], pcv, AX.X, ALU.add))
            step(nc.vector.reciprocal(pcm[:, 0, :], pcm[:, 1, :]))
            step(nc.vector.tensor_tensor(out=pcm[:, 1, :].rearrange("p (h t) -> p h t", h=8), in0=pcm[:, 0, :].rearrange("p (h t) -> p h t", h=8),
                                         in1=gate[:, :, 0:24:3].rearrange("p t h -> p h t"), op=ALU.mult))
            step(nc.vector.tensor_tensor(out=pcv, in0=pcv, in1=pcm[:, 1, :].unsqueeze(2).to_broadcast([P, 32, N_CMP]), op=ALU.mult))
            for h in range(8):
                step(nc.vector.tensor_tensor(out=PC[:, h, :, :], in0=PC[:, h, :, :], in1=okt, op=ALU.mult), wait=False)
            mark("pcmp")
            for h in range(8):
                dve.wait_ge(s_smallp, 7 + 2 * h)
                step(nc.vector.tensor_copy(O[:, :, 512 + h * HD:512 + (h + 1) * HD], OB[h % 2][:, 0:256].rearrange("p (t d) -> p t d", t=TT)), wait=False)
            dve.wait_ge(s_small, small[0])

            def fin_diff(i, j, at):
                o = O[:, :, bass.ds(i * P + (j // 2) * P, P)] if not isinstance(i, int) else O[:, :, i * P:(i + 1) * P]
                ps = OB[j % 2][:, :].rearrange("p (t d) -> p t d", t=TT)
                if j == 0:
                    nc.vector.tensor_tensor(out=o, in0=ps, in1=rs[:, 0, :].unsqueeze(2).to_broadcast([P, TT, P]), op=ALU.mult).then_inc(o_used, 1)
                else:
                    nc.vector.tensor_scalar(rs[:, 1, :], rs[:, 1, :], lam[:, 5:6], None, ALU.mult).then_inc(o_steps, 1)
                    dve.wait_ge(o_steps, at + 1)
                    nc.vector.tensor_tensor(out=og[:, :, :], in0=ps, in1=rs[:, 1, :].unsqueeze(2).to_broadcast([P, TT, P]), op=ALU.mult).then_inc(o_steps, 1)
                    dve.wait_ge(o_steps, at + 2)
                    nc.vector.tensor_tensor(out=o, in0=o, in1=og[:, :, :], op=ALU.add).then_inc(o_used, 1)

            def fin_nsa(r, j, at):
                g, par, kind = j // 4, (j // 2) % 2, j % 2
                if isinstance(r, int):
                    c = 512 + (4 * g + 2 * r + par) * HD
                    o = O[:, :, c:c + HD]
                    c = 3 * (4 * g + 2 * r + par) + 1 + kind
                    gt = gate[:, :, c:c + 1]
                else:
                    o = O[:, :, bass.ds(r * (2 * HD) + (512 + (4 * g + par) * HD), HD)]
                    gt = gate[:, :, bass.ds(r * 6 + (3 * (4 * g + par) + 1 + kind), 1)]
                ps = OB[kind][:, 0:256].rearrange("p (t d) -> p t d", t=TT)
                nc.vector.tensor_tensor(out=rs[:, kind, :].unsqueeze(2), in0=rs[:, kind, :].unsqueeze(2), in1=gt, op=ALU.mult).then_inc(o_steps, 1)
                dve.wait_ge(o_steps, at + 1)
                nc.vector.tensor_tensor(out=og[:, :, 0:HD], in0=ps, in1=rs[:, kind, :].unsqueeze(2).to_broadcast([P, TT, HD]), op=ALU.mult).then_inc(o_steps, 1)
                dve.wait_ge(o_steps, at + 2)
                nc.vector.tensor_tensor(out=o, in0=o, in1=og[:, :, 0:HD], op=ALU.add).then_inc(o_used, 1)

            def fin_fox(i, j, at):
                o = O[:, :, bass.ds(i * P + j * HD, HD)] if not isinstance(i, int) else O[:, :, i * P + j * HD:i * P + (j + 1) * HD]
                ps = OB[j % 2][:, 0:256].rearrange("p (t d) -> p t d", t=TT)
                nc.vector.tensor_tensor(out=o, in0=ps, in1=rs[:, j % 2, :].unsqueeze(2).to_broadcast([P, TT, HD]), op=ALU.mult).then_inc(o_used, 1)

            dve_attend(dve, "diff", 4, 2, P, fin_diff)
            dve_attend(dve, "nsa", 2, 8, HD, fin_nsa)
            dve.wait_ge(o_used, 24)
            sq = SC[:, 0, :, :]
            step(nc.vector.tensor_tensor(out=sq, in0=O[:, :, 0:512], in1=O[:, :, 0:512], op=ALU.mult))
            step(nc.vector.tensor_reduce(rmsq[:, 0, :], sq.rearrange("p t (h d) -> p (t h) d", h=4), AX.X, ALU.add))
            step(nc.vector.tensor_scalar(rmsq[:, 1, :], rmsq[:, 0, :], 1.0 / P, LN_EPS, ALU.mult, ALU.add))
            step(nc.vector.reciprocal(rmsq[:, 0, :], rmsq[:, 1, :]))
            mark("rms")
            dve.wait_ge(s_smalla, 13)
            for t in range(TT):
                o = O[:, t, 0:512].rearrange("p (h d) -> p h d", h=4)
                step(nc.vector.tensor_tensor(out=o, in0=o, in1=rmsq[:, 1, 4 * t:4 * t + 4].unsqueeze(2).to_broadcast([P, 4, P]), op=ALU.mult))
                step(nc.vector.tensor_tensor(out=o, in0=o, in1=subln[:, :].unsqueeze(1).to_broadcast([P, 4, P]), op=ALU.mult), wait=False)
            mark("mixed0")
            cc = csil[:, 0, :, :].rearrange("p a k -> p (a k)")
            cs_ = csil[:, 1, :, :].rearrange("p a k -> p (a k)")
            dve.wait_ge(s_smalla, SMALLA["silu"])
            step(nc.vector.tensor_scalar(cc, cc, 1.0, None, ALU.add))
            step(nc.vector.reciprocal(cc, cc))
            step(nc.vector.tensor_tensor(out=cs_, in0=cc, in1=cols2[:, 0:16], op=ALU.mult))
            step(nc.vector.memset(ones[:, :], 1.0))
            residual("out0", ALPHA)
            layer_norm("out0", LN_EPS)
            xt_low("x1", 0)
            mlp("mlp0", ALPHA, ada=0)
            layer_norm("mlp0", LN_EPS)
            dve.wait_ge(act_out, st("proj1", "act") + 25)
            step(nc.vector.tensor_scalar(crow[:, 2, :], crow[:, 0, :], -1.0, None, ALU.mult))
            step(nc.vector.tensor_tensor(out=crow[:, 1, :], in0=crow[:, 0, :], in1=crow[:, 2, :], op=ALU.max))
            mark("fabs")
            dve.wait_ge(s_smalla, SMALLA["fexp"])
            step(nc.vector.tensor_scalar(crow[:, 0, :], crow[:, 0, :], 0.0, None, ALU.min))
            dve.wait_ge(s_smalla, SMALLA["fexp"] + 1)
            step(nc.vector.tensor_tensor(out=crow[:, 0, :], in0=crow[:, 0, :], in1=crow[:, 1, :], op=ALU.subtract))
            step(nc.vector.tensor_tensor_scan(out=crow[:, 1, :], data0=crow[:, 0, :], data1=crow[:, 0, :], initial=0.0,
                                              op0=ALU.add, op1=ALU.bypass))
            step(nc.vector.tensor_scalar(crow[:, 2, :], crow[:, 1, :], -1.0, None, ALU.mult))
            mark("fox")
            dve_attend(dve, "fox", 8, 2, HD, fin_fox)
            residual("out1", ALPHA)
            layer_norm("out1", LN_EPS)
            xt_low("x3", 8)
            mlp("mlp1", ALPHA, ada=2)
            layer_norm("mlp1", LN_EPS)
            vector_second(dve, residual, layer_norm)


def slab_layout(w, width=512):
    K, n = w.shape
    w = np.pad(w, ((0, 0), (0, -n % width)))
    out = []
    for c in range(0, w.shape[1], width):
        for r in range(0, K, 1024):
            out.append(w[r:r + 1024, c:c + width].reshape(8, P, width).transpose(1, 0, 2).reshape(P, 4096))
    return out


def up_chunks(w):
    n = w.shape[1] // 256
    return list(w.reshape(KT, P, n, 2, P).transpose(2, 1, 3, 0, 4).reshape(n, P, 2048))


def down_chunks(w, parts):
    out = []
    for first, last in parts:
        for r in range(first, last, 2):
            c = w[r * P:(r + 2) * P].reshape(2, P, 2, 512).transpose(1, 2, 0, 3)
            if r < last - 2:
                c = c[:, ::-1]
            out.append(c.reshape(P, 2048))
    return out


def kernel(**inputs):
    import concourse.bacc as bacc
    from concourse.bass_utils import run_bass_kernel_spmd

    a = {k: np.asarray(v) for k, v in inputs.items()}
    table, where, dft_len, dft_ch, heads = shape_constants()
    we, wo = a["w_in_even"][0], a["w_in_odd"][0]
    chunks = []
    for i in range(2):
        up, down = up_chunks(a["mlp_w_up"][i]), down_chunks(a["mlp_w_down"][i], ((0, 16), (16, 32)))
        chunks += up[0:8] + down[0:8] + up[8:] + down[8:]
    kv = np.concatenate([we[:, 2048:2176], we[:, 2176:2304], we[:, 2304:2432], we[:, 2560:2688]], axis=1)
    vg = np.concatenate([we[:, 2432:2560], we[:, 2688:2816], we[:, 2816:2840]], axis=1)
    w1 = a["nsa_cmp_w1"][0]
    slabs = (slab_layout(we[:, 512:1024]) + slab_layout(we[:, 0:512]) + slab_layout(we[:, 1536:2048])
             + slab_layout(we[:, 1024:1536]) + slab_layout(kv) + slab_layout(vg)
             + [w1[j].reshape(16, P, 256).transpose(1, 0, 2).reshape(P, 4096) for j in range(2)]
             + slab_layout(a["w_out_even"][0])
             + slab_layout(wo[:, 1024:2048]) + slab_layout(wo[:, 0:1024]) + slab_layout(wo[:, 2048:3072]) + slab_layout(wo[:, 3072:])
             + slab_layout(a["w_out_odd"][0]))
    cols = np.zeros((P, 37), np.float32)
    cols[:, 0:4] = a["nsa_cmp_b1"][0].reshape(4, P).T
    cols[0:16, 4] = a["fox_f_bias"][0]
    cols[:, 5:37] = a["nsa_pe"][0].reshape(2 * 16, P).T

    wi = a["w_in_2"][0]
    up = up_chunks(a["ffn_w_up_2"][0].reshape(D, 2, 22, P).transpose(0, 2, 1, 3).reshape(D, 2 * D_FF_2))
    down = down_chunks(a["ffn_w_down_2"][0], ((0, 12), (12, 22)))
    chunks += up[0:12] + down[0:6] + up[12:] + down[6:]
    slabs += (slab_layout(wi[:, OFF_DT:OFF_DT + 16]) + slab_layout(wi[:, OFF_XS:OFF_BC]) + slab_layout(wi[:, OFF_BC:OFF_DT])
              + slab_layout(wi[:, OFF_FP:]) + slab_layout(wi[:, 0:512])
              + [dft_len.reshape(8, P, S).transpose(1, 0, 2).reshape(P, 4096)]
              + slab_layout(a["w_out_2"][0]))
    bada = a["b_ada_2"][0].reshape(48, P).T
    cols2 = np.zeros((P, 122 + 480), np.float32)
    cols2[:, 0:8] = a["c_2"].reshape(KT, P).T
    cols2[:, 8:16] = a["c_ctx_2"].reshape(KT, P).T
    cols2[:, 16:64] = bada
    cols2[:, 64:80] = bada[:, 0:16]
    cols2[0:16, 80] = a["ssd_dt_bias_2"].reshape(16)
    cols2[0:16, 81] = a["ssd_a_log_2"].reshape(16)
    cols2[0:8, 82] = 1
    cols2[8:16, 83] = 1
    cols2[:, 84:108] = a["ssd_conv_w_2"][0].reshape(3, 8, P).transpose(2, 1, 0).reshape(P, 24)
    cols2[:, 108:116] = a["ssd_conv_b_2"].reshape(8, P).T
    cols2[:, 116:120] = a["ssd_norm_w_2"].reshape(4, P).T
    cols2[:, 120:122] = a["pool_scale_2"].reshape(2, P).T
    ffn = np.concatenate([a["ffn_conv_w_2"][0].reshape(9, 2 * D_FF_2), a["ffn_conv_b_2"]])
    ffn = ffn.reshape(10, 2, 11, 2, P).transpose(4, 2, 3, 1, 0)
    cols2[:, 122:562] = ffn.reshape(P, 440)
    ada = np.stack(slab_layout(a["w_ada_2"][0]))

    nc = bacc.Bacc("TRN2", target_bir_lowering=False, num_devices=1)
    arrays = {"slabs": np.stack(slabs), "chunks": np.stack(chunks), "cols": cols, "table": table, "ones": np.ones((2, S), np.float32),
              "cols2": cols2, "ada": ada, "dft_ch": np.concatenate([dft_ch, dft_ch], axis=2).transpose(1, 0, 2).copy()}
    for n in ("x", "ln_gain", "ln_bias", "diff_lambda", "diff_subln", "nsa_cmp_w2", "ctx_2", "fnet_w_2", "pool_w_2",
              "ssd_d_2", "ln1_g_2", "ln1_b_2", "ln2_g_2", "ln2_b_2"):
        arrays[n] = a[n]
    A = {n: nc.dram_tensor(n, v.shape, F32, kind="ExternalInput").ap() for n, v in arrays.items()}
    A["where"] = where
    A["crow"] = nc.dram_tensor("forget_rows", (16, 2, S), F32, kind="Internal").ap()
    out = nc.dram_tensor("out", (1, S, D), F32, kind="ExternalOutput").ap()
    build(nc, A, out)
    r = run_bass_kernel_spmd(nc, [arrays], core_ids=[0])
    return r.results[0]["out"]
```

```python
import math
from contextlib import ExitStack

import numpy as np
import concourse.bass as bass
from concourse import mybir

F32 = mybir.dt.float32
F32R = mybir.dt.float32r
ALU = mybir.AluOpType
ACT = mybir.ActivationFunctionType
AX = mybir.AxisListType

P = 128
D = 1024
S = 512
TT = S // P
KT = D // P
HD = 64
D_FF = 4 * D
N_EVEN_COLS = 2840
ALPHA = 4.0 ** 0.25
LN_EPS = 1e-5
BIG = 2.0 ** 100
N_CMP = 31
LAM_INIT = 0.8 - 0.6 * math.exp(0.0)

D_FF_2 = 2816
CTX = 256
ALPHA_2 = 2.0 ** 0.25
EPS_2 = 1e-6
N_IN = 2064
OFF_XS, OFF_BC, OFF_DT, OFF_FP = 512, 1024, 1536, 1552
GRID_W = 64


def shape_constants():
    half = 8
    inv = (np.float32(500000.0) ** (-np.arange(half, dtype=np.float32) / np.float32(half))).astype(np.float32)

    def rope(pos):
        ang = pos.astype(np.float32)[:, None] * inv[None, :]
        c, s = np.cos(ang), np.sin(ang)
        cos, sin = np.ones((P, len(pos)), np.float32), np.zeros((P, len(pos)), np.float32)
        for p in range(P):
            d = p % HD
            if d < 2 * half:
                cos[p] = c[:, d % half]
                sin[p] = s[:, d % half] * (-1 if d < half else 1)
        return cos, sin

    cos, sin = rope(np.arange(S))
    cmp_end = np.arange(N_CMP) * 16 + 31
    cc, cs = rope(np.concatenate([cmp_end, cmp_end]))
    swap = np.zeros((P, P), np.float32)
    for m in range(P):
        d = m % HD
        if d < 16:
            swap[(m - 8 if d >= 8 else m + 8), m] = 1
    q, k = np.arange(P)[:, None], np.arange(P)[None, :]
    causal = np.zeros((P, S), np.float32)
    causal[:, S - P:] = np.where(k > q, BIG, 0)
    tok = np.arange(TT)[None, :, None] * P + np.arange(P)[:, None, None]
    ok = cmp_end[None, None, :] <= tok
    inv_count = np.zeros((P, 2, S), np.float32)
    t = np.arange(S)
    for g, w in enumerate((2, 4, 8, 16)):
        n = np.minimum(t + (w - 1 - w // 2) + 1, S) - np.maximum(t - w // 2, 0)
        inv_count[(g % 2) * HD:(g % 2) * HD + HD, g // 2] = 1.0 / n.astype(np.float32)
    parts = [("cos", cos), ("sin", sin), ("ident", np.eye(P)), ("swap", swap), ("causal", causal),
             ("cmp_cos", cc), ("cmp_sin", cs),
             ("cmp_mask", np.where(ok, 0, BIG).reshape(P, -1)), ("cmp_ok", ok.reshape(P, -1)),
             ("lower", (q >= k)), ("upper", (q <= k)), ("inv_count", inv_count.reshape(P, -1))]
    at, where = 0, {}
    for name, a in parts:
        where[name] = (at, at + a.shape[1])
        at += a.shape[1]
    table = np.concatenate([np.asarray(a, np.float32) for _, a in parts], axis=1)
    n = np.arange(S)
    ang = 2 * np.pi * ((n[:, None] * n[None, :]) % S) / S
    scale = 1.0 / math.sqrt(S * HD)
    dft_len = np.stack([np.cos(ang) * scale, -np.sin(ang) * scale]).astype(np.float32)
    c = np.arange(HD)
    angc = 2 * np.pi * ((c[:, None] * c[None, :]) % HD) / HD
    dft_ch = np.stack([np.cos(angc), np.sin(angc)]).astype(np.float32)
    heads = np.zeros((16, 16 * P), np.float32)
    for h in range(16):
        heads[h, h * P:(h + 1) * P] = 1
    return table, where, dft_len, dft_ch, heads


class Stages:

    def __init__(self):
        self.total, self.base, self.before, self.own = {}, {}, {}, {}

    def add(self, stage, **counts):
        self.before[stage] = dict(self.total)
        for what, n in counts.items():
            self.base[stage, what] = self.total.get(what, 0)
            self.own[stage, what] = n
            self.total[what] = self.total.get(what, 0) + n

    def total_until(self, stage, what, rest):
        return self.base[stage, what] + self.own[stage, what] - rest

    def __call__(self, stage, what):
        return self.base[stage, what]


def build(nc, A, out, debug=None):
    where = A["where"]
    st = Stages()
    st.add("x0", tr=8)
    st.add("proj0", quarters=24, act=24)
    st.add("cmp", quarters=8, act=4)
    st.add("diff", units=8, loads=2)
    st.add("nsa", units=16, loads=1)
    st.add("mixed0", tr=8)
    st.add("out0", quarters=8, dve=8, ln=28, std=4)
    st.add("x1", tr=8)
    st.add("mlp0", quarters=64, act=32, hidden=32, dve=16, ln=28, std=4)
    st.add("x2", tr=8)
    st.add("proj1", quarters=28, act=25)
    st.add("fox", units=16)
    st.add("mixed1", tr=8)
    st.add("out1", quarters=8, dve=8, ln=28, std=4)
    st.add("x3", tr=8)
    st.add("mlp1", quarters=64, act=32, hidden=32, dve=16, ln=52, std=8, norm=4)
    st.add("ln_ctx", ln=12, std=2, norm=2)
    st.add("x4", tr=8)
    st.add("x_ctx", tr=8)
    st.add("w_in", quarters=20)
    st.add("dft", quarters=4)
    st.add("out2", quarters=8, dve=8, ln=52, std=8, norm=4)
    st.add("x5", tr=8)
    st.add("ffn2", quarters=66, act=44, hidden=22, dve=16, ln=28, std=4)
    SLAB = {}
    for stage, n in (("cmp", 2), ("w_in", 5), ("dft", 1), ("out2", 2)):
        SLAB[stage] = sum(n_ for _, n_ in SLAB.values()), n
    PLAIN = ("s0", "s1", "ag", "ve", "rc", "nm")
    FULL = PLAIN[:5] + ("ga", "bi")
    LN_ORDER = {stage: [(op, t) for t in range(TT) for op in FULL] for stage in ("out0", "mlp0", "out1", "ffn2")}
    for stage in ("mlp1", "out2"):
        LN_ORDER[stage] = [(op, t) for t in range(TT) for op, t in
                           [("s0", t), ("s1", t)] + ([("nm'", t - 1)] if t else []) + [(op, t) for op in FULL[2:]]
                           + [(op + "'", t) for op in PLAIN[:5]]] + [("nm'", TT - 1)]
    LN_ORDER["ln_ctx"] = [(op, t) for t in range(2) for op in PLAIN[:2]] + [(op, t) for op in PLAIN[2:] for t in range(2)]
    LN_SCALAR = {stage: [("root" if op[:2] == "rc" else "apply", t, op[2:]) for op, t in order if op[:2] in ("rc", "nm")]
                 for stage, order in LN_ORDER.items()}

    def scalar_place(stage, kind, t, mark):
        base = st(stage, "std" if kind == "root" else "norm")
        return base + [x for x in LN_SCALAR[stage] if x[0] == kind].index((kind, t, mark)) + 1

    LN_PLACE = {(stage, *x): st(stage, "ln") + i + 1 for stage, order in LN_ORDER.items() for i, x in enumerate(order)}
    for stage, order in LN_ORDER.items():
        assert len(order) == {"out2": 52, "mlp1": 52, "ln_ctx": 12}.get(stage, 28)
    NORMS = ("out0", "mlp0", "out1", "mlp1", "out2", "ffn2")
    PARTS = {"mlp0": ((16, 16), (16, 16)), "mlp1": ((16, 16), (16, 16)), "ffn2": ((24, 12), (20, 10))}
    SPLIT0, TILE0, at, tiles_at = {}, {}, 0, 0
    for stage, n, n_tiles in (("proj0", 24, 6), ("out0", 8, 6), ("mlp0", 64, 3), ("proj1", 28, 6), ("out1", 8, 6), ("mlp1", 64, 3),
                              ("ffn2", 66, 3)):
        SPLIT0[stage], TILE0[stage] = at, tiles_at
        at, tiles_at = at + n, tiles_at + n_tiles
    FORGET = 4

    CONSTS = 3 * 16
    SMALL_INPUTS = 5 * 16
    GROUPS0 = ([("F", (m * P, m * P + P), (None, 1.0)) for m in range(4)]
               + [("F", (m * P, m * P + P), (None, -0.125)) for m in range(4)] * 2
               + [("T", (0, 512), (("V", t, 0, 512), 1.0)) for t in range(TT)]
               + [("F", (m * P, m * P + P), (("K", 4 + m) if m < 2 else None, 1.0)) for m in range(4)]
               + [("T", (0, 280), (("V", t, 512, 792), 1.0)) for t in range(TT)])
    ROPED0 = ([(g, "k", g) for g in range(4)] + [(4 + g, "q", g) for g in range(8)]
              + [(18, "k", 6), (19, "k", 7)])
    SMALL = dict(lam=2, windows=7, gelu_in=12, gelu=14, kraw=16, krope=19, scmp=29, pcmp=41, rms=53,
                 mixed0=61, fabs=67, fox=71)
    SMALLA = dict(ptc=4, silu=14, fexp=15)
    LOADS = {"diff": 0, "nsa": 128, "fox": 256}
    STEP0 = {"diff": 0, "nsa": 8, "fox": 40}

    ctx = ExitStack()
    with ctx:
        def sb(name, shape):
            return ctx.enter_context(nc.sbuf_tensor(name + "_sb", shape, F32))

        def pb(name):
            return ctx.enter_context(nc.psum_tensor(name, [P, 512], F32))

        def sem(name):
            return ctx.enter_context(nc.semaphore(name))

        X = sb("X", [P, TT, D])
        with ExitStack() as overlay:
            Hh, Hl, Wh, Wl, XTh, XTl = (overlay.enter_context(nc.sbuf_tensor(name, shape, F32R)) for name, shape in (
                ("hidden_high", [P, 16, S]), ("hidden_low", [P, 16, S]), ("weights_high", [P, 4, 1024]),
                ("weights_low", [P, 4, 1024]), ("xt_high", [P, KT, S]), ("xt_low", [P, KT, S])))
        wide = sb("wide", [P, 32, S])
        SC = sb("SC", [P, 2, TT, S])
        PT = sb("PT", [P, TT, S])
        qb = sb("qb", [P, 2, S])
        kb = sb("kb", [P, 2, S])
        XT = sb("XT", [P, KT, S])
        ring = sb("ring", [P, 2, 4096])
        raw = ring[:, 1, :].rearrange("p (s q n) -> p s q n", s=2, q=2)
        QT, KTT = wide[:, 0:8, :], wide[:, 8:16, :]
        V = wide[:, 16:24, :].rearrange("p (t h) n -> p t (h n)", t=TT)
        O = wide[:, 24:32, :].rearrange("p (t h) n -> p t (h n)", t=TT)
        table = sb("table", [P, A["table"].shape[1]])
        cols = sb("cols", [P, A["cols"].shape[1]])
        rows = sb("rows", [P, 2, D])
        stat = sb("stat", [P, TT, 2, 6])
        agg = sb("agg", [P, TT, 2])
        rstd = sb("rstd", [P, 4, TT])
        mn = sb("mn", [P, 2, TT])
        sm = sb("sm", [P, 2, TT])
        rs = sb("rs", [P, 2, TT])
        og = sb("og", [P, TT, P])
        lamrow = og[:, 0:2, :].rearrange("p a (b n) -> p a b n", b=2)
        KS4 = sb("KS4", [P, 4, S])
        KSW = KS4[0:HD, :, :].rearrange("p (a b) n -> p a b n", a=2)
        lam = sb("lam", [P, 8])
        subln = sb("subln", [P, P])
        gate = sb("gate", [P, TT, 24])
        w2 = sb("w2", [P, 2, 2, P])
        hc = SC[:, 1, 3, 0:248].rearrange("p (a b) -> p a b", a=4)
        hc2 = SC[:, 1, 3, 248:496].rearrange("p (a b) -> p a b", a=4)
        kcc = sb("kcc", [P, 2, 62])
        vcc = sb("vcc", [N_CMP, 2, HD])
        crow = rows[0:16, :, :].rearrange("p a (b n) -> p (a b) n", n=S)
        ones = sb("ones", [P, P])
        cols2 = sb("cols2", [P, A["cols2"].shape[1]])
        modc = sb("modc", [P, 64])
        csil = sb("csil", [P, 2, 2, KT])
        bd = sb("bd", [P, 2, 256])
        poolw = sb("poolw", [P, 2, P])
        tks = sb("tks", [P, 160])
        ncs = sb("ncs", [P, TT, 16])
        ecs = sb("ecs", [P, TT, 16])
        nega = sb("nega", [16, 4])
        drow = sb("drow", [P, 8])
        ys = sb("ys", [P, 3, TT, 2])
        pcm = sb("pcm", [P, 2, 32])
        rmsq = sb("rmsq", [P, 2, 16])
        PC = SC[:, 0, 0:2, :].rearrange("p a b -> p (a b)")[:, 0:8 * TT * N_CMP].rearrange("p (h t n) -> p h t n", h=8, t=TT)

        def WIN(j):
            w = PT[:, 2 * j:2 * j + 2, :].rearrange("p a b -> p (a b)")
            return w[:, 0:16 * 62].rearrange("p (m n) -> p m n", m=16)

        G = [pb(f"G{i}") for i in range(4)]
        TR = [pb(f"TR{i}") for i in range(2)]
        OB = [pb(f"OB{i}") for i in range(2)]

        def tab(name, n=P):
            a, b = where[name]
            return table[0:n, a:b]

        act_buf = [tab("cos"), tab("sin")]
        ogf = og[:, :, :].rearrange("p a b -> p (a b)")

        ident = tab("ident")
        BANKS = [G, [TR[0], TR[1], OB[1], OB[0]]]

        s_const = sem("constants_in")
        s_small_in = sem("small_inputs_in")
        ident_in = sem("ident_in")
        x_in = [sem(f"x_tile_{t}_in") for t in range(TT)]
        slab_in = [sem("slab_in_even"), sem("slab_in_odd")]
        quarters = sem("slab_quarters_used")
        act_out = sem("psum_emptied_by_scalar")
        dve_out = sem("psum_emptied_by_vector")
        tr_ready = sem("transposed_in_psum")
        tr_out = sem("transposed_copied")
        rope_swapped = sem("rope_partners_in_psum")
        rope_cos = sem("rope_cos_products")
        rope_dve = sem("rope_vector_steps")
        gb_in = sem("gain_bias_in")
        ln_dve = sem("layer_norm_vector_steps")
        ln_std = sem("layer_norm_deviations")
        ln_norm = sem("layer_norm_normalized")
        tile_done = sem("token_tiles_in_psum")
        raw_in = [sem("raw_even_in"), sem("raw_odd_in")]
        w_hi = sem("weight_high_parts")
        w_lo = sem("weight_low_parts")
        xt_hi = sem("xt_high_parts")
        hid_hi = sem("hidden_high_parts")
        hid_steps = sem("hidden_float32")
        hidden = sem("hidden_low_parts")
        ada_moved = sem("ada_columns_moved")
        qk_in = [sem("qk_in_even"), sem("qk_in_odd")]
        sc_seen = sem("scores_seen_by_vector")
        sc_ready = sem("scores_in_psum")
        sc_used = sem("scores_copied_with_min")
        pr_ready = sem("probabilities_ready")
        pt_ready = sem("probabilities_transposed")
        pt_dve = sem("transposed_probabilities_by_vector")
        pt_act = sem("transposed_probabilities_by_scalar")
        pv_ready = sem("attended_in_psum")
        o_steps = sem("attended_vector_steps")
        rec_done = sem("sums_inverted")
        o_used = sem("attended_copied")
        s_small = sem("vector_small_steps")
        s_smalla = sem("scalar_small_steps")
        s_smallp = sem("tensor_small_steps")
        ksw_in = sem("shared_keys_moved")
        cmp_in = sem("compression_windows_in")
        crow_in = sem("forget_rows_stored")
        s_out = sem("stored")
        ada_in = [sem("ada_half_0_in"), sem("ada_half_1_in")]
        ada_steps = sem("ada_accumulated")
        ada_cols = sem("ada_columns_summed")
        s_two = sem("vector_steps_second")
        s_twoa = sem("scalar_steps_second")
        s_twop = sem("tensor_steps_second")
        s_twog = sem("gpsimd_steps_second")
        s_twod = sem("second_inputs_in")
        conv_first = sem("ffn_conv_padded")
        conv_steps = sem("ffn_conv_taps")
        gelu_done = sem("ffn_gelu")
        x_val = sem("modulated_float32")
        res_steps = sem("residual_gated")
        s_ctx = sem("context_in")

        def ADW(h):
            return KS4[:, 2 * h:2 * h + 2, :].rearrange("p k c -> p (k c)")

        STEPS = {"diff": (0, 0, 2), "nsa": tuple(range(0, 17, 2)), "fox": (0, 0, 0)}

        block = ctx.enter_context(nc.Block())

        def slab(s):
            return ring[:, s % 2, :].rearrange("p (k c) -> p k c", k=KT)

        def split_products(out, terms):
            n = 3 * len(terms)
            for i, (ah, al, bh, bl) in enumerate(terms):
                for j, (a, b) in enumerate(((ah, bh), (ah, bl), (al, bh))):
                    mm = nc.tensor.matmul(out, lhsT=a, rhs=b, start=(3 * i + j == 0), stop=(3 * i + j == n - 1))
            return mm

        def raw_quarter(Q):
            return raw[:, (Q // 2) % 2, Q % 2, :]

        def columns(stage, n):
            return slice(0, 8) if stage == "proj1" and 0 < n < FORGET else slice(0, 1024)

        def high_split(act, stage, n, i=0, first=False):
            Q = SPLIT0[stage] + n
            act.wait_ge(raw_in[(Q // 2) % 2], i * 16 + 16 * (Q // 4 + 1))
            if not first:
                act.wait_ge(quarters, i * 4 + (st(stage, "quarters") + n - 3))
            c = columns(stage, n)
            nc.scalar.activation(Wh[:, n % 4, c], raw_quarter(Q)[:, c], ACT.Copy).then_inc(w_hi, 1)

        def low_split(eng, tt_, stage, n, i=0):
            Q = SPLIT0[stage] + n
            eng.wait_ge(w_hi, i * 4 + (Q + 1))
            c = columns(stage, n)
            tt_(out=Wl[:, n % 4, c], in0=raw_quarter(Q)[:, c], in1=Wh[:, n % 4, c], op=ALU.subtract).then_inc(w_lo, 1)

        def tile_wait(eng, stage, n0, slab_, t):
            if t < TT - 1:
                eng.wait_ge(tile_done, TILE0[stage] + (TT - 1) * slab_ + t + 1)
            else:
                eng.wait_ge(quarters, st(stage, "quarters") + n0 + 4)

        def n_quarters(stage):
            return sum(a + b for a, b in PARTS[stage])

        C2 = dict(bada=16, dt_bias=80, a_log=81, fwd=82, bwd=83, conv=84, conv_b=108, norm=116, pool=120, ffn=122)

        def col(name, n=0, rows_=P):
            return cols2[0:rows_, C2[name] + n:C2[name] + n + 1]

        def tiles(a, b):
            return wide[:, a:b, :].rearrange("p a b -> p (a b)")

        xbcT, Z, Btok = wide[:, 0:8, :], wide[:, 11:15, :], wide[:, 15, :]
        CX = tiles(8, 11).rearrange("p (a b) -> p a b", b=CTX)
        STATE = wide[:, 8:10, :]
        CT = tiles(16, 20).rearrange("p (a b) -> p a b", b=CTX)
        fnetT, CXT = wide[:, 16:18, :], wide[:, 18:20, :]
        ctok = tiles(20, 24).rearrange("p (t n) -> p t n", t=2)
        XW = wide[:, 20:24, :]
        Hn = O
        XS, Y, FAB = wide[:, 24:28, :], wide[:, 28:32, :], wide[:, 28:32, :]
        XF, XB = wide[:, 0:4, :], wide[:, 16:20, :]
        MB = [PT, wide[:, 20:24, :]]
        gbc = KS4[:, :, :].rearrange("p a b -> p (a b)")
        SCF = SC[:, :, :, :].rearrange("p a b c -> p (a b c)")
        PAD_L = 528
        PB, D1, D2 = (SCF[:, n * 2 * PAD_L:(n + 1) * 2 * PAD_L].rearrange("p (a b) -> p a b", a=2) for n in range(3))
        D8 = SCF[:, 6 * PAD_L:7 * PAD_L]
        R = kb
        CR = rows[0:16, :, :].rearrange("p a b -> p (a b)")
        DT, DA = CR[:, 0:768], CR[:, 768:1536]
        PTF = PT[0:16, :, :].rearrange("p a b -> p (a b)")
        CF, RV = PTF[:, 0:768], PTF[:, 768:1536]
        PAIR = [wide[:, a:a + 4, :].rearrange("p a b -> p (a b)") for a in (12, 28)]
        PADS = [PAIR[m // 2][:, (m % 2) * 660:(m % 2 + 1) * 660].rearrange("p (r c) -> p r c", r=10) for m in range(4)]
        SUMS = [PAIR[m // 2][:, 1320:1832] if m % 2 == 0 else KS4[:, m // 2, :] for m in range(4)]
        dch = w2[0:HD, 0, :, :]
        fw = w2[0:HD, 1, :, :].rearrange("p a b -> p (a b)")

        class Steps:

            def __init__(self, sem_, names):
                self.sem, self.names, self.next = sem_, names, 0
                self.place = {n: i + 1 for i, n in enumerate(names)}
                assert len(self.place) == len(names)

            def do(self, name, ins):
                assert self.names[self.next] == name, (name, self.names[self.next])
                self.next += 1
                ins.then_inc(self.sem, 1)

            def of(self, name):
                return self.place[name]

        def names(*parts):
            out_ = []
            for x in parts:
                out_ += [x] if isinstance(x, str) else list(x)
            return out_

        CONV = [(m, who) for m in range(8) for who in ("c", "l") if who == "l" or m < 6]

        def conv_order(first, second):
            out_ = []
            for m in range(9):
                for k, w in CONV:
                    if k == m:
                        out_ += [x.format(w=w, m=m) for x in first]
                for k, w in CONV:
                    if k == m - 1:
                        out_ += [x.format(w=w, m=m - 1) for x in second]
            return out_

        V2 = Steps(s_two, names(
            "mod1", "mod2", "mod3", [f"dgb{b}" for b in range(16)], "halfw", "bdz", "pwz",
            conv_order(["{w}{m}a", "{w}{m}b"], ["{w}{m}s"]),
            "dneg", "dabs", "dmax", "dt", "nega", "dA", "cf", "cfc", "rv", "rvc", "c0", "cs", "tt0", "tt1", "wc",
            [f"bd{n}" for n in range(8)], [f"z{t}" for t in range(4)], "tks", "ncs", [f"xw{n}" for n in range(8)],
            [f"xf{t}" for t in range(4)], [f"xb{t}" for t in range(4)],
            [f"yo{g}{t}{x}" for g in range(2) for t in range(4) for x in "abc"],
            "da0", "db0", "dm0", [x for h in range(8) for x in ([f"da{h+1}", f"db{h+1}", f"dm{h+1}"] if h < 7 else [])
                                  + [f"mm{h}", f"df{h}", f"dr{h}"] + ([f"ya{h-1}"] if h else [])], "ya7",
            [f"{x}{t}" for t in range(4) for x in ("sk", "sa", "sz", "sq", "sr")], "sv", "si", [f"sn{t}" for t in range(4)]))
        A2 = Steps(s_twoa, names(
            [f"gb{q}" for q in range(4)], "dtc", "dtl", conv_order(["{w}{m}f"], ["{w}{m}t"]),
            "alog", "dexp", "dln", "fn0", "fn1", "po0", "po1", "wexp",
            [f"z{t}{x}" for t in range(4) for x in "ht"], [f"fab{t}" for t in range(4)], "yf0", "yf1", "ecs",
            [f"xt{t}" for t in range(4)], "ct0", "ct1", "bt", "yp0", "yp1", "st0", "st1", [f"g{g}{j}" for g in range(2) for j in range(4)],
            [f"{x}{h}" for h in range(8) for x in ("of", "ed")], "ss", [f"ym{b}" for b in range(4)]))
        P2 = Steps(s_twop, names(
            [f"gb{q}" for q in range(4)], "dtc", "bdp", "tks", [f"fab{t}" for t in range(4)],
            [f"xt{t}" for t in range(4)], "ct0", "ct1", "bt", "yp0", "yp1", "st0", "st1",
            [f"g{g}{j}" for g in range(2) for j in range(4)], [f"yo{g}{t}" for g in range(2) for t in range(4)],
            "rw0", "rw1", [x for h in range(8) for x in ([f"rw{h+2}"] if h < 6 else []) + [f"y{h}"]], [f"ym{b}" for b in range(4)]))
        G2 = Steps(s_twog, names("pz", "d2", "d4", "d8", "d16", "m0", "m1", "m2", "m3", "sub", "padz"))

        def XBC(w, m):
            return xbcT[:, m, :] if w == "l" else CX[:, m, :]

        def TH(w, m):
            return qb[:, m % 2, :] if w == "l" else PT[:, 3, (m % 2) * CTX:(m % 2 + 1) * CTX]

        def DGB(b):
            return qb[:, (b % 8) // 4, (b % 4) * P:(b % 4 + 1) * P]

        def DFB(h):
            return (kb[:, 0, :], kb[:, 1, :]) if h % 2 == 0 else (XT[:, 0, :], XT[:, 1, :])

        def diagonal(m):
            a = m[:, 0, 0:P]
            return bass.AP(tensor=a.tensor, offset=a.offset, ap=[list(a.ap[0]), [S + P, TT], [1, P]])

        def gpsimd_second(gp, gain_bias):
            gp.wait_ge(quarters, st("mlp1", "quarters") + 64)
            gp.dma_start(ctok, A["ctx_2"].rearrange("o (t p) d -> p (o t) d", p=P)).then_inc(s_ctx, 16)
            gp.dma_start(dch, A["dft_ch"]).then_inc(s_twod, 16)
            gp.dma_start(fw.rearrange("p (g d) -> p g d", g=4), A["fnet_w_2"].rearrange("o g c d -> c (o g) d")).then_inc(s_twod, 16)
            gp.dma_start(drow[:, :], A["ssd_d_2"].partition_broadcast(P).rearrange("p o h -> p (o h)")).then_inc(s_twod, 16)
            gp.wait_ge(s_two, V2.of("pwz"))
            for g in range(4):
                r = (g % 2) * HD
                gp.dma_start(poolw[r:r + HD, g // 2, r:r + HD], A["pool_w_2"][0, g, :, :]).then_inc(s_twod, 16)
            gp.wait_ge(quarters, st("mlp1", "quarters") + 64)
            G2.do("pz", nc.gpsimd.memset(SCF[:, 0:2 * PAD_L], 0.0))
            gp.wait_ge(s_twoa, A2.of("po1"))
            tt = nc.gpsimd.tensor_tensor
            G2.do("d2", tt(out=D1[:, :, 0:526], in0=PB[:, :, 0:526], in1=PB[:, :, 1:527], op=ALU.add))
            gp.wait_ge(s_twog, G2.of("d2"))
            G2.do("d4", tt(out=D2[:, :, 0:524], in0=D1[:, :, 0:524], in1=D1[:, :, 2:526], op=ALU.add))
            gp.wait_ge(s_twog, G2.of("d4"))
            G2.do("d8", tt(out=D8[:, 0:520], in0=D2[:, 1, 0:520], in1=D2[:, 1, 4:524], op=ALU.add))
            gp.wait_ge(s_twog, G2.of("d8"))
            G2.do("d16", tt(out=D1[:, 1, 0:S], in0=D8[:, 0:S], in1=D8[:, 8:S + 8], op=ALU.add))
            gp.wait_ge(s_twog, G2.of("d16"))
            inv = tab("inv_count").rearrange("p (a n) -> p a n", a=2)
            for n, (p0, i, src) in enumerate([(0, 0, D1[0:HD, 0, 7:7 + S]), (HD, 0, D2[HD:P, 0, 6:6 + S]),
                                              (0, 1, D8[0:HD, 4:4 + S]), (HD, 1, D1[HD:P, 1, 0:S])]):
                G2.do(f"m{n}", tt(out=R[p0:p0 + HD, i, :], in0=src, in1=inv[p0:p0 + HD, i, :], op=ALU.mult))
            gp.wait_ge(s_twog, G2.of("m3"))
            G2.do("sub", tt(out=R[:, :, :], in0=R[:, :, :], in1=PB[:, :, 8:8 + S], op=ALU.subtract))
            gp.wait_ge(s_twop, P2.of("y7"))
            gp.wait_ge(s_two, V2.of("mm7"))
            gain_bias(4, A["ln1_g_2"][0, :], A["ln1_b_2"][0, :])
            gain_bias(5, A["ln2_g_2"][0, :], A["ln2_b_2"][0, :])
            gp.wait_ge(tr_ready, st("x5", "tr") + 8)
            nc.gpsimd.memset(PAIR[0][:, 0:1320], 0.0)
            G2.do("padz", nc.gpsimd.memset(PAIR[1][:, 0:1320], 0.0))
            for n in range(3):
                low_split(gp, tt, "ffn2", n)
            n0 = 0
            for up, down in PARTS["ffn2"]:
                with gp.Fori(0, up // 4) as i:
                    for m in range(4):
                        low_split(gp, tt, "ffn2", n0 + m + 3, i)
                n0 += up
                for n in range(n0, n0 + down):
                    if n + 3 < n_quarters("ffn2"):
                        low_split(gp, tt, "ffn2", n + 3)
                n0 += down

        def tensor_second(pe, stage_start, slab_wait, mlp_products, out_products):
            mm_, tr_ = nc.tensor.matmul, nc.tensor.transpose

            def by_feature(stage, src, n_tiles, ready):
                base = st(stage, "tr")
                ready()
                for b in range(KT):
                    if base + b >= 2:
                        pe.wait_ge(tr_out, base + b - 1)
                    for t in range(n_tiles):
                        m = tr_(TR[b % 2][:, t * P:(t + 1) * P], src[:, t, b * P:(b + 1) * P], ident)
                    m.then_inc(tr_ready, 1)

            by_feature("x4", Hn, TT, lambda: pe.wait_ge(ln_norm, st("mlp1", "norm") + 4))
            by_feature("x_ctx", ctok, 2, lambda: pe.wait_ge(ln_norm, st("ln_ctx", "norm") + 2))
            for q in range(4):
                pe.wait_ge(s_two, V2.of(f"dgb{4 * q + 3}"))
                pe.wait_ge(ln_dve, st("ln_ctx", "ln"))
                for n in range(4):
                    m = mm_(G[q][:, n * P:(n + 1) * P], lhsT=ones[:, :], rhs=DGB(4 * q + n), start=True, stop=True)
                P2.do(f"gb{q}", m)

            s0 = SLAB["w_in"][0]
            pe.wait_ge(tr_out, st("x_ctx", "tr") + 8)
            pe.wait_ge(s_twoa, A2.of("gb3"))
            slab_wait(s0)
            for k in range(KT):
                m = mm_(G[2][0:16, 0:CTX], lhsT=slab(s0)[:, k, 0:16], rhs=CT[:, k, :], start=(k == 0), stop=(k == KT - 1))
            P2.do("dtc", m)
            for k in range(KT):
                m = mm_(G[0][0:16, :], lhsT=slab(s0)[:, k, 0:16], rhs=XT[:, k, :], start=(k == 0), stop=(k == KT - 1))
            m.then_inc(quarters, 4)
            for n in range(16):
                if n % 4 == 0:
                    slab_wait(s0 + 1 + n // 4)
                sl = slab(s0 + 1 + n // 4)
                c = slice((n % 4) * P, (n % 4 + 1) * P)
                if n < 2:
                    pe.wait_ge(s_twoa, A2.of("dtl"))
                elif n < 10:
                    pe.wait_ge(s_two, V2.of(f"l{n - 2}b"))
                elif n < 14:
                    pe.wait_ge(s_twoa, A2.of(("fn0", "fn1", "po0", "po1")[n - 10]))
                else:
                    pe.wait_ge(s_twoa, A2.of(f"z{n - 14}h"))
                if n < 6:
                    for k in range(KT):
                        mm_(G[2 + n % 2][:, 0:CTX], lhsT=sl[:, k, c], rhs=CT[:, k, :], start=(k == 0), stop=(k == KT - 1))
                for k in range(KT):
                    if n < 12:
                        m = mm_(G[n % 2][:, :], lhsT=sl[:, k, c], rhs=XT[:, k, :], start=(k == 0), stop=(k == KT - 1))
                    else:
                        m = mm_(G[n % 2][:, :], lhsT=XT[:, k, c], rhs=sl[:, k, :], start=(k == 0), stop=(k == KT - 1))
                m.then_inc(quarters, 1)

            pe.wait_ge(s_twod, 112)
            for cs in range(2):
                m = mm_(TR[0][:, cs * 256:(cs + 1) * 256], lhsT=dch[:, cs, :], rhs=fw, start=True, stop=True)
            P2.do("bdp", m)
            pe.wait_ge(s_two, V2.of("wc"))
            for n in range(10):
                src = DA[:, n * P:(n + 1) * P] if n < 4 else DT[:, (n - 4) * P:(n - 3) * P] if n < 8 else CF[:, S + (n - 8) * P:S + (n - 7) * P]
                m = tr_(OB[1][:, n * 16:(n + 1) * 16], src, ident[0:16, 0:16])
            P2.do("tks", m)
            pe.wait_ge(s_two, V2.of("bd7"))
            for t in range(TT):
                pe.wait_ge(s_twoa, A2.of("z3h"))
                for ft in range(2):
                    m = mm_(G[t][:, ft * 256:(ft + 1) * 256], lhsT=fnetT[:, ft, t * P:(t + 1) * P], rhs=bd[:, ft, :], start=True, stop=True)
                P2.do(f"fab{t}", m)
            sd = SLAB["dft"][0]
            slab_wait(sd)
            for ft in range(2):
                for n in range(8):
                    cs, t = n // 4, n % 4
                    pe.wait_ge(s_twoa, A2.of("fab3"))
                    m = mm_(TR[ft][:, :], lhsT=FAB[:, t, ft * 256 + cs * P:ft * 256 + (cs + 1) * P], rhs=slab(sd)[:, n, :],
                            start=(n == 0), stop=(n == 7))
                m.then_inc(quarters, 2)
            pe.wait_ge(s_two, V2.of("l7s"))
            for t in range(TT):
                for b in range(4):
                    m = tr_(G[t][:, b * P:(b + 1) * P], xbcT[:, b, t * P:(t + 1) * P], ident)
                P2.do(f"xt{t}", m)
            for t in range(2):
                pe.wait_ge(s_twoa, A2.of(f"yf{t}"))
                for b in range(4):
                    m = tr_(TR[t][:, b * P:(b + 1) * P], CX[:, b, t * P:(t + 1) * P], ident)
                P2.do(f"ct{t}", m)
            for n in range(4):
                m = tr_(OB[0][:, n * P:(n + 1) * P], CX[:, 4 + n % 2, (n // 2) * P:(n // 2 + 1) * P], ident)
            P2.do("bt", m)
            pe.wait_ge(s_twog, G2.of("sub"))
            pe.wait_ge(s_twod, 112)
            for i in range(2):
                pe.wait_ge(s_twoa, A2.of(f"xt{i}"))
                P2.do(f"yp{i}", mm_(G[i][:, :], lhsT=poolw[:, i, :], rhs=R[:, i, :], start=True, stop=True))
            pe.wait_ge(s_two, V2.of("xw7"))
            pe.wait_ge(s_twoa, A2.of("bt"))
            for g in range(2):
                for t in range(2):
                    m = mm_(OB[g][:, :], lhsT=Btok[:, (2 * t + g) * P:(2 * t + g + 1) * P], rhs=XW[:, 2 * t + g, :], start=(t == 0), stop=(t == 1))
                P2.do(f"st{g}", m)
            for g in range(2):
                for j in range(TT):
                    if g == 0:
                        pe.wait_ge(s_twoa, A2.of(f"yp{j}" if j < 2 else f"xt{j}"))
                    else:
                        pe.wait_ge(s_twoa, A2.of(f"g0{j}"))
                    P2.do(f"g{g}{j}", mm_(G[j][:, :], lhsT=xbcT[:, 4 + g, j * P:(j + 1) * P], rhs=xbcT[:, 6 + g, :], start=True, stop=True))
            pe.wait_ge(s_twoa, A2.of("st1"))
            for g in range(2):
                for t in range(TT):
                    if g or t >= 2:
                        pe.wait_ge(s_two, V2.of(f"yo{g if t >= 2 else 0}{(t - 2) % 4}b"))
                    P2.do(f"yo{g}{t}", mm_(TR[t % 2][:, :], lhsT=xbcT[:, 6 + g, t * P:(t + 1) * P], rhs=STATE[:, g, :], start=True, stop=True))

            def decay_rows(h):
                if h >= 2:
                    pe.wait_ge(s_two, V2.of(f"db{h - 2}"))
                    pe.wait_ge(s_twoa, A2.of(f"of{h - 2}"))
                else:
                    pe.wait_ge(s_twoa, A2.of("g13"))
                for x in range(2):
                    m = mm_(G[2 * (h % 2) + x][:, :], lhsT=ident[0:16, 8 * x + h:8 * x + h + 1].to_broadcast([16, P]), rhs=DA[:, 0:S],
                            start=True, stop=True)
                P2.do(f"rw{h}", m)

            decay_rows(0)
            decay_rows(1)
            for h in range(8):
                if h < 6:
                    decay_rows(h + 2)
                pe.wait_ge(s_two, V2.of(f"dr{h}"))
                if h >= 2:
                    pe.wait_ge(s_two, V2.of(f"ya{h - 2}"))
                M = MB[h % 2]
                c = slice(h // 2 * P, (h // 2 + 1) * P)
                for t in range(TT):
                    T_ = slice(t * P, (t + 1) * P)
                    terms = [(M[:, j, T_], (XF if j < t else XB)[:, j, c]) for j in range(TT) if j != t]
                    terms += [(DFB(h)[0][:, T_], XF[:, t, c]), (DFB(h)[1][:, T_], XB[:, t, c])]
                    for n, (a, b) in enumerate(terms):
                        m = mm_(OB[h % 2][:, t * P:(t + 1) * P], lhsT=a, rhs=b, start=(n == 0), stop=(n == len(terms) - 1))
                P2.do(f"y{h}", m)
            pe.wait_ge(s_two, V2.of("sn3"))
            for b in range(4):
                if b >= 2:
                    pe.wait_ge(s_twoa, A2.of(f"ym{b - 2}"))
                for t in range(TT):
                    m = tr_(TR[b % 2][:, t * P:(t + 1) * P], Y[:, t, b * P:(b + 1) * P], ident)
                P2.do(f"ym{b}", m)

            pe.wait_ge(s_twoa, A2.of("ym3"))
            out_products("out2", "x4")
            by_feature("x5", Hn, TT, lambda: pe.wait_ge(ln_norm, st("out2", "norm") + 4))

            mlp_products("ffn2", "x5")

        def hidden_tile(x, i, e):
            at = 2 * i + e if isinstance(i, int) else i * 2 + e if e >= 0 else (i - 1) * 2 + (e + 2)
            return x[:, at:at + 1, :] if isinstance(at, int) else x[:, bass.ds(at, 1), :]

        def scalar_second(act, first_splits, normalize):
            ac = nc.scalar.activation

            def modulated(stage, dst, n_tiles, scale0, shift0):
                base = st(stage, "tr")
                act.wait_ge(s_two, V2.of("mod3"))
                for b in range(KT):
                    act.wait_ge(tr_ready, base + b + 1)
                    ac(dst[:, b, :], TR[b % 2][:, 0:n_tiles * P], ACT.Identity, scale=modc[:, scale0 + b:scale0 + b + 1],
                       bias=modc[:, shift0 + b:shift0 + b + 1]).then_inc(tr_out, 1)

            modulated("x4", XT, TT, 8, 0)
            normalize("ln_ctx", ctok, ctok)
            modulated("x_ctx", CT, 2, 56, 48)
            for q in range(4):
                act.wait_ge(s_twop, P2.of(f"gb{q}"))
                A2.do(f"gb{q}", ac(gbc[:, q * 512:(q + 1) * 512], G[q][:, :], ACT.Copy))
            q0 = st("w_in", "quarters")
            act.wait_ge(s_twop, P2.of("dtc"))
            A2.do("dtc", ac(DT[:, S:S + CTX], G[2][0:16, 0:CTX], ACT.Identity, bias=col("dt_bias", 0, 16)))
            act.wait_ge(quarters, q0 + 4)
            A2.do("dtl", ac(DT[:, 0:S], G[0][0:16, :], ACT.Identity, bias=col("dt_bias", 0, 16)))

            def conv_tanh(m, w):
                act.wait_ge(s_two, V2.of(f"{w}{m}b"))
                if m >= 2:
                    act.wait_ge(s_two, V2.of(f"{w}{m - 2}s"))
                A2.do(f"{w}{m}t", ac(TH(w, m), XBC(w, m), ACT.Tanh))

            act.wait_ge(s_two, V2.of("halfw"))
            for m in range(9):
                if m < 8:
                    act.wait_ge(quarters, q0 + 4 + m + 1)
                for k, w in CONV:
                    if k == m:
                        ps = G[m % 2][:, :] if w == "l" else G[2 + m % 2][:, 0:CTX]
                        A2.do(f"{w}{m}f", ac(XBC(w, m), ps, ACT.Identity, scale=col("conv", 3 * m + 1), bias=col("conv_b", m)))
                for k, w in CONV:
                    if k == m - 1:
                        conv_tanh(k, w)
            A2.do("alog", ac(nega[:, 0:1], col("a_log", 0, 16), ACT.Exp))
            act.wait_ge(s_two, V2.of("dabs"))
            A2.do("dexp", ac(DA, DA, ACT.Exp, scale=-1.0))
            act.wait_ge(s_twoa, A2.of("dexp"))
            A2.do("dln", ac(DA, DA, ACT.Ln, bias=1.0))
            for n in range(4):
                act.wait_ge(quarters, q0 + 12 + n + 1)
                if n < 2:
                    A2.do(f"fn{n}", ac(fnetT[:, n, :], G[n % 2][:, :], ACT.Copy))
                else:
                    act.wait_ge(s_twog, G2.of("pz"))
                    A2.do(f"po{n - 2}", ac(PB[:, n - 2, 8:8 + S], G[n % 2][:, :], ACT.Copy))
            act.wait_ge(s_two, V2.of("tt1"))
            A2.do("wexp", ac(CF[:, S:S + CTX], DA[:, S:S + CTX], ACT.Exp, scale=-1.0, bias=nega[:, 3:4]))
            for t in range(TT):
                act.wait_ge(quarters, q0 + 16 + t + 1)
                A2.do(f"z{t}h", ac(Z[:, t, :], G[t % 2][:, :], ACT.Copy, scale=0.5))
                act.wait_ge(s_twoa, A2.of(f"z{t}h"))
                act.wait_ge(s_two, V2.of("l7s") if t < 2 else V2.of(f"z{t - 2}"))
                A2.do(f"z{t}t", ac(qb[:, t % 2, :], Z[:, t, :], ACT.Tanh))
            for t in range(TT):
                act.wait_ge(s_twop, P2.of(f"fab{t}"))
                A2.do(f"fab{t}", ac(FAB[:, t, :], G[t][:, :], ACT.Copy))
            for ft in range(2):
                act.wait_ge(quarters, st("dft", "quarters") + 2 * ft + 2)
                A2.do(f"yf{ft}", ac(XT[:, 4 + ft, :], TR[ft][:, :], ACT.Copy))
            act.wait_ge(s_two, V2.of("tks"))
            A2.do("ecs", ac(ecs[:, :, :].rearrange("p a b -> p (a b)"), tks[:, 0:64], ACT.Exp))
            for t in range(TT):
                act.wait_ge(s_twop, P2.of(f"xt{t}"))
                A2.do(f"xt{t}", ac(XS[:, t, :], G[t][:, :], ACT.Copy))
            for t in range(2):
                act.wait_ge(s_twop, P2.of(f"ct{t}"))
                A2.do(f"ct{t}", ac(CXT[:, t, :], TR[t][:, :], ACT.Copy))
            act.wait_ge(s_twop, P2.of("bt"))
            A2.do("bt", ac(Btok, OB[0][:, :], ACT.Copy))
            for i in range(2):
                act.wait_ge(s_twop, P2.of(f"yp{i}"))
                A2.do(f"yp{i}", ac(XT[:, 6 + i, :], G[i][:, :], ACT.Copy, scale=col("pool", i)))
            for g in range(2):
                act.wait_ge(s_twop, P2.of(f"st{g}"))
                A2.do(f"st{g}", ac(STATE[:, g, :], OB[g][:, :], ACT.Copy))
            act.wait_ge(s_twog, G2.of("sub"))
            for g in range(2):
                for j in range(TT):
                    act.wait_ge(s_twop, P2.of(f"g{g}{j}"))
                    A2.do(f"g{g}{j}", ac(SC[:, g, j, :], G[j][:, :], ACT.Copy))
            for h in range(8):
                act.wait_ge(s_two, V2.of(f"db{h}"))
                if h >= 2:
                    act.wait_ge(s_twop, P2.of(f"y{h - 2}"))
                elif h == 1:
                    act.wait_ge(s_twop, P2.of("st1"))
                M = MB[h % 2]
                for j in range(TT):
                    if j:
                        m = ac(M[:, j, 0:j * P], G[2 * (h % 2) + 1][:, 0:j * P], ACT.Exp, bias=ncs[:, j, 8 + h:9 + h])
                    if j < 3:
                        m = ac(M[:, j, (j + 1) * P:S], G[2 * (h % 2)][:, (j + 1) * P:S], ACT.Exp, bias=ncs[:, j, h:h + 1])
                A2.do(f"of{h}", m)
                act.wait_ge(s_two, V2.of(f"dm{h}"))
                A2.do(f"ed{h}", ac(diagonal(M), qb[:, h % 2, :].rearrange("p (a b) -> p a b", a=TT), ACT.Exp))
            act.wait_ge(s_two, V2.of("si"))
            A2.do("ss", ac(ys[:, 2, :, :], ys[:, 0, :, :], ACT.Sqrt))
            for b in range(4):
                act.wait_ge(s_twop, P2.of(f"ym{b}"))
                A2.do(f"ym{b}", ac(XT[:, b, :], TR[b % 2][:, :], ACT.Copy, scale=col("norm", b)))
            normalize("out2", then=Hn)
            base, v = st("x5", "tr"), 0
            for b in range(KT):
                act.wait_ge(tr_ready, base + b + 1)
                if b >= 2:
                    act.wait_ge(tr_out, base + b - 1)
                for dst, sem_ in ((act_buf[b % 2], x_val), (XTh[:, b, :], xt_hi)):
                    ac(dst, TR[b % 2][:, :], ACT.Identity, scale=modc[:, 32 + b:33 + b], bias=modc[:, 24 + b:25 + b]).then_inc(sem_, 1)
            first_splits("ffn2")

            n, u, q, a0, h = 0, 0, st("ffn2", "quarters"), st("ffn2", "act"), st("ffn2", "hidden")
            Q = SPLIT0["ffn2"]

            def grids(i, first=False):
                pads(i, 0)
                pads(i, 1)
                if not first:
                    gelu(i, -1)
                    high_hidden(i, -1)
                pads(i, 2)
                pads(i, 3)
                gelu(i, 1)
                high_hidden(i, 0)

            def pads(i, m):
                high_split(act, "ffn2", n + m + 3, i)
                act.wait_ge(quarters, i * 4 + (q + n + m + 1))
                if m % 2 == 0:
                    act.wait_ge(hidden, i * 2 + (h + (u + m) // 2 - 1))
                ps = G[m][:, :].rearrange("p (r c) -> p r c", c=GRID_W)
                ac(PADS[m][:, 1:9, 1:65], ps, ACT.Copy).then_inc(conv_first, 1)
                f = C2["ffn"] + 10 * (u + m)
                w, b = (cols2[:, bass.ds(i * 40 + (f + x), 1)] for x in (4, 9))
                ac(SUMS[m], G[m][:, :], ACT.Identity, scale=w, bias=b).then_inc(act_out, 1)

            def gelu(i, m):
                act.wait_ge(conv_steps, i * 32 + 8 * (u + m + 1))
                ac(SUMS[m % 4], SUMS[m % 4], ACT.Gelu_apprx_tanh).then_inc(gelu_done, 1)

            def high_hidden(i, e):
                act.wait_ge(hid_steps, i * 2 + (h + u // 2 + e + 1))
                ac(hidden_tile(Hh, i, e), SUMS[2 * (e % 2)].unsqueeze(1), ACT.Copy).then_inc(hid_hi, 1)

            act.wait_ge(s_twog, G2.of("padz"))
            for up, down in PARTS["ffn2"]:
                grids(0, True)
                with act.Fori(1, up // 4) as i:
                    grids(i)
                gelu(up // 4, -1)
                high_hidden(up // 4, -1)
                n, u = n + up, u + up
                for j in range(down):
                    if n + j + 3 < n_quarters("ffn2"):
                        high_split(act, "ffn2", n + j + 3)
                n += down
            normalize("ffn2")

        def vector_second(dve, down_wait, layer_norm):
            tt, ts, stt = nc.vector.tensor_tensor, nc.vector.tensor_scalar, nc.vector.scalar_tensor_tensor

            def own(name):
                dve.wait_ge(s_two, V2.of(name))

            own("mod3")
            dve.wait_ge(s_ctx, 16)
            layer_norm("ln_ctx", EPS_2, src=ctok)
            for b in range(16):
                c = 16 + b if b < 8 else 32 + b
                if b >= 8:
                    dve.wait_ge(s_twop, P2.of(f"gb{(b - 8) // 4}"))
                V2.do(f"dgb{b}", ts(DGB(b), ident, modc[:, c:c + 1], None, ALU.mult))
            V2.do("halfw", ts(cols2[:, 84:116], cols2[:, 84:116], 0.5, None, ALU.mult))
            V2.do("bdz", nc.vector.memset(bd[:, :, :], 0.0))
            V2.do("pwz", nc.vector.memset(poolw[:, :, :], 0.0))

            own("halfw")
            for m in range(9):
                for k, w in CONV:
                    if k == m:
                        n = S if w == "l" else CTX
                        ps = G[m % 2] if w == "l" else G[2 + m % 2]
                        y = XBC(w, m)
                        dve.wait_ge(s_twoa, A2.of(f"{w}{m}f"))
                        V2.do(f"{w}{m}a", stt(out=y[:, 1:n], in0=ps[:, 0:n - 1], scalar=col("conv", 3 * m), in1=y[:, 1:n], op0=ALU.mult, op1=ALU.add))
                        own(f"{w}{m}a")
                        V2.do(f"{w}{m}b", stt(out=y[:, 0:n - 1], in0=ps[:, 1:n], scalar=col("conv", 3 * m + 2), in1=y[:, 0:n - 1], op0=ALU.mult, op1=ALU.add))
                for k, w in CONV:
                    if k == m - 1:
                        y = XBC(w, k)
                        dve.wait_ge(s_twoa, A2.of(f"{w}{k}t"))
                        V2.do(f"{w}{k}s", stt(out=y, in0=TH(w, k), scalar=1.0, in1=y, op0=ALU.add, op1=ALU.mult))
            dve.wait_ge(s_twoa, A2.of("dtl"))
            V2.do("dneg", ts(DA, DT, -1.0, None, ALU.mult))
            own("dneg")
            V2.do("dabs", tt(out=DA, in0=DA, in1=DT, op=ALU.max))
            own("dabs")
            V2.do("dmax", ts(DT, DT, 0.0, None, ALU.max))
            dve.wait_ge(s_twoa, A2.of("dln"))
            own("dmax")
            V2.do("dt", tt(out=DT, in0=DT, in1=DA, op=ALU.add))
            V2.do("nega", ts(nega[:, 1:2], nega[:, 0:1], -1.0, None, ALU.mult))
            own("nega")
            V2.do("dA", ts(DA, DT, nega[:, 1:2], None, ALU.mult))
            own("dA")
            scan = nc.vector.tensor_tensor_scan
            for name, o, a, b, flip in (("cf", CF, 0, S, 0), ("cfc", CF, S, S + CTX, 0), ("rv", RV, 0, S, 1), ("rvc", RV, S, S + CTX, 1)):
                src, dst = DA[:, a:b], o[:, a:b]
                if flip:
                    src, dst = src[:, ::-1], dst[:, ::-1]
                V2.do(name, scan(out=dst, data0=src, data1=src, initial=0.0, op0=ALU.add, op1=ALU.bypass))
            own("rvc")
            V2.do("c0", ts(CF, CF, col("fwd", 0, 16), None, ALU.mult))
            own("c0")
            V2.do("cs", stt(out=DA, in0=RV, scalar=col("bwd", 0, 16), in1=CF, op0=ALU.mult, op1=ALU.add))
            own("cs")
            V2.do("tt0", ts(nega[:, 2:3], DA[:, S + CTX - 1:S + CTX], col("fwd", 0, 16), None, ALU.mult))
            own("tt0")
            V2.do("tt1", stt(out=nega[:, 3:4], in0=DA[:, S:S + 1], scalar=col("bwd", 0, 16), in1=nega[:, 2:3], op0=ALU.mult, op1=ALU.add))
            dve.wait_ge(s_twoa, A2.of("wexp"))
            V2.do("wc", tt(out=CF[:, S:S + CTX], in0=CF[:, S:S + CTX], in1=DT[:, S:S + CTX], op=ALU.mult))
            dve.wait_ge(s_twop, P2.of("bdp"))
            own("bdz")
            for n in range(8):
                cs, g = n // 4, n % 4
                r = (g % 2) * HD
                V2.do(f"bd{n}", nc.vector.tensor_copy(bd[r:r + HD, g // 2, cs * P + r:cs * P + r + HD],
                                                      TR[0][r:r + HD, cs * 256 + g * HD:cs * 256 + (g + 1) * HD]))
            for t in range(TT):
                dve.wait_ge(s_twoa, A2.of(f"z{t}t"))
                V2.do(f"z{t}", stt(out=Z[:, t, :], in0=qb[:, t % 2, :], scalar=1.0, in1=Z[:, t, :], op0=ALU.add, op1=ALU.mult))
            dve.wait_ge(s_twop, P2.of("tks"))
            V2.do("tks", nc.vector.tensor_copy(tks[:, :], OB[1][:, 0:160]))
            own("tks")
            V2.do("ncs", ts(ncs[:, :, :].rearrange("p a b -> p (a b)"), tks[:, 0:64], -1.0, None, ALU.mult))
            dtt = tks[:, 64:128].rearrange("p (t n) -> p t n", t=TT)
            wct = tks[:, 128:160].rearrange("p (t n) -> p t n", t=2)

            def heads_(ap, n=4):
                return ap.rearrange("p (h d) -> p h d", h=n)

            def over(ap, n, d):
                return ap.unsqueeze(2).to_broadcast([P, n, d])

            for n in range(8):
                t, g, x = n // 4, (n // 2) % 2, n % 2
                dve.wait_ge(s_twoa, A2.of(f"ct{t}"))
                V2.do(f"xw{n}", tt(out=heads_(XW[:, 2 * t + g, x * 256:(x + 1) * 256]), in0=heads_(CXT[:, t, g * 256:(g + 1) * 256]),
                                   in1=over(wct[:, t, 8 * x + 4 * g:8 * x + 4 * g + 4], 4, HD), op=ALU.mult))
            own("xw7")
            dve.wait_ge(s_twoa, A2.of("fab3"))
            for x, dst in ((0, XF), (1, XB)):
                for t in range(TT):
                    dve.wait_ge(s_twoa, A2.of(f"xt{t}"))
                    V2.do(f"x{'fb'[x]}{t}", tt(out=heads_(dst[:, t, :], 8), in0=heads_(XS[:, t, :], 8),
                                              in1=over(dtt[:, t, 8 * x:8 * x + 8], 8, HD), op=ALU.mult))
            dve.wait_ge(s_twoa, A2.of("ecs"))
            for g in range(2):
                for t in range(TT):
                    dve.wait_ge(s_twop, P2.of(f"yo{g}{t}"))
                    y = heads_(Y[:, t, g * 256:(g + 1) * 256])
                    if g or t:
                        own(f"yo{g if t else g - 1}{(t - 1) % 4}c")
                    V2.do(f"yo{g}{t}a", tt(out=y, in0=heads_(TR[t % 2][:, 0:256]), in1=over(ecs[:, t, 4 * g:4 * g + 4], 4, HD), op=ALU.mult))
                    V2.do(f"yo{g}{t}b", tt(out=heads_(ogf[:, 0:256]), in0=heads_(TR[t % 2][:, 256:512]), in1=over(ecs[:, t, 8 + 4 * g:12 + 4 * g], 4, HD), op=ALU.mult))
                    own(f"yo{g}{t}b")
                    V2.do(f"yo{g}{t}c", tt(out=y, in0=y, in1=heads_(ogf[:, 0:256]), op=ALU.add))

            def head_out(h):
                y = Y[:, :, h * HD:(h + 1) * HD]
                dve.wait_ge(s_twop, P2.of(f"y{h}"))
                V2.do(f"ya{h}", tt(out=y, in0=y, in1=OB[h % 2][:, :].rearrange("p (t d) -> p t d", t=TT)[:, :, (h % 2) * HD:(h % 2 + 1) * HD], op=ALU.add))

            def diagonal_exponents(h):
                q = [qb[:, h % 2, :].rearrange("p (a b) -> p a b", a=TT), ogf.rearrange("p (a b) -> p a b", a=TT)]
                dve.wait_ge(s_twop, P2.of(f"rw{h}"))
                own(f"dm{h - 1}" if h else "yo13c")
                if h >= 2:
                    dve.wait_ge(s_twoa, A2.of(f"ed{h - 2}"))
                for x, name in enumerate(("da", "db")):
                    V2.do(f"{name}{h}", tt(out=q[x], in0=G[2 * (h % 2) + x][:, :].rearrange("p (a b) -> p a b", a=TT),
                                           in1=over(ncs[:, :, 8 * x + h], TT, P), op=ALU.add))
                own(f"db{h}")
                V2.do(f"dm{h}", tt(out=q[0], in0=q[0], in1=q[1], op=ALU.min))

            diagonal_exponents(0)
            for h in range(8):
                if h < 7:
                    diagonal_exponents(h + 1)
                M = MB[h % 2]
                dve.wait_ge(s_twoa, A2.of(f"ed{h}"))
                V2.do(f"mm{h}", tt(out=M[:, :, :], in0=M[:, :, :], in1=SC[:, h // 4, :, :], op=ALU.mult))
                own(f"mm{h}")
                if h >= 2:
                    dve.wait_ge(s_twop, P2.of(f"y{h - 2}"))
                for x, (name, mask) in enumerate((("df", "upper"), ("dr", "lower"))):
                    V2.do(f"{name}{h}", tt(out=DFB(h)[x].rearrange("p (a b) -> p a b", a=TT), in0=diagonal(M),
                                           in1=tab(mask).unsqueeze(1).to_broadcast([P, TT, P]), op=ALU.mult))
                if h:
                    head_out(h - 1)
            head_out(7)
            for t in range(TT):
                y = Y[:, t, :]
                own(f"sr{t - 1}" if t else "ya7")
                V2.do(f"sk{t}", tt(out=heads_(ogf, 8), in0=heads_(XS[:, t, :], 8), in1=over(drow[:, :], 8, HD), op=ALU.mult))
                own(f"sk{t}")
                V2.do(f"sa{t}", tt(out=y, in0=y, in1=ogf, op=ALU.add))
                own(f"sa{t}")
                V2.do(f"sz{t}", tt(out=y, in0=y, in1=Z[:, t, :], op=ALU.mult))
                own(f"sz{t}")
                V2.do(f"sq{t}", tt(out=ogf, in0=y, in1=y, op=ALU.mult))
                own(f"sq{t}")
                V2.do(f"sr{t}", nc.vector.tensor_reduce(ys[:, 0, t, :], heads_(ogf, 2), AX.X, ALU.add))
            own("sr3")
            V2.do("sv", ts(ys[:, 1, :, :], ys[:, 0, :, :], 1.0 / 256, EPS_2, ALU.mult, ALU.add))
            own("sv")
            V2.do("si", nc.vector.reciprocal(ys[:, 0, :, :], ys[:, 1, :, :]))
            dve.wait_ge(s_twoa, A2.of("ss"))
            for t in range(TT):
                V2.do(f"sn{t}", tt(out=heads_(Y[:, t, :], 2), in0=heads_(Y[:, t, :], 2), in1=over(ys[:, 2, t, :], 2, 256), op=ALU.mult))

            def gated_residual(x, ps, g, at, alpha=ALPHA_2):
                dve.wait_ge(dve_out, at + (st("out2", "dve") - 1))
                tt(out=ogf, in0=ps, in1=g, op=ALU.mult).then_inc(res_steps, 1)
                dve.wait_ge(res_steps, at)
                stt(out=x, in0=x, scalar=alpha, in1=ogf, op0=ALU.mult, op1=ALU.add).then_inc(dve_out, 1)

            q0 = st("out2", "quarters")

            def mixed(h, t):
                n = 4 * h + t
                dve.wait_ge(quarters, q0 + n + 1)
                gated_residual(X[:, t, h * 512:(h + 1) * 512], G[t][:, :], gbc[:, h * 512:(h + 1) * 512], n + 1)

            for t in range(TT):
                mixed(0, t)
            layer_norm("out2", EPS_2, residual_of=lambda t: mixed(1, t), eps_then=EPS_2)

            base = st("x5", "tr")
            for b in range(KT):
                dve.wait_ge(x_val, b + 1)
                dve.wait_ge(xt_hi, 48 + b + 1)
                tt(out=XTl[:, b, :], in0=act_buf[b % 2], in1=XTh[:, b, :], op=ALU.subtract).then_inc(tr_out, 1)

            a0, q0, h0, u = st("ffn2", "act"), st("ffn2", "quarters"), st("ffn2", "hidden"), 0

            def taps(i, pair, xs):
                for x in xs:
                    for e in range(2):
                        m = 2 * pair + e
                        if x == 0:
                            dve.wait_ge(act_out, i * 4 + (a0 + u + m + 1))
                        else:
                            dve.wait_ge(conv_steps, i * 32 + (8 * u + 16 * pair + 2 * x + e - 1))
                        tap = (0, 1, 2, 3, 5, 6, 7, 8)[x]
                        r, c = tap // 3, tap % 3
                        w = cols2[:, bass.ds(i * 40 + (C2["ffn"] + 10 * (u + m) + tap), 1)] if not isinstance(i, int) else \
                            cols2[:, C2["ffn"] + 10 * (u + m) + tap:C2["ffn"] + 10 * (u + m) + tap + 1]
                        y = SUMS[m].rearrange("p (r c) -> p r c", c=GRID_W)
                        stt(out=y, in0=PADS[m][:, r:r + 8, c:c + GRID_W], scalar=w, in1=y, op0=ALU.mult, op1=ALU.add).then_inc(conv_steps, 1)

            def product(i, e):
                dve.wait_ge(gelu_done, i * 2 + (u // 2 + e + 1))
                m = 2 * (e % 2)
                tt(out=SUMS[m], in0=SUMS[m], in1=SUMS[m + 1], op=ALU.mult).then_inc(hid_steps, 1)

            def low_hidden(i, e):
                dve.wait_ge(hid_hi, i * 2 + (h0 + u // 2 + e + 1))
                tt(out=hidden_tile(Hl, i, e), in0=SUMS[2 * (e % 2)].unsqueeze(1), in1=hidden_tile(Hh, i, e), op=ALU.subtract).then_inc(hidden, 1)

            def four_tiles(i, first=False):
                for pair in range(2):
                    taps(i, pair, range(0, 2))
                    if not (first and pair == 0):
                        product(i, pair - 1)
                    taps(i, pair, range(2, 5))
                    if not (first and pair == 0):
                        low_hidden(i, pair - 1)
                    taps(i, pair, range(5, 8))

            def fed(half, t, alpha, at):
                c = slice(half * 512, (half + 1) * 512)
                gated_residual(X[:, t, c], BANKS[half][t][:, :], gbc[:, 1024 + half * 512:1536 + half * 512], at, alpha)

            q = q0
            for part, (up, down) in enumerate(PARTS["ffn2"]):
                four_tiles(0, True)
                with dve.Fori(1, up // 4) as i:
                    four_tiles(i)
                product(up // 4, -1)
                low_hidden(up // 4, -1)
                q, u = q + up + down, u + up
                if part == 0:
                    for half in range(2):
                        dve.wait_ge(quarters, q - 1 + half)
                        for t in range(TT):
                            fed(half, t, ALPHA_2, 8 + 4 * half + t + 1)

            def last_tile(t):
                down_wait("ffn2", t)
                for half in range(2):
                    fed(half, t, 1.0, 16 + 2 * t + half + 1)

            layer_norm("ffn2", EPS_2, residual_of=last_tile)

        @block.sync
        def _(sp):
            a, b = where["ident"]
            sp.dma_start(table[:, a:b], A["table"][:, a:b]).then_inc(ident_in, 16)
            for t in range(TT):
                sp.dma_start(X[:, t, :], A["x"][0, t * P:(t + 1) * P, :]).then_inc(x_in[t], 16)
            def load(s):
                sp.dma_start(ring[:, s % 2, :], A["slabs"][s]).then_inc(slab_in[s % 2], 16)

            def slabs(first, last, q0):
                with sp.Fori(0, (last - first) // 2) as i:
                    for e in range(2):
                        s = first + e
                        sp.wait_ge(quarters, i * 8 + (q0 + 4 * e - 4))
                        sp.wait_ge(x_in[0], 16)
                        sp.dma_start(ring[:, s % 2, :], A["slabs"][bass.ds(i * 2 + s, 1), :, :].rearrange("o p c -> p (o c)")).then_inc(slab_in[s % 2], 16)
                if (last - first) % 2:
                    sp.wait_ge(quarters, q0 + 4 * (last - first) - 8)
                    load(last - 1)

            def raw_chunks(first, last):
                with sp.Fori(0, (last - first) // 2) as i:
                    for s in range(2):
                        sp.wait_ge(w_lo, i * 4 + (2 * first + 2 * s - 2))
                        sp.wait_ge(x_in[0], 16)
                        sp.dma_start(ring[:, 1, s * 2048:(s + 1) * 2048], A["chunks"][bass.ds(i * 2 + (first + s), 1), :, :].rearrange("o p c -> p (o c)")).then_inc(raw_in[s], 16)

            def raw_chunk(c):
                sp.dma_start(ring[:, 1, (c % 2) * 2048:(c % 2 + 1) * 2048], A["chunks"][c]).then_inc(raw_in[c % 2], 16)

            def after_mlp(stage, s):
                for e in range(2):
                    if (s + e) % 2:
                        sp.wait_ge(w_lo, SPLIT0[stage] + 64)
                    else:
                        sp.wait_ge(quarters, st(stage, "quarters") + 48)
                    load(s + e)

            def tile(ap):
                return ap.rearrange("p o n -> p (o n)")

            def feed(name, n_iter, n, loads, lead=None):
                def unit(i, j):
                    u0 = st(name, "units")
                    aps = [(d, s) for d, s in loads(i, j)]
                    for d, s in aps:
                        sp.dma_start(d, s).then_inc(qk_in[j % 2], 16)
                for j in range(2):
                    if st(name, "units"):
                        sp.wait_ge(sc_ready, 4 * (st(name, "units") + j - 1))
                    unit(0, j)
                for j in range(2, n):
                    sp.wait_ge(sc_ready, 4 * (st(name, "units") + j - 1))
                    unit(0, j)
                with sp.Fori(1, n_iter) as i:
                    for j in range(n):
                        sp.wait_ge(sc_ready, i * (4 * n) + 4 * (st(name, "units") + j - 1))
                        unit(i, j)

            raw_chunk(0)
            raw_chunk(1)
            sp.dma_start(table[:, 0:a], A["table"][:, 0:a]).then_inc(s_const, 16)
            sp.dma_start(table[:, b:], A["table"][:, b:]).then_inc(s_const, 16)
            sp.dma_start(cols[:, :], A["cols"]).then_inc(s_const, 16)
            raw_chunks(2, SPLIT0["out0"] // 2)
            sp.wait_ge(act_out, st("proj0", "act") + 24)
            sp.wait_ge(quarters, 24)
            for j in range(2):
                for g in range(2):
                    src = KTT[g * HD:(g + 1) * HD, 4 + j, :]
                    sp.dma_start(XT[0:HD, 2 * j + g, :], src).then_inc(cmp_in, 16)
                    sp.dma_start(XT[HD:P, 2 * j + g, 0:S - 1], src[:, 1:S]).then_inc(cmp_in, 16)
            sp.wait_ge(quarters, st("cmp", "quarters"))
            load(0)
            sp.wait_ge(w_lo, SPLIT0["out0"])
            load(1)
            sp.wait_ge(quarters, st("out0", "quarters"))
            c = SPLIT0["out0"] // 2
            raw_chunk(c)
            raw_chunk(c + 1)
            sp.wait_ge(act_out, st("proj0", "act") + 24)
            sp.wait_ge(rope_dve, 2 * len(ROPED0))
            feed("diff", 4, 2, lambda i, c: [
                (qb[0:HD, c, :], tile(QT[c * HD:(c + 1) * HD, bass.ds(i, 1), :])),
                (kb[0:HD, c, :], tile(KTT[c * HD:(c + 1) * HD, bass.ds(i, 1), :]))])
            feed("nsa", 2, 8, lambda r, j: [
                (qb[0:HD, j % 2, :], tile(QT[((j // 2) % 2) * HD:((j // 2) % 2) * HD + HD, bass.ds(r + (4 + 2 * (j // 4)), 1), :]))])
            raw_chunks(c + 2, SPLIT0["out1"] // 2 + 2)
            sp.wait_ge(quarters, st("proj1", "quarters") + 28)
            sp.wait_ge(act_out, st("proj1", "act") + 17)
            sp.wait_ge(crow_in, 16)
            feed("fox", 8, 2, lambda i, e: [
                (qb[0:HD, e, :], tile(QT[e * HD:(e + 1) * HD, bass.ds(i, 1), :])),
                (kb[0:HD, e, :], tile(KTT[e * HD:(e + 1) * HD, bass.ds(i, 1), :])),
                (qb[HD + 1:HD + 2, e, :], A["crow"][bass.ds(i * 2 + e, 1), 1, :]),
                (kb[HD:HD + 1, e, :], A["crow"][bass.ds(i * 2 + e, 1), 0, :])])
            raw_chunks(SPLIT0["out1"] // 2 + 2, SPLIT0["ffn2"] // 2)
            after_mlp("mlp1", SLAB["w_in"][0])
            slabs(SLAB["w_in"][0] + 2, SLAB["out2"][0] + 2, st("w_in", "quarters") + 8)
            sp.wait_ge(quarters, st("ffn2", "quarters"))
            c, n = SPLIT0["ffn2"] // 2, n_quarters("ffn2") // 2
            raw_chunk(c)
            raw_chunk(c + 1)
            raw_chunks(c + 2, c + n - n % 2)
            if n % 2:
                sp.wait_ge(w_lo, 2 * (c + n - 1) - 2)
                raw_chunk(c + n - 1)
            sp.wait_ge(ln_dve, st.total["ln"])
            sp.dma_start(out.rearrange("o (t p) d -> p (o t) d", p=P), X[:, :, :]).then_inc(s_out, 16)
            sp.wait_ge(s_out, 16)

        @block.gpsimd
        def _(gp):
            gp.dma_start(w2[:, :, :, 0:HD], A["nsa_cmp_w2"].rearrange("o j (h p) d -> p (o j) h d", p=P)).then_inc(s_small_in, 16)
            gp.dma_start(w2[:, :, :, HD:P], A["nsa_cmp_w2"].rearrange("o j (h p) d -> p (o j) h d", p=P)).then_inc(s_small_in, 16)
            gp.dma_start(lamrow[:, :, :, :], A["diff_lambda"].rearrange("o (a b) d -> o (a b d)", a=2).partition_broadcast(P)
                         .rearrange("p o (a b d) -> p (o a) b d", a=2, b=2)).then_inc(s_small_in, 16)
            gp.dma_start(subln[:, :], A["diff_subln"].partition_broadcast(P).rearrange("p o d -> p (o d)")).then_inc(s_small_in, 16)
            gp.dma_start(cols2[:, :], A["cols2"]).then_inc(s_small_in, 16)

            def gain_bias(n, gain, bias):
                if n:
                    gp.wait_ge(ln_dve, LN_PLACE[NORMS[n - 1], "bi", TT - 1])
                gp.dma_start(rows[:, 0, :], gain.partition_broadcast(P)).then_inc(gb_in, 16)
                gp.dma_start(rows[:, 1, :], bias.partition_broadcast(P)).then_inc(gb_in, 16)

            gain_bias(0, A["ln_gain"][0, 0, :], A["ln_bias"][0, 0, :])

            gp.wait_ge(s_const, CONSTS)
            for r, (g, *_) in enumerate(ROPED0):
                gp.wait_ge(act_out, st("proj0", "act") + g + 1)
                if r >= 2:
                    gp.wait_ge(rope_dve, 2 * (r - 2) + 2)
                nc.gpsimd.tensor_tensor(out=wide[:, 26 + r % 2, :], in0=wide[:, 24 + r % 2, :], in1=tab("cos"),
                                        op=ALU.mult).then_inc(rope_cos, 1)

            gp.wait_ge(rope_dve, 2 * len(ROPED0))
            for kind in range(2):
                for g in range(2):
                    gp.dma_start(KSW[:, kind, g, :], KTT[g * HD:(g + 1) * HD, 6 + kind, :]).then_inc(ksw_in, 16)

            gp.wait_ge(gb_in, 32)
            gain_bias(1, A["ln_gain"][0, 1, :], A["ln_bias"][0, 1, :])

            def ada_loads(parts):
                def job(part, j):
                    for q in range(4):
                        if part or q > 1 or not isinstance(j, int) or j:
                            gp.wait_ge(ada_steps, j * 8 + (32 * part + 2 * q - 2))
                        src = A["ada"][part if isinstance(j, int) and j == 3 else j + 3 * part if isinstance(j, int) else bass.ds(j + 3 * part, 1), :, q * 1024:(q + 1) * 1024]
                        if len(src.shape) == 3:
                            src = src.rearrange("o p c -> p (o c)")
                        gp.dma_start(ADW(q % 2), src).then_inc(ada_in[q % 2], 16)

                for part in parts:
                    job(part, 0)
                    with gp.Fori(1, 3) as j:
                        job(part, j)
                    job(part, 3)

            gp.wait_ge(o_used, 24)
            ada_loads((0, 1))
            gp.wait_ge(s_small, SMALL["fox"])
            gp.wait_ge(s_small_in, SMALL_INPUTS)
            gp.dma_start(A["crow"], crow[:, 1:3, :]).then_inc(crow_in, 16)
            gp.wait_ge(crow_in, 16)
            gp.wait_ge(quarters, st("proj1", "quarters") + 28)
            for e in range(2):
                gp.dma_start(qb[HD:HD + 1, e, :], A["ones"][0:1, :]).then_inc(crow_in, 16)
                gp.dma_start(kb[HD + 1:HD + 2, e, :], A["ones"][1:2, :]).then_inc(crow_in, 16)
            gain_bias(2, A["ln_gain"][1, 0, :], A["ln_bias"][1, 0, :])
            ada_loads((2, 3))
            gain_bias(3, A["ln_gain"][1, 1, :], A["ln_bias"][1, 1, :])
            gpsimd_second(gp, gain_bias)

        PTS = [XT[:, 0:4, :], XT[:, 4:8, :]]
        TRS = [TR[0], TR[1], G[2], G[3]]

        def units(engine, n_iter, n, slot):
            for j in range(n):
                slot(0, j, (0, j + 1) if j + 1 < n else (1, 0), (0, j - 1) if j else None)
            if n_iter > 2:
                with engine.Fori(1, n_iter - 1) as i:
                    for j in range(n):
                        slot(i, j, (i, j + 1) if j + 1 < n else (i + 1, 0), (i, j - 1))
            i = n_iter - 1
            for j in range(n):
                slot(i, j, (i, j + 1) if j + 1 < n else None, (i, j - 1) if j else (i - 1, n - 1))

        def pe_attend(pe, name, n_iter, n, depth, q_of, k_of, v_of, hd, per_slot):
            u0 = st(name, "units")
            in0 = LOADS[name]

            def number(i, j, times):
                return i * (times * n) + times * (u0 + j)

            def first(i, j, before):
                return isinstance(i, int) and i * n + u0 + j < before

            def score(unit, t):
                if unit is None:
                    return
                i, j = unit
                if t == 0:
                    pe.wait_ge(qk_in[j % 2], in0 + i * (per_slot * 16 * (n // 2)) + per_slot * 16 * (j // 2 + 1))
                if not first(i, j, 1) or t >= 2:
                    pe.wait_ge(sc_used, number(i, j, 4) + t - 1)
                nc.tensor.matmul(G[t % 2][:, 0:(t + 1) * P], lhsT=q_of(i, j)[0:depth, t * P:(t + 1) * P],
                                 rhs=k_of(i, j)[0:depth, 0:(t + 1) * P], start=True, stop=True).then_inc(sc_ready, 1)

            def transposed(i, j, t):
                pe.wait_ge(pr_ready, number(i, j, 4) + t + 1)
                if not first(i, j, 1):
                    pe.wait_ge(pt_dve if t < 2 else pt_act, number(i, j, 2) + t % 2 - 1)
                for b in range(t + 1):
                    mm = nc.tensor.transpose(TRS[t][:, b * P:(b + 1) * P], SC[:, j % 2, t, b * P:(b + 1) * P], ident)
                mm.then_inc(pt_ready, 1)

            def attended(unit):
                if unit is None:
                    return
                i, j = unit
                if not first(i, j, 2):
                    pe.wait_ge(o_used, number(i, j, 1) - 1)
                for t in range(TT):
                    pe.wait_ge(pt_dve if t < 2 else pt_act, number(i, j, 2) + t % 2 + 1)
                    for b in range(t + 1):
                        mm = nc.tensor.matmul(OB[j % 2][:, t * hd:(t + 1) * hd], lhsT=PTS[j % 2][:, t, b * P:(b + 1) * P],
                                              rhs=v_of(i, j, b), start=(b == 0), stop=(b == t))
                mm.then_inc(pv_ready, 1)

            def slot(i, j, after, before):
                score(after, 0)
                score(after, 1)
                transposed(i, j, 0)
                transposed(i, j, 1)
                score(after, 2)
                score(after, 3)
                transposed(i, j, 2)
                transposed(i, j, 3)
                attended(before)

            for t in range(TT):
                score((0, 0), t)
            units(pe, n_iter, n, slot)
            attended((n_iter - 1, n - 1))

        def act_attend(act, name, n_iter, n):
            u0 = st(name, "units")

            def number(i, j, times):
                return i * (times * n) + times * (u0 + j)

            def exp(unit, t):
                if unit is None:
                    return
                i, j = unit
                e = j % 2
                act.wait_ge(sc_used, number(i, j, 4) + t + 1)
                if t == 0 and not (isinstance(i, int) and i * n + u0 + j < 2):
                    act.wait_ge(rec_done, number(i, j, 1) - 1)
                nc.scalar.activation(SC[:, e, t, 0:(t + 1) * P], SC[:, e, t, 0:(t + 1) * P], ACT.Exp,
                                     scale=-1.0, bias=mn[:, e, t:t + 1], accum_out=sm[:, e, t:t + 1]).then_inc(pr_ready, 1)

            def copy(i, j, t):
                act.wait_ge(pt_ready, number(i, j, 4) + t + 1)
                if t == 2 and not (isinstance(i, int) and i * n + u0 + j < 2):
                    act.wait_ge(pv_ready, number(i, j, 1) - 1)
                nc.scalar.activation(PTS[j % 2][:, t, 0:(t + 1) * P], TRS[t][:, 0:(t + 1) * P], ACT.Copy).then_inc(pt_act, 1)

            def slot(i, j, after, before):
                exp(after, 0)
                exp(after, 1)
                exp(after, 2)
                copy(i, j, 2)
                exp(after, 3)
                copy(i, j, 3)

            for t in range(TT):
                exp((0, 0), t)
            units(act, n_iter, n, slot)

        def dve_attend(dve, name, n_iter, n, hd, finish):
            u0 = st(name, "units")
            step0, per = STEP0[name], STEPS[name]

            def number(i, j, times):
                return i * (times * n) + times * (u0 + j)

            def first(i, j):
                return isinstance(i, int) and i * n + u0 + j < 2

            def least(unit, t):
                if unit is None:
                    return
                i, j = unit
                e = j % 2
                if t == 0 and not first(i, j):
                    dve.wait_ge(pt_ready, number(i, j, 4) - 4)
                dve.wait_ge(sc_ready, number(i, j, 4) + t + 1)
                dve.sem_inc(sc_seen, 1)
                a, b = where["causal"]
                nc.vector.tensor_tensor_reduce(
                    out=SC[:, e, t, 0:(t + 1) * P], in0=G[t % 2][:, 0:(t + 1) * P], in1=table[:, b - (t + 1) * P:b],
                    scale=1.0, scalar=3.0e38, op0=ALU.add, op1=ALU.min, accum_out=mn[:, e, t:t + 1]).then_inc(sc_used, 1)

            def copy(i, j, t):
                if t == 0 and not first(i, j):
                    dve.wait_ge(pv_ready, number(i, j, 1) - 1)
                dve.wait_ge(pt_ready, number(i, j, 4) + t + 1)
                nc.vector.tensor_copy(PTS[j % 2][:, t, 0:(t + 1) * P], TRS[t][:, 0:(t + 1) * P]).then_inc(pt_dve, 1)

            def invert(i, j):
                dve.wait_ge(pr_ready, number(i, j, 4) + 4)
                if not first(i, j):
                    dve.wait_ge(o_used, number(i, j, 1) - 1)
                nc.vector.reciprocal(rs[:, j % 2, :], sm[:, j % 2, :]).then_inc(rec_done, 1)

            def output(unit):
                if unit is None:
                    return
                i, j = unit
                dve.wait_ge(pv_ready, number(i, j, 1) + 1)
                dve.wait_ge(rec_done, number(i, j, 1) + 1)
                finish(i, j, i * per[n] + (step0 + (per[j] if j >= 0 else per[n - 1] - per[n])))

            def slot(i, j, after, before):
                least(after, 0)
                least(after, 1)
                copy(i, j, 0)
                copy(i, j, 1)
                least(after, 2)
                least(after, 3)
                invert(i, j)
                output(before)

            for t in range(TT):
                least((0, 0), t)
            units(dve, n_iter, n, slot)
            output((n_iter - 1, n - 1))

        @block.tensor
        def _(pe):
            def slab_wait(s, pairs=0):
                pe.wait_ge(slab_in[s % 2], pairs * 16 + 16 * (s // 2 + 1))

            def stage_start(stage):
                a = st.before[stage].get("act", 0)
                v = st.before[stage].get("dve", 0)
                if a:
                    pe.wait_ge(act_out, a)
                if v:
                    pe.wait_ge(dve_out, v)

            def transposes(stage, src, ready):
                base = st(stage, "tr")
                for t in range(TT):
                    ready(t)
                    for h in range(2):
                        n = base + 2 * t + h
                        if n >= 2:
                            pe.wait_ge(tr_out, n - 1)
                        for b in range(4):
                            c = (4 * h + b) * P
                            mm = nc.tensor.transpose(TR[h][:, b * P:(b + 1) * P], src[:, t, c:c + P], ident)
                        mm.then_inc(tr_ready, 1)

            def token_groups(stage, s, bank0, half, pos):
                for t in range(TT):
                    if bank0 + t >= 4:
                        pe.wait_ge(dve_out, st(stage, "dve") + bank0 + t - 3)
                    for k in range(KT):
                        mm = nc.tensor.matmul(G[t][:, :], lhsT=XT[:, k, t * P:(t + 1) * P], rhs=slab(s)[:, k, :],
                                              start=(k == 0), stop=(k == KT - 1))
                    mm.then_inc(quarters, 1)

            def feature_tile(stage, n, out, rows_=P):
                pe.wait_ge(w_lo, SPLIT0[stage] + n + 1)
                w = [x[:, n % 4, :].rearrange("p (k c) -> p k c", k=KT)[:, :, 0:rows_] for x in (Wh, Wl)]
                return split_products(out, [(w[0][:, k, :], w[1][:, k, :], XTh[:, k, :], XTl[:, k, :]) for k in range(KT)])

            def token_slab(stage, n0, banks, ready, width=512, between=None):
                for p in range(4):
                    pe.wait_ge(w_lo, SPLIT0[stage] + n0 + p + 1)
                    w = [x[:, (n0 + p) % 4, :].rearrange("p (k c) -> p k c", k=2) for x in (Wh, Wl)]
                    pairs = [(t, k) for k in range(2) for t in range(TT)] if p < 3 else [(t, k) for t in range(TT) for k in range(2)]
                    for t, k in pairs:
                        if p == 0 and k == 0:
                            ready(t)
                        T_ = slice(t * P, (t + 1) * P)
                        for x, (a, b) in enumerate(((XTh, w[0]), (XTh, w[1]), (XTl, w[0]))):
                            mm = nc.tensor.matmul(banks[t][:, 0:width], lhsT=a[:, 2 * p + k, T_], rhs=b[:, k, 0:width],
                                                  start=(p == 0 and k == 0 and x == 0), stop=(p == 3 and k == 1 and x == 2))
                        if p == 3 and k == 1 and t < TT - 1:
                            mm.then_inc(tile_done, 1)
                    mm.then_inc(quarters, 1)
                    if p == 0 and between is not None:
                        between()

            def token_slab_by_tile(stage, n0, banks):
                for t in range(TT):
                    T_ = slice(t * P, (t + 1) * P)
                    for p in range(4):
                        if t == 0:
                            pe.wait_ge(w_lo, SPLIT0[stage] + n0 + p + 1)
                        w = [x[:, (n0 + p) % 4, :].rearrange("p (k c) -> p k c", k=2) for x in (Wh, Wl)]
                        for k in range(2):
                            for x, (a, b) in enumerate(((XTh, w[0]), (XTh, w[1]), (XTl, w[0]))):
                                mm = nc.tensor.matmul(banks[t][:, :], lhsT=a[:, 2 * p + k, T_], rhs=b[:, k, :],
                                                      start=(p == 0 and k == 0 and x == 0), stop=(p == 3 and k == 1 and x == 2))
                    mm.then_inc(tile_done if t < TT - 1 else quarters, 1 if t < TT - 1 else 4)

            def split_out(stage, tr_stage):
                stage_start(stage)
                pe.wait_ge(tr_out, st(tr_stage, "tr") + 8)
                token_slab(stage, 0, BANKS[1], lambda t: None)
                token_slab_by_tile(stage, 4, BANKS[0])

            def out_products(stage, tr_stage):
                stage_start(stage)
                pe.wait_ge(tr_out, st(tr_stage, "tr") + 8)
                s = SLAB[stage][0]
                for h in range(2):
                    slab_wait(s + h)
                    token_groups(stage, s + h, 4 * h, h, 0)

            def ada_sums(part, j):
                pe.wait_ge(ada_steps, j * 8 + (32 * part + 8))
                for q in range(4):
                    mm = nc.tensor.matmul(OB[0][:, q:q + 1], lhsT=ogf[:, q * P:(q + 1) * P], rhs=ones[:, 0:1], start=True, stop=True)
                mm.then_inc(ada_cols, 1)

            def mlp_products(stage, tr_stage, ada=None):
                stage_start(stage)
                pe.wait_ge(tr_out, st(tr_stage, "tr") + 8)
                Q, a, v, h = SPLIT0[stage], st(stage, "act"), st(stage, "dve"), st(stage, "hidden")
                per = 2 if stage == "ffn2" else 1
                for part, (up, down) in enumerate(PARTS[stage]):
                    if part:
                        pe.wait_ge(dve_out, v + 4)
                    with pe.Fori(0, up // 4) as i:
                        for m in range(4):
                            pe.wait_ge(w_lo, i * 4 + (Q + m + 1))
                            pe.wait_ge(act_out, i * 4 + (a + m - 3))
                            w = [x[:, m, :].rearrange("p (k c) -> p k c", k=KT) for x in (Wh, Wl)]
                            split_products(G[m][:, :], [(w[0][:, k, :], w[1][:, k, :], XTh[:, k, :], XTl[:, k, :])
                                                        for k in range(KT)]).then_inc(quarters, 1)
                        if ada is not None:
                            ada_sums(ada + part, i)
                    Q, a = Q + up, a + up
                    if ada is not None:
                        pe.wait_ge(ada_moved, 4 * (ada + part) + 4)
                    if part:
                        pe.wait_ge(dve_out, v + 8)
                    for j in range(down - 2 * part):
                        half = 1 - j % 2 if j < down - 2 else j % 2
                        pe.wait_ge(w_lo, Q + j + 1)
                        if j == 1:
                            pe.wait_ge(act_out, a)
                        w = [x[:, (Q + j) % 4, :].rearrange("p (k c) -> p k c", k=2) for x in (Wh, Wl)]
                        for k in range(2):
                            n = 2 * (j // 2) + k
                            pe.wait_ge(hidden, h + n + 1)
                            for t in range(TT):
                                T_ = slice(t * P, (t + 1) * P)
                                for x, (lh, wx) in enumerate(((Hh, w[0]), (Hh, w[1]), (Hl, w[0]))):
                                    mm = nc.tensor.matmul(BANKS[half][t][:, :], lhsT=lh[:, n, T_], rhs=wx[:, k, :],
                                                          start=(n == 0 and x == 0), stop=(n == down - 1 and x == 2))
                        mm.then_inc(quarters, 1)
                    if part:
                        pe.wait_ge(w_lo, Q + down)
                        pe.wait_ge(hidden, h + down)
                        for t in range(TT):
                            T_ = slice(t * P, (t + 1) * P)
                            for half in range(2):
                                w = [x[:, (Q + down - 2 + half) % 4, :].rearrange("p (k c) -> p k c", k=2) for x in (Wh, Wl)]
                                for k in range(2):
                                    n = down - 2 + k
                                    for x, (lh, wx) in enumerate(((Hh, w[0]), (Hh, w[1]), (Hl, w[0]))):
                                        mm = nc.tensor.matmul(BANKS[half][t][:, :], lhsT=lh[:, n, T_], rhs=wx[:, k, :],
                                                              start=False, stop=(k == 1 and x == 2))
                            mm.then_inc(tile_done if t < TT - 1 else quarters, 1 if t < TT - 1 else 2)
                    Q, h = Q + down, h + up // per

            pe.wait_ge(ident_in, 16)
            transposes("x0", X, lambda t: pe.wait_ge(x_in[t], 16))

            pe.wait_ge(tr_out, 8)
            roped = {g: r for r, (g, *_) in enumerate(ROPED0)}

            def rope_swap(g):
                r = roped[g]
                if r == 0:
                    pe.wait_ge(s_const, CONSTS)
                pe.wait_ge(act_out, g + 1)
                if r >= 2:
                    pe.wait_ge(rope_dve, 2 * (r - 2) + 1)
                else:
                    pe.wait_ge(tr_out, 8)
                nc.tensor.matmul(TR[r % 2][:, :], lhsT=tab("swap"), rhs=wide[:, 24 + r % 2, :], start=True, stop=True).then_inc(rope_swapped, 1)

            def bank_ready(g):
                if g >= 4:
                    pe.wait_ge(act_out, g - 3)

            for g in range(24):
                def swap_before():
                    if g - 1 in roped:
                        rope_swap(g - 1)

                if GROUPS0[g][0] == "F":
                    bank_ready(g)
                    feature_tile("proj0", g, G[g % 4][:, :]).then_inc(quarters, 1)
                    swap_before()
                elif g % 4 == 0:
                    token_slab("proj0", g, G, lambda t: bank_ready(g + t), GROUPS0[g][1][1], swap_before)

            a0 = st("cmp", "act")
            pe.wait_ge(act_out, 24)
            for j in range(2):
                pe.wait_ge(s_small, SMALL["windows"] + j + 1)
                slab_wait(SLAB["cmp"][0] + j)
                for h in range(2):
                    for m in range(16):
                        mm = nc.tensor.matmul(G[2 * j + h][:, 0:62], lhsT=ring[:, j, m * 256 + h * P:m * 256 + (h + 1) * P],
                                              rhs=WIN(j)[:, m, :], start=(m == 0), stop=(m == 15))
                    mm.then_inc(quarters, 2)
            pe.wait_ge(s_small, SMALL["gelu"])
            pe.wait_ge(s_small_in, SMALL_INPUTS)
            pe.wait_ge(rope_dve, 2 * len(ROPED0))
            for h in range(2):
                mm = nc.tensor.matmul(TR[0][:, 0:62], lhsT=w2[:, 0, h, :], rhs=hc2[:, h, :], start=(h == 0), stop=(h == 1))
            mm.then_inc(s_smallp, 1)
            for g in range(2):
                for h in range(2):
                    mm = nc.tensor.matmul(TR[1][0:N_CMP, g * HD:(g + 1) * HD], lhsT=hc2[:, 2 + h, g * N_CMP:(g + 1) * N_CMP],
                                          rhs=w2[:, 1, h, 0:HD], start=(h == 0), stop=(h == 1))
            mm.then_inc(s_smallp, 1)
            pe.wait_ge(s_small, SMALL["kraw"])
            nc.tensor.matmul(TR[0][:, 0:62], lhsT=tab("swap"), rhs=kcc[:, 0, :], start=True, stop=True).then_inc(s_smallp, 1)
            pe.wait_ge(s_small, SMALL["krope"])
            for h in range(8):
                r = (h % 2) * HD
                for t in range(TT):
                    c = (h // 2) * P + t * 32
                    mm = nc.tensor.matmul(G[h % 2][:, c:c + N_CMP], lhsT=QT[r:r + HD, 4 + h // 2, t * P:(t + 1) * P],
                                          rhs=kcc[r:r + HD, 1, (h // 4) * N_CMP:(h // 4 + 1) * N_CMP], start=True, stop=True)
                if h >= 6:
                    mm.then_inc(s_smallp, 1)
            for h in range(8):
                pe.wait_ge(s_small, SMALL["pcmp"])
                if h >= 2:
                    pe.wait_ge(s_smalla, SMALLA["ptc"] + h - 1)
                for t in range(TT):
                    mm = nc.tensor.transpose(TR[h % 2][0:N_CMP, t * P:(t + 1) * P], PC[:, h, t, 0:N_CMP], ident)
                mm.then_inc(s_smallp, 1)
                pe.wait_ge(s_smalla, SMALLA["ptc"] + h + 1)
                if h >= 2:
                    pe.wait_ge(s_small, SMALL["pcmp"] + h - 1)
                for t in range(TT):
                    mm = nc.tensor.matmul(OB[h % 2][:, t * HD:(t + 1) * HD], lhsT=PT[0:N_CMP, h % 2, t * P:(t + 1) * P],
                                          rhs=vcc[:, h // 4, :], start=True, stop=True)
                mm.then_inc(s_smallp, 1)

            pe.wait_ge(s_small, SMALL["pcmp"] + 8)
            pe_attend(pe, "diff", 4, 2, HD, lambda i, j: qb[:, j % 2, :], lambda i, j: kb[:, j % 2, :],
                      lambda i, j, b: V[:, b, bass.ds(i * P + (j // 2) * P, P)] if not isinstance(i, int) else V[:, b, i * P:(i + 1) * P], P, 2)
            pe.wait_ge(ksw_in, 64)
            pe_attend(pe, "nsa", 2, 8, HD, lambda i, j: qb[:, j % 2, :], lambda i, j: KSW[:, j % 2, j // 4, :],
                      lambda i, j, b: V[:, b, 512 + (j % 2) * P:512 + (j % 2) * P + P], P, 1)

            transposes("mixed0", O, lambda t: pe.wait_ge(s_small, SMALL["rms"] + 2 * (t + 1)))
            split_out("out0", "mixed0")
            transposes("x1", X, lambda t: pe.wait_ge(ln_dve, LN_PLACE["out0", "bi", t]))
            mlp_products("mlp0", "x1", ada=0)
            pe.wait_ge(dve_out, st("mlp0", "dve") + 12)
            transposes("x2", X, lambda t: pe.wait_ge(ln_dve, LN_PLACE["mlp0", "bi", t]))

            stage_start("proj1")
            pe.wait_ge(tr_out, st("x2", "tr") + 8)
            a0 = st("proj1", "act")
            feature_tile("proj1", 0, G[0][0:16, :], 16).then_inc(quarters, FORGET)
            for g in range(16):
                if g >= 3:
                    pe.wait_ge(act_out, a0 + g - 2)
                feature_tile("proj1", FORGET + g, G[(g + 1) % 4][:, :]).then_inc(quarters, 1)
            for g in (16, 20):
                token_slab("proj1", FORGET + g, [G[(t + 1) % 4] for t in range(TT)], lambda t: pe.wait_ge(act_out, a0 + g + t - 2))
            pe.wait_ge(act_out, a0 + 25)
            pe.wait_ge(tr_out, st("x2", "tr") + 8)
            pe.wait_ge(crow_in, 80)
            pe_attend(pe, "fox", 8, 2, HD + 2, lambda i, j: qb[:, j % 2, :], lambda i, j: kb[:, j % 2, :],
                      lambda i, j, b: V[:, b, bass.ds(i * P + (j // 2) * P, P)] if not isinstance(i, int) else V[:, b, i * P:(i + 1) * P], P, 4)
            transposes("mixed1", O, lambda t: pe.wait_ge(o_used, st("fox", "units") + 16))
            split_out("out1", "mixed1")
            transposes("x3", X, lambda t: pe.wait_ge(ln_dve, LN_PLACE["out1", "bi", t]))
            mlp_products("mlp1", "x3", ada=2)
            tensor_second(pe, stage_start, slab_wait, mlp_products, out_products)

        @block.scalar
        def _(act):
            def normalize(stage, src=X, dst=X, then=None):
                def root(t, mark=""):
                    act.wait_ge(ln_dve, LN_PLACE[stage, "rc" + mark, t])
                    nc.scalar.activation(rstd[:, 2, t:t + 1], rstd[:, 1, t:t + 1], ACT.Sqrt).then_inc(ln_std, 1)

                def apply(t, dst, mark=""):
                    act.wait_ge(ln_dve, LN_PLACE[stage, "nm" + mark, t])
                    nc.scalar.activation(dst[:, t, :], src[:, t, :], ACT.Identity, scale=rstd[:, 2, t:t + 1],
                                         bias=rstd[:, 3, t:t + 1]).then_inc(ln_norm, 1)

                for kind, t, mark in LN_SCALAR[stage]:
                    if kind == "root":
                        root(t, mark)
                    else:
                        apply(t, then if mark else dst, mark)

            def first_splits(stage):
                for n in range(3):
                    high_split(act, stage, n, first=True)

            def out_splits(stage):
                first_splits(stage)
                for n in range(3, 8):
                    high_split(act, stage, n)

            def split_copies(stage):
                base = st(stage, "tr")
                for n in range(8):
                    act.wait_ge(tr_ready, base + n + 1)
                    t, h = n // 2, n % 2
                    nc.scalar.activation(XTh[:, 4 * h:4 * h + 4, t * P:(t + 1) * P], TR[h][:, :].rearrange("p (b c) -> p b c", b=4),
                                         ACT.Copy).then_inc(xt_hi, 1)

            def relu(stage):
                n, u = 0, 0
                q, a, h = st(stage, "quarters"), st(stage, "act"), st(stage, "hidden")

                def four(i):
                    for m in range(4):
                        high_split(act, stage, n + m + 3, i)
                        act.wait_ge(quarters, i * 4 + (q + n + m + 1))
                        if h + u + m >= 2 or not (isinstance(i, int) and i == 0):
                            act.wait_ge(hidden, i * 4 + (h + u + m - 1))
                        nc.scalar.activation(act_buf[m % 2], G[m][:, :], ACT.Relu).then_inc(act_out, 1)
                        act.wait_ge(act_out, i * 4 + (a + u + m + 1))
                        nc.scalar.activation(Hh[:, bass.ds(i * 4 + m, 1), :] if not isinstance(i, int) else Hh[:, m:m + 1, :],
                                             act_buf[m % 2].unsqueeze(1), ACT.Square).then_inc(hid_hi, 1)

                for up, down in PARTS[stage]:
                    first = h + u < 2
                    if first:
                        four(0)
                    with act.Fori(1 if first else 0, up // 4) as i:
                        four(i)
                    n, u = n + up, u + up
                    for j in range(down):
                        if n + j + 3 < n_quarters(stage):
                            high_split(act, stage, n + j + 3)
                    n += down

            split_copies("x0")
            first_splits("proj0")
            act.wait_ge(s_const, CONSTS)
            r = 0
            for g in range(24):
                kind, c, (dst, scale) = GROUPS0[g]
                for n in ((g + 3,) if kind == "F" else range(g + 3, g + 7) if g % 4 == 0 else ()):
                    if n < 24:
                        high_split(act, "proj0", n)
                if kind == "F":
                    act.wait_ge(quarters, g + 1)
                else:
                    tile_wait(act, "proj0", g // 4 * 4, 0 if g < 16 else 1, g % 4)
                if dst is None:
                    if r >= 2:
                        act.wait_ge(rope_swapped, r - 1)
                        act.wait_ge(rope_cos, r - 1)
                    dst_ap, r = wide[:, 24 + r % 2, :], r + 1
                else:
                    dst_ap = KTT[:, dst[1], :] if dst[0] == "K" else V[:, dst[1], dst[2]:dst[3]]
                nc.scalar.activation(dst_ap, G[g % 4][:, 0:dst_ap.free_size()], ACT.Copy, scale=scale).then_inc(act_out, 1)
            act.wait_ge(s_small, SMALL["lam"])
            nc.scalar.activation(lam[:, 2:4], lam[:, 0:2], ACT.Exp).then_inc(s_smalla, 1)
            act.wait_ge(act_out, 24)
            nc.scalar.activation(gate[:, :, :], V[:, :, 768:792], ACT.Exp, scale=-1.0).then_inc(s_smalla, 1)
            for n in range(4):
                act.wait_ge(quarters, 24 + 2 * (n + 1))
                nc.scalar.activation(hc[:, n, :], G[n][:, 0:62], ACT.Identity, bias=cols[:, n:n + 1]).then_inc(act_out, 1)
            act.wait_ge(s_small, SMALL["gelu_in"])
            nc.scalar.activation(SC[:, 1, 2, 0:248], SC[:, 1, 1, 0:248], ACT.Tanh, scale=math.sqrt(2 / math.pi)).then_inc(s_smalla, 1)
            act.wait_ge(s_small, SMALL["scmp"])
            nc.scalar.activation(PC[:, :, :, :], PC[:, :, :, :], ACT.Exp, scale=-1.0).then_inc(s_smalla, 1)
            for h in range(8):
                act.wait_ge(s_smallp, 6 + 2 * h)
                if h >= 2:
                    act.wait_ge(s_smallp, 7 + 2 * (h - 2))
                nc.scalar.activation(PT[0:N_CMP, h % 2, :], TR[h % 2][0:N_CMP, :], ACT.Copy).then_inc(s_smalla, 1)
            act.wait_ge(s_smallp, 21)
            act_attend(act, "diff", 4, 2)
            act_attend(act, "nsa", 2, 8)
            act.wait_ge(s_small, SMALL["rms"])
            nc.scalar.activation(rmsq[:, 1, :], rmsq[:, 0, :], ACT.Sqrt).then_inc(s_smalla, 1)
            nc.scalar.activation(csil[:, 0, :, :].rearrange("p a k -> p (a k)"), cols2[:, 0:16], ACT.Exp, scale=-1.0).then_inc(s_smalla, 1)
            split_copies("mixed0")
            out_splits("out0")
            normalize("out0")
            split_copies("x1")
            first_splits("mlp0")
            relu("mlp0")
            normalize("mlp0")
            split_copies("x2")
            first_splits("proj1")
            q0 = st("proj1", "quarters")
            high_split(act, "proj1", 3)
            act.wait_ge(quarters, q0 + FORGET)
            nc.scalar.activation(crow[:, 0, :], G[0][0:16, :], ACT.Identity, bias=cols[0:16, 4:5]).then_inc(act_out, 1)
            for n in range(4, 7):
                high_split(act, "proj1", n)
            for g in range(24):
                for n in ((g + 7,) if g < 16 else range(g + 7, g + 11) if g % 4 == 0 else ()):
                    if n < 28:
                        high_split(act, "proj1", n)
                if g < 16:
                    act.wait_ge(quarters, q0 + FORGET + g + 1)
                else:
                    tile_wait(act, "proj1", FORGET + g // 4 * 4, g // 4 - 4, g % 4)
                if g < 8:
                    o, sc_ = KTT[:, g, :], 1.0
                elif g < 16:
                    o, sc_ = QT[:, g - 8, :], -0.125
                else:
                    o, sc_ = V[:, g % 4, ((g - 16) // 4) * 512:((g - 16) // 4 + 1) * 512], 1.0
                nc.scalar.activation(o, G[(g + 1) % 4][:, :], ACT.Copy, scale=sc_).then_inc(act_out, 1)
                if g == 0:
                    act.wait_ge(s_small, SMALL["fabs"])
                    nc.scalar.activation(crow[:, 2, :], crow[:, 1, :], ACT.Exp, scale=-1.0).then_inc(s_smalla, 1)
                elif g == 1:
                    act.wait_ge(s_smalla, SMALLA["fexp"])
                    nc.scalar.activation(crow[:, 1, :], crow[:, 2, :], ACT.Ln, bias=1.0).then_inc(s_smalla, 1)
            act_attend(act, "fox", 8, 2)
            split_copies("mixed1")
            out_splits("out1")
            normalize("out1")
            split_copies("x3")
            first_splits("mlp1")
            relu("mlp1")
            normalize("mlp1", then=Hn)
            scalar_second(act, first_splits, normalize)

        @block.vector
        def _(dve):
            small = [0]

            def step(ins, wait=True):
                small[0] += 1
                ins.then_inc(s_small, 1)
                if wait:
                    dve.wait_ge(s_small, small[0])

            def mark(name, add=0):
                assert SMALL[name] == small[0] + add, (name, SMALL[name], small[0] + add)

            def low_splits(stage, ns):
                for n in ns:
                    low_split(dve, nc.vector.tensor_tensor, stage, n)

            def residual(stage, alpha, h, t):
                tile_wait(dve, stage, 4 * h, h, t)
                nc.vector.scalar_tensor_tensor(out=X[:, t, h * 512:(h + 1) * 512], in0=X[:, t, h * 512:(h + 1) * 512], scalar=alpha,
                                               in1=BANKS[1 - h][t][:, :], op0=ALU.mult, op1=ALU.add).then_inc(dve_out, 1)

            def out_norm(stage):
                low_splits(stage, range(8))
                for t in range(TT):
                    residual(stage, ALPHA, 0, t)
                layer_norm(stage, LN_EPS, residual_of=lambda t: residual(stage, ALPHA, 1, t))

            def ada_steps_of(part, j, ks):
                for k in ks:
                    if k % 2 == 0:
                        dve.wait_ge(ada_in[(k // 2) % 2], j * 32 + 16 * (8 * part + k // 4 + 1))
                    w = ADW((k // 2) % 2)[:, (k % 2) * 512:(k % 2 + 1) * 512]
                    ctx_part = isinstance(j, int) and j == 3
                    c = csil[:, 1, 1 if ctx_part else 0, k:k + 1]
                    if k == 0:
                        nc.vector.tensor_scalar(ogf, w, c, None, ALU.mult).then_inc(ada_steps, 1)
                    else:
                        dve.wait_ge(ada_steps, j * 8 + (32 * part + k))
                        nc.vector.scalar_tensor_tensor(out=ogf, in0=w, scalar=c, in1=ogf, op0=ALU.mult, op1=ALU.add).then_inc(ada_steps, 1)

            def ada_move(part, j, less=0):
                dve.wait_ge(ada_cols, j + (4 * part + 1 - less))
                at = 48 + 4 * part if isinstance(j, int) and j - less == 3 else j * 4 + (12 * part - 4 * less)
                dst, bias = ((x[:, bass.ds(at + o, 4)] if not isinstance(at, int) else x[:, at + o:at + o + 4]) for x, o in ((modc, 0), (cols2, 16)))
                nc.vector.tensor_tensor(out=dst, in0=OB[0][:, 0:4], in1=bias, op=ALU.add).then_inc(ada_moved, 1)

            def xt_low(stage, done):
                for n in range(8):
                    dve.wait_ge(xt_hi, done + n + 1)
                    t, h = n // 2, n % 2
                    x = [y[:, 4 * h:4 * h + 4, t * P:(t + 1) * P] for y in (XTl, XTh)]
                    nc.vector.tensor_tensor(out=x[0], in0=TR[h][:, :].rearrange("p (b c) -> p b c", b=4), in1=x[1],
                                            op=ALU.subtract).then_inc(tr_out, 1)

            def down_wait(stage, t):
                if t < TT - 1:
                    dve.wait_ge(tile_done, TILE0[stage] + t + 1)
                else:
                    dve.wait_ge(quarters, st(stage, "quarters") + n_quarters(stage))

            def scale_columns():
                dve.wait_ge(ada_moved, 16)
                for n, c in enumerate((8, 32, 56)):
                    V2.do(f"mod{n + 1}", nc.vector.tensor_scalar(modc[:, c:c + 8], modc[:, c:c + 8], 1.0, None, ALU.add))

            def mlp(stage, alpha, ada):
                n, u = 0, 0
                q, h = st(stage, "quarters"), st(stage, "hidden")

                def four(part, i):
                    if not (isinstance(i, int) and i == 0):
                        ada_move(part, i, 1)
                    for m in range(4):
                        low_split(dve, nc.vector.tensor_tensor, stage, n + m + 3, i)
                        r = act_buf[m % 2]
                        dve.wait_ge(hid_hi, i * 4 + (h + u + m + 1))
                        nc.vector.tensor_tensor(out=r, in0=r, in1=r, op=ALU.mult).then_inc(hid_steps, 1)
                        dve.wait_ge(hid_steps, i * 4 + (h + u + m + 1))
                        at = bass.ds(i * 4 + m, 1) if not isinstance(i, int) else slice(4 * i + m, 4 * i + m + 1)
                        nc.vector.tensor_tensor(out=Hl[:, at, :], in0=r.unsqueeze(1), in1=Hh[:, at, :],
                                                op=ALU.subtract).then_inc(hidden, 1)
                        ada_steps_of(part, i, ((0, 1, 2), (3, 4, 5), (6, 7), ())[m])

                for n_ in range(3):
                    low_split(dve, nc.vector.tensor_tensor, stage, n_)
                for part, (up, down) in enumerate(PARTS[stage]):
                    four(ada + part, 0)
                    with dve.Fori(1, 3) as i:
                        four(ada + part, i)
                    four(ada + part, 3)
                    n, u = n + up, u + up
                    ada_move(ada + part, 3)
                    for j in range(down):
                        if n + j + 3 < n_quarters(stage):
                            low_split(dve, nc.vector.tensor_tensor, stage, n + j + 3)
                    n += down
                    def add(half, t, scale):
                        nc.vector.scalar_tensor_tensor(out=X[:, t, half * 512:(half + 1) * 512], in0=X[:, t, half * 512:(half + 1) * 512],
                                                       scalar=scale, in1=BANKS[half][t][:, :],
                                                       op0=ALU.mult, op1=ALU.add).then_inc(dve_out, 1)

                    if part == 0:
                        for half in range(2):
                            dve.wait_ge(quarters, q + n - 1 + half)
                            for t in range(TT):
                                add(half, t, alpha)

                def last_tile(t):
                    down_wait(stage, t)
                    dve.wait_ge(dve_out, st(stage, "dve") + 8)
                    for half in range(2):
                        add(half, t, 1.0)

                if stage == "mlp1":
                    scale_columns()
                layer_norm(stage, LN_EPS, residual_of=last_tile, eps_then=EPS_2)

            norms = [0]

            def layer_norm(stage, eps, src=X, residual_of=None, eps_then=None):
                def own(op, t):
                    dve.wait_ge(ln_dve, LN_PLACE[stage, op, t])

                for op, t in LN_ORDER[stage]:
                    mark = op[2:]
                    r = rstd[:, :, t:t + 1]
                    op = op[:2]
                    if op in ("s0", "s1"):
                        h = int(op[1])
                        if h == 0 and not mark and residual_of is not None:
                            residual_of(t)
                            dve.wait_ge(dve_out, st.total_until(stage, "dve", (TT - 1 - t) * (1 if stage[:3] == "out" else 2)))
                        if h == 0 and mark:
                            own("bi", t)
                        ins = nc.vector.bn_stats(stat[:, t, h, :], src[:, t, h * 512:(h + 1) * 512])
                    elif op == "ag":
                        own("s1" + mark, t)
                        ins = nc.vector.bn_aggr(agg[:, t, :], stat[:, t, :, :])
                    elif op == "ve":
                        own("ag" + mark, t)
                        ins = nc.vector.tensor_scalar(r[:, 0, :], agg[:, t, 1:2], eps if not mark else eps_then, None, ALU.add)
                    elif op == "rc":
                        own("ve" + mark, t)
                        ins = nc.vector.reciprocal(r[:, 1, :], r[:, 0, :])
                    elif op == "nm":
                        dve.wait_ge(ln_std, scalar_place(stage, "root", t, mark))
                        ins = nc.vector.scalar_tensor_tensor(out=r[:, 3, :], in0=agg[:, t, 0:1], scalar=-1.0, in1=r[:, 2, :],
                                                             op0=ALU.mult, op1=ALU.mult)
                    elif op == "ga":
                        if t == 0:
                            norms[0] += 1
                            dve.wait_ge(gb_in, 32 * norms[0])
                        own("ag", t)
                        ins = nc.vector.scalar_tensor_tensor(out=X[:, t, :], in0=X[:, t, :], scalar=agg[:, t, 0:1], in1=rows[:, 0, :],
                                                             op0=ALU.subtract, op1=ALU.mult)
                    else:
                        own("ga", t)
                        dve.wait_ge(ln_std, scalar_place(stage, "root", t, ""))
                        ins = nc.vector.scalar_tensor_tensor(out=X[:, t, :], in0=X[:, t, :], scalar=r[:, 2, :], in1=rows[:, 1, :],
                                                             op0=ALU.mult, op1=ALU.add)
                    ins.then_inc(ln_dve, 1)

            xt_low("x0", 0)
            low_splits("proj0", range(3))
            dve.wait_ge(s_const, CONSTS)
            dve.wait_ge(s_small_in, SMALL_INPUTS)
            step(nc.vector.tensor_tensor(out=lamrow[:, :, 0, :], in0=lamrow[:, :, 0, :], in1=lamrow[:, :, 1, :], op=ALU.mult))
            step(nc.vector.tensor_reduce(lam[:, 0:2], lamrow[:, :, 0, :], AX.X, ALU.add))
            mark("lam")
            step(nc.vector.tensor_scalar(subln[:, :], subln[:, :], 1.0 - LAM_INIT, None, ALU.mult))

            n = 3
            for r, (g, *dst) in enumerate(ROPED0):
                which, idx = dst
                low_splits("proj0", range(n, min(24, g + 5)))
                n = max(n, g + 5)
                o = (QT if which == "q" else KTT)[:, idx, :]
                dve.wait_ge(rope_swapped, r + 1)
                if r >= 2:
                    dve.wait_ge(rope_dve, 2 * (r - 2) + 2)
                nc.vector.tensor_tensor(out=wide[:, 28 + r % 2, :], in0=TR[r % 2][:, :], in1=tab("sin"), op=ALU.mult).then_inc(rope_dve, 1)
                dve.wait_ge(rope_cos, r + 1)
                dve.wait_ge(rope_dve, 2 * r + 1)
                nc.vector.tensor_tensor(out=o, in0=wide[:, 26 + r % 2, :], in1=wide[:, 28 + r % 2, :], op=ALU.add).then_inc(rope_dve, 1)
            low_splits("proj0", range(n, 24))
            dve.wait_ge(rope_dve, 2 * len(ROPED0))
            dve.wait_ge(s_smalla, 2)
            step(nc.vector.tensor_tensor(out=lam[:, 4:5], in0=lam[:, 3:4], in1=lam[:, 2:3], op=ALU.subtract))
            step(nc.vector.tensor_scalar(lam[:, 5:6], lam[:, 4:5], -LAM_INIT, None, ALU.add))
            step(nc.vector.tensor_scalar(gate[:, :, :], gate[:, :, :], 1.0, None, ALU.add))
            step(nc.vector.reciprocal(gate[:, :, :], gate[:, :, :]))
            mark("windows")
            dve.wait_ge(cmp_in, 128)
            for j in range(2):
                for g in range(2):
                    src = XT[:, 2 * j + g, :]
                    for m in range(16):
                        ins = nc.vector.tensor_scalar(WIN(j)[:, m, g * N_CMP:(g + 1) * N_CMP], src[:, 2 * m:2 * m + 16 * 30 + 1:16],
                                                      cols[:, 5 + 16 * j + m:6 + 16 * j + m], None, ALU.add)
                step(ins, wait=False)
            dve.wait_ge(act_out, 28)
            x_ = hc[:, :, :].rearrange("p a b -> p (a b)")
            a_, b_ = SC[:, 1, 0, 0:248], SC[:, 1, 1, 0:248]
            step(nc.vector.tensor_tensor(out=a_, in0=x_, in1=x_, op=ALU.mult))
            step(nc.vector.tensor_scalar(a_, a_, 0.044715, 1.0, ALU.mult, ALU.add))
            step(nc.vector.tensor_tensor(out=b_, in0=a_, in1=x_, op=ALU.mult))
            mark("gelu_in")
            dve.wait_ge(s_smalla, 3)
            step(nc.vector.tensor_scalar(a_, SC[:, 1, 2, 0:248], 1.0, 0.5, ALU.add, ALU.mult))
            step(nc.vector.tensor_tensor(out=hc2[:, :, :].rearrange("p a b -> p (a b)"), in0=a_, in1=x_, op=ALU.mult))
            mark("gelu")
            dve.wait_ge(s_smallp, 2)
            step(nc.vector.tensor_copy(vcc[:, :, :], TR[1][0:N_CMP, 0:P].rearrange("p (g d) -> p g d", g=2)))
            step(nc.vector.tensor_copy(kcc[:, 0, :], TR[0][:, 0:62]))
            mark("kraw")
            step(nc.vector.tensor_tensor(out=SC[:, 1, 0, 0:62], in0=kcc[:, 0, :], in1=tab("cmp_cos"), op=ALU.mult))
            dve.wait_ge(s_smallp, 3)
            step(nc.vector.tensor_tensor(out=SC[:, 1, 1, 0:62], in0=TR[0][:, 0:62], in1=tab("cmp_sin"), op=ALU.mult))
            step(nc.vector.tensor_tensor(out=kcc[:, 1, :], in0=SC[:, 1, 0, 0:62], in1=SC[:, 1, 1, 0:62], op=ALU.add))
            mark("krope")
            okt = tab("cmp_ok").rearrange("p (t n) -> p t n", t=TT)
            mkt = tab("cmp_mask").rearrange("p (t n) -> p t n", t=TT)
            for b in range(2):
                dve.wait_ge(s_smallp, 4 + b)
                for h in range(4):
                    ins = nc.vector.tensor_tensor(out=PC[:, 2 * h + b, :, :], in0=G[b][:, h * P:(h + 1) * P].rearrange("p (t n) -> p t n", t=TT)[:, :, 0:N_CMP],
                                                  in1=mkt, op=ALU.add)
                    step(ins, wait=False)
            dve.wait_ge(s_small, small[0])
            step(nc.vector.tensor_reduce(pcm[:, 0, :], PC[:, :, :, :].rearrange("p h t n -> p (h t) n"), AX.X, ALU.min))
            pcv = PC[:, :, :, :].rearrange("p h t n -> p (h t) n")
            step(nc.vector.tensor_tensor(out=pcv, in0=pcv, in1=pcm[:, 0, :].unsqueeze(2).to_broadcast([P, 32, N_CMP]), op=ALU.subtract))
            mark("scmp")
            dve.wait_ge(s_smalla, 4)
            step(nc.vector.tensor_reduce(pcm[:, 1, :], pcv, AX.X, ALU.add))
            step(nc.vector.reciprocal(pcm[:, 0, :], pcm[:, 1, :]))
            step(nc.vector.tensor_tensor(out=pcm[:, 1, :].rearrange("p (h t) -> p h t", h=8), in0=pcm[:, 0, :].rearrange("p (h t) -> p h t", h=8),
                                         in1=gate[:, :, 0:24:3].rearrange("p t h -> p h t"), op=ALU.mult))
            step(nc.vector.tensor_tensor(out=pcv, in0=pcv, in1=pcm[:, 1, :].unsqueeze(2).to_broadcast([P, 32, N_CMP]), op=ALU.mult))
            for h in range(8):
                step(nc.vector.tensor_tensor(out=PC[:, h, :, :], in0=PC[:, h, :, :], in1=okt, op=ALU.mult), wait=False)
            mark("pcmp")
            for h in range(8):
                dve.wait_ge(s_smallp, 7 + 2 * h)
                step(nc.vector.tensor_copy(O[:, :, 512 + h * HD:512 + (h + 1) * HD], OB[h % 2][:, 0:256].rearrange("p (t d) -> p t d", t=TT)), wait=False)
            dve.wait_ge(s_small, small[0])

            def fin_diff(i, j, at):
                o = O[:, :, bass.ds(i * P + (j // 2) * P, P)] if not isinstance(i, int) else O[:, :, i * P:(i + 1) * P]
                ps = OB[j % 2][:, :].rearrange("p (t d) -> p t d", t=TT)
                if j == 0:
                    nc.vector.tensor_tensor(out=o, in0=ps, in1=rs[:, 0, :].unsqueeze(2).to_broadcast([P, TT, P]), op=ALU.mult).then_inc(o_used, 1)
                else:
                    nc.vector.tensor_scalar(rs[:, 1, :], rs[:, 1, :], lam[:, 5:6], None, ALU.mult).then_inc(o_steps, 1)
                    dve.wait_ge(o_steps, at + 1)
                    nc.vector.tensor_tensor(out=og[:, :, :], in0=ps, in1=rs[:, 1, :].unsqueeze(2).to_broadcast([P, TT, P]), op=ALU.mult).then_inc(o_steps, 1)
                    dve.wait_ge(o_steps, at + 2)
                    nc.vector.tensor_tensor(out=o, in0=o, in1=og[:, :, :], op=ALU.add).then_inc(o_used, 1)

            def fin_nsa(r, j, at):
                g, par, kind = j // 4, (j // 2) % 2, j % 2
                if isinstance(r, int):
                    c = 512 + (4 * g + 2 * r + par) * HD
                    o = O[:, :, c:c + HD]
                    c = 3 * (4 * g + 2 * r + par) + 1 + kind
                    gt = gate[:, :, c:c + 1]
                else:
                    o = O[:, :, bass.ds(r * (2 * HD) + (512 + (4 * g + par) * HD), HD)]
                    gt = gate[:, :, bass.ds(r * 6 + (3 * (4 * g + par) + 1 + kind), 1)]
                ps = OB[kind][:, :].rearrange("p (t d) -> p t d", t=TT)[:, :, g * HD:(g + 1) * HD]
                nc.vector.tensor_tensor(out=rs[:, kind, :].unsqueeze(2), in0=rs[:, kind, :].unsqueeze(2), in1=gt, op=ALU.mult).then_inc(o_steps, 1)
                dve.wait_ge(o_steps, at + 1)
                nc.vector.tensor_tensor(out=og[:, :, 0:HD], in0=ps, in1=rs[:, kind, :].unsqueeze(2).to_broadcast([P, TT, HD]), op=ALU.mult).then_inc(o_steps, 1)
                dve.wait_ge(o_steps, at + 2)
                nc.vector.tensor_tensor(out=o, in0=o, in1=og[:, :, 0:HD], op=ALU.add).then_inc(o_used, 1)

            def fin_fox(i, j, at):
                o = O[:, :, bass.ds(i * P + j * HD, HD)] if not isinstance(i, int) else O[:, :, i * P + j * HD:i * P + (j + 1) * HD]
                ps = OB[j % 2][:, :].rearrange("p (t d) -> p t d", t=TT)[:, :, (j % 2) * HD:(j % 2 + 1) * HD]
                nc.vector.tensor_tensor(out=o, in0=ps, in1=rs[:, j % 2, :].unsqueeze(2).to_broadcast([P, TT, HD]), op=ALU.mult).then_inc(o_used, 1)

            dve_attend(dve, "diff", 4, 2, P, fin_diff)
            dve_attend(dve, "nsa", 2, 8, HD, fin_nsa)
            dve.wait_ge(o_used, 24)
            sq = SC[:, 0, :, :]
            step(nc.vector.tensor_tensor(out=sq, in0=O[:, :, 0:512], in1=O[:, :, 0:512], op=ALU.mult))
            step(nc.vector.tensor_reduce(rmsq[:, 0, :], sq.rearrange("p t (h d) -> p (t h) d", h=4), AX.X, ALU.add))
            step(nc.vector.tensor_scalar(rmsq[:, 1, :], rmsq[:, 0, :], 1.0 / P, LN_EPS, ALU.mult, ALU.add))
            step(nc.vector.reciprocal(rmsq[:, 0, :], rmsq[:, 1, :]))
            mark("rms")
            dve.wait_ge(s_smalla, 13)
            for t in range(TT):
                o = O[:, t, 0:512].rearrange("p (h d) -> p h d", h=4)
                step(nc.vector.tensor_tensor(out=o, in0=o, in1=rmsq[:, 1, 4 * t:4 * t + 4].unsqueeze(2).to_broadcast([P, 4, P]), op=ALU.mult))
                step(nc.vector.tensor_tensor(out=o, in0=o, in1=subln[:, :].unsqueeze(1).to_broadcast([P, 4, P]), op=ALU.mult), wait=False)
            mark("mixed0")
            cc = csil[:, 0, :, :].rearrange("p a k -> p (a k)")
            cs_ = csil[:, 1, :, :].rearrange("p a k -> p (a k)")
            dve.wait_ge(s_smalla, SMALLA["silu"])
            step(nc.vector.tensor_scalar(cc, cc, 1.0, None, ALU.add))
            step(nc.vector.reciprocal(cc, cc))
            step(nc.vector.tensor_tensor(out=cs_, in0=cc, in1=cols2[:, 0:16], op=ALU.mult))
            step(nc.vector.memset(ones[:, :], 1.0))
            xt_low("mixed0", 8)
            out_norm("out0")
            xt_low("x1", 16)
            mlp("mlp0", ALPHA, ada=0)
            xt_low("x2", 24)
            low_splits("proj1", range(4))
            dve.wait_ge(act_out, st("proj1", "act") + 1)
            step(nc.vector.tensor_scalar(crow[:, 2, :], crow[:, 0, :], -1.0, None, ALU.mult))
            step(nc.vector.tensor_tensor(out=crow[:, 1, :], in0=crow[:, 0, :], in1=crow[:, 2, :], op=ALU.max))
            mark("fabs")
            low_splits("proj1", range(4, 9))
            dve.wait_ge(s_smalla, SMALLA["fexp"])
            step(nc.vector.tensor_scalar(crow[:, 0, :], crow[:, 0, :], 0.0, None, ALU.min))
            dve.wait_ge(s_smalla, SMALLA["fexp"] + 1)
            step(nc.vector.tensor_tensor(out=crow[:, 0, :], in0=crow[:, 0, :], in1=crow[:, 1, :], op=ALU.subtract))
            step(nc.vector.tensor_tensor_scan(out=crow[:, 1, :], data0=crow[:, 0, :], data1=crow[:, 0, :], initial=0.0,
                                              op0=ALU.add, op1=ALU.bypass))
            step(nc.vector.tensor_scalar(crow[:, 2, :], crow[:, 1, :], -1.0, None, ALU.mult))
            mark("fox")
            low_splits("proj1", range(9, 28))
            dve_attend(dve, "fox", 8, 2, HD, fin_fox)
            xt_low("mixed1", 32)
            out_norm("out1")
            xt_low("x3", 40)
            mlp("mlp1", ALPHA, ada=2)
            vector_second(dve, down_wait, layer_norm)


def slab_layout(w, width=512):
    K, n = w.shape
    w = np.pad(w, ((0, 0), (0, -n % width)))
    out = []
    for c in range(0, w.shape[1], width):
        for r in range(0, K, 1024):
            out.append(w[r:r + 1024, c:c + width].reshape(8, P, width).transpose(1, 0, 2).reshape(P, 4096))
    return out


def up_chunks(w):
    n = w.shape[1] // 256
    return list(w.reshape(KT, P, n, 2, P).transpose(2, 1, 3, 0, 4).reshape(n, P, 2048))


def token_chunks(w):
    out = []
    for c in range(0, w.shape[1], 512):
        x = np.pad(w[:, c:c + 512], ((0, 0), (0, max(0, c + 512 - w.shape[1]))))
        out += list(x.reshape(2, 2, 2, P, 512).transpose(0, 3, 1, 2, 4).reshape(2, P, 2048))
    return out


def down_chunks(w, parts):
    out = []
    for first, last in parts:
        for r in range(first, last, 2):
            c = w[r * P:(r + 2) * P].reshape(2, P, 2, 512).transpose(1, 2, 0, 3)
            if r < last - 2:
                c = c[:, ::-1]
            out.append(c.reshape(P, 2048))
    return out


def kernel(**inputs):
    import concourse.bacc as bacc
    from concourse.bass_utils import run_bass_kernel_spmd

    a = {k: np.asarray(v) for k, v in inputs.items()}
    table, where, dft_len, dft_ch, heads = shape_constants()
    we, wo = a["w_in_even"][0], a["w_in_odd"][0]
    kv = np.concatenate([we[:, 2048:2176], we[:, 2176:2304], we[:, 2304:2432], we[:, 2560:2688]], axis=1)
    vg = np.concatenate([we[:, 2432:2560], we[:, 2688:2816], we[:, 2816:2840]], axis=1)
    w1 = a["nsa_cmp_w1"][0]
    slabs = [w1[j].reshape(16, P, 256).transpose(1, 0, 2).reshape(P, 4096) for j in range(2)]
    mlps = []
    for i in range(2):
        up, down = up_chunks(a["mlp_w_up"][i]), down_chunks(a["mlp_w_down"][i], ((0, 16), (16, 32)))
        mlps.append(up[0:8] + down[0:8] + up[8:] + down[8:])
    chunks = (up_chunks(we[:, 512:1024]) + up_chunks(we[:, 0:512]) + up_chunks(we[:, 1536:2048]) + token_chunks(we[:, 1024:1536])
              + up_chunks(kv) + token_chunks(vg) + token_chunks(a["w_out_even"][0]) + mlps[0]
              + up_chunks(np.pad(wo[:, 3072:], ((0, 0), (0, 512 - 16)))) + up_chunks(wo[:, 1024:2048]) + up_chunks(wo[:, 0:1024])
              + token_chunks(wo[:, 2048:3072]) + token_chunks(a["w_out_odd"][0]) + mlps[1])
    cols = np.zeros((P, 37), np.float32)
    cols[:, 0:4] = a["nsa_cmp_b1"][0].reshape(4, P).T
    cols[0:16, 4] = a["fox_f_bias"][0]
    cols[:, 5:37] = a["nsa_pe"][0].reshape(2 * 16, P).T

    wi = a["w_in_2"][0]
    up = up_chunks(a["ffn_w_up_2"][0].reshape(D, 2, 22, P).transpose(0, 2, 1, 3).reshape(D, 2 * D_FF_2))
    down = down_chunks(a["ffn_w_down_2"][0], ((0, 12), (12, 22)))
    chunks += up[0:12] + down[0:6] + up[12:] + down[6:]
    slabs += (slab_layout(wi[:, OFF_DT:OFF_DT + 16]) + slab_layout(wi[:, OFF_XS:OFF_BC]) + slab_layout(wi[:, OFF_BC:OFF_DT])
              + slab_layout(wi[:, OFF_FP:]) + slab_layout(wi[:, 0:512])
              + [dft_len.reshape(8, P, S).transpose(1, 0, 2).reshape(P, 4096)]
              + slab_layout(a["w_out_2"][0]))
    bada = a["b_ada_2"][0].reshape(48, P).T
    cols2 = np.zeros((P, 122 + 480), np.float32)
    cols2[:, 0:8] = a["c_2"].reshape(KT, P).T
    cols2[:, 8:16] = a["c_ctx_2"].reshape(KT, P).T
    cols2[:, 16:64] = bada
    cols2[:, 64:80] = bada[:, 0:16]
    cols2[0:16, 80] = a["ssd_dt_bias_2"].reshape(16)
    cols2[0:16, 81] = a["ssd_a_log_2"].reshape(16)
    cols2[0:8, 82] = 1
    cols2[8:16, 83] = 1
    cols2[:, 84:108] = a["ssd_conv_w_2"][0].reshape(3, 8, P).transpose(2, 1, 0).reshape(P, 24)
    cols2[:, 108:116] = a["ssd_conv_b_2"].reshape(8, P).T
    cols2[:, 116:120] = a["ssd_norm_w_2"].reshape(4, P).T
    cols2[:, 120:122] = a["pool_scale_2"].reshape(2, P).T
    ffn = np.concatenate([a["ffn_conv_w_2"][0].reshape(9, 2 * D_FF_2), a["ffn_conv_b_2"]])
    ffn = ffn.reshape(10, 2, 11, 2, P).transpose(4, 2, 3, 1, 0)
    cols2[:, 122:562] = ffn.reshape(P, 440)
    ada = np.stack(slab_layout(a["w_ada_2"][0]))

    nc = bacc.Bacc("TRN2", target_bir_lowering=False, num_devices=1)
    arrays = {"slabs": np.stack(slabs), "chunks": np.stack(chunks), "cols": cols, "table": table, "ones": np.ones((2, S), np.float32),
              "cols2": cols2, "ada": ada, "dft_ch": np.concatenate([dft_ch, dft_ch], axis=2).transpose(1, 0, 2).copy()}
    for n in ("x", "ln_gain", "ln_bias", "diff_lambda", "diff_subln", "nsa_cmp_w2", "ctx_2", "fnet_w_2", "pool_w_2",
              "ssd_d_2", "ln1_g_2", "ln1_b_2", "ln2_g_2", "ln2_b_2"):
        arrays[n] = a[n]
    A = {n: nc.dram_tensor(n, v.shape, F32, kind="ExternalInput").ap() for n, v in arrays.items()}
    A["where"] = where
    A["crow"] = nc.dram_tensor("forget_rows", (16, 2, S), F32, kind="Internal").ap()
    out = nc.dram_tensor("out", (1, S, D), F32, kind="ExternalOutput").ap()
    build(nc, A, out)
    r = run_bass_kernel_spmd(nc, [arrays], core_ids=[0])
    return r.results[0]["out"]
```
